# Optimizing a Trainium2 kernel written in Bass

```python
import math
import jax, jax.numpy as jnp
from jax import lax
import numpy as np

D_MODEL = 1024
BATCH = 1
SEQ = 256
DEPTH = 2

N_MOD = 6
EPS = 1e-6
SSM_EXPAND = 2
SSM_D_INNER = SSM_EXPAND * D_MODEL
SSM_HEAD_DIM = 64
SSM_HEADS = SSM_D_INNER // SSM_HEAD_DIM
SSM_GROUPS = 4
SSM_STATE = 128
SSM_CONV = 4
SSM_CHUNK = 128
SSM_CONV_DIM = SSM_D_INNER + 2 * SSM_GROUPS * SSM_STATE
ATT_HEAD_DIM = 64
ATT_KV_HEADS = D_MODEL // ATT_HEAD_DIM
ATT_PATTERNS = ((128, 1), (512, 4), (2048, 16))
ATT_GROUPS = len(ATT_PATTERNS)
ATT_Q_HEADS = ATT_GROUPS * ATT_KV_HEADS
ATT_WIDTH = ATT_KV_HEADS * ATT_HEAD_DIM
REL_BUCKETS = 32
REL_MAX_DIST = 2048
HY_SIZES = (SSM_D_INNER, SSM_CONV_DIM, SSM_HEADS, ATT_Q_HEADS * ATT_HEAD_DIM, ATT_WIDTH, ATT_WIDTH)
HY_SPLITS = tuple(int(v) for v in np.cumsum(HY_SIZES)[:-1])
HY_IN_DIM = sum(HY_SIZES)
HY_OUT_DIM = SSM_D_INNER + ATT_WIDTH
CONV_WIDTH = 31
FFN_HIDDEN = -(-8 * D_MODEL // (3 * 256)) * 256
N_EVEN = (DEPTH + 1) // 2
N_ODD = DEPTH // 2


def rms_norm(x, g):
    xf = x.astype(jnp.float32)
    y = xf * lax.rsqrt(jnp.mean(xf * xf, -1, keepdims=True) + EPS)
    return (y * g.astype(jnp.float32)).astype(x.dtype)

def layer_norm(x, g, b):
    xf = x.astype(jnp.float32)
    mu = jnp.mean(xf, -1, keepdims=True)
    var = jnp.mean(jnp.square(xf - mu), -1, keepdims=True)
    y = (xf - mu) * lax.rsqrt(var + EPS)
    return (y * g.astype(jnp.float32) + b.astype(jnp.float32)).astype(x.dtype)

def causal_depthwise_conv(x, w, b):
    k = w.shape[0]
    out = lax.conv_general_dilated(
        x, w[:, None, :].astype(x.dtype), window_strides=(1,), padding=[(k - 1, 0)],
        dimension_numbers=('NWC', 'WIO', 'NWC'), feature_group_count=x.shape[-1])
    return out + b

def t5_bucket(dist):
    max_exact = REL_BUCKETS // 2
    n = jnp.maximum(dist, 1).astype(jnp.float32)
    large = max_exact + jnp.log(n / max_exact) / math.log(REL_MAX_DIST / max_exact) * (REL_BUCKETS - max_exact)
    large = jnp.minimum(large.astype(jnp.int32), REL_BUCKETS - 1)
    return jnp.where(dist < max_exact, dist, large)

def ssd_chunked(x, dt, A, Bm, Cm):
    f32 = jnp.float32
    b_, s, h, p = x.shape
    g, n = Bm.shape[2], Bm.shape[3]
    r, q = h // g, SSM_CHUNK
    nc = s // q
    x = x.astype(f32).reshape(b_, nc, q, g, r, p)
    dt = dt.astype(f32).reshape(b_, nc, q, g, r)
    Bm = Bm.astype(f32).reshape(b_, nc, q, g, n)
    Cm = Cm.astype(f32).reshape(b_, nc, q, g, n)
    a_cs = jnp.cumsum(dt * A.astype(f32).reshape(g, r), axis=2)
    xdt = x * dt[..., None]
    seg = a_cs[:, :, :, None] - a_cs[:, :, None, :]
    causal = jnp.tril(jnp.ones((q, q), bool))[:, :, None, None]
    decay = jnp.exp(jnp.where(causal, seg, -jnp.inf))
    cb = jnp.einsum('bclgn,bcsgn->bclsg', Cm, Bm)
    y_diag = jnp.einsum('bclsgr,bcsgrp->bclgrp', cb[..., None] * decay, xdt)
    decay_end = jnp.exp(a_cs[:, :, -1:] - a_cs)
    states = jnp.einsum('bcsgn,bcsgrp->bcgrpn', Bm, xdt * decay_end[..., None])
    chunk_decay = jnp.exp(a_cs[:, :, -1])

    def step(hs, inp):
        st, dec = inp
        return dec[..., None, None] * hs + st, hs

    h0 = jnp.zeros((b_, g, r, p, n), f32)
    _, prev = lax.scan(step, h0, (jnp.moveaxis(states, 1, 0), jnp.moveaxis(chunk_decay, 1, 0)))
    prev = jnp.moveaxis(prev, 0, 1)
    y_off = jnp.einsum('bclgn,bcgrpn->bclgrp', Cm, prev) * jnp.exp(a_cs)[..., None]
    return (y_diag + y_off).reshape(b_, s, h, p)

def dilated_branch(q, k, v, bias_tab, window, dil):
    b_, s, h, dh = q.shape
    blk = window // dil
    L = s // dil
    nb = -(-L // blk)
    lp = nb * blk

    def blocks(t):
        t = t.reshape(b_, L, dil, h, dh)
        t = jnp.pad(t, ((0, 0), (0, lp - L), (0, 0), (0, 0), (0, 0)))
        return t.reshape(b_, nb, blk, dil, h, dh)

    def band_keys(t):
        prev = jnp.pad(t, ((0, 0), (1, 0), (0, 0), (0, 0), (0, 0), (0, 0)))[:, :-1]
        return jnp.concatenate([prev, t], axis=2)

    qb = blocks(q)
    kw, vw = band_keys(blocks(k)), band_keys(blocks(v))
    i = jnp.arange(blk)[:, None]
    j = jnp.arange(2 * blk)[None, :]
    delta = blk + i - j
    band = (delta >= 0) & (delta <= blk)
    kpos = jnp.arange(nb)[:, None] * blk + jnp.arange(2 * blk)[None, :] - blk
    mask = band[None] & (kpos >= 0)[:, None, :]
    bias = jnp.transpose(bias_tab[t5_bucket(jnp.maximum(delta, 0) * dil)], (2, 0, 1)).astype(jnp.float32)
    sc = jnp.einsum('bnirhd,bnjrhd->bnrhij', qb, kw).astype(jnp.float32) * (dh ** -0.5) + bias
    sc = jnp.where(mask[None, :, None, None], sc, -jnp.inf)
    m = jnp.max(sc, -1, keepdims=True)
    pr = jnp.exp(sc - m)
    l = jnp.sum(pr, -1, keepdims=True)
    o = jnp.einsum('bnrhij,bnjrhd->bnirhd', (pr / l).astype(v.dtype), vw)
    lse = jnp.transpose((m + jnp.log(l))[..., 0], (0, 1, 4, 2, 3))
    lse = lse.reshape(b_, lp, dil, h)[:, :L].reshape(b_, s, h)
    o = o.reshape(b_, lp, dil, h, dh)[:, :L].reshape(b_, s, h, dh)
    return o, lse

def dilated_attention(q, k, v, rel_table):
    b_, s, _, h, dh = q.shape
    outs, lses = [], []
    for gi, (w, d) in enumerate(ATT_PATTERNS):
        o, lse = dilated_branch(q[:, :, gi], k, v, rel_table[:, gi * h:(gi + 1) * h], w, d)
        outs.append(o)
        lses.append(lse)
    wgt = jax.nn.softmax(jnp.stack(lses, 0), axis=0)
    o = jnp.einsum('gbsh,gbshd->bshd', wgt.astype(outs[0].dtype), jnp.stack(outs, 0))
    return o.reshape(b_, s, h * dh)

def hybrid_mixer(h, w_in, conv_w, conv_b, dt_bias, a_log, d_skip, ssm_norm_g, w_out, rel_table):
    b_, s, _ = h.shape
    z, xbc, dt_raw, q, k, v = jnp.split(h @ w_in, HY_SPLITS, axis=-1)
    xbc = jax.nn.silu(causal_depthwise_conv(xbc, conv_w, conv_b))
    xs, bm, cm = jnp.split(xbc, (SSM_D_INNER, SSM_D_INNER + SSM_GROUPS * SSM_STATE), axis=-1)
    xs = xs.reshape(b_, s, SSM_HEADS, SSM_HEAD_DIM)
    dt = jax.nn.softplus((dt_raw + dt_bias).astype(jnp.float32))
    A = -jnp.exp(a_log.astype(jnp.float32))
    y = ssd_chunked(xs, dt, A, bm.reshape(b_, s, SSM_GROUPS, SSM_STATE), cm.reshape(b_, s, SSM_GROUPS, SSM_STATE))
    y = y + d_skip.astype(jnp.float32)[:, None] * xs.astype(jnp.float32)
    y = y.reshape(b_, s, SSM_D_INNER).astype(h.dtype)
    y = rms_norm(y * jax.nn.silu(z), ssm_norm_g)
    att = dilated_attention(q.reshape(b_, s, ATT_GROUPS, ATT_KV_HEADS, ATT_HEAD_DIM),
                            k.reshape(b_, s, ATT_KV_HEADS, ATT_HEAD_DIM),
                            v.reshape(b_, s, ATT_KV_HEADS, ATT_HEAD_DIM), rel_table)
    return jnp.concatenate([y, att.astype(y.dtype)], axis=-1) @ w_out

def conformer_conv(h, w1, b1, w_dw, b_dw, ln_g, ln_b, w2, b2):
    a, gt = jnp.split(h @ w1 + b1, 2, axis=-1)
    u = a * jax.nn.sigmoid(gt)
    u = causal_depthwise_conv(u, w_dw, b_dw)
    u = jax.nn.silu(layer_norm(u, ln_g, ln_b))
    return u @ w2 + b2

def swiglu(h, wg, wu, wd):
    return (jax.nn.silu(h @ wg) * (h @ wu)) @ wd

def first_inputs(seed: int = 0) -> dict:
    key = jax.random.key(seed)
    ks = iter(jax.random.split(key, 40))
    f32 = jnp.float32

    def nrm(shape, scale=1.0):
        return jax.random.normal(next(ks), shape, f32) * scale

    D = D_MODEL
    dt0 = jnp.exp(jax.random.uniform(next(ks), (N_EVEN, SSM_HEADS), f32, math.log(1e-3), math.log(1e-1)))
    return {
        "x": nrm((BATCH, SEQ, D)),
        "c": nrm((BATCH, D)),
        "ada_w": nrm((DEPTH, D, N_MOD * D), 0.5 * D ** -0.5),
        "ada_b": nrm((DEPTH, N_MOD * D), 0.02),
        "norm_mix_g": 1.0 + nrm((DEPTH, D), 0.05),
        "norm_ffn_g": 1.0 + nrm((DEPTH, D), 0.05),
        "hy_w_in": nrm((N_EVEN, D, HY_IN_DIM), D ** -0.5),
        "hy_conv_w": nrm((N_EVEN, SSM_CONV, SSM_CONV_DIM), SSM_CONV ** -0.5),
        "hy_conv_b": nrm((N_EVEN, SSM_CONV_DIM), 0.02),
        "hy_dt_bias": dt0 + jnp.log(-jnp.expm1(-dt0)),
        "hy_a_log": jnp.log(jax.random.uniform(next(ks), (N_EVEN, SSM_HEADS), f32, 1.0, 16.0)),
        "hy_d_skip": 1.0 + nrm((N_EVEN, SSM_HEADS), 0.1),
        "hy_ssm_norm_g": 1.0 + nrm((N_EVEN, SSM_D_INNER), 0.05),
        "hy_w_out": nrm((N_EVEN, HY_OUT_DIM, D), HY_OUT_DIM ** -0.5),
        "rel_table": nrm((REL_BUCKETS, ATT_Q_HEADS), 0.2),
        "cv_w_pw1": nrm((N_ODD, D, 2 * D), D ** -0.5),
        "cv_b_pw1": nrm((N_ODD, 2 * D), 0.02),
        "cv_w_dw": nrm((N_ODD, CONV_WIDTH, D), CONV_WIDTH ** -0.5),
        "cv_b_dw": nrm((N_ODD, D), 0.02),
        "cv_ln_g": 1.0 + nrm((N_ODD, D), 0.05),
        "cv_ln_b": nrm((N_ODD, D), 0.02),
        "cv_w_pw2": nrm((N_ODD, D, D), D ** -0.5),
        "cv_b_pw2": nrm((N_ODD, D), 0.02),
        "ffn_w_gate": nrm((DEPTH, D, FFN_HIDDEN), D ** -0.5),
        "ffn_w_up": nrm((DEPTH, D, FFN_HIDDEN), D ** -0.5),
        "ffn_w_down": nrm((DEPTH, FFN_HIDDEN, D), FFN_HIDDEN ** -0.5),
        "final_norm_g": 1.0 + nrm((D,), 0.05),
    }

def first_block(x, c, ada_w, ada_b, norm_mix_g, norm_ffn_g, hy_w_in, hy_conv_w, hy_conv_b, hy_dt_bias,
              hy_a_log, hy_d_skip, hy_ssm_norm_g, hy_w_out, rel_table, cv_w_pw1, cv_b_pw1, cv_w_dw,
              cv_b_dw, cv_ln_g, cv_ln_b, cv_w_pw2, cv_b_pw2, ffn_w_gate, ffn_w_up, ffn_w_down,
              final_norm_g):
    cs = jax.nn.silu(c)
    for i in range(DEPTH):
        mod = cs @ ada_w[i] + ada_b[i]
        sh1, sc1, g1, sh2, sc2, g2 = [m[:, None, :] for m in jnp.split(mod, N_MOD, axis=-1)]
        h = rms_norm(x, norm_mix_g[i]) * (1 + sc1) + sh1
        j = i // 2
        if i % 2 == 0:
            mix = hybrid_mixer(h, hy_w_in[j], hy_conv_w[j], hy_conv_b[j], hy_dt_bias[j], hy_a_log[j],
                               hy_d_skip[j], hy_ssm_norm_g[j], hy_w_out[j], rel_table)
        else:
            mix = conformer_conv(h, cv_w_pw1[j], cv_b_pw1[j], cv_w_dw[j], cv_b_dw[j], cv_ln_g[j],
                                 cv_ln_b[j], cv_w_pw2[j], cv_b_pw2[j])
        x = x + g1 * mix
        h = rms_norm(x, norm_ffn_g[i]) * (1 + sc2) + sh2
        x = x + g2 * swiglu(h, ffn_w_gate[i], ffn_w_up[i], ffn_w_down[i])
    return rms_norm(x, final_norm_g)


GRID_W = 64
CTX_LEN = 256
N_MIXERS = 2
N_RWKV = (DEPTH + N_MIXERS - 1) // N_MIXERS
N_MLA = DEPTH // N_MIXERS
NORM_EPS = 1e-6
RWKV_HEAD = 64
RWKV_HEADS = D_MODEL // RWKV_HEAD
DECAY_LORA = 64
ICLR_LORA = 64
GN_EPS = 64e-5
N_DIR = 2
MLA_HEADS = 16
QK_NOPE = 64
QK_ROPE = 32
V_HEAD = 64
Q_LORA = 384
KV_LORA = 256
MLA_GATE = MLA_HEADS * V_HEAD
MLA_IN = Q_LORA + KV_LORA + QK_ROPE + MLA_GATE
ROPE_THETA = 10000.0
Q_BLOCK = 128


def rmsnorm(x, g, eps=NORM_EPS):
    xf = x.astype(jnp.float32)
    y = xf * lax.rsqrt(jnp.mean(xf * xf, axis=-1, keepdims=True) + eps)
    return (y * g.astype(jnp.float32)).astype(x.dtype)

def centred_shift(h):
    prev = jnp.pad(h[:, :-1], ((0, 0), (1, 0), (0, 0)))
    nxt = jnp.pad(h[:, 1:], ((0, 0), (0, 1), (0, 0)))
    return 0.5 * (prev + nxt) - h

def rwkv_prepare(h, mu, w_in, w0, w1, w2, a0, a1, a2, k_k, k_a):
    B, T, D = h.shape
    xx = centred_shift(h)
    lerp = lambda j: h + xx * mu[j]
    heads = lambda t: t.reshape(t.shape[:-1] + (RWKV_HEADS, RWKV_HEAD))
    r = heads(lerp(0) @ w_in[0])
    k = heads(lerp(1) @ w_in[1])
    v = heads(lerp(2) @ w_in[2])
    gate = lerp(3) @ w_in[3]
    xw, xa = lerp(4), lerp(5)
    wpre = w0[:, None, None, :] + jnp.einsum('nbtr,nrd->nbtd', jnp.tanh(jnp.einsum('btd,ndr->nbtr', xw, w1)), w2)
    wpre = wpre.astype(jnp.float32)
    logw = heads(-jnp.exp(-jax.nn.softplus(-wpre) - 0.5))
    a = heads(jax.nn.sigmoid(a0[:, None, None, :] + jnp.einsum('nbtr,nrd->nbtd', jnp.einsum('btd,ndr->nbtr', xa, a1), a2)))
    kkf = (k * k_k.reshape(RWKV_HEADS, RWKV_HEAD)).astype(jnp.float32)
    kk = (kkf / jnp.maximum(jnp.linalg.norm(kkf, axis=-1, keepdims=True), 1e-12)).astype(h.dtype)
    k_dir = k[None] * (1.0 + (a - 1.0) * k_a.reshape(RWKV_HEADS, RWKV_HEAD))
    b = kk[None] * a
    return r, logw, k_dir, v, -kk, b, gate

def orient_shared(t):
    return jnp.stack([t, jnp.flip(t, 1)])

def orient_dir(t):
    return jnp.stack([t[0], jnp.flip(t[1], 1)])

def wkv_scan(r, logw, k, v, a, b, s0):
    tm = lambda t: jnp.moveaxis(t.astype(jnp.float32), 2, 0)

    def step(s, inp):
        r_t, lw_t, k_t, v_t, a_t, b_t = inp
        sa = jnp.einsum('dbhij,dbhj->dbhi', s, a_t)
        s = s * jnp.exp(lw_t)[..., None, :] + sa[..., None] * b_t[..., None, :] + v_t[..., None] * k_t[..., None, :]
        return s, jnp.einsum('dbhij,dbhj->dbhi', s, r_t)

    s_fin, y = lax.scan(step, s0, (tm(r), tm(logw), tm(k), tm(v), tm(a), tm(b)))
    return jnp.moveaxis(y, 0, 2), s_fin

def rwkv_run(prep, s0):
    r, logw, k_dir, v, a_vec, b, gate = prep
    return wkv_scan(orient_shared(r), orient_dir(logw), orient_dir(k_dir), orient_shared(v),
                    orient_shared(a_vec), orient_dir(b), s0)

def rwkv_readout(y, prep, r_k, lnx_g, lnx_b, w_out):
    r, logw, k_dir, v, a_vec, b, gate = prep
    B, T, D = gate.shape
    yf = y[0] + jnp.flip(y[1], 1)
    mean = jnp.mean(yf, axis=-1, keepdims=True)
    var = jnp.mean(jnp.square(yf - mean), axis=-1, keepdims=True)
    yn = ((yf - mean) * lax.rsqrt(var + GN_EPS)).reshape(B, T, D).astype(gate.dtype) * lnx_g + lnx_b
    bonus = jnp.sum(r[None] * k_dir * r_k, axis=(0, -1))[..., None] * v
    o = (yn + bonus.reshape(B, T, D)) * jax.nn.silu(gate)
    return o @ w_out

def rwkv_mixer(h_x, h_c, mu, w_in, w0, w1, w2, a0, a1, a2, k_k, k_a, r_k, lnx_g, lnx_b, w_out, need_ctx):
    B = h_x.shape[0]
    p_c = rwkv_prepare(h_c, mu, w_in, w0, w1, w2, a0, a1, a2, k_k, k_a)
    p_x = rwkv_prepare(h_x, mu, w_in, w0, w1, w2, a0, a1, a2, k_k, k_a)
    s0 = jnp.zeros((N_DIR, B, RWKV_HEADS, RWKV_HEAD, RWKV_HEAD), jnp.float32)
    y_c, s_c = rwkv_run(p_c, s0)
    y_x, _ = rwkv_run(p_x, s_c)
    d_x = rwkv_readout(y_x, p_x, r_k, lnx_g, lnx_b, w_out)
    d_c = rwkv_readout(y_c, p_c, r_k, lnx_g, lnx_b, w_out) if need_ctx else None
    return d_x, d_c

def axial_rope_angles(T, rows):
    row = jnp.broadcast_to(jnp.arange(rows)[:, None], (rows, GRID_W)).reshape(T).astype(jnp.float32)
    col = jnp.broadcast_to(jnp.arange(GRID_W)[None, :], (rows, GRID_W)).reshape(T).astype(jnp.float32)
    n_axis = QK_ROPE // 2
    inv = 1.0 / (ROPE_THETA ** (jnp.arange(0, n_axis, 2, dtype=jnp.float32) / n_axis))
    ang = jnp.concatenate([row[:, None] * inv, col[:, None] * inv], axis=-1)
    return jnp.cos(ang), jnp.sin(ang)

def apply_rope(x, cos, sin):
    half = QK_ROPE // 2
    x1, x2 = x[..., :half], x[..., half:]
    c = cos[:, None, :].astype(x.dtype)
    s = sin[:, None, :].astype(x.dtype)
    return jnp.concatenate([x1 * c - x2 * s, x1 * s + x2 * c], axis=-1)

def mla_project(h, w_in, q_norm_g, w_qb, kv_norm_g, w_kvb, cos=None, sin=None):
    B, T, D = h.shape
    p = h @ w_in
    q_c, kv_c, k_pe, gate = jnp.split(p, [Q_LORA, Q_LORA + KV_LORA, Q_LORA + KV_LORA + QK_ROPE], axis=-1)
    q = (rmsnorm(q_c, q_norm_g) @ w_qb).reshape(B, T, MLA_HEADS, QK_NOPE + QK_ROPE)
    kv = (rmsnorm(kv_c, kv_norm_g) @ w_kvb).reshape(B, T, MLA_HEADS, QK_NOPE + V_HEAD)
    q_nope, q_pe = q[..., :QK_NOPE], q[..., QK_NOPE:]
    k_nope, v = kv[..., :QK_NOPE], kv[..., QK_NOPE:]
    k_pe = k_pe[:, :, None, :]
    if cos is not None:
        q_pe = apply_rope(q_pe, cos, sin)
        k_pe = apply_rope(k_pe, cos, sin)
    q = jnp.concatenate([q_nope, q_pe], axis=-1)
    k = jnp.concatenate([k_nope, jnp.broadcast_to(k_pe, (B, T, MLA_HEADS, QK_ROPE))], axis=-1)
    return q, k, v, gate

def attend(q, k, v):
    s = jnp.einsum('bqhd,bkhd->bhqk', q, k, preferred_element_type=jnp.float32) * (1.0 / math.sqrt(QK_NOPE + QK_ROPE))
    p = jax.nn.softmax(s, axis=-1).astype(v.dtype)
    return jnp.einsum('bhqk,bkhd->bqhd', p, v, preferred_element_type=jnp.float32).astype(q.dtype)

def mla_mixer(h_x, h_c, cos, sin, w_in, q_norm_g, w_qb, kv_norm_g, w_kvb, w_out, need_ctx):
    B, T, D = h_x.shape
    L = h_c.shape[1]
    q_x, k_x, v_x, g_x = mla_project(h_x, w_in, q_norm_g, w_qb, kv_norm_g, w_kvb, cos, sin)
    q_c, k_c, v_c, g_c = mla_project(h_c, w_in, q_norm_g, w_qb, kv_norm_g, w_kvb)
    k_all = jnp.concatenate([k_x, k_c], axis=1)
    v_all = jnp.concatenate([v_x, v_c], axis=1)
    qb = q_x.reshape(B, T // Q_BLOCK, Q_BLOCK, MLA_HEADS, QK_NOPE + QK_ROPE).swapaxes(0, 1)
    o = lax.map(lambda qblk: attend(qblk, k_all, v_all), qb)
    o = o.swapaxes(0, 1).reshape(B, T, MLA_GATE)
    d_x = (o * jax.nn.silu(g_x)) @ w_out
    d_c = None
    if need_ctx:
        o_c = attend(q_c, k_c, v_c).reshape(B, L, MLA_GATE)
        d_c = (o_c * jax.nn.silu(g_c)) @ w_out
    return d_x, d_c

def second_inputs(seed: int = 0) -> dict:
    key = jax.random.key(seed)
    ks = iter(jax.random.split(key, 40))
    nrm = lambda shape, scale: scale * jax.random.normal(next(ks), shape, jnp.float32)
    D, NR, NM = D_MODEL, N_RWKV, N_MLA
    return {
        'x': nrm((BATCH, SEQ, D), 1.0),
        'c': nrm((BATCH, D), 1.0),
        'ctx': nrm((BATCH, CTX_LEN, D), 1.0),
        'c_ctx': nrm((D,), 1.0),
        'norm_g': 1.0 + nrm((DEPTH, D), 0.05),
        'mod_w': nrm((DEPTH, D, 3 * D), 0.5 * D ** -0.5),
        'mod_b': nrm((DEPTH, 3 * D), 0.05),
        'rwkv_mu': jax.random.uniform(next(ks), (NR, 6, D), jnp.float32),
        'rwkv_w_in': nrm((NR, 4, D, D), D ** -0.5),
        'rwkv_w0': jax.random.uniform(next(ks), (NR, N_DIR, D), jnp.float32, -6.0, -1.0),
        'rwkv_w1': nrm((NR, N_DIR, D, DECAY_LORA), D ** -0.5),
        'rwkv_w2': nrm((NR, N_DIR, DECAY_LORA, D), 0.5 * DECAY_LORA ** -0.5),
        'rwkv_a0': nrm((NR, N_DIR, D), 0.1),
        'rwkv_a1': nrm((NR, N_DIR, D, ICLR_LORA), D ** -0.5),
        'rwkv_a2': nrm((NR, N_DIR, ICLR_LORA, D), 0.5 * ICLR_LORA ** -0.5),
        'rwkv_k_k': 0.85 + nrm((NR, D), 0.05),
        'rwkv_k_a': 1.0 + nrm((NR, D), 0.05),
        'rwkv_r_k': nrm((NR, RWKV_HEADS, RWKV_HEAD), 0.1),
        'rwkv_lnx_g': 1.0 + nrm((NR, D), 0.05),
        'rwkv_lnx_b': nrm((NR, D), 0.02),
        'rwkv_w_out': nrm((NR, D, D), D ** -0.5),
        'mla_w_in': nrm((NM, D, MLA_IN), D ** -0.5),
        'mla_q_norm_g': 1.0 + nrm((NM, Q_LORA), 0.05),
        'mla_w_qb': nrm((NM, Q_LORA, MLA_HEADS * (QK_NOPE + QK_ROPE)), Q_LORA ** -0.5),
        'mla_kv_norm_g': 1.0 + nrm((NM, KV_LORA), 0.05),
        'mla_w_kvb': nrm((NM, KV_LORA, MLA_HEADS * (QK_NOPE + V_HEAD)), KV_LORA ** -0.5),
        'mla_w_out': nrm((NM, MLA_GATE, D), MLA_GATE ** -0.5),
        'final_g': 1.0 + nrm((D,), 0.05),
    }

def second_block(x, c, ctx, c_ctx, norm_g, mod_w, mod_b, rwkv_mu, rwkv_w_in, rwkv_w0, rwkv_w1, rwkv_w2,
              rwkv_a0, rwkv_a1, rwkv_a2, rwkv_k_k, rwkv_k_a, rwkv_r_k, rwkv_lnx_g, rwkv_lnx_b, rwkv_w_out,
              mla_w_in, mla_q_norm_g, mla_w_qb, mla_kv_norm_g, mla_w_kvb, mla_w_out, final_g):
    T = x.shape[1]
    ROWS = T // GRID_W
    cos, sin = axial_rope_angles(T, ROWS)
    for i in range(DEPTH):
        last = i == DEPTH - 1
        mod_x = jax.nn.silu(c) @ mod_w[i] + mod_b[i]
        mod_c = jax.nn.silu(c_ctx) @ mod_w[i] + mod_b[i]
        sh_x, sc_x, g_x = jnp.split(mod_x[:, None, :], 3, axis=-1)
        sh_c, sc_c, g_c = jnp.split(mod_c, 3, axis=-1)
        h_x = rmsnorm(x, norm_g[i]) * (1.0 + sc_x) + sh_x
        h_c = rmsnorm(ctx, norm_g[i]) * (1.0 + sc_c) + sh_c
        j = i // N_MIXERS
        if i % N_MIXERS == 0:
            d_x, d_c = rwkv_mixer(h_x, h_c, rwkv_mu[j], rwkv_w_in[j], rwkv_w0[j], rwkv_w1[j], rwkv_w2[j],
                                  rwkv_a0[j], rwkv_a1[j], rwkv_a2[j], rwkv_k_k[j], rwkv_k_a[j], rwkv_r_k[j],
                                  rwkv_lnx_g[j], rwkv_lnx_b[j], rwkv_w_out[j], not last)
        else:
            d_x, d_c = mla_mixer(h_x, h_c, cos, sin, mla_w_in[j], mla_q_norm_g[j], mla_w_qb[j],
                                 mla_kv_norm_g[j], mla_w_kvb[j], mla_w_out[j], not last)
        x = x + g_x * d_x
        if not last:
            ctx = ctx + g_c * d_c
    return rmsnorm(x, final_g)


def setup_inputs(seed=0):
    out = dict(first_inputs(seed))
    for name, value in second_inputs(seed + 1).items():
        if name != "x":
            out[name + "_2"] = value
    return out


def reference(
    x, c, ada_w, ada_b, norm_mix_g, norm_ffn_g, hy_w_in, hy_conv_w, hy_conv_b, hy_dt_bias,
    hy_a_log, hy_d_skip, hy_ssm_norm_g, hy_w_out, rel_table, cv_w_pw1, cv_b_pw1, cv_w_dw,
    cv_b_dw, cv_ln_g, cv_ln_b, cv_w_pw2, cv_b_pw2, ffn_w_gate, ffn_w_up, ffn_w_down,
    final_norm_g, c_2, ctx_2, c_ctx_2, norm_g_2, mod_w_2, mod_b_2, rwkv_mu_2, rwkv_w_in_2,
    rwkv_w0_2, rwkv_w1_2, rwkv_w2_2, rwkv_a0_2, rwkv_a1_2, rwkv_a2_2, rwkv_k_k_2, rwkv_k_a_2,
    rwkv_r_k_2, rwkv_lnx_g_2, rwkv_lnx_b_2, rwkv_w_out_2, mla_w_in_2, mla_q_norm_g_2,
    mla_w_qb_2, mla_kv_norm_g_2, mla_w_kvb_2, mla_w_out_2, final_g_2,
):
    x = first_block(
        x, c, ada_w, ada_b, norm_mix_g, norm_ffn_g, hy_w_in, hy_conv_w, hy_conv_b, hy_dt_bias,
        hy_a_log, hy_d_skip, hy_ssm_norm_g, hy_w_out, rel_table, cv_w_pw1, cv_b_pw1, cv_w_dw,
        cv_b_dw, cv_ln_g, cv_ln_b, cv_w_pw2, cv_b_pw2, ffn_w_gate, ffn_w_up, ffn_w_down,
        final_norm_g,
    )
    return second_block(
        x, c_2, ctx_2, c_ctx_2, norm_g_2, mod_w_2, mod_b_2, rwkv_mu_2, rwkv_w_in_2, rwkv_w0_2,
        rwkv_w1_2, rwkv_w2_2, rwkv_a0_2, rwkv_a1_2, rwkv_a2_2, rwkv_k_k_2, rwkv_k_a_2,
        rwkv_r_k_2, rwkv_lnx_g_2, rwkv_lnx_b_2, rwkv_w_out_2, mla_w_in_2, mla_q_norm_g_2,
        mla_w_qb_2, mla_kv_norm_g_2, mla_w_kvb_2, mla_w_out_2, final_g_2,
    )


_drawn_inputs = setup_inputs


def setup_inputs(seed=0):
    import zlib

    import numpy as np

    out = dict(_drawn_inputs(seed))
    spreads = {}
    factors = {'hy_conv_b': 8.0,
     'hy_d_skip': 3.451,
     'hy_ssm_norm_g': 4.3,
     'rel_table': 8.0,
     'cv_b_pw1': 8.0,
     'cv_b_dw': 7.63,
     'cv_ln_g': 4.998,
     'cv_ln_b': 8.0,
     'cv_b_pw2': 8.0,
     'norm_g_2': 3.548,
     'rwkv_w1_2': 8.0,
     'rwkv_w2_2': 8.0,
     'rwkv_a0_2': 8.0,
     'rwkv_k_k_2': 3.28,
     'rwkv_k_a_2': 3.434,
     'rwkv_lnx_g_2': 7.622,
     'rwkv_lnx_b_2': 8.0,
     'mla_q_norm_g_2': 8.0,
     'mla_w_qb_2': 3.243,
     'mla_kv_norm_g_2': 8.0}
    for name, (base, spread) in spreads.items():
        noise = np.random.default_rng([zlib.crc32(name.encode()), seed]).standard_normal(out[name].shape)
        drawn = base * np.exp(spread * noise) if base else spread * noise
        out[name] = __import__('jax').numpy.asarray(drawn.astype(out[name].dtype))
    for name, factor in factors.items():
        out[name] = (out[name] * factor).astype(out[name].dtype)
    return out
```

```python
import math
from contextlib import ExitStack

import numpy as np

import concourse.bass as bass
from concourse import mybir

F32 = mybir.dt.float32
U8 = mybir.dt.uint8
I32 = mybir.dt.int32
ACT = mybir.ActivationFunctionType
ALU = mybir.AluOpType
AX = mybir.AxisListType.X

P = 128
D = 1024
T = 256
KT = D // P
RING = 4
SLOT = KT * 512
EPS = 1e-6
NEG = -1e30

DI = 2048
CONV_DIM = 3072
HEADS = 32
ST_Z, ST_XS, ST_B, ST_C, ST_Q, ST_K, ST_V = 0, 16, 32, 36, 40, 64, 72
NY = 80
FFN = 2816
FT = FFN // P
TAPS = 31

_PAR_SIZES = [("c", 8), ("c2", 8), ("cctx", 8), ("adab0", 48), ("adab1", 48), ("modb0", 24), ("modb1", 24),
              ("nmix0", 8), ("nmix1", 8), ("nffn0", 8), ("nffn1", 8), ("final1", 8),
              ("conv", 24 * 5), ("dskip", 16), ("ssmg", 16), ("pw1b", 16), ("dw", 8 * 32), ("lng", 8),
              ("lnb", 8), ("pw2b", 8), ("norm2_0", 8), ("norm2_1", 8), ("mu", 48), ("final2", 8), ("qg", 3),
              ("kvg", 2), ("rw", 8 * 9)]
PAR = {}
NPAR = 0
for _name, _n in _PAR_SIZES:
    PAR[_name] = NPAR
    NPAR += _n

_SLOTS = [("mod0", 12), ("hyin", 20), ("hyout", 6), ("up0", 11), ("down0", 6), ("mod1", 12), ("pw1", 4), ("pw2", 2),
          ("up1", 11), ("down1", 6), ("mod2", 12), ("rkvg", 8), ("rwout", 2), ("mlain", 4), ("mlab", 3),
          ("mlaout", 2)]
FIRST = {}
NSLOTS = 0
for _name, _n in _SLOTS:
    FIRST[_name] = NSLOTS
    NSLOTS += _n

_CONST_SIZES = [("ident", 128), ("ones", 128), ("headones", 128), ("tri", 128), ("neg", 128), ("flip", 128)]
CON = {}
NCON = 0
for _name, _n in _CONST_SIZES:
    CON[_name] = NCON
    NCON += _n


class Steps:

    def __init__(self, eng, sem, done=0):
        self.eng, self.sem, self.done, self.n = eng, sem, done, 0

    def __call__(self, ins):
        self.n += 1
        ins.then_inc(self.sem, 1)
        self.eng.wait_ge(self.sem, self.done + self.n)


class Core:
    pass


def psum_tiles(k):
    return [k.psum[b] for b in range(8)]


def wait_slot(k, eng, n, turn=0):
    eng.wait_ge(k.slot_landed[n % RING], turn * 16 + 16 * (n // RING + 1))


def load_ahead(k, sp, first, count):
    def one(n, turn):
        sp.wait_ge(k.slot_used, turn * RING + (n + 1))
        sp.dma_start(k.ring[:, n % RING, :], k.stream[turn * RING + (n + RING)]).then_inc(
            k.slot_landed[n % RING], 16)

    count = min(count, NSLOTS - RING - first)
    turns = count // RING
    if turns > 1:
        with sp.Fori(0, turns) as t:
            for j in range(RING):
                one(first + j, t)
        for j in range(turns * RING, count):
            one(first + j, 0)
    else:
        for j in range(count):
            one(first + j, 0)


def ring_tile(k, n, kt, col, width=P):
    return k.ring[:, n % RING, kt * 512 + col:kt * 512 + col + width]


def row(k, name, i=0, n=1):
    c = PAR[name] + i
    return k.par[:, c:c + n]


def const(k, name):
    return k.con[:, CON[name]:CON[name] + P]


def stage_setup(nc, k, a):
    with ExitStack() as ctx:
        landed = ctx.enter_context(nc.semaphore("setup_landed"))
        silu_done = ctx.enter_context(nc.semaphore("setup_silu"))
        block = ctx.enter_context(nc.Block())

        @block.sync
        def _(sp):
            sp.dma_start(k.par[:], a["par"]).then_inc(landed, 16)
            sp.dma_start(k.con[:], a["con"]).then_inc(landed, 16)
            for n in range(RING):
                sp.dma_start(k.ring[:, n, :], k.stream[n]).then_inc(k.slot_landed[n], 16)
            sp.dma_start(k.x[:], a["xt"]).then_inc(landed, 16)
            sp.dma_start(k.ctx[:], a["ctxt"]).then_inc(landed, 16)
            sp.wait_ge(landed, 64)

        @block.scalar
        def _(act):
            act.wait_ge(landed, 64)
            nc.scalar.activation(k.cs[:], row(k, "c", 0, 24), ACT.Silu).then_inc(silu_done, 1)


def stage_mod(nc, k, slots, vectors, out, bias):
    first, count = slots
    nv = len(vectors)
    with ExitStack() as ctx:
        part = ctx.enter_context(nc.sbuf_tensor(f"mod_part{first}", [P, 2, nv, 512], F32))
        summed = ctx.enter_context(nc.semaphore("mod_summed"))
        step = ctx.enter_context(nc.semaphore("mod_step"))
        stored = ctx.enter_context(nc.semaphore("mod_stored"))
        block = ctx.enter_context(nc.Block())
        turns = count // RING

        @block.sync
        def _(sp):
            load_ahead(k, sp, first, count)

        @block.vector
        def _(dve):
            with dve.Fori(0, turns) as t:
                s = Steps(dve, step, t * (RING * (KT - 1) * nv))
                for j in range(RING):
                    wait_slot(k, dve, first + j, t)
                    dve.wait_ge(k.slot_used, t * RING + max(first + j - 1, j))
                    w = k.ring[:, (first + j) % RING, :]
                    for kt in range(KT):
                        for v, vec in enumerate(vectors):
                            acc = part[:, j % 2, v, :]
                            if kt == 0:
                                ins = nc.vector.tensor_scalar(acc, w[:, 0:512], vec[:, 0:1], None, ALU.mult)
                            else:
                                ins = nc.vector.scalar_tensor_tensor(
                                    acc, w[:, kt * 512:kt * 512 + 512], vec[:, kt:kt + 1], acc, ALU.mult, ALU.add)
                            if kt < KT - 1:
                                ins.then_inc(step, 1)
                                s.n += 1
                            elif v == nv - 1:
                                ins.then_inc(summed, 1)
                        if kt < KT - 1:
                            dve.wait_ge(step, s.done + s.n)

        @block.tensor
        def _(pe):
            with pe.Fori(0, turns) as t:
                for j in range(RING):
                    pe.wait_ge(summed, t * RING + (j + 1))
                    if j == 0:
                        pe.wait_ge(stored, t * nv)
                    for v in range(nv):
                        for q in range(4):
                            mm = pe.matmul(k.psum[v][:, j * 4 + q:j * 4 + q + 1],
                                           part[:, j % 2, v, q * P:(q + 1) * P], const(k, "ones")[:, 0:1],
                                           start=True, stop=True)
                    mm.then_inc(k.slot_used, 1)

        @block.scalar
        def _(act):
            with act.Fori(0, turns) as t:
                act.wait_ge(k.slot_used, t * RING + (first + RING))
                for v in range(nv):
                    nc.scalar.copy(out[v][:, bass.ds(t * 16, 16)], k.psum[v][:, 0:16]).then_inc(stored, 1)

    with nc.Block() as block:
        @block.vector
        def _(dve):
            for v in range(nv):
                nc.vector.tensor_tensor(out[v], out[v], bias, ALU.add)


def stage_norm(nc, k, src, nt, width, scale, bias, dst, count, name):
    with ExitStack() as ctx:
        sq = ctx.enter_context(nc.sbuf_tensor(f"norm_sq_{name}", [P, nt, width], F32))
        rstd = ctx.enter_context(nc.sbuf_tensor(f"norm_rstd_{name}", [P, 1, width], F32))
        squared = ctx.enter_context(nc.semaphore("norm_squared"))
        summed = ctx.enter_context(nc.semaphore("norm_summed"))
        step = ctx.enter_context(nc.semaphore("norm_step"))
        rooted = ctx.enter_context(nc.semaphore("norm_rooted"))
        block = ctx.enter_context(nc.Block())
        half = nt // 2

        @block.scalar
        def _(act):
            for lo, hi in ((0, half), (half, nt)):
                nc.scalar.activation(sq[:, lo:hi, :], src[:, lo:hi, :], ACT.Square).then_inc(squared, 1)
            act.wait_ge(step, 1)
            nc.scalar.activation(rstd[:, 0, :], rstd[:, 0, :], ACT.Sqrt).then_inc(rooted, 1)
            if bias is not None:
                act.wait_ge(step, 3)
                for i in range(1, nt, 2):
                    nc.scalar.activation(dst[:, i, :], sq[:, i, :], ACT.Identity, bias=bias[:, i:i + 1],
                                         scale=scale[:, i:i + 1])

        @block.tensor
        def _(pe):
            for i in range(nt):
                if i == 0:
                    pe.wait_ge(squared, 1)
                if i == half:
                    pe.wait_ge(squared, 2)
                mm = pe.matmul(k.psum[0][:, 0:width], const(k, "ones"), sq[:, i, :], start=(i == 0),
                               stop=(i == nt - 1))
            mm.then_inc(summed, 1)

        @block.vector
        def _(dve):
            s = Steps(dve, step)
            dve.wait_ge(summed, 1)
            s(nc.vector.tensor_scalar(rstd[:, 0, :], k.psum[0][:, 0:width], 1.0 / (nt * P) if count is None
                                      else 1.0 / count, EPS, ALU.mult, ALU.add))
            dve.wait_ge(rooted, 1)
            s(nc.vector.reciprocal(rstd[:, 0, :], rstd[:, 0, :]))
            s(nc.vector.tensor_tensor(sq[:], src, rstd[:].to_broadcast([P, nt, width]), ALU.mult))
            for i in range(0, nt, 2 if bias is not None else 1):
                if bias is not None:
                    nc.vector.tensor_scalar(dst[:, i, :], sq[:, i, :], scale[:, i:i + 1], bias[:, i:i + 1],
                                            ALU.mult, ALU.add)
                else:
                    nc.vector.tensor_scalar(dst[:, i, :], sq[:, i, :], scale[:, i:i + 1], None, ALU.mult)


def stage_scales(nc, k, pairs):
    with ExitStack() as ctx:
        block = ctx.enter_context(nc.Block())

        @block.vector
        def _(dve):
            for out, sc, g in pairs:
                nc.vector.scalar_tensor_tensor(out, sc, 1.0, g, ALU.add, ALU.mult)


def slot_products(k, pe, n, turn, rhs, outs, kts=range(KT), start=True, stop=True, width=P):
    wait_slot(k, pe, n, turn)
    for i, out in enumerate(outs):
        for kt in kts:
            mm = pe.matmul(out, ring_tile(k, n, kt, i * P), rhs[kt], start=start and kt == kts[0],
                           stop=stop and kt == kts[-1])
    return mm


def stage_hyin(nc, k, h, y, a, dtok):
    first = FIRST["hyin"]
    turns = 20 // RING
    with ExitStack() as ctx:
        wdt = ctx.enter_context(nc.sbuf_tensor("hyin_wdt", [P, KT, HEADS], F32))
        wdt_landed = ctx.enter_context(nc.semaphore("wdt_landed"))
        stored_dve = ctx.enter_context(nc.semaphore("hyin_stored_dve"))
        stored_act = ctx.enter_context(nc.semaphore("hyin_stored_act"))
        dt_done = ctx.enter_context(nc.semaphore("hyin_dt"))
        block = ctx.enter_context(nc.Block())

        @block.sync
        def _(sp):
            sp.dma_start(wdt[:], a["wdt"]).then_inc(wdt_landed, 16)
            load_ahead(k, sp, first, 20)

        @block.tensor
        def _(pe):
            rhs = [h[:, kt, :] for kt in range(KT)]
            pe.wait_ge(wdt_landed, 16)
            for c in range(2):
                for kt in range(KT):
                    mm = pe.matmul(k.psum[7][:, c * HEADS:(c + 1) * HEADS], h[:, kt, c * P:(c + 1) * P],
                                   wdt[:, kt, :], start=(kt == 0), stop=(kt == KT - 1))
            mm.then_inc(dt_done, 1)
            with pe.Fori(0, turns) as t:
                for j in range(RING):
                    pe.wait_ge(stored_dve, t * RING + (j + 1))
                    pe.wait_ge(stored_act, t * RING + (j + 1))
                    b = 2 * (j % 2)
                    outs = [k.psum[b + i // 2][:, (i % 2) * T:(i % 2 + 1) * T] for i in range(4)]
                    slot_products(k, pe, first + j, t, rhs, outs).then_inc(k.slot_used, 1)

        @block.vector
        def _(dve):
            dve.wait_ge(dt_done, 1)
            nc.vector.tensor_copy(dtok[:], k.psum[7][:, 0:2 * HEADS])
            dve.sem_inc(stored_dve, 2)
            with dve.Fori(0, turns) as t:
                for j in range(RING):
                    dve.wait_ge(k.slot_used, t * RING + (first + j + 1))
                    nc.vector.tensor_copy(y[:, bass.ds(t * 16 + 4 * j, 2), :],
                                          k.psum[2 * (j % 2)][:]).then_inc(stored_dve, 1)

        @block.scalar
        def _(act):
            act.sem_inc(stored_act, 2)
            with act.Fori(0, turns) as t:
                for j in range(RING):
                    act.wait_ge(k.slot_used, t * RING + (first + j + 1))
                    nc.scalar.copy(y[:, bass.ds(t * 16 + 4 * j + 2, 2), :],
                                   k.psum[2 * (j % 2) + 1][:]).then_inc(stored_act, 1)


def stage_conv4(nc, k, y):
    nt = 24
    with ExitStack() as ctx:
        acc = ctx.enter_context(nc.sbuf_tensor("conv_acc", [P, 2, T], F32))
        step = ctx.enter_context(nc.semaphore("conv_step"))
        summed = ctx.enter_context(nc.semaphore("conv_summed"))
        stored = ctx.enter_context(nc.semaphore("conv_stored"))
        block = ctx.enter_context(nc.Block())

        @block.vector
        def _(dve):
            dve.sem_inc(stored, 2)
            with dve.Fori(0, nt // 2) as t:
                s = Steps(dve, step, t * 6)
                for tap in range(4):
                    for j in range(2):
                        i = t * 2 + j
                        src = y[:, bass.ds(i + ST_XS, 1), :]
                        a = acc[:, j:j + 1, :]

                        def w(c):
                            return k.par[:, bass.ds(i * 5 + (PAR["conv"] + c), 1)]
                        if tap == 0:
                            dve.wait_ge(stored, t * 2 + (j + 1))
                            ins = nc.vector.tensor_scalar(a, src, w(3), w(4), ALU.mult, ALU.add)
                        else:
                            ins = nc.vector.scalar_tensor_tensor(
                                a[:, :, tap:], src[:, :, :T - tap], w(3 - tap), a[:, :, tap:], ALU.mult, ALU.add)
                        if tap == 3:
                            ins.then_inc(summed, 1)
                        else:
                            ins.then_inc(step, 1)
                            s.n += 1
                    if tap < 3:
                        dve.wait_ge(step, s.done + s.n)

        @block.scalar
        def _(act):
            for q in range(4):
                nc.scalar.activation(y[:, 4 * q:4 * q + 4, :], y[:, 4 * q:4 * q + 4, :], ACT.Silu)
            with act.Fori(0, nt // 2) as t:
                for j in range(2):
                    act.wait_ge(summed, t * 2 + (j + 1))
                    nc.scalar.activation(y[:, bass.ds(t * 2 + (j + ST_XS), 1), :], acc[:, j:j + 1, :],
                                         ACT.Silu).then_inc(stored, 1)


DT, DA, ACS, TOTAL, DT_END = range(5)


def stage_dt(nc, k, a, dtok, hd):
    with ExitStack() as ctx:
        hrow = ctx.enter_context(nc.sbuf_tensor("headrow", [P, 2, HEADS], F32))
        w = ctx.enter_context(nc.sbuf_tensor("dt_work", [P, 8, 2 * HEADS], F32))
        landed = ctx.enter_context(nc.semaphore("headrow_landed"))
        step = ctx.enter_context(nc.semaphore("dt_step"))
        done = ctx.enter_context(nc.semaphore("dt_act"))
        summed = ctx.enter_context(nc.semaphore("dt_summed"))
        dt_ready = ctx.enter_context(nc.semaphore("dt_ready"))
        block = ctx.enter_context(nc.Block())
        RAW, ABS, EXPD, ONEP, LOG1, BACK, ZERO, AROW = range(8)

        def both(ap):
            return ap.unsqueeze(1).to_broadcast([P, 2, HEADS])

        def v(i):
            return w[:, i, :].rearrange("p (c h) -> p c h", c=2)

        @block.sync
        def _(sp):
            sp.dma_start(hrow[:], a["headrow"].rearrange("p (r h) -> p r h", r=2)).then_inc(landed, 16)

        @block.scalar
        def _(act):
            act.wait_ge(landed, 16)
            nc.scalar.activation(w[:, AROW, 0:HEADS], hrow[:, 1, :], ACT.Exp).then_inc(done, 1)
            act.wait_ge(step, 2)
            nc.scalar.activation(w[:, EXPD, :], w[:, ABS, :], ACT.Exp, scale=-1.0).then_inc(done, 1)
            act.wait_ge(step, 3)
            nc.scalar.activation(w[:, LOG1, :], w[:, ONEP, :], ACT.Ln).then_inc(done, 1)
            act.wait_ge(step, 13)
            nc.scalar.activation(w[:, EXPD, :], w[:, BACK, :], ACT.Exp).then_inc(done, 1)

        @block.tensor
        def _(pe):
            pe.wait_ge(step, 11)
            pe.matmul(k.psum[0][:, 0:64], const(k, "tri"), hd[:, DA, :], start=True, stop=True)
            pe.matmul(k.psum[1][:, 0:64], const(k, "ones"), hd[:, DA, :], start=True, stop=True).then_inc(summed, 1)

        @block.vector
        def _(dve):
            s = Steps(dve, step)
            dve.wait_ge(landed, 16)
            s(nc.vector.tensor_tensor(v(RAW), dtok[:].rearrange("p (c h) -> p c h", c=2), both(hrow[:, 0, :]), ALU.add))
            s(nc.vector.scalar_tensor_tensor(w[:, ABS, :], w[:, RAW, :], -1.0, w[:, RAW, :], ALU.mult, ALU.max))
            dve.wait_ge(done, 2)
            s(nc.vector.tensor_scalar(w[:, ONEP, :], w[:, EXPD, :], 1.0, None, ALU.add))
            s(nc.vector.tensor_scalar(w[:, BACK, :], w[:, ONEP, :], -1.0, None, ALU.add))
            s(nc.vector.tensor_scalar(w[:, ZERO, :], w[:, BACK, :], 0.0, None, ALU.is_equal))
            s(nc.vector.tensor_tensor(w[:, BACK, :], w[:, BACK, :], w[:, ZERO, :], ALU.add))
            dve.wait_ge(done, 3)
            s(nc.vector.tensor_tensor(w[:, LOG1, :], w[:, LOG1, :], w[:, ZERO, :], ALU.add))
            s(nc.vector.reciprocal(w[:, BACK, :], w[:, BACK, :]))
            s(nc.vector.tensor_tensor(w[:, LOG1, :], w[:, LOG1, :], w[:, BACK, :], ALU.mult))
            s(nc.vector.tensor_tensor(w[:, LOG1, :], w[:, LOG1, :], w[:, EXPD, :], ALU.mult))
            nc.vector.scalar_tensor_tensor(hd[:, DT, :], w[:, RAW, :], 0.0, w[:, LOG1, :], ALU.max,
                                           ALU.add).then_inc(dt_ready, 1)
            dve.wait_ge(dt_ready, 1)
            dve.wait_ge(done, 1)
            s(nc.vector.scalar_tensor_tensor(hd[:, DA, :].rearrange("p (c h) -> p c h", c=2),
                                             hd[:, DT, :].rearrange("p (c h) -> p c h", c=2), -1.0,
                                             both(w[:, AROW, 0:HEADS]), ALU.mult, ALU.mult))
            dve.wait_ge(summed, 1)
            s(nc.vector.tensor_copy(hd[:, ACS, :], k.psum[0][:, 0:64]))
            s(nc.vector.tensor_tensor(w[:, BACK, :], k.psum[1][:, 0:64], hd[:, ACS, :], ALU.subtract))
            dve.wait_ge(done, 4)
            s(nc.vector.tensor_tensor(hd[:, DT_END, :], hd[:, DT, :], w[:, EXPD, :], ALU.mult))



def stage_ssd(nc, k, y, hd):
    with ExitStack() as ctx:
        def sb(name, shape):
            return ctx.enter_context(nc.sbuf_tensor("ssd_" + name, shape, F32))

        def sem(name):
            return ctx.enter_context(nc.semaphore("ssd_" + name))
        bt, ct, xs = sb("b", [P, T]), sb("c", [P, T]), sb("x", [P, 4, T])
        hv = sb("hv", [P, 5, 2, 8])
        bt_tok = sb("b_tok", [P, P])
        xdt = sb("xdt", [P, 2, 8, 64])
        xend = sb("xend", [P, 8, 64])
        cb = sb("cb", [P, 2, P])
        seg = sb("seg", [P, 4, 4, P])
        cdec = sb("cdec", [P, 2, 4, P])
        state = sb("state", [P, 512])
        staged, turned, rows_up = sem("staged"), sem("turned"), sem("rows_up")
        evac, masked, decayed, weighted = sem("evac"), sem("masked"), sem("decayed"), sem("weighted")
        cdone, states_up, state_down, y_up, y_down = sem("cdone"), sem("states_up"), sem("state_down"), sem("y_up"), \
            sem("y_down")
        rowed = sem("rowed")
        ident = const(k, "ident")
        block = ctx.enter_context(nc.Block())

        @block.gpsimd
        def _(pool):
            with pool.Fori(0, 4) as g:
                pool.wait_ge(y_down, g * 2)
                nc.gpsimd.tensor_copy(bt[:].unsqueeze(1), y[:, bass.ds(g + ST_B, 1), :]).then_inc(staged, 1)
                nc.gpsimd.tensor_copy(ct[:].unsqueeze(1), y[:, bass.ds(g + ST_C, 1), :]).then_inc(staged, 1)
                for r in (DT, DA, ACS, DT_END):
                    nc.gpsimd.tensor_copy(hv[:, r, :, :], hd[:, r, :].rearrange("p (c h) -> p c h", c=2)[
                        :, :, bass.ds(g * 8, 8)]).then_inc(staged, 1)
                nc.gpsimd.tensor_copy(xs[:], y[:, bass.ds(g * 4 + ST_XS, 4), :]).then_inc(staged, 1)

        @block.tensor
        def _(pe):
            with pe.Fori(0, 4) as g:
                pe.wait_ge(staged, g * 7 + 7)
                for c in range(2):
                    for i in range(4):
                        pe.transpose(k.psum[c][:, i * P:(i + 1) * P], xs[:, i, c * P:(c + 1) * P], ident)
                for c in range(2):
                    pe.matmul(k.psum[2][:, c * P:(c + 1) * P], bt[:, c * P:(c + 1) * P], ct[:, c * P:(c + 1) * P],
                              start=True, stop=True)
                pe.transpose(k.psum[2][:, 2 * P:3 * P], bt[:, 0:P], ident).then_inc(turned, 1)
                for b in range(4):
                    c, half = b // 2, b % 2
                    for i in range(4):
                        col = hv[:, DA, c, half * 4 + i:half * 4 + i + 1].to_broadcast([P, P])
                        mm = pe.matmul(k.psum[4 + b][:, i * P:(i + 1) * P], col, const(k, "tri"), start=True,
                                       stop=True)
                    mm.then_inc(rows_up, 1)
                pe.wait_ge(evac, g * 5 + 5)
                pe.matmul(k.psum[3][:], bt_tok[:], xend[:].rearrange("p h d -> p (h d)"), start=True,
                          stop=True).then_inc(states_up, 1)
                for c in range(2):
                    for i in range(4):
                        if i % 2 == 0:
                            pe.wait_ge(weighted, g * 4 + (2 * c + i // 2 + 1))
                        if c == 1 and i == 0:
                            pe.wait_ge(state_down, g + 1)
                            pe.wait_ge(cdone, g * 2 + 2)
                        for e in range(2):
                            hh = 2 * i + e
                            out = k.psum[c][e * 64:(e + 1) * 64, i * P:(i + 1) * P]
                            mm = pe.matmul(out, xdt[:, c, hh, :], seg[:, 2 * c + hh // 4, hh % 4, :], start=True,
                                           stop=(c == 0), skip_group_check=True)
                            if c == 1:
                                mm = pe.matmul(out, state[:, hh * 64:(hh + 1) * 64], cdec[:, hh // 4, hh % 4, :],
                                               start=False, stop=True, skip_group_check=True)
                    mm.then_inc(y_up, 1)

        @block.vector
        def _(dve):
            with dve.Fori(0, 4) as g:
                dve.wait_ge(turned, g + 1)
                for c in range(2):
                    xt = k.psum[c][:].rearrange("p (h d) -> p h d", h=8)
                    nc.vector.tensor_tensor(xdt[:, c, :, :], xt, hv[:, DT, c, :].unsqueeze(2).to_broadcast(
                        [P, 8, 64]), ALU.mult).then_inc(evac, 1)
                nc.vector.tensor_tensor(xend[:], k.psum[0][:].rearrange("p (h d) -> p h d", h=8),
                                        hv[:, DT_END, 0, :].unsqueeze(2).to_broadcast([P, 8, 64]),
                                        ALU.mult).then_inc(evac, 1)
                nc.vector.tensor_copy(cb[:].rearrange("p c l -> p (c l)"), k.psum[2][:, 0:2 * P]).then_inc(evac, 1)
                nc.vector.tensor_copy(bt_tok[:], k.psum[2][:, 2 * P:3 * P]).then_inc(evac, 1)
                for b in range(4):
                    c, half = b // 2, b % 2
                    dve.wait_ge(rows_up, g * 4 + (b + 1))
                    for i in range(4):
                        ins = nc.vector.scalar_tensor_tensor(
                            seg[:, b, i, :], k.psum[4 + b][:, i * P:(i + 1) * P],
                            hv[:, ACS, c, half * 4 + i:half * 4 + i + 1], const(k, "neg"), ALU.subtract, ALU.add)
                    ins.then_inc(masked, 1)
                for b in range(4):
                    dve.wait_ge(decayed, g * 4 + (b + 1))
                    if b == 0:
                        dve.wait_ge(evac, g * 5 + 5)
                    nc.vector.tensor_tensor(seg[:, b, :, :], seg[:, b, :, :], cb[:, b // 2, :].unsqueeze(
                        1).to_broadcast([P, 4, P]), ALU.mult).then_inc(weighted, 1)
                for half in range(2):
                    dve.wait_ge(rowed, g * 2 + (half + 1))
                    nc.vector.tensor_tensor(cdec[:, half, :, :], cdec[:, half, :, :], ct[:, P:2 * P].unsqueeze(
                        1).to_broadcast([P, 4, P]), ALU.mult).then_inc(cdone, 1)
                for c in range(2):
                    dve.wait_ge(y_up, g * 2 + (c + 1))
                    for i in range(4):
                        ins = nc.vector.scalar_tensor_tensor(
                            y[:, bass.ds(g * 4 + (ST_XS + i), 1), c * P:(c + 1) * P],
                            xs[:, i:i + 1, c * P:(c + 1) * P],
                            k.par[:, bass.ds(g * 4 + (PAR["dskip"] + i), 1)],
                            k.psum[c][:, i * P:(i + 1) * P].unsqueeze(1), ALU.mult, ALU.add)
                    ins.then_inc(y_down, 1)

        @block.scalar
        def _(act):
            with act.Fori(0, 4) as g:
                for b in range(4):
                    act.wait_ge(masked, g * 4 + (b + 1))
                    nc.scalar.activation(seg[:, b, :, :], seg[:, b, :, :], ACT.Exp).then_inc(decayed, 1)
                    if b >= 2:
                        nc.scalar.activation(cdec[:, b - 2, :, :].rearrange("p h l -> p (h l)"),
                                             k.psum[4 + b][:], ACT.Exp).then_inc(rowed, 1)
                act.wait_ge(states_up, g + 1)
                nc.scalar.copy(state[:], k.psum[3][:]).then_inc(state_down, 1)


def stage_ssm_gate(nc, k, y):
    with ExitStack() as ctx:
        half_done = ctx.enter_context(nc.semaphore("gate_done"))
        block = ctx.enter_context(nc.Block())

        @block.vector
        def _(dve):
            for lo, hi in ((0, 4), (4, 8), (8, 12), (12, 16)):
                nc.vector.tensor_tensor(y[:, ST_XS + lo:ST_XS + hi, :], y[:, ST_XS + lo:ST_XS + hi, :],
                                        y[:, lo:hi, :], ALU.mult)
    stage_norm(nc, k, y[:, ST_XS:ST_XS + 16, :], 16, T, row(k, "ssmg", 0, 16), None,
               y[:, ST_XS:ST_XS + 16, :], None, "ssm")


def stage_bias_table(nc, k, a, table):
    with ExitStack() as ctx:
        rel = ctx.enter_context(nc.sbuf_tensor("bias_rel", [32, 48], F32))
        onehot = ctx.enter_context(nc.sbuf_tensor("bias_onehot", [32, 384], F32))
        neg = ctx.enter_context(nc.sbuf_tensor("bias_neg", [48, 384], F32))
        flat = ctx.enter_context(nc.sbuf_tensor("bias_flat", [48, 384], F32))
        landed = ctx.enter_context(nc.semaphore("bias_landed"))
        looked_up = ctx.enter_context(nc.semaphore("bias_looked_up"))
        masked = ctx.enter_context(nc.semaphore("bias_masked"))
        kept = ctx.enter_context(nc.semaphore("bias_kept"))
        block = ctx.enter_context(nc.Block())

        @block.sync
        def _(sp):
            sp.dma_start(rel[:], a["rel_table"]).then_inc(landed, 16)
            sp.dma_start(onehot[:], a["bias_onehot"]).then_inc(landed, 16)
            sp.dma_start(neg[:], a["bias_neg"]).then_inc(landed, 16)
            sp.wait_ge(masked, 1)
            sp.dma_start(table, flat[:]).then_inc(kept, 16)
            sp.wait_ge(kept, 16)

        @block.tensor
        def _(pe):
            pe.wait_ge(landed, 48)
            pe.matmul(k.psum[0][0:48, 0:384], rel[:], onehot[:], start=True, stop=True).then_inc(looked_up, 1)

        @block.vector
        def _(dve):
            dve.wait_ge(looked_up, 1)
            nc.vector.tensor_tensor(flat[:], k.psum[0][0:48, 0:384], neg[:], ALU.add).then_inc(masked, 1)


def stage_attention(nc, k, a, y):
    table = nc.dram_tensor("bias_table", (48, 384), F32)
    stage_bias_table(nc, k, a, table.ap())
    NQ = 3 * T + 3 * P
    with ExitStack() as ctx:
        def sb(name, shape):
            return ctx.enter_context(nc.sbuf_tensor("att_" + name, shape, F32))

        def sem(name):
            return ctx.enter_context(nc.semaphore("att_" + name))
        half = sb("half", [P, 6])
        q2 = sb("q", [P, 2, 3, T])
        kst, vst = sb("k", [P, T]), sb("v", [P, T])
        vtok = sb("vtok", [P, 2, P])
        bias = y[:, 0:12, :].rearrange("p (u e g) v -> p u e g v", u=2, e=2)
        prob = sb("prob", [P, 2, NQ])
        stat = sb("stat", [P, 2, 6])
        diag = sb("diag", [P, 2, 2, P])
        ptok = sb("ptok", [P, 2, 3 * P])
        landed0, landed1 = sem("bias_even"), sem("bias_odd")
        half_landed = sem("half_landed")
        staged, q_up, scored, added = sem("staged"), sem("q_up"), sem("scored"), sem("added")
        maxed, exped, normed = sem("maxed"), sem("exped"), sem("normed")
        v_up, v_down, turned, p_down, o_up, o_down = sem("v_up"), sem("v_down"), sem("turned"), sem("p_down"), \
            sem("o_up"), sem("o_down")
        step = sem("step")
        ident = const(k, "ident")
        TURNS = 4

        with nc.Block() as block:
            @block.sync
            def _(sp):
                sp.dma_start(half[:], a["half_masks"]).then_inc(half_landed, 16)
                sp.wait_ge(half_landed, 16)
        block = ctx.enter_context(nc.Block())

        @block.sync
        def _(sp):
            with sp.Fori(0, TURNS) as t:
                for u in range(2):
                    sp.wait_ge(added, t * 4 + 0)
                    for e in range(2):
                        for g in range(3):
                            src = bass.AP(table, (t * 2 + u) * 768 + (g * 16 * 384 + e * 384),
                                          [[1, P], [1, T]])
                            sp.dma_start(bias[:, u, e, g, :], src).then_inc(landed0 if u == 0 else landed1, 16)

        @block.scalar
        def _(act):
            with act.Fori(0, TURNS) as t:
                for u in range(2):
                    i = t * 2 + u
                    act.wait_ge(o_up, i * 2)
                    act.wait_ge(v_up, i)
                    for e in range(2):
                        nc.scalar.activation(
                            q2[:, e, :, ::-1], y[:, ST_Q:ST_Q + 24, :].rearrange("p (g h) t -> p g h t", g=3)[
                                :, :, bass.ds(i, 1), :].rearrange("p g o t -> p g (o t)"),
                            ACT.Copy, scale=half[:, e:e + 1]).then_inc(q_up, 1)
                    for e in range(2):
                        n = i * 2 + e
                        act.wait_ge(maxed, n + 1)
                        p0 = prob[:, e, 3 * T:]
                        nc.scalar.activation(prob[:, e, 0:3 * T], prob[:, e, 0:3 * T], ACT.Exp,
                                             bias=stat[:, e, 1:2], accum_out=stat[:, e, 3:4])
                        nc.scalar.activation(p0, p0, ACT.Exp, bias=stat[:, e, 0:1],
                                             accum_out=stat[:, e, 2:3]).then_inc(exped, 1)
                    for e in range(2):
                        n = i * 2 + e
                        act.wait_ge(turned, n + 1)
                        nc.scalar.copy(ptok[:, e, :], k.psum[6][:, 0:3 * P]).then_inc(p_down, 1)

        @block.gpsimd
        def _(pool):
            with pool.Fori(0, TURNS) as t:
                for u in range(2):
                    i = t * 2 + u
                    pool.wait_ge(o_up, i * 2)
                    pool.wait_ge(v_up, i)
                    nc.gpsimd.tensor_copy(kst[:].unsqueeze(1), y[:, bass.ds(i + ST_K, 1), :]).then_inc(staged, 1)
                    nc.gpsimd.tensor_copy(vst[:].unsqueeze(1), y[:, bass.ds(i + ST_V, 1), :]).then_inc(staged, 1)

        @block.tensor
        def _(pe):
            with pe.Fori(0, TURNS) as t:
                for u in range(2):
                    i = t * 2 + u
                    pe.wait_ge(staged, i * 2 + 2)
                    for e in range(2):
                        pe.wait_ge(q_up, i * 2 + (e + 1))
                        pe.wait_ge(added, i * 2)
                        for g in range(3):
                            pe.matmul(k.psum[3 * e + g // 2][:, (g % 2) * T:(g % 2 + 1) * T], q2[:, e, g, 0:P],
                                      kst[:], start=True, stop=True)
                        for g in range(3):
                            mm = pe.matmul(k.psum[3 * e + 2][:, g * P:(g + 1) * P], q2[:, e, g, P:2 * P], kst[:, 0:P],
                                           start=True, stop=True)
                        mm.then_inc(scored, 1)
                    pe.wait_ge(o_down, i)
                    for c in range(2):
                        mm = pe.transpose(k.psum[7][:, c * P:(c + 1) * P], vst[:, c * P:(c + 1) * P], ident)
                    mm.then_inc(v_up, 1)
                    for e in range(2):
                        n = i * 2 + e
                        pe.wait_ge(normed, n + 1)
                        if e == 1:
                            pe.wait_ge(p_down, i * 2 + 1)
                        for blk, keys in ((0, 1), (1, 2)):
                            for kb in range(keys):
                                at = (blk + kb) * P
                                for g in range(3):
                                    lo = (3 * T + g * P) if blk == 0 else (g * T + kb * P)
                                    mm = pe.matmul(k.psum[6][:, at:at + P], prob[:, e, lo:lo + P],
                                                   diag[:, e, blk, :], start=(g == 0), stop=(g == 2))
                        mm.then_inc(turned, 1)
                    for e in range(2):
                        n = i * 2 + e
                        pe.wait_ge(p_down, n + 1)
                        pe.wait_ge(v_down, i + 1)
                        out = k.psum[7][e * 64:(e + 1) * 64, :]
                        pe.matmul(out[:, 0:P], vtok[:, 0, e * 64:(e + 1) * 64], ptok[:, e, 0:P], start=True,
                                  stop=True)
                        for kb in range(2):
                            mm = pe.matmul(out[:, P:2 * P], vtok[:, kb, e * 64:(e + 1) * 64],
                                           ptok[:, e, (1 + kb) * P:(2 + kb) * P], start=(kb == 0), stop=(kb == 1))
                        mm.then_inc(o_up, 1)

        @block.vector
        def _(dve):
            with dve.Fori(0, TURNS) as t:
                s = Steps(dve, step, t * 8)
                for u in range(2):
                    i = t * 2 + u
                    dve.wait_ge(landed0 if u == 0 else landed1, t * 96 + 96)
                    for e in range(2):
                        dve.wait_ge(scored, i * 2 + (e + 1))
                        dve.wait_ge(turned, i * 2)
                        pe1 = prob[:, e, 0:3 * T].rearrange("p (g v) -> p g v", g=3)
                        pe0 = prob[:, e, 3 * T:].rearrange("p (g v) -> p g v", g=3)
                        nc.vector.scalar_tensor_tensor(pe1[:, 0:2, :], k.psum[3 * e][:].rearrange(
                            "p (g v) -> p g v", g=2), 0.125, bias[:, u, e, 0:2, :], ALU.mult, ALU.add)
                        nc.vector.scalar_tensor_tensor(pe1[:, 2:3, :], k.psum[3 * e + 1][:, 0:T].unsqueeze(1),
                                                       0.125, bias[:, u, e, 2:3, :], ALU.mult, ALU.add)
                        nc.vector.scalar_tensor_tensor(pe0, k.psum[3 * e + 2][:, 0:3 * P].rearrange(
                            "p (g v) -> p g v", g=3), 0.125, bias[:, u, e, :, P:2 * P], ALU.mult,
                            ALU.add).then_inc(added, 1)
                        dve.wait_ge(added, i * 2 + (e + 1))
                        nc.vector.tensor_reduce(stat[:, e, 4:5], prob[:, e, 3 * T:], AX, ALU.max)
                        s(nc.vector.tensor_reduce(stat[:, e, 5:6], prob[:, e, 0:3 * T], AX, ALU.max))
                        nc.vector.tensor_scalar(stat[:, e, 0:2], stat[:, e, 4:6], -1.0, None,
                                                ALU.mult).then_inc(maxed, 1)
                    dve.wait_ge(v_up, i + 1)
                    nc.vector.tensor_copy(vtok[:].rearrange("p c v -> p (c v)"), k.psum[7][:, 0:T]).then_inc(
                        v_down, 1)
                    for e in range(2):
                        dve.wait_ge(exped, i * 2 + (e + 1))
                        s(nc.vector.reciprocal(stat[:, e, 4:6], stat[:, e, 2:4]))
                        nc.vector.tensor_scalar(diag[:, e, 0, :], const(k, "flip"), stat[:, e, 4:5], None, ALU.mult)
                        nc.vector.tensor_scalar(diag[:, e, 1, :], const(k, "flip"), stat[:, e, 5:6], None,
                                                ALU.mult).then_inc(normed, 1)
                    dve.wait_ge(o_up, i * 2 + 2)
                    nc.vector.tensor_copy(y[:, bass.ds(i + ST_Q, 1), :], k.psum[7][:, 0:T].unsqueeze(
                        1)).then_inc(o_down, 1)
                assert s.n == 8


def stage_out(nc, k, first, rhs, gain):
    groups = 2
    per = -(-len(rhs) // KT)
    with ExitStack() as ctx:
        done = ctx.enter_context(nc.semaphore("out_done"))
        block = ctx.enter_context(nc.Block())

        @block.sync
        def _(sp):
            load_ahead(k, sp, first, groups * per)

        @block.tensor
        def _(pe):
            n = first
            for grp in range(groups):
                for part in range(per):
                    kts = range(min(KT, len(rhs) - part * KT))
                    wait_slot(k, pe, n)
                    for i in range(4):
                        for kt in kts:
                            mm = pe.matmul(k.psum[grp * 4 + i][:, 0:T], ring_tile(k, n, kt, i * P),
                                           rhs[part * KT + kt], start=(part == 0 and kt == 0),
                                           stop=(part == per - 1 and kt == kts[-1]))
                    mm.then_inc(k.slot_used, 1)
                    n += 1

        @block.vector
        def _(dve):
            for grp in range(groups):
                dve.wait_ge(k.slot_used, first + (grp + 1) * per)
                for i in range(4):
                    m = grp * 4 + i
                    nc.vector.scalar_tensor_tensor(k.x[:, m, :], k.psum[m][:, 0:T], gain[:, m:m + 1], k.x[:, m, :],
                                                   ALU.mult, ALU.add)


def stage_ffn(nc, k, h, up, down, gain, which):
    count = FT // 2
    turns = count // RING
    with ExitStack() as lay:
        hid = lay.enter_context(nc.sbuf_tensor(f"ffn_hidden{which}", [P, FT, T], F32))
        with ExitStack() as ctx:
            gate = ctx.enter_context(nc.sbuf_tensor(f"ffn_gate{which}", [P, 2, 512], F32))
            gated = ctx.enter_context(nc.semaphore("ffn_gated"))
            stored = ctx.enter_context(nc.semaphore("ffn_stored"))
            block = ctx.enter_context(nc.Block())

            def over_slots(eng, one):
                with eng.Fori(0, turns) as t:
                    for j in range(RING):
                        one(j, t)
                for j in range(turns * RING, count):
                    one(j, 0)

            @block.sync
            def _(sp):
                load_ahead(k, sp, up, count)

            @block.tensor
            def _(pe):
                rhs = [h[:, kt, :] for kt in range(KT)]

                def one(j, t):
                    pe.wait_ge(stored, t * RING + (j + 1))
                    b = 2 * (j % 2)
                    outs = [k.psum[b + i // 2][:, (i % 2) * T:(i % 2 + 1) * T] for i in range(4)]
                    slot_products(k, pe, up + j, t, rhs, outs).then_inc(k.slot_used, 1)
                over_slots(pe, one)

            @block.scalar
            def _(act):
                def one(j, t):
                    act.wait_ge(k.slot_used, t * RING + (up + j + 1))
                    act.wait_ge(stored, t * RING + (j + 1))
                    nc.scalar.activation(gate[:, j % 2, :], k.psum[2 * (j % 2)][:], ACT.Silu).then_inc(gated, 1)
                over_slots(act, one)

            @block.vector
            def _(dve):
                dve.sem_inc(stored, 2)

                def one(j, t):
                    dve.wait_ge(gated, t * RING + (j + 1))
                    nc.vector.tensor_tensor(hid[:, bass.ds(t * 8 + 2 * j, 2), :].rearrange("p a t -> p (a t)"),
                                            gate[:, j % 2, :], k.psum[2 * (j % 2) + 1][:], ALU.mult).then_inc(
                                                stored, 1)
                over_slots(dve, one)
        stage_out(nc, k, down, [hid[:, i, :] for i in range(FT)], gain)


def stage_conformer(nc, k, h):
    NS = 4
    with ExitStack() as lay:
        u = lay.enter_context(nc.sbuf_tensor("cv_u", [P, KT, T], F32))
        v = lay.enter_context(nc.sbuf_tensor("cv_v", [P, KT, T], F32))
        sq = lay.enter_context(nc.sbuf_tensor("cv_sq", [P, KT, T], F32))
        first = FIRST["pw1"]
        with ExitStack() as ctx:
            sig = ctx.enter_context(nc.sbuf_tensor("cv_sig", [P, KT, T], F32))
            gated = ctx.enter_context(nc.semaphore("cv_gated"))
            block = ctx.enter_context(nc.Block())

            @block.sync
            def _(sp):
                load_ahead(k, sp, first, NS)

            @block.tensor
            def _(pe):
                rhs = [h[:, kt, :] for kt in range(KT)]
                for j in range(NS):
                    outs = [k.psum[2 * j + i // 2][:, (i % 2) * T:(i % 2 + 1) * T] for i in range(4)]
                    slot_products(k, pe, first + j, 0, rhs, outs).then_inc(k.slot_used, 1)

            @block.scalar
            def _(act):
                for j in range(NS):
                    act.wait_ge(k.slot_used, first + j + 1)
                    for i in range(2):
                        m = 2 * j + i
                        nc.scalar.activation(sig[:, m, :], k.psum[2 * j + 1][:, i * T:(i + 1) * T], ACT.Sigmoid,
                                             bias=row(k, "pw1b", 8 + m)).then_inc(gated, 1)

            @block.vector
            def _(dve):
                for m in range(KT):
                    dve.wait_ge(gated, m + 1)
                    nc.vector.scalar_tensor_tensor(u[:, m, :], k.psum[2 * (m // 2)][:, (m % 2) * T:(m % 2 + 1) * T],
                                                   row(k, "pw1b", m), sig[:, m, :], ALU.add, ALU.mult)
        with ExitStack() as ctx:
            step = ctx.enter_context(nc.semaphore("cv_step"))
            block = ctx.enter_context(nc.Block())

            @block.vector
            def _(dve):
                G = 2
                with dve.Fori(0, KT // G) as t:
                    s = Steps(dve, step, t * (TAPS * G))
                    for tap in range(TAPS):
                        for j in range(G):
                            i = t * G + j
                            src, acc = u[:, bass.ds(i, 1), :], v[:, bass.ds(i, 1), :]

                            def w(c):
                                return k.par[:, bass.ds(i * (TAPS + 1) + (PAR["dw"] + c), 1)]
                            if tap == 0:
                                ins = nc.vector.tensor_scalar(acc, src, w(TAPS - 1), w(TAPS), ALU.mult, ALU.add)
                            else:
                                ins = nc.vector.scalar_tensor_tensor(
                                    v[:, bass.ds(i, 1), tap:], u[:, bass.ds(i, 1), :T - tap], w(TAPS - 1 - tap),
                                    v[:, bass.ds(i, 1), tap:], ALU.mult, ALU.add)
                            ins.then_inc(step, 1)
                            s.n += 1
                        dve.wait_ge(step, s.done + s.n)
        with ExitStack() as ctx:
            mean = ctx.enter_context(nc.sbuf_tensor("cv_mean", [P, 2, T], F32))
            meant = ctx.enter_context(nc.semaphore("cv_meant"))
            centred = ctx.enter_context(nc.semaphore("cv_centred"))
            squared = ctx.enter_context(nc.semaphore("cv_squared"))
            summed = ctx.enter_context(nc.semaphore("cv_summed"))
            step = ctx.enter_context(nc.semaphore("cv_lnstep"))
            rooted = ctx.enter_context(nc.semaphore("cv_rooted"))
            scaled = ctx.enter_context(nc.semaphore("cv_scaled"))
            block = ctx.enter_context(nc.Block())

            @block.tensor
            def _(pe):
                for i in range(KT):
                    mm = pe.matmul(k.psum[0][:, 0:T], const(k, "ones"), v[:, i, :], start=(i == 0), stop=(i == 7))
                mm.then_inc(meant, 1)
                pe.wait_ge(squared, 1)
                for i in range(KT):
                    mm = pe.matmul(k.psum[1][:, 0:T], const(k, "ones"), sq[:, i, :], start=(i == 0), stop=(i == 7))
                mm.then_inc(summed, 1)

            @block.vector
            def _(dve):
                s = Steps(dve, step)
                dve.wait_ge(meant, 1)
                s(nc.vector.tensor_scalar(mean[:, 0, :], k.psum[0][:, 0:T], 1.0 / D, None, ALU.mult))
                nc.vector.tensor_tensor(v[:], v[:], mean[:, 0:1, :].to_broadcast([P, KT, T]),
                                        ALU.subtract).then_inc(centred, 1)
                dve.wait_ge(summed, 1)
                s(nc.vector.tensor_scalar(mean[:, 1, :], k.psum[1][:, 0:T], 1.0 / D, EPS, ALU.mult, ALU.add))
                dve.wait_ge(rooted, 1)
                s(nc.vector.reciprocal(mean[:, 1, :], mean[:, 1, :]))
                nc.vector.tensor_tensor(v[:], v[:], mean[:, 1:2, :].to_broadcast([P, KT, T]),
                                        ALU.mult).then_inc(scaled, 1)

            @block.scalar
            def _(act):
                act.wait_ge(centred, 1)
                nc.scalar.activation(sq[:], v[:], ACT.Square).then_inc(squared, 1)
                act.wait_ge(step, 2)
                nc.scalar.activation(mean[:, 1, :], mean[:, 1, :], ACT.Sqrt).then_inc(rooted, 1)
                act.wait_ge(scaled, 1)
                for i in range(KT):
                    nc.scalar.activation(u[:, i, :], v[:, i, :], ACT.Silu, bias=row(k, "lnb", i),
                                         scale=row(k, "lng", i))
        first = FIRST["pw2"]
        with ExitStack() as ctx:
            biased = ctx.enter_context(nc.semaphore("cv_biased"))
            block = ctx.enter_context(nc.Block())

            @block.sync
            def _(sp):
                load_ahead(k, sp, first, 2)

            @block.tensor
            def _(pe):
                rhs = [u[:, kt, :] for kt in range(KT)]
                for j in range(2):
                    outs = [k.psum[4 * j + i][:, 0:T] for i in range(4)]
                    slot_products(k, pe, first + j, 0, rhs, outs).then_inc(k.slot_used, 1)

            @block.scalar
            def _(act):
                for m in range(KT):
                    act.wait_ge(k.slot_used, first + m // 4 + 1)
                    nc.scalar.activation(v[:, m, :], k.psum[m][:, 0:T], ACT.Identity,
                                         bias=row(k, "pw2b", m)).then_inc(biased, 1)

            @block.vector
            def _(dve):
                for m in range(KT):
                    dve.wait_ge(biased, m + 1)
                    nc.vector.scalar_tensor_tensor(k.x[:, m, :], v[:, m, :], k.mod[:, 64 + m:65 + m], k.x[:, m, :],
                                                   ALU.mult, ALU.add)


GN_EPS = 64e-5
CH = 128
NCH = 2 * T // CH
SH, SC, GT = 0, 8, 16


def mod2(k, layer, part, ctx=False):
    c = 48 * ctx + 24 * layer + part
    return k.mod[:, c:c + 8]


def stage_shift(nc, k, h, xx):
    hs, xs = (b[:].rearrange("p k (s t) -> p (k s) t", s=2) for b in (h, xx))
    with ExitStack() as ctx:
        step = ctx.enter_context(nc.semaphore("shift_step"))
        block = ctx.enter_context(nc.Block())

        @block.vector
        def _(dve):
            s = Steps(dve, step)
            s(nc.vector.tensor_scalar(xs, hs, -1.0, None, ALU.mult))
            s(nc.vector.scalar_tensor_tensor(xs[:, :, 1:], hs[:, :, :T - 1], 0.5, xs[:, :, 1:], ALU.mult, ALU.add))
            s(nc.vector.scalar_tensor_tensor(xs[:, :, :T - 1], hs[:, :, 1:], 0.5, xs[:, :, :T - 1], ALU.mult,
                                             ALU.add))


def stage_rwkv_in(nc, k, a, h, xx, lora, kept):
    R, K, V, G, W, A = range(6)
    first = FIRST["rkvg"]
    with ExitStack() as ctx:
        l0 = ctx.enter_context(nc.sbuf_tensor("mixed0", [P, KT, 512], F32))
        l1 = ctx.enter_context(nc.sbuf_tensor("mixed1", [P, KT, 512], F32))
        w1 = ctx.enter_context(nc.sbuf_tensor("lora_in_sb", [P, KT, 256], F32))
        outb = ctx.enter_context(nc.sbuf_tensor("proj_out", [P, 2, 4, 512], F32))
        w1_landed = ctx.enter_context(nc.semaphore("lora_in_landed"))
        mixed = ctx.enter_context(nc.semaphore("mixed"))
        lora_up = ctx.enter_context(nc.semaphore("lora_up"))
        evac = ctx.enter_context(nc.semaphore("proj_evac"))
        kept0 = ctx.enter_context(nc.semaphore("proj_kept_even"))
        kept1 = ctx.enter_context(nc.semaphore("proj_kept_odd"))
        block = ctx.enter_context(nc.Block())
        order = [(W, l0), (A, l1), (R, l0), (K, l1), (V, l0), (G, xx)]

        @block.sync
        def _(sp):
            sp.dma_start(w1[:], a["lora_in"]).then_inc(w1_landed, 16)
            load_ahead(k, sp, first, 8)

        @block.vector
        def _(dve):
            for n, (j, buf) in enumerate(order):
                if n in (2, 3):
                    dve.wait_ge(lora_up, n - 1)
                if n == 4:
                    dve.wait_ge(k.slot_used, first + 2)
                if n == 5:
                    dve.wait_ge(mixed, KT * n)
                for i in range(KT):
                    nc.vector.scalar_tensor_tensor(buf[:, i, :], xx[:, i, :], row(k, "mu", 8 * j + i), h[:, i, :],
                                                   ALU.mult, ALU.add).then_inc(mixed, 1)

        @block.tensor
        def _(pe):
            pe.wait_ge(w1_landed, 16)
            for n in range(2):
                pe.wait_ge(mixed, KT * (n + 1))
                for kt in range(KT):
                    mm = pe.matmul(k.psum[n][:], w1[:, kt, n * P:(n + 1) * P], order[n][1][:, kt, :],
                                   start=(kt == 0), stop=(kt == KT - 1))
                mm.then_inc(lora_up, 1)
            for j in range(8):
                n = 2 + j // 2
                pe.wait_ge(mixed, KT * (n + 1))
                if j >= 2:
                    pe.wait_ge(evac, 2 + 4 * (j - 1))
                elif j == 0:
                    pe.wait_ge(evac, 2)
                outs = [k.psum[4 * (j % 2) + i][:] for i in range(4)]
                rhs = [order[n][1][:, kt, :] for kt in range(KT)]
                slot_products(k, pe, first + j, 0, rhs, outs).then_inc(k.slot_used, 1)

        @block.scalar
        def _(act):
            act.wait_ge(lora_up, 1)
            nc.scalar.activation(lora[:, 0, :], k.psum[0][:], ACT.Tanh).then_inc(evac, 1)
            act.wait_ge(lora_up, 2)
            nc.scalar.copy(lora[:, 1, :], k.psum[1][:]).then_inc(evac, 1)
            for j in range(8):
                act.wait_ge(k.slot_used, first + j + 1)
                if j >= 2:
                    act.wait_ge((kept0, kept1)[j % 2], 16 * (j // 2))
                for i in range(4):
                    nc.scalar.copy(outb[:, j % 2, i, :], k.psum[4 * (j % 2) + i][:]).then_inc(evac, 1)

        @block.gpsimd
        def _(pool):
            for j in range(8):
                pool.wait_ge(evac, 2 + 4 * (j + 1))
                pool.dma_start(kept[4 * (j % 2):4 * (j % 2) + 4, :, j // 2, :].rearrange("t p n -> p t n"),
                               outb[:, j % 2, :, :]).then_inc((kept0, kept1)[j % 2], 16)
            pool.wait_ge(kept0, 64)
            pool.wait_ge(kept1, 64)


class Track:

    def __init__(self, sem, names):
        self.sem, self.names, self.n = sem, names, 0
        self.at = {name: i + 1 for i, name in enumerate(names)}
        assert len(self.at) == len(names)

    def start(self, eng):
        eng.sem_inc(self.sem, len(self.names))

    def mark(self, ins, name):
        assert self.names[self.n] == name, (self.names[self.n], name)
        self.n += 1
        ins.then_inc(self.sem, 1)

    def wait(self, eng, turn, name, before=0, apart=False):
        eng.wait_ge(self.sem, turn * len(self.names) + (self.at[name] + (1 - before) * len(self.names)))
        if apart:
            eng.nop(nofuse=True)


def rwkv_milestones():
    m0, m1 = "ABs", "MT0"
    dve = ["one_ka", "kk_raw", "kk_sq", "kk_max", "kk_rec", "kk"]
    act = ["v_tok", "norm", "silu_g"]
    pe = ["v_up", "sq_up"]
    pool = ["staged"]
    for d in range(2):
        pool += [f"eye{d}{e}" for e in range(2)]
        pe += [f"lora{d}", f"b_up{d}", f"k_up{d}"]
        act += [f"sig_w{d}", f"sig_a{d}", f"eh{d}", f"ee{d}", f"ei{d}", f"en{d}", f"b_tok{d}", f"k_tok{d}"]
        dve += [f"{n}{d}" for n in ("lw", "cum", "half", "mid", "dif", "blend", "kd", "b", "ksum", "at", "rt",
                                    "bt", "kt", "E0", "E1", "E2", "z_init")]
        for e in range(2):
            pe += [f"g{d}{e}{m}" for m in range(5)]
            dve += [f"m{d}{e}{m}" for m in range(5)] + [f"inv{d}{e}0"]
        for lv in range(1, 7):
            pe += [f"W{d}{lv}{e}" for e in range(2)]
            act += [f"Wc{d}{lv}{e}" for e in range(2)]
            for e in range(2):
                pe += [f"Pt{d}{lv}{e}"] + ([f"Pm{d}{lv}{e}"] if lv < 6 else [])
                dve += [f"t{d}{lv}{e}"] + ([f"inv{d}{e}{lv}"] if lv < 6 else [])
        for q in range(NCH):
            pe += [f"X{d}{q}0", f"X{d}{q}1", f"SA{d}{q}"] + ([f"U{d}{q}"] if q < 3 else []) + [f"Y{d}{q}"]
            act += [f"xs{d}{q}"]
            dve += ([f"ze{d}{q}"] if q < 3 else []) + [f"xs{d}{q}", f"sa{d}{q}"] + \
                ([f"z{d}{q}"] if q < 3 else []) + [f"y{d}{q}0", f"y{d}{q}1"]
    dve += ["rk", "mean", "xc", "var", "y_rec", "yn", "ynl", "bon", "sum", "o"]
    act += ["y_sq", "y_root"]
    pe += ["mean", "bon", "var"]
    return dve, act, pe, pool


def stage_rwkv_scan(nc, k, a, lora, kept, o):
    dve_names, act_names, pe_names, pool_names = rwkv_milestones()
    HALF_E = -math.exp(-0.5)
    with ExitStack() as ctx:
        def sb(name, shape, dt=F32):
            return ctx.enter_context(nc.sbuf_tensor("rw_" + name, shape, dt))

        def sem(name):
            return ctx.enter_context(nc.semaphore("rw_" + name))
        lora_out = sb("lora_out", [P, 2, D])
        tri = sb("tri", [P, 4, P])
        lvl = sb("lvl", [P, 2, 7, P], U8)
        starts = sb("starts", [P, 512])
        pre = sb("pre", [P, 4, 512])
        tin = sb("tin", [P, 4, 512])
        w2 = sb("w2", [P, 2, P])
        rp = sb("rp", [P, 9])
        omka = sb("omka", [P, 1])
        kk, sq = sb("kk", [P, 512]), sb("sq", [P, 512])
        lw, av = sb("lw", [P, 512]), sb("av", [P, 512])
        mid, dif = sb("mid", [P, 512]), sb("dif", [P, 512])
        half, eh, dec = sb("half", [P, NCH]), sb("eh", [P, NCH]), sb("dec", [P, NCH])
        kd, bb, ksum = sb("kd", [P, 512]), sb("bb", [P, 512]), sb("ksum", [P, 512])
        ee, ei, en = sb("ee", [P, 512]), sb("ei", [P, 512]), sb("en", [P, 512])
        at, rt, bt, kt_ = sb("at", [P, 512]), sb("rt", [P, 512]), sb("bt", [P, 512]), sb("kt", [P, 512])
        btok, ktok, vtok = sb("btok", [P, NCH, P]), sb("ktok", [P, NCH, P]), sb("vtok", [P, NCH, P])
        AB, AKT, RBT, RKT, M, MT, Wb = (sb(n, [P, 2, NCH, P]) for n in ("AB", "AKT", "RBT", "RKT", "M", "MT", "W"))
        xs, sas = sb("xs", [P, P]), sb("sas", [P, P])
        z, ze = sb("z", [P, 64]), sb("ze", [P, 64])
        yf = sb("yf", [P, 512])
        consts, pre_landed = sem("consts"), sem("pre_landed")
        dv, ac, pt, pl = (Track(sem(n), names) for n, names in (
            ("dve_done", dve_names), ("act_done", act_names), ("pe_done", pe_names), ("pool_done", pool_names)))
        ident, headones = const(k, "ident"), const(k, "headones")
        W0, A0, KK_, KA, RK_, LG, LB = 0, 2, 4, 5, 6, 7, 8
        rr, kx, vv, gg = (tin[:, i, :] for i in range(4))
        ORDER = [[0, 1, 2, 3], [1, 0, 3, 2]]
        b = k.psum

        def chunks(ap):
            return ap.rearrange("p (c t) -> p c t", c=NCH)

        def head(ap, e, c):
            return ap[e * 64:(e + 1) * 64, c * CH:(c + 1) * CH]

        def bank(i):
            return k.psum[i][:].rearrange("p (c t) -> p c t", c=NCH)

        wide = pre[:].rearrange("p j n -> p (j n)")[:, 0:14 * P].bitcast(I32)
        with nc.Block() as block:
            @block.sync
            def _(sp):
                sp.dma_start(lora_out[:], a["lora_out"]).then_inc(consts, 16)
                sp.dma_start(tri[:].rearrange("p m f -> p (m f)"), a["tri_masks"]).then_inc(consts, 16)
                sp.dma_start(wide, a["level_masks"]).then_inc(consts, 16)
                sp.dma_start(starts[:], a["chunk_starts"]).then_inc(consts, 16)
                sp.wait_ge(consts, 64)

            @block.vector
            def _(dve):
                dve.wait_ge(consts, 64)
                nc.vector.tensor_copy(lvl[:].rearrange("p u l f -> p (u l f)"), wide)
        block = ctx.enter_context(nc.Block())

        @block.sync
        def _(sp):
            with sp.Fori(0, KT) as t:
                pl.wait(sp, t, "staged", before=1)
                sp.dma_start(pre[:].unsqueeze(1), kept[bass.ds(t, 1), :, :, :].rearrange(
                    "o p j n -> p o j n")).then_inc(pre_landed, 16)

        @block.gpsimd
        def _(pool):
            pl.start(pool)
            with pool.Fori(0, KT) as t:
                pool.wait_ge(pre_landed, t * 16 + 16)
                dv.wait(pool, t, "o", before=1, apart=True)
                nc.gpsimd.tensor_copy(tin[:], pre[:])
                nc.gpsimd.tensor_copy(w2[:], lora_out[:, :, bass.ds(t * P, P)])
                pl.mark(nc.gpsimd.tensor_copy(rp[:], k.par[:, bass.ds(t * 9 + PAR["rw"], 9)]), "staged")
                for d in range(2):
                    for e in range(2):
                        if d == 1:
                            pt.wait(pool, t, "SA03", apart=True)
                        src = ident.unsqueeze(1).to_broadcast([P, NCH, P])
                        nc.gpsimd.tensor_copy(M[:, e, :, :], src)
                        pl.mark(nc.gpsimd.tensor_copy(MT[:, e, :, :], src), f"eye{d}{e}")

        @block.scalar
        def _(act):
            ac.start(act)
            with act.Fori(0, KT) as t:
                pt.wait(act, t, "v_up")
                ac.mark(nc.scalar.copy(vtok[:].rearrange("p c t -> p (c t)"), b[0][:]), "v_tok")
                pt.wait(act, t, "sq_up")
                ac.mark(nc.scalar.activation(sq[:], b[1][:], ACT.Sqrt), "norm")
                ac.mark(nc.scalar.activation(gg, gg, ACT.Silu), "silu_g")
                for d in range(2):
                    pt.wait(act, t, f"lora{d}")
                    dv.wait(act, t, "kt0" if d else "kt1", before=1 - d)
                    ac.mark(nc.scalar.activation(lw[:], b[2][:], ACT.Sigmoid, bias=rp[:, W0 + d:W0 + d + 1]),
                            f"sig_w{d}")
                    ac.mark(nc.scalar.activation(av[:], b[3][:], ACT.Sigmoid, bias=rp[:, A0 + d:A0 + d + 1]),
                            f"sig_a{d}")
                    dv.wait(act, t, f"half{d}")
                    ac.mark(nc.scalar.activation(eh[:], half[:], ACT.Exp), f"eh{d}")
                    dv.wait(act, t, f"dif{d}")
                    before, upto, sign = (dif, mid, 1.0) if d == 0 else (mid, dif, -1.0)
                    ac.mark(nc.scalar.activation(ee[:], before[:], ACT.Exp, scale=sign), f"ee{d}")
                    ac.mark(nc.scalar.activation(ei[:], upto[:], ACT.Exp, scale=sign), f"ei{d}")
                    ac.mark(nc.scalar.activation(en[:], upto[:], ACT.Exp, scale=-sign), f"en{d}")
                    pt.wait(act, t, f"b_up{d}")
                    ac.mark(nc.scalar.copy(btok[:].rearrange("p c t -> p (c t)"), b[0][:]), f"b_tok{d}")
                    pt.wait(act, t, f"k_up{d}")
                    ac.mark(nc.scalar.copy(ktok[:].rearrange("p c t -> p (c t)"), b[1][:]), f"k_tok{d}")
                    for lv in range(1, 7):
                        for e in range(2):
                            pt.wait(act, t, f"W{d}{lv}{e}")
                            ac.mark(nc.scalar.copy(Wb[:, e, :, :].rearrange("p c t -> p (c t)"), b[e][:]),
                                    f"Wc{d}{lv}{e}")
                    for q in range(NCH):
                        pt.wait(act, t, f"X{d}{q}1")
                        ac.mark(nc.scalar.copy(xs[:, 64:], b[1][:, 0:64]), f"xs{d}{q}")
                dv.wait(act, t, "xc")
                ac.mark(nc.scalar.activation(sq[:], yf[:], ACT.Square), "y_sq")
                dv.wait(act, t, "var")
                ac.mark(nc.scalar.activation(mid[:], mid[:], ACT.Sqrt), "y_root")

        @block.tensor
        def _(pe):
            pt.start(pe)
            with pe.Fori(0, KT) as t:
                pl.wait(pe, t, "staged")
                dv.wait(pe, t, "o", before=1)
                for c in range(NCH):
                    mm = pe.transpose(b[0][:, c * CH:(c + 1) * CH], vv[:, c * CH:(c + 1) * CH], ident)
                pt.mark(mm, "v_up")
                dv.wait(pe, t, "kk_sq")
                pt.mark(pe.matmul(b[1][:], headones, sq[:], start=True, stop=True), "sq_up")
                for d in range(2):
                    if d == 1:
                        dv.wait(pe, t, "y031")
                    rows = slice(d * 64, d * 64 + 64)
                    pe.matmul(b[2][:], w2[rows, 0, :], lora[rows, 0, :], start=True, stop=True)
                    pt.mark(pe.matmul(b[3][:], w2[rows, 1, :], lora[rows, 1, :], start=True, stop=True), f"lora{d}")
                    if d == 0:
                        ac.wait(pe, t, "norm")
                    for src, bk, dn, up in ((bt, 0, "bt", "b_up"), (kt_, 1, "kt", "k_up")):
                        dv.wait(pe, t, f"{dn}{d}")
                        for c in range(NCH):
                            mm = pe.transpose(b[bk][:, c * CH:(c + 1) * CH], src[:, c * CH:(c + 1) * CH], ident)
                        pt.mark(mm, f"{up}{d}")
                    for e in range(2):
                        for m, (lhs, rhs) in enumerate(((at, bt), (bt, at), (kt_, at), (bt, rt), (kt_, rt))):
                            s = e * 5 + m
                            if s >= 6:
                                dv.wait(pe, t, f"m{d}{(s - 6) // 5}{(s - 6) % 5}")
                            for c in range(NCH):
                                mm = pe.matmul(b[2 + s % 6][:, c * CH:(c + 1) * CH], head(lhs, e, c),
                                               head(rhs, e, c), start=True, stop=True)
                            pt.mark(mm, f"g{d}{e}{m}")
                    ac.wait(pe, t, f"k_tok{d}")
                    for lv in range(1, 7):
                        for e in range(2):
                            dv.wait(pe, t, f"inv{d}{e}{lv - 1}")
                            for c in range(NCH):
                                mm = pe.matmul(b[e][:, c * CH:(c + 1) * CH], AB[:, e, c, :], MT[:, e, c, :],
                                               start=True, stop=True)
                            pt.mark(mm, f"W{d}{lv}{e}")
                        for e in range(2):
                            ac.wait(pe, t, f"Wc{d}{lv}{e}")
                            if lv == 1:
                                dv.wait(pe, t, f"inv{d}10")
                            for c in range(NCH):
                                mm = pe.matmul(b[2 + e][:, c * CH:(c + 1) * CH], M[:, e, c, :], Wb[:, e, c, :],
                                               start=True, stop=True)
                            pt.mark(mm, f"Pt{d}{lv}{e}")
                            if lv < 6:
                                for c in range(NCH):
                                    mm = pe.matmul(b[4 + e][:, c * CH:(c + 1) * CH], Wb[:, e, c, :],
                                                   M[:, e, c, :], start=True, stop=True)
                                pt.mark(mm, f"Pm{d}{lv}{e}")
                    for q, c in enumerate(ORDER[d]):
                        yb = [b[4 + 2 * (q % 2) + e][e * 64:(e + 1) * 64, 0:CH] for e in range(2)]
                        hs = [slice(e * 64, e * 64 + 64) for e in range(2)]
                        dv.wait(pe, t, f"z{d}{q - 1}" if q else f"z_init{d}")
                        if q == 0:
                            dv.wait(pe, t, f"t{d}61")
                        for e in range(2):
                            pe.matmul(b[e][:, 0:64], head(at, e, c), z[hs[e], :], start=True, stop=False)
                            pt.mark(pe.matmul(b[e][:, 0:64], AKT[:, e, c, :], vtok[:, c, hs[e]], start=False,
                                              stop=True), f"X{d}{q}{e}")
                        if q >= 2:
                            dv.wait(pe, t, f"y{d}{q - 2}1", apart=True)
                        for e in range(2):
                            pe.matmul(yb[e], z[hs[e], :], head(rt, e, c), start=True, stop=False)
                            pe.matmul(yb[e], vtok[:, c, hs[e]], RKT[:, e, c, :], start=False, stop=False)
                            if q < 3:
                                pe.matmul(b[3][hs[e], 0:64], ktok[:, c, hs[e]], vtok[:, c, hs[e]], start=True,
                                          stop=False)
                        for e in range(2):
                            (ac if e else dv).wait(pe, t, f"xs{d}{q}")
                            mm = pe.matmul(b[2][:, hs[e]], MT[:, e, c, :], xs[:, hs[e]], start=True, stop=True)
                        pt.mark(mm, f"SA{d}{q}")
                        dv.wait(pe, t, f"sa{d}{q}")
                        if q < 3:
                            for e in range(2):
                                mm = pe.matmul(b[3][hs[e], 0:64], btok[:, c, hs[e]], sas[:, hs[e]], start=False,
                                               stop=True)
                            pt.mark(mm, f"U{d}{q}")
                        for e in range(2):
                            mm = pe.matmul(yb[e], sas[:, hs[e]], RBT[:, e, c, :], start=False, stop=True)
                        pt.mark(mm, f"Y{d}{q}")
                dv.wait(pe, t, "y131")
                pt.mark(pe.matmul(b[0][:], headones, yf[:], start=True, stop=True), "mean")
                dv.wait(pe, t, "rk")
                pt.mark(pe.matmul(b[2][:], headones, ksum[:], start=True, stop=True), "bon")
                ac.wait(pe, t, "y_sq")
                pt.mark(pe.matmul(b[1][:], headones, sq[:], start=True, stop=True), "var")

        @block.vector
        def _(dve):
            v = nc.vector
            dv.start(dve)
            with dve.Fori(0, KT) as t:
                def do(ins, name, wait=True):
                    dv.mark(ins, name)
                    if wait:
                        dv.wait(dve, t, name)
                pl.wait(dve, t, "staged")
                do(v.tensor_scalar(omka[:], rp[:, KA:KA + 1], -1.0, 1.0, ALU.mult, ALU.add), "one_ka", False)
                do(v.tensor_scalar(kk[:], kx, rp[:, KK_:KK_ + 1], None, ALU.mult), "kk_raw")
                do(v.tensor_tensor(sq[:], kk[:], kk[:], ALU.mult), "kk_sq", False)
                ac.wait(dve, t, "norm")
                do(v.tensor_scalar(sq[:], sq[:], 1e-12, None, ALU.max), "kk_max")
                do(v.reciprocal(sq[:], sq[:]), "kk_rec")
                do(v.tensor_tensor(kk[:], kk[:], sq[:], ALU.mult), "kk")
                for d in range(2):
                    ac.wait(dve, t, f"sig_w{d}")
                    do(v.tensor_scalar(lw[:], lw[:], HALF_E, None, ALU.mult), f"lw{d}")
                    do(v.tensor_tensor_scan(mid[:], starts[:], lw[:], 0.0, ALU.mult, ALU.add), f"cum{d}")
                    do(v.tensor_scalar(half[:], chunks(mid[:])[:, :, CH - 1], 0.5, None, ALU.mult), f"half{d}")
                    do(v.tensor_tensor(chunks(mid[:]), chunks(mid[:]), half[:].unsqueeze(2).to_broadcast(
                        [P, NCH, CH]), ALU.subtract), f"mid{d}")
                    do(v.tensor_tensor(dif[:], mid[:], lw[:], ALU.subtract), f"dif{d}", False)
                    ac.wait(dve, t, f"sig_a{d}")
                    do(v.tensor_scalar(kd[:], av[:], rp[:, KA:KA + 1], omka[:, 0:1], ALU.mult, ALU.add), f"blend{d}")
                    do(v.tensor_tensor(kd[:], kx, kd[:], ALU.mult), f"kd{d}")
                    do(v.tensor_tensor(bb[:], kk[:], av[:], ALU.mult), f"b{d}")
                    if d == 0:
                        do(v.tensor_copy(ksum[:], kd[:]), f"ksum{d}", False)
                    else:
                        do(v.tensor_tensor(ksum[:], ksum[:], kd[:], ALU.add), f"ksum{d}", False)
                        pt.wait(dve, t, "Y03")
                    ac.wait(dve, t, f"en{d}")
                    do(v.scalar_tensor_tensor(at[:], kk[:], -1.0, ee[:], ALU.mult, ALU.mult), f"at{d}", False)
                    do(v.tensor_tensor(rt[:], rr, ei[:], ALU.mult), f"rt{d}", False)
                    do(v.tensor_tensor(bt[:], bb[:], en[:], ALU.mult), f"bt{d}", False)
                    do(v.tensor_tensor(kt_[:], kd[:], en[:], ALU.mult), f"kt{d}", False)
                    for q in range(3):
                        c0, c1 = ORDER[d][q:q + 2]
                        do(v.tensor_tensor(dec[:, q:q + 1], eh[:, c0:c0 + 1], eh[:, c1:c1 + 1], ALU.mult),
                           f"E{q}{d}", False)
                    do(v.memset(z[:], 0.0), f"z_init{d}", False)
                    up, lo = (0, 1) if d == 0 else (1, 0)
                    strict, incl, ab = (0, 1, 2) if d == 0 else (2, 3, 0)
                    for e in range(2):
                        for m, (dst, mask) in enumerate(((AB, ab), (MT, None), (AKT, strict), (RBT, incl),
                                                         (RKT, incl))):
                            pt.wait(dve, t, f"g{d}{e}{m}")
                            src = bank(2 + (e * 5 + m) % 6)
                            if mask is None:
                                pl.wait(dve, t, f"eye{d}{e}", apart=True)
                                ins = v.copy_predicated(MT[:, e, :, :], lvl[:, up, 0:1, :].to_broadcast(
                                    [P, NCH, P]), src)
                            else:
                                ins = v.tensor_tensor(dst[:, e, :, :], src, tri[:, mask:mask + 1, :].to_broadcast(
                                    [P, NCH, P]), ALU.mult)
                            do(ins, f"m{d}{e}{m}", False)
                        dv.wait(dve, t, f"m{d}{e}4", apart=True)
                        do(v.copy_predicated(M[:, e, :, :], lvl[:, lo, 0:1, :].to_broadcast([P, NCH, P]),
                                             AB[:, e, :, :]), f"inv{d}{e}0", False)
                    for lv in range(1, 7):
                        for e in range(2):
                            pt.wait(dve, t, f"Pt{d}{lv}{e}", apart=True)
                            do(v.copy_predicated(MT[:, e, :, :], lvl[:, up, lv:lv + 1, :].to_broadcast(
                                [P, NCH, P]), bank(2 + e)), f"t{d}{lv}{e}", False)
                            if lv < 6:
                                pt.wait(dve, t, f"Pm{d}{lv}{e}", apart=True)
                                do(v.copy_predicated(M[:, e, :, :], lvl[:, lo, lv:lv + 1, :].to_broadcast(
                                    [P, NCH, P]), bank(4 + e)), f"inv{d}{e}{lv}", False)
                    for q, c in enumerate(ORDER[d]):
                        if q < 3:
                            dv.wait(dve, t, f"z{d}{q - 1}" if q else f"z_init{d}")
                            do(v.tensor_scalar(ze[:], z[:], dec[:, q:q + 1], None, ALU.mult), f"ze{d}{q}", False)
                        pt.wait(dve, t, f"X{d}{q}0")
                        do(v.tensor_copy(xs[:, 0:64], b[0][:, 0:64]), f"xs{d}{q}", False)
                        pt.wait(dve, t, f"SA{d}{q}")
                        do(v.tensor_copy(sas[:], b[2][:, 0:P]), f"sa{d}{q}", False)
                        if q < 3:
                            pt.wait(dve, t, f"U{d}{q}")
                            dv.wait(dve, t, f"ze{d}{q}")
                            do(v.scalar_tensor_tensor(z[:], b[3][:, 0:64], dec[:, q:q + 1], ze[:], ALU.mult,
                                                      ALU.add), f"z{d}{q}", False)
                        pt.wait(dve, t, f"Y{d}{q}")
                        for e in range(2):
                            hsl = slice(e * 64, e * 64 + 64)
                            src, dst = b[4 + 2 * (q % 2) + e][hsl, 0:CH], yf[hsl, c * CH:(c + 1) * CH]
                            if d == 0:
                                do(v.tensor_copy(dst, src), f"y{d}{q}{e}", False)
                            else:
                                do(v.tensor_tensor(dst, src, dst, ALU.add), f"y{d}{q}{e}", False)
                do(v.scalar_tensor_tensor(ksum[:], rr, rp[:, RK_:RK_ + 1], ksum[:], ALU.mult, ALU.mult), "rk", False)
                pt.wait(dve, t, "mean")
                do(v.tensor_scalar(mid[:], b[0][:], 1.0 / 64, None, ALU.mult), "mean")
                do(v.tensor_tensor(yf[:], yf[:], mid[:], ALU.subtract), "xc")
                pt.wait(dve, t, "var")
                do(v.tensor_scalar(mid[:], b[1][:], 1.0 / 64, GN_EPS, ALU.mult, ALU.add), "var", False)
                ac.wait(dve, t, "y_root")
                do(v.reciprocal(mid[:], mid[:]), "y_rec")
                do(v.tensor_tensor(yf[:], yf[:], mid[:], ALU.mult), "yn")
                do(v.tensor_scalar(yf[:], yf[:], rp[:, LG:LG + 1], rp[:, LB:LB + 1], ALU.mult, ALU.add), "ynl", False)
                pt.wait(dve, t, "bon")
                do(v.tensor_tensor(dif[:], b[2][:], vv, ALU.mult), "bon")
                do(v.tensor_tensor(yf[:], yf[:], dif[:], ALU.add), "sum")
                do(v.tensor_tensor(o[:, bass.ds(t, 1), :], yf[:].unsqueeze(1), gg.unsqueeze(1), ALU.mult), "o",
                   False)


def stage_rwkv_out(nc, k, o):
    first = FIRST["rwout"]
    with ExitStack() as ctx:
        block = ctx.enter_context(nc.Block())

        @block.sync
        def _(sp):
            load_ahead(k, sp, first, 2)

        @block.tensor
        def _(pe):
            rhs = [o[:, kt, :] for kt in range(KT)]
            for j in range(2):
                slot_products(k, pe, first + j, 0, rhs, [k.psum[4 * j + i][:] for i in range(4)]).then_inc(
                    k.slot_used, 1)

        @block.vector
        def _(dve):
            for m in range(KT):
                dve.wait_ge(k.slot_used, first + m // 4 + 1)
                for dst, cols, c in ((k.ctx, slice(0, T), True), (k.x, slice(T, 2 * T), False)):
                    nc.vector.scalar_tensor_tensor(dst[:, m, :], k.psum[m][:, cols],
                                                   mod2(k, 0, GT, c)[:, m:m + 1], dst[:, m, :], ALU.mult, ALU.add)


def second_block(nc, k, a):
    stage_mod(nc, k, (FIRST["mod2"], 12), [k.cs[:, 8:16], k.cs[:, 16:24]], [k.mod[:, 0:48], k.mod[:, 48:96]],
              row(k, "modb0", 0, 48))
    stage_scales(nc, k, [(k.gain[:, 8 * i:8 * i + 8], mod2(k, i // 2, SC, i % 2 == 1),
                          row(k, f"norm2_{i // 2}", 0, 8)) for i in range(4)])
    kept = nc.dram_tensor("rwkv_projections", (KT, P, 4, 512), F32).ap()
    with ExitStack() as lay:
        lora = lay.enter_context(nc.sbuf_tensor("lora", [P, 2, 512], F32))
        with ExitStack() as inner:
            h = inner.enter_context(nc.sbuf_tensor("h_both", [P, KT, 512], F32))
            stage_norm(nc, k, k.ctx[:], KT, T, k.gain[:, 8:16], mod2(k, 0, SH, True), h[:, :, 0:T], None, "rwc")
            stage_norm(nc, k, k.x[:], KT, T, k.gain[:, 0:8], mod2(k, 0, SH), h[:, :, T:2 * T], None, "rwx")
            xx = inner.enter_context(nc.sbuf_tensor("shifted", [P, KT, 512], F32))
            stage_shift(nc, k, h, xx)
            stage_rwkv_in(nc, k, a, h, xx, lora, kept)
        o = lay.enter_context(nc.sbuf_tensor("rwkv_o", [P, KT, 512], F32))
        stage_rwkv_scan(nc, k, a, lora, kept, o)
        stage_rwkv_out(nc, k, o)
    stage_mla(nc, k, a)
    stage_norm(nc, k, k.x[:], KT, T, row(k, "final2", 0, 8), None, k.x, None, "final2")


def stage_mla_in(nc, k, a, h, rope, qc, kvc, kpe, gate):
    first = FIRST["mlain"]
    X = slice(T, 2 * T)
    with ExitStack() as ctx:
        turned = ctx.enter_context(nc.sbuf_tensor("kpe_turned", [P, T], F32))
        act_evac = ctx.enter_context(nc.semaphore("mlain_act_evac"))
        step = ctx.enter_context(nc.semaphore("mlain_step"))
        b = k.psum
        block = ctx.enter_context(nc.Block())

        @block.sync
        def _(sp):
            load_ahead(k, sp, first, 4)

        @block.tensor
        def _(pe):
            both, x_only = [h[:, kt, :] for kt in range(KT)], [h[:, kt, X] for kt in range(KT)]

            def tile(n, i, out, rhs):
                for kt in range(KT):
                    mm = pe.matmul(out, ring_tile(k, n, kt, i * P), rhs[kt], start=(kt == 0), stop=(kt == KT - 1))
                return mm
            wait_slot(k, pe, first)
            for i in range(3):
                tile(first, i, b[i // 2][:, (i % 2) * T:(i % 2 + 1) * T], x_only)
            tile(first, 3, b[2][:], both).then_inc(k.slot_used, 1)
            wait_slot(k, pe, first + 1)
            for i in range(3):
                mm = tile(first + 1, i, b[3 + i][:], both)
            mm.then_inc(k.slot_used, 1)
            for j in range(2):
                wait_slot(k, pe, first + 2 + j)
                if j == 1:
                    pe.wait_ge(act_evac, 2)
                for i in range(4):
                    mm = tile(first + 2 + j, i, b[(6, 0)[j] + i // 2][:, (i % 2) * T:(i % 2 + 1) * T], x_only)
                mm.then_inc(k.slot_used, 1)

        @block.scalar
        def _(act):
            act.wait_ge(k.slot_used, first + 1)
            nc.scalar.copy(qc[:, 0:2, :].rearrange("p i t -> p (i t)"), b[0][:]).then_inc(act_evac, 1)
            nc.scalar.copy(qc[:, 2, :], b[1][:, 0:T]).then_inc(act_evac, 1)
            act.wait_ge(k.slot_used, first + 2)
            for i in range(2):
                nc.scalar.copy(kvc[:, i, :], b[3 + i][:])
            for j in range(2):
                act.wait_ge(k.slot_used, first + 3 + j)
                for i in range(2):
                    nc.scalar.activation(gate[:, 4 * j + 2 * i:4 * j + 2 * i + 2, :].rearrange("p i t -> p (i t)"),
                                         b[(6, 0)[j] + i][:], ACT.Silu)

        @block.vector
        def _(dve):
            s = Steps(dve, step)
            dve.wait_ge(k.slot_used, first + 2)
            nc.vector.tensor_copy(kpe[:, 0:T], b[2][:, 0:T])
            nc.vector.tensor_tensor(kpe[:, X], b[2][:, X], rope[:, 0, :], ALU.mult)
            s(nc.vector.tensor_tensor(turned[:], b[5][:, X], rope[:, 1, :], ALU.mult))
            nc.vector.tensor_tensor(kpe[:, X], kpe[:, X], turned[:], ALU.add)


def stage_mla_up(nc, k, rope, qc, kvc, kn, v, qn, qp):
    first = FIRST["mlab"]
    with ExitStack() as ctx:
        turned = ctx.enter_context(nc.sbuf_tensor("qp_turned", [P, 4, T], F32))
        act_evac = ctx.enter_context(nc.semaphore("mlaup_act"))
        dve_evac = ctx.enter_context(nc.semaphore("mlaup_dve"))
        done = ctx.enter_context(nc.semaphore("mlaup_pe"))
        b = k.psum
        block = ctx.enter_context(nc.Block())

        @block.sync
        def _(sp):
            load_ahead(k, sp, first, 3)

        @block.tensor
        def _(pe):
            w = k.ring[:, first % RING, :]
            wait_slot(k, pe, first)
            for m in range(8):
                for kt in range(2):
                    mm = pe.matmul(b[m][:], w[:, kt * D + m * P:kt * D + (m + 1) * P], kvc[:, kt, :],
                                   start=(kt == 0), stop=(kt == 1))
                mm.then_inc(done, 1)
            for c in range(4):
                for n in range(2):
                    pe.wait_ge(act_evac, 2 * c + n + 1)
                    for kt in range(2):
                        mm = pe.matmul(b[2 * c + n][:], kvc[:, kt, c * P:(c + 1) * P],
                                       w[:, 2 * D + kt * D + n * 512:2 * D + kt * D + (n + 1) * 512],
                                       start=(kt == 0), stop=(kt == 1))
                    mm.then_inc(done, 1)
            for sl, (lo, tiles, banks) in enumerate((((0, D), 8, range(0, 4)), ((0, 512), 8, range(4, 8)))):
                wait_slot(k, pe, first + 1 + sl)
                w = k.ring[:, (first + 1 + sl) % RING, :]
                for m in range(tiles):
                    bk = banks[m // 2]
                    if m % 2 == 0:
                        pe.wait_ge(dve_evac, bk + 1)
                    for kt in range(3):
                        if sl == 0:
                            at = kt * D + m * P
                        else:
                            at = (m // 4) * 1536 + kt * 512 + (m % 4) * P
                        mm = pe.matmul(b[bk][:, (m % 2) * T:(m % 2 + 1) * T], w[:, at:at + P], qc[:, kt, :],
                                       start=(kt == 0), stop=(kt == 2))
                if sl == 0:
                    mm.then_inc(k.slot_used, 2)
                else:
                    mm.then_inc(k.slot_used, 1)

        @block.scalar
        def _(act):
            for m in range(8):
                act.wait_ge(done, m + 1)
                nc.scalar.copy(kn[:, m, :], b[m][:]).then_inc(act_evac, 1)
            act.wait_ge(k.slot_used, first + 2)
            for i in range(4):
                nc.scalar.copy(qn[:, 2 * i:2 * i + 2, :].rearrange("p i t -> p (i t)"), b[i][:])

        @block.vector
        def _(dve):
            for c in range(4):
                for n in range(2):
                    dve.wait_ge(done, 8 + 2 * c + n + 1)
                    nc.vector.tensor_copy(v[:, c, n * 512:(n + 1) * 512], b[2 * c + n][:]).then_inc(dve_evac, 1)
            dve.wait_ge(k.slot_used, first + 3)
            cos, sin = (rope[:, i:i + 1, :].to_broadcast([P, 2, T]) for i in range(2))
            for i in range(2):
                nc.vector.tensor_tensor(qp[:, 2 * i:2 * i + 2, :], b[4 + i][:].rearrange("p (i t) -> p i t", i=2),
                                        cos, ALU.mult)
                nc.vector.tensor_tensor(turned[:, 2 * i:2 * i + 2, :], b[6 + i][:].rearrange(
                    "p (i t) -> p i t", i=2), sin, ALU.mult).then_inc(dve_evac, 1)
            dve.wait_ge(dve_evac, 10)
            nc.vector.tensor_tensor(qp[:], qp[:], turned[:], ALU.add)


def stage_mla_attention(nc, k, half, kn, v, qn, qp, kpe, gate):
    SCALE = 1.0 / math.sqrt(96.0)
    NK = 2 * T
    with ExitStack() as ctx:
        def sb(name, shape):
            return ctx.enter_context(nc.sbuf_tensor("mla_" + name, shape, F32))

        def sem(name):
            return ctx.enter_context(nc.semaphore("mla_" + name))
        qm = sb("q", [P, 4, 2, T])
        kst, vst = sb("k", [P, 2, NK]), sb("v", [P, 4, 2 * P])
        prob = sb("prob", [P, 2, NK])
        stat = sb("stat", [P, 8, 3])
        diag = sb("diag", [P, 2, P])
        ptok = sb("ptok", [P, 2, NK])
        staged, q_up, scored, maxed, exped, normed = (sem(n) for n in ("staged", "q_up", "scored", "maxed", "exped",
                                                                        "normed"))
        turned, p_down, o_up, o_down, step = (sem(n) for n in ("turned", "p_down", "o_up", "o_down", "step"))
        ident = const(k, "ident")
        U = 8
        block = ctx.enter_context(nc.Block())

        @block.gpsimd
        def _(pool):
            with pool.Fori(0, 4) as t:
                pool.wait_ge(o_up, t * U)
                pool.nop(nofuse=True)
                nc.gpsimd.tensor_copy(kst[:], kn[:, bass.ds(t * 2, 2), :]).then_inc(staged, 1)
                nc.gpsimd.tensor_copy(vst[:], v[:, :, bass.ds(t * 2 * P, 2 * P)]).then_inc(staged, 1)

        @block.scalar
        def _(act):
            with act.Fori(0, 4) as t:
                act.wait_ge(o_up, t * U)
                for hh in range(4):
                    nc.scalar.activation(qm[:, hh, 0:1, :], qn[:, bass.ds(t * 2 + hh // 2, 1), :], ACT.Copy,
                                         scale=half[:, hh % 2:hh % 2 + 1])
                    nc.scalar.activation(qm[:, hh, 1:2, :], qp[:, bass.ds(t, 1), :], ACT.Copy,
                                         scale=half[:, 2 + hh:3 + hh]).then_inc(q_up, 1)
                for u in range(U + 1):
                    if u < U:
                        act.wait_ge(maxed, t * U + (u + 1))
                        act.wait_ge(turned, t * U + max(u - 1, 0))
                        nc.scalar.activation(prob[:, u % 2, :], k.psum[u % 4][:], ACT.Exp, scale=SCALE,
                                             bias=stat[:, u, 0:1], accum_out=stat[:, u, 1:2]).then_inc(exped, 1)
                    if u >= 1:
                        act.wait_ge(turned, t * U + u)
                        nc.scalar.copy(ptok[:, (u - 1) % 2, :], k.psum[4 + (u - 1) % 2][:]).then_inc(p_down, 1)

        @block.tensor
        def _(pe):
            with pe.Fori(0, 4) as t:
                pe.wait_ge(staged, t * 2 + 2)

                def turn(u):
                    pe.wait_ge(normed, t * U + (u + 1))
                    pe.wait_ge(p_down, t * U + max(u - 1, 0))
                    for c in range(4):
                        mm = pe.matmul(k.psum[4 + u % 2][:, c * P:(c + 1) * P], prob[:, u % 2, c * P:(c + 1) * P],
                                       diag[:, u % 2, :], start=True, stop=True)
                    mm.then_inc(turned, 1)

                def values(u):
                    hh, e, qb = u // 2, (u // 2) % 2, u % 2
                    pe.wait_ge(p_down, t * U + (u + 1))
                    if u % 4 == 0:
                        pe.wait_ge(o_down, t * 2 + 0)
                    for c in range(4):
                        mm = pe.matmul(k.psum[6 + hh // 2][e * 64:(e + 1) * 64, qb * P:(qb + 1) * P],
                                       vst[:, c, hh * 64:(hh + 1) * 64], ptok[:, u % 2, c * P:(c + 1) * P],
                                       start=(c == 0), stop=(c == 3))
                    mm.then_inc(o_up, 1)
                for u in range(U + 2):
                    if u < U:
                        hh, qb = u // 2, u % 2
                        pe.wait_ge(q_up, t * 4 + (hh + 1))
                        pe.wait_ge(exped, t * U + max(u - 3, 0))
                        pe.matmul(k.psum[u % 4][:], qm[:, hh, 0, qb * P:(qb + 1) * P], kst[:, hh // 2, :],
                                  start=True, stop=False)
                        pe.matmul(k.psum[u % 4][:], qm[:, hh, 1, qb * P:(qb + 1) * P], kpe[:], start=False,
                                  stop=True).then_inc(scored, 1)
                    if u >= 1 and u - 1 < U:
                        turn(u - 1)
                    if u >= 2:
                        values(u - 2)

        @block.vector
        def _(dve):
            with dve.Fori(0, 4) as t:
                s = Steps(dve, step, t * 16)

                def output(i):
                    dve.wait_ge(o_up, t * U + 4 * (i + 1))
                    g = gate[:, bass.ds(t * 2 + i, 1), :]
                    nc.vector.tensor_tensor(g, k.psum[6 + i][:, 0:T].unsqueeze(1), g, ALU.mult).then_inc(o_down, 1)

                def norm(u):
                    dve.wait_ge(exped, t * U + (u + 1))
                    s(nc.vector.reciprocal(stat[:, u, 2:3], stat[:, u, 1:2]))
                    dve.wait_ge(turned, t * U + max(u - 1, 0))
                    nc.vector.tensor_scalar(diag[:, u % 2, :], ident, stat[:, u, 2:3], None,
                                            ALU.mult).then_inc(normed, 1)
                for u in range(U + 1):
                    if u < U:
                        dve.wait_ge(scored, t * U + (u + 1))
                        s(nc.vector.tensor_reduce(stat[:, u, 2:3], k.psum[u % 4][:], AX, ALU.max))
                        nc.vector.tensor_scalar(stat[:, u, 0:1], stat[:, u, 2:3], -SCALE, None,
                                                ALU.mult).then_inc(maxed, 1)
                    if u >= 1:
                        norm(u - 1)
                for i in range(2):
                    output(i)


def stage_mla(nc, k, a):
    with ExitStack() as lay:
        def sb(name, shape):
            return lay.enter_context(nc.sbuf_tensor("mla_" + name, shape, F32))
        rope, half = sb("rope", [P, 2, T]), sb("half", [P, 6])
        qc, kvc, kpe, gate = sb("qc", [P, 3, T]), sb("kvc", [P, 2, 512]), sb("kpe", [P, 512]), sb("gate", [P, KT, T])
        with nc.semaphore("mla_consts") as landed, nc.Block() as block:
            @block.sync
            def _(sp):
                sp.dma_start(rope[:], a["rope"].rearrange("p (i t) -> p i t", i=2)).then_inc(landed, 16)
                sp.dma_start(half[:], a["half_masks"]).then_inc(landed, 16)
                sp.wait_ge(landed, 32)
        with ExitStack() as inner:
            h = inner.enter_context(nc.sbuf_tensor("mla_h", [P, KT, 512], F32))
            stage_norm(nc, k, k.ctx[:], KT, T, k.gain[:, 24:32], mod2(k, 1, SH, True), h[:, :, 0:T], None, "mlac")
            stage_norm(nc, k, k.x[:], KT, T, k.gain[:, 16:24], mod2(k, 1, SH), h[:, :, T:2 * T], None, "mlax")
            stage_mla_in(nc, k, a, h, rope, qc, kvc, kpe, gate)
        stage_norm(nc, k, qc[:], 3, T, row(k, "qg", 0, 3), None, qc, None, "mlaq")
        stage_norm(nc, k, kvc[:], 2, 512, row(k, "kvg", 0, 2), None, kvc, None, "mlakv")
        kn, v, qn, qp = sb("kn", [P, KT, 512]), sb("vt", [P, 4, D]), sb("qn", [P, KT, T]), sb("qp", [P, 4, T])
        stage_mla_up(nc, k, rope, qc, kvc, kn, v, qn, qp)
        stage_mla_attention(nc, k, half, kn, v, qn, qp, kpe, gate)
        stage_out(nc, k, FIRST["mlaout"], [gate[:, i, :] for i in range(KT)], mod2(k, 1, GT))


def build(nc, a, out):
    with ExitStack() as top:
        k = Core()
        k.stream = a["stream"]
        k.ring = top.enter_context(nc.sbuf_tensor("ring", [P, RING, SLOT], F32))
        k.par = top.enter_context(nc.sbuf_tensor("par", [P, NPAR], F32))
        k.con = top.enter_context(nc.sbuf_tensor("con", [P, NCON], F32))
        k.cs = top.enter_context(nc.sbuf_tensor("cs", [P, 24], F32))
        k.x = top.enter_context(nc.sbuf_tensor("x", [P, KT, T], F32))
        k.ctx = top.enter_context(nc.sbuf_tensor("ctx", [P, KT, T], F32))
        k.mod = top.enter_context(nc.sbuf_tensor("mod", [P, 96], F32))
        k.gain = top.enter_context(nc.sbuf_tensor("gain", [P, 32], F32))
        k.psum = [top.enter_context(nc.psum_tensor(f"bank{b}", [P, 512], F32)) for b in range(8)]
        k.slot_landed = [top.enter_context(nc.semaphore(f"slot_landed{s}")) for s in range(RING)]
        k.slot_used = top.enter_context(nc.semaphore("slot_used"))
        k.first_stage_sem = k.slot_used.num + 1

        stage_setup(nc, k, a)
        first_block(nc, k, a)
        stage_clear(nc, k)
        second_block(nc, k, a)
        stage_store(nc, k, out)


def stage_clear(nc, k):
    with nc.Block() as block:
        @block.sync
        def _(sp):
            sp.sem_clear(range(k.first_stage_sem, 256))


def stage_store(nc, k, out):
    with nc.semaphore("out_stored") as stored, nc.Block() as block:
        @block.sync
        def _(sp):
            sp.dma_start(out, k.x[:]).then_inc(stored, 16)
            sp.wait_ge(stored, 16)


def first_block(nc, k, a):
    with ExitStack() as lay:
        h = lay.enter_context(nc.sbuf_tensor("h", [P, KT, T], F32))
        stage_mod(nc, k, (FIRST["mod0"], 12), [k.cs[:, 0:8]], [k.mod[:, 0:48]], row(k, "adab0", 0, 48))
        stage_scales(nc, k, [(k.gain[:, 0:8], k.mod[:, 8:16], row(k, "nmix0", 0, 8)),
                             (k.gain[:, 8:16], k.mod[:, 32:40], row(k, "nffn0", 0, 8))])
        stage_norm(nc, k, k.x[:], KT, T, k.gain[:, 0:8], k.mod[:, 0:8], h, None, "mix0")
        stage_hybrid(nc, k, a, h)
        stage_norm(nc, k, k.x[:], KT, T, k.gain[:, 8:16], k.mod[:, 24:32], h, None, "ffn0")
        stage_ffn(nc, k, h, FIRST["up0"], FIRST["down0"], k.mod[:, 40:48], 0)
        stage_mod(nc, k, (FIRST["mod1"], 12), [k.cs[:, 0:8]], [k.mod[:, 48:96]], row(k, "adab1", 0, 48))
        stage_scales(nc, k, [(k.gain[:, 0:8], k.mod[:, 56:64], row(k, "nmix1", 0, 8)),
                             (k.gain[:, 8:16], k.mod[:, 80:88], row(k, "nffn1", 0, 8))])
        stage_norm(nc, k, k.x[:], KT, T, k.gain[:, 0:8], k.mod[:, 48:56], h, None, "mix1")
        stage_conformer(nc, k, h)
        stage_norm(nc, k, k.x[:], KT, T, k.gain[:, 8:16], k.mod[:, 72:80], h, None, "ffn1")
        stage_ffn(nc, k, h, FIRST["up1"], FIRST["down1"], k.mod[:, 88:96], 1)
        stage_norm(nc, k, k.x[:], KT, T, row(k, "final1", 0, 8), None, k.x, None, "final1")


def stage_hybrid(nc, k, a, h):
    with ExitStack() as lay:
        y = lay.enter_context(nc.sbuf_tensor("y", [P, NY, T], F32))
        dtok = lay.enter_context(nc.sbuf_tensor("dtok", [P, 2 * HEADS], F32))
        stage_hyin(nc, k, h, y, a, dtok)
        stage_conv4(nc, k, y)
        with ExitStack() as inner:
            hd = inner.enter_context(nc.sbuf_tensor("headvals", [P, 8, 2 * HEADS], F32))
            stage_dt(nc, k, a, dtok, hd)
            stage_ssd(nc, k, y, hd)
        stage_ssm_gate(nc, k, y)
        stage_attention(nc, k, a, y)
        rhs = [y[:, ST_XS + i, :] for i in range(16)] + [y[:, ST_Q + i, :] for i in range(8)]
        stage_out(nc, k, FIRST["hyout"], rhs, k.mod[:, 16:24])


def _cols(w):
    return w.reshape(w.shape[0] // P, P, w.shape[1]).transpose(1, 0, 2)


def _slots(w, groups=None):
    kk, n = w.shape
    kslots, nslots = -(-kk // D), -(-n // 512)
    full = np.zeros((kslots * D, nslots * 512), w.dtype)
    full[:kk, :n] = w
    return full.reshape(kslots, KT, P, nslots, 512).transpose(3, 0, 2, 1, 4).reshape(-1, P, SLOT)


def _pairs(a, b, width=256):
    n = a.shape[1] // width
    both = np.stack([a.reshape(D, n, width), b.reshape(D, n, width)], 2)
    return both.reshape(D, 2 * a.shape[1])


def _one_slot(parts):
    flat = np.concatenate([p.reshape(P, -1) for p in parts], 1)
    out = np.zeros((1, P, SLOT), flat.dtype)
    out[0, :, :flat.shape[1]] = flat
    return out


def lay_stream(i):
    s = [_slots(i["ada_w"][0]), None, _slots(i["hy_w_out"][0]),
         _slots(_pairs(i["ffn_w_gate"][0], i["ffn_w_up"][0])), _slots(i["ffn_w_down"][0]),
         _slots(i["ada_w"][1]), _slots(_pairs(*np.split(i["cv_w_pw1"][0], 2, 1))), _slots(i["cv_w_pw2"][0]),
         _slots(_pairs(i["ffn_w_gate"][1], i["ffn_w_up"][1])), _slots(i["ffn_w_down"][1]),
         _slots(i["mod_w_2"][0]), _slots(i["mod_w_2"][1])]
    w = i["hy_w_in"][0]
    s[1] = _slots(np.concatenate([w[:, :DI + CONV_DIM], w[:, DI + CONV_DIM + HEADS:]], 1))
    s += [_slots(i["rwkv_w_in_2"][0][j]) for j in range(4)] + [_slots(i["rwkv_w_out_2"][0])]
    w = i["mla_w_in_2"][0]
    qc, kvc, kpe, gate = w[:, :384], w[:, 384:640], w[:, 640:672], w[:, 672:]
    swapped = np.concatenate([kpe[:, 16:], kpe[:, :16]], 1)
    s += [_slots(np.concatenate([qc] + [kpe] * 4, 1)), _slots(np.concatenate([kvc] + [swapped] * 4, 1)),
          _slots(gate)]
    kvb = i["mla_w_kvb_2"][0].reshape(256, 16, 2, 64)
    qb = i["mla_w_qb_2"][0].reshape(384, 16, 96)
    s += [_one_slot([_cols(kvb[:, :, 0].reshape(256, 1024)), _cols(kvb[:, :, 1].reshape(256, 1024))]),
          _one_slot([_cols(qb[:, :, :64].reshape(384, 1024))]),
          _one_slot([_cols(qb[:, :, 64:].reshape(384, 512)),
                     _cols(np.concatenate([qb[:, :, 80:], qb[:, :, 64:80]], 2).reshape(384, 512))]),
          _slots(i["mla_w_out_2"][0])]
    stream = np.concatenate(s, 0)
    assert stream.shape == (NSLOTS, P, SLOT), (stream.shape, NSLOTS)
    return stream


def _rows(*vectors):
    return np.concatenate([v.reshape(-1, P).T for v in vectors], 1)


def lay_par(i):
    conv = np.stack([*i["hy_conv_w"][0], i["hy_conv_b"][0]], 0)
    dw = np.stack([*i["cv_w_dw"][0], i["cv_b_dw"][0]], 0)
    rw = np.stack([i["rwkv_w0_2"][0, 0], i["rwkv_w0_2"][0, 1], i["rwkv_a0_2"][0, 0], i["rwkv_a0_2"][0, 1],
                   i["rwkv_k_k_2"][0], i["rwkv_k_a_2"][0], i["rwkv_r_k_2"][0].reshape(-1),
                   i["rwkv_lnx_g_2"][0], i["rwkv_lnx_b_2"][0]], 0)

    def tilewise(m):
        return m.reshape(m.shape[0], -1, P).transpose(1, 0, 2)
    par = _rows(i["c"], i["c_2"], i["c_ctx_2"], i["ada_b"][0], i["ada_b"][1], i["mod_b_2"][0], i["mod_b_2"][1],
                i["norm_mix_g"][0], i["norm_mix_g"][1], i["norm_ffn_g"][0], i["norm_ffn_g"][1],
                i["final_norm_g"], tilewise(conv), np.repeat(i["hy_d_skip"][0], 64), i["hy_ssm_norm_g"][0],
                i["cv_b_pw1"][0], tilewise(dw), i["cv_ln_g"][0], i["cv_ln_b"][0], i["cv_b_pw2"][0],
                i["norm_g_2"][0], i["norm_g_2"][1], i["rwkv_mu_2"][0], i["final_g_2"], i["mla_q_norm_g_2"][0],
                i["mla_kv_norm_g_2"][0], tilewise(rw))
    assert par.shape == (P, NPAR), (par.shape, NPAR)
    return par


def t5_bucket(dist):
    n = np.maximum(dist, 1).astype(np.float32)
    large = np.float32(16) + np.log(n / np.float32(16)) / np.float32(math.log(2048 / 16)) * np.float32(16)
    return np.where(dist < 16, dist, np.minimum(large.astype(np.int32), 31))


def constants():
    p, f = np.arange(P)[:, None], np.arange(P)[None, :]
    f32 = np.float32
    out = {}
    out["con"] = np.concatenate([(p == f), np.ones((P, P)), (p // 64 == f // 64), (p <= f),
                                 np.where(f >= p, 0.0, NEG), (p + f == P - 1)], 1).astype(f32)
    dist = 255 - np.arange(384)
    bucket = t5_bucket(np.maximum(dist, 0))
    onehot = ((np.arange(32)[:, None] == bucket[None]) & (dist >= 0)[None]).astype(f32)
    allowed = [(dist >= 0) & (dist <= 128), (dist >= 0) & (dist % 4 == 0), (dist >= 0) & (dist % 16 == 0)]
    negs = np.concatenate([np.where(np.tile(a, (16, 1)), 0.0, NEG) for a in allowed], 0).astype(f32)
    out["bias_onehot"], out["bias_neg"] = onehot, negs
    out["tri_masks"] = np.concatenate([p < f, p <= f, p > f, p >= f], 1).astype(f32)
    levels = []
    for upper in (True, False):
        for lv in range(7):
            i, j = p >> lv, f >> lv
            levels.append((i % 2 == 0) & (j == i + 1) if upper else (j % 2 == 0) & (i == j + 1))
    out["level_masks"] = np.concatenate(levels, 1).astype(np.int32)
    out["chunk_starts"] = np.broadcast_to((np.arange(512) % P != 0), (P, 512)).astype(f32).copy()
    out["half_masks"] = np.concatenate([p < 64, p >= 64] + [p // 32 == q for q in range(4)], 1).astype(f32)
    tok = np.arange(T)
    inv = (1.0 / (f32(10000.0) ** (np.arange(0, 16, 2, dtype=f32) / f32(16)))).astype(f32)
    ang = np.concatenate([(tok // 64).astype(f32)[:, None] * inv, (tok % 64).astype(f32)[:, None] * inv], 1)
    cos, sin = np.cos(ang).T.astype(f32), np.sin(ang).T.astype(f32)
    out["rope"] = np.tile(np.concatenate([np.concatenate([cos, cos]), np.concatenate([-sin, sin])], 1), (4, 1))
    return out


def lay_inputs(i):
    def tokens(x):
        return _cols(np.ascontiguousarray(x.reshape(T, D).T))
    w = i["hy_w_in"][0]
    out = constants()
    out["stream"] = lay_stream(i)
    out["par"] = lay_par(i)
    out["xt"], out["ctxt"] = tokens(i["x"]), tokens(i["ctx_2"])
    out["wdt"] = _cols(w[:, DI + CONV_DIM:DI + CONV_DIM + HEADS])
    out["headrow"] = np.concatenate([np.broadcast_to(i["hy_dt_bias"][0], (P, HEADS)),
                                     np.broadcast_to(i["hy_a_log"][0], (P, HEADS))], 1)
    out["rel_table"] = i["rel_table"]
    w1 = np.concatenate([*i["rwkv_w1_2"][0], *i["rwkv_a1_2"][0]], 1)
    out["lora_in"] = _cols(w1)
    out["lora_out"] = np.stack([i["rwkv_w2_2"][0].reshape(P, D), i["rwkv_a2_2"][0].reshape(P, D)], 1)
    return {n: np.ascontiguousarray(v) for n, v in out.items()}


def kernel(**inputs):
    import concourse.bacc as bacc
    from concourse.bass_utils import run_bass_kernel_spmd

    nc = bacc.Bacc("TRN2", target_bir_lowering=False, num_devices=1)
    arrays = lay_inputs({n: np.asarray(v) for n, v in inputs.items()})
    aps = {n: nc.dram_tensor("in_" + n, v.shape, mybir.dt.from_np(v.dtype), kind="ExternalInput").ap()
           for n, v in arrays.items()}
    out = nc.dram_tensor("out_0_dram", (P, KT, T), F32, kind="ExternalOutput").ap()
    build(nc, aps, out)
    r = run_bass_kernel_spmd(nc, [{"in_" + n: v for n, v in arrays.items()}], core_ids=[0])
    got = r.results[0]["out_0_dram"]
    return got.transpose(2, 1, 0).reshape(1, T, D)
```

```python
import math
from contextlib import ExitStack

import numpy as np

import concourse.bass as bass
from concourse import mybir

F32 = mybir.dt.float32
U8 = mybir.dt.uint8
I32 = mybir.dt.int32
ACT = mybir.ActivationFunctionType
ALU = mybir.AluOpType
AX = mybir.AxisListType.X

P = 128
D = 1024
T = 256
KT = D // P
RING = 4
SLOT = KT * 512
EPS = 1e-6
NEG = -1e30

DI = 2048
CONV_DIM = 3072
HEADS = 32
ST_Z, ST_XS, ST_B, ST_C, ST_Q, ST_K, ST_V = 0, 16, 32, 36, 40, 64, 72
NY = 80
FFN = 2816
FT = FFN // P
TAPS = 31

_PAR_SIZES = [("c", 8), ("c2", 8), ("cctx", 8), ("adab0", 48), ("adab1", 48), ("modb0", 24), ("modb1", 24),
              ("nmix0", 8), ("nmix1", 8), ("nffn0", 8), ("nffn1", 8), ("final1", 8),
              ("conv", 24 * 5), ("dskip", 16), ("ssmg", 16), ("pw1b", 16), ("dw", 8 * 32), ("lng", 8),
              ("lnb", 8), ("pw2b", 8), ("norm2_0", 8), ("norm2_1", 8), ("mu", 48), ("final2", 8), ("qg", 3),
              ("kvg", 2), ("rw", 9 * 9)]
PAR = {}
NPAR = 0
for _name, _n in _PAR_SIZES:
    PAR[_name] = NPAR
    NPAR += _n

_SLOTS = [("mod0", 12), ("hyin", 20), ("hyout", 6), ("up0", 11), ("down0", 6), ("mod1", 12), ("pw1", 4), ("pw2", 2),
          ("up1", 11), ("down1", 6), ("mod2", 12), ("rkvg", 8), ("rwout", 2), ("mlain", 4), ("mlab", 3),
          ("mlaout", 2)]
FIRST = {}
NSLOTS = 0
for _name, _n in _SLOTS:
    FIRST[_name] = NSLOTS
    NSLOTS += _n

_CONST_SIZES = [("ident", 128), ("ones", 128), ("headones", 128), ("tri", 128), ("neg", 128), ("flip", 128)]
CON = {}
NCON = 0
for _name, _n in _CONST_SIZES:
    CON[_name] = NCON
    NCON += _n


class Steps:

    def __init__(self, eng, sem, done=0):
        self.eng, self.sem, self.done, self.n = eng, sem, done, 0

    def __call__(self, ins):
        self.n += 1
        ins.then_inc(self.sem, 1)
        self.eng.wait_ge(self.sem, self.done + self.n)


class Core:
    pass


def psum_tiles(k):
    return [k.psum[b] for b in range(8)]


def wait_slot(k, eng, n, turn=0):
    eng.wait_ge(k.slot_landed[n % RING], turn * 16 + 16 * (n // RING + 1))


def load_ahead(k, sp, first, count):
    def one(n, turn):
        sp.wait_ge(k.slot_used, turn * RING + (n + 1))
        sp.dma_start(k.ring[:, n % RING, :], k.stream[turn * RING + (n + RING)]).then_inc(
            k.slot_landed[n % RING], 16)

    count = min(count, NSLOTS - RING - first)
    turns = count // RING
    if turns > 1:
        with sp.Fori(0, turns) as t:
            for j in range(RING):
                one(first + j, t)
        for j in range(turns * RING, count):
            one(first + j, 0)
    else:
        for j in range(count):
            one(first + j, 0)


def ring_tile(k, n, kt, col, width=P):
    return k.ring[:, n % RING, kt * 512 + col:kt * 512 + col + width]


def row(k, name, i=0, n=1):
    c = PAR[name] + i
    return k.par[:, c:c + n]


def const(k, name):
    return k.con[:, CON[name]:CON[name] + P]


def stage_setup(nc, k, a):
    with ExitStack() as ctx:
        landed = ctx.enter_context(nc.semaphore("setup_landed"))
        silu_done = ctx.enter_context(nc.semaphore("setup_silu"))
        block = ctx.enter_context(nc.Block())

        @block.sync
        def _(sp):
            sp.dma_start(k.par[:], a["par"]).then_inc(landed, 16)
            sp.dma_start(k.con[:], a["con"]).then_inc(landed, 16)
            for n in range(RING):
                sp.dma_start(k.ring[:, n, :], k.stream[n]).then_inc(k.slot_landed[n], 16)
            sp.dma_start(k.x[:], a["xt"]).then_inc(landed, 16)
            sp.dma_start(k.ctx[:], a["ctxt"]).then_inc(landed, 16)
            sp.wait_ge(landed, 64)

        @block.scalar
        def _(act):
            act.wait_ge(landed, 64)
            nc.scalar.activation(k.cs[:], row(k, "c", 0, 24), ACT.Silu).then_inc(silu_done, 1)


def stage_mod(nc, k, slots, vectors, out, bias):
    first, count = slots
    nv = len(vectors)
    with ExitStack() as ctx:
        part = ctx.enter_context(nc.sbuf_tensor(f"mod_part{first}", [P, 2, nv, 512], F32))
        summed = ctx.enter_context(nc.semaphore("mod_summed"))
        step = ctx.enter_context(nc.semaphore("mod_step"))
        stored = ctx.enter_context(nc.semaphore("mod_stored"))
        block = ctx.enter_context(nc.Block())
        turns = count // RING

        @block.sync
        def _(sp):
            load_ahead(k, sp, first, count)

        @block.vector
        def _(dve):
            with dve.Fori(0, turns) as t:
                s = Steps(dve, step, t * (RING * (KT - 1) * nv))
                for j in range(RING):
                    wait_slot(k, dve, first + j, t)
                    dve.wait_ge(k.slot_used, t * RING + max(first + j - 1, j))
                    w = k.ring[:, (first + j) % RING, :]
                    for kt in range(KT):
                        for v, vec in enumerate(vectors):
                            acc = part[:, j % 2, v, :]
                            if kt == 0:
                                ins = nc.vector.tensor_scalar(acc, w[:, 0:512], vec[:, 0:1], None, ALU.mult)
                            else:
                                ins = nc.vector.scalar_tensor_tensor(
                                    acc, w[:, kt * 512:kt * 512 + 512], vec[:, kt:kt + 1], acc, ALU.mult, ALU.add)
                            if kt < KT - 1:
                                ins.then_inc(step, 1)
                                s.n += 1
                            elif v == nv - 1:
                                ins.then_inc(summed, 1)
                        if kt < KT - 1:
                            dve.wait_ge(step, s.done + s.n)

        @block.tensor
        def _(pe):
            with pe.Fori(0, turns) as t:
                for j in range(RING):
                    pe.wait_ge(summed, t * RING + (j + 1))
                    if j == 0:
                        pe.wait_ge(stored, t * nv)
                    for v in range(nv):
                        for q in range(4):
                            mm = pe.matmul(k.psum[v][:, j * 4 + q:j * 4 + q + 1],
                                           part[:, j % 2, v, q * P:(q + 1) * P], const(k, "ones")[:, 0:1],
                                           start=True, stop=True)
                    mm.then_inc(k.slot_used, 1)

        @block.scalar
        def _(act):
            with act.Fori(0, turns) as t:
                act.wait_ge(k.slot_used, t * RING + (first + RING))
                for v in range(nv):
                    nc.scalar.copy(out[v][:, bass.ds(t * 16, 16)], k.psum[v][:, 0:16]).then_inc(stored, 1)

    with nc.Block() as block:
        @block.vector
        def _(dve):
            for v in range(nv):
                nc.vector.tensor_tensor(out[v], out[v], bias, ALU.add)


def stage_norm(nc, k, src, nt, width, scale, bias, dst, count, name):
    with ExitStack() as ctx:
        sq = ctx.enter_context(nc.sbuf_tensor(f"norm_sq_{name}", [P, nt, width], F32))
        rstd = ctx.enter_context(nc.sbuf_tensor(f"norm_rstd_{name}", [P, 1, width], F32))
        squared = ctx.enter_context(nc.semaphore("norm_squared"))
        summed = ctx.enter_context(nc.semaphore("norm_summed"))
        step = ctx.enter_context(nc.semaphore("norm_step"))
        rooted = ctx.enter_context(nc.semaphore("norm_rooted"))
        block = ctx.enter_context(nc.Block())
        half = nt // 2

        @block.scalar
        def _(act):
            for lo, hi in ((0, half), (half, nt)):
                nc.scalar.activation(sq[:, lo:hi, :], src[:, lo:hi, :], ACT.Square).then_inc(squared, 1)
            act.wait_ge(step, 1)
            nc.scalar.activation(rstd[:, 0, :], rstd[:, 0, :], ACT.Sqrt).then_inc(rooted, 1)
            if bias is not None:
                act.wait_ge(step, 3)
                for i in range(1, nt, 2):
                    nc.scalar.activation(dst[:, i, :], sq[:, i, :], ACT.Identity, bias=bias[:, i:i + 1],
                                         scale=scale[:, i:i + 1])

        @block.tensor
        def _(pe):
            for i in range(nt):
                if i == 0:
                    pe.wait_ge(squared, 1)
                if i == half:
                    pe.wait_ge(squared, 2)
                mm = pe.matmul(k.psum[0][:, 0:width], const(k, "ones"), sq[:, i, :], start=(i == 0),
                               stop=(i == nt - 1))
            mm.then_inc(summed, 1)

        @block.vector
        def _(dve):
            s = Steps(dve, step)
            dve.wait_ge(summed, 1)
            s(nc.vector.tensor_scalar(rstd[:, 0, :], k.psum[0][:, 0:width], 1.0 / (nt * P) if count is None
                                      else 1.0 / count, EPS, ALU.mult, ALU.add))
            dve.wait_ge(rooted, 1)
            s(nc.vector.reciprocal(rstd[:, 0, :], rstd[:, 0, :]))
            s(nc.vector.tensor_tensor(sq[:], src, rstd[:].to_broadcast([P, nt, width]), ALU.mult))
            for i in range(0, nt, 2 if bias is not None else 1):
                if bias is not None:
                    nc.vector.tensor_scalar(dst[:, i, :], sq[:, i, :], scale[:, i:i + 1], bias[:, i:i + 1],
                                            ALU.mult, ALU.add)
                else:
                    nc.vector.tensor_scalar(dst[:, i, :], sq[:, i, :], scale[:, i:i + 1], None, ALU.mult)


def stage_scales(nc, k, pairs):
    with ExitStack() as ctx:
        block = ctx.enter_context(nc.Block())

        @block.vector
        def _(dve):
            for out, sc, g in pairs:
                nc.vector.scalar_tensor_tensor(out, sc, 1.0, g, ALU.add, ALU.mult)


def slot_products(k, pe, n, turn, rhs, outs, kts=range(KT), start=True, stop=True, width=P):
    wait_slot(k, pe, n, turn)
    for i, out in enumerate(outs):
        for kt in kts:
            mm = pe.matmul(out, ring_tile(k, n, kt, i * P), rhs[kt], start=start and kt == kts[0],
                           stop=stop and kt == kts[-1])
    return mm


def stage_hyin(nc, k, h, y, a, dtok):
    first = FIRST["hyin"]
    turns = 20 // RING
    with ExitStack() as ctx:
        wdt = ctx.enter_context(nc.sbuf_tensor("hyin_wdt", [P, KT, HEADS], F32))
        wdt_landed = ctx.enter_context(nc.semaphore("wdt_landed"))
        stored_dve = ctx.enter_context(nc.semaphore("hyin_stored_dve"))
        stored_act = ctx.enter_context(nc.semaphore("hyin_stored_act"))
        dt_done = ctx.enter_context(nc.semaphore("hyin_dt"))
        block = ctx.enter_context(nc.Block())

        @block.sync
        def _(sp):
            sp.dma_start(wdt[:], a["wdt"]).then_inc(wdt_landed, 16)
            load_ahead(k, sp, first, 20)

        @block.tensor
        def _(pe):
            rhs = [h[:, kt, :] for kt in range(KT)]
            pe.wait_ge(wdt_landed, 16)
            for c in range(2):
                for kt in range(KT):
                    mm = pe.matmul(k.psum[7][:, c * HEADS:(c + 1) * HEADS], h[:, kt, c * P:(c + 1) * P],
                                   wdt[:, kt, :], start=(kt == 0), stop=(kt == KT - 1))
            mm.then_inc(dt_done, 1)
            with pe.Fori(0, turns) as t:
                for j in range(RING):
                    pe.wait_ge(stored_dve, t * RING + (j + 1))
                    pe.wait_ge(stored_act, t * RING + (j + 1))
                    b = 2 * (j % 2)
                    outs = [k.psum[b + i // 2][:, (i % 2) * T:(i % 2 + 1) * T] for i in range(4)]
                    slot_products(k, pe, first + j, t, rhs, outs).then_inc(k.slot_used, 1)

        @block.vector
        def _(dve):
            dve.wait_ge(dt_done, 1)
            nc.vector.tensor_copy(dtok[:], k.psum[7][:, 0:2 * HEADS])
            dve.sem_inc(stored_dve, 2)
            with dve.Fori(0, turns) as t:
                for j in range(RING):
                    dve.wait_ge(k.slot_used, t * RING + (first + j + 1))
                    nc.vector.tensor_copy(y[:, bass.ds(t * 16 + 4 * j, 2), :],
                                          k.psum[2 * (j % 2)][:]).then_inc(stored_dve, 1)

        @block.scalar
        def _(act):
            act.sem_inc(stored_act, 2)
            with act.Fori(0, turns) as t:
                for j in range(RING):
                    act.wait_ge(k.slot_used, t * RING + (first + j + 1))
                    nc.scalar.copy(y[:, bass.ds(t * 16 + 4 * j + 2, 2), :],
                                   k.psum[2 * (j % 2) + 1][:]).then_inc(stored_act, 1)


def stage_conv4(nc, k, y):
    nt = 24
    with ExitStack() as ctx:
        acc = ctx.enter_context(nc.sbuf_tensor("conv_acc", [P, 2, T], F32))
        step = ctx.enter_context(nc.semaphore("conv_step"))
        summed = ctx.enter_context(nc.semaphore("conv_summed"))
        stored = ctx.enter_context(nc.semaphore("conv_stored"))
        block = ctx.enter_context(nc.Block())

        @block.vector
        def _(dve):
            dve.sem_inc(stored, 2)
            with dve.Fori(0, nt // 2) as t:
                s = Steps(dve, step, t * 6)
                for tap in range(4):
                    for j in range(2):
                        i = t * 2 + j
                        src = y[:, bass.ds(i + ST_XS, 1), :]
                        a = acc[:, j:j + 1, :]

                        def w(c):
                            return k.par[:, bass.ds(i * 5 + (PAR["conv"] + c), 1)]
                        if tap == 0:
                            dve.wait_ge(stored, t * 2 + (j + 1))
                            ins = nc.vector.tensor_scalar(a, src, w(3), w(4), ALU.mult, ALU.add)
                        else:
                            ins = nc.vector.scalar_tensor_tensor(
                                a[:, :, tap:], src[:, :, :T - tap], w(3 - tap), a[:, :, tap:], ALU.mult, ALU.add)
                        if tap == 3:
                            ins.then_inc(summed, 1)
                        else:
                            ins.then_inc(step, 1)
                            s.n += 1
                    if tap < 3:
                        dve.wait_ge(step, s.done + s.n)

        @block.scalar
        def _(act):
            for q in range(4):
                nc.scalar.activation(y[:, 4 * q:4 * q + 4, :], y[:, 4 * q:4 * q + 4, :], ACT.Silu)
            with act.Fori(0, nt // 2) as t:
                for j in range(2):
                    act.wait_ge(summed, t * 2 + (j + 1))
                    nc.scalar.activation(y[:, bass.ds(t * 2 + (j + ST_XS), 1), :], acc[:, j:j + 1, :],
                                         ACT.Silu).then_inc(stored, 1)


DT, DA, ACS, TOTAL, DT_END = range(5)


def stage_dt(nc, k, a, dtok, hd):
    with ExitStack() as ctx:
        hrow = ctx.enter_context(nc.sbuf_tensor("headrow", [P, 2, HEADS], F32))
        w = ctx.enter_context(nc.sbuf_tensor("dt_work", [P, 8, 2 * HEADS], F32))
        landed = ctx.enter_context(nc.semaphore("headrow_landed"))
        step = ctx.enter_context(nc.semaphore("dt_step"))
        done = ctx.enter_context(nc.semaphore("dt_act"))
        summed = ctx.enter_context(nc.semaphore("dt_summed"))
        dt_ready = ctx.enter_context(nc.semaphore("dt_ready"))
        block = ctx.enter_context(nc.Block())
        RAW, ABS, EXPD, ONEP, LOG1, BACK, ZERO, AROW = range(8)

        def both(ap):
            return ap.unsqueeze(1).to_broadcast([P, 2, HEADS])

        def v(i):
            return w[:, i, :].rearrange("p (c h) -> p c h", c=2)

        @block.sync
        def _(sp):
            sp.dma_start(hrow[:], a["headrow"].rearrange("p (r h) -> p r h", r=2)).then_inc(landed, 16)

        @block.scalar
        def _(act):
            act.wait_ge(landed, 16)
            nc.scalar.activation(w[:, AROW, 0:HEADS], hrow[:, 1, :], ACT.Exp).then_inc(done, 1)
            act.wait_ge(step, 2)
            nc.scalar.activation(w[:, EXPD, :], w[:, ABS, :], ACT.Exp, scale=-1.0).then_inc(done, 1)
            act.wait_ge(step, 3)
            nc.scalar.activation(w[:, LOG1, :], w[:, ONEP, :], ACT.Ln).then_inc(done, 1)
            act.wait_ge(step, 13)
            nc.scalar.activation(w[:, EXPD, :], w[:, BACK, :], ACT.Exp).then_inc(done, 1)

        @block.tensor
        def _(pe):
            pe.wait_ge(step, 11)
            pe.matmul(k.psum[0][:, 0:64], const(k, "tri"), hd[:, DA, :], start=True, stop=True)
            pe.matmul(k.psum[1][:, 0:64], const(k, "ones"), hd[:, DA, :], start=True, stop=True).then_inc(summed, 1)

        @block.vector
        def _(dve):
            s = Steps(dve, step)
            dve.wait_ge(landed, 16)
            s(nc.vector.tensor_tensor(v(RAW), dtok[:].rearrange("p (c h) -> p c h", c=2), both(hrow[:, 0, :]), ALU.add))
            s(nc.vector.scalar_tensor_tensor(w[:, ABS, :], w[:, RAW, :], -1.0, w[:, RAW, :], ALU.mult, ALU.max))
            dve.wait_ge(done, 2)
            s(nc.vector.tensor_scalar(w[:, ONEP, :], w[:, EXPD, :], 1.0, None, ALU.add))
            s(nc.vector.tensor_scalar(w[:, BACK, :], w[:, ONEP, :], -1.0, None, ALU.add))
            s(nc.vector.tensor_scalar(w[:, ZERO, :], w[:, BACK, :], 0.0, None, ALU.is_equal))
            s(nc.vector.tensor_tensor(w[:, BACK, :], w[:, BACK, :], w[:, ZERO, :], ALU.add))
            dve.wait_ge(done, 3)
            s(nc.vector.tensor_tensor(w[:, LOG1, :], w[:, LOG1, :], w[:, ZERO, :], ALU.add))
            s(nc.vector.reciprocal(w[:, BACK, :], w[:, BACK, :]))
            s(nc.vector.tensor_tensor(w[:, LOG1, :], w[:, LOG1, :], w[:, BACK, :], ALU.mult))
            s(nc.vector.tensor_tensor(w[:, LOG1, :], w[:, LOG1, :], w[:, EXPD, :], ALU.mult))
            nc.vector.scalar_tensor_tensor(hd[:, DT, :], w[:, RAW, :], 0.0, w[:, LOG1, :], ALU.max,
                                           ALU.add).then_inc(dt_ready, 1)
            dve.wait_ge(dt_ready, 1)
            dve.wait_ge(done, 1)
            s(nc.vector.scalar_tensor_tensor(hd[:, DA, :].rearrange("p (c h) -> p c h", c=2),
                                             hd[:, DT, :].rearrange("p (c h) -> p c h", c=2), -1.0,
                                             both(w[:, AROW, 0:HEADS]), ALU.mult, ALU.mult))
            dve.wait_ge(summed, 1)
            s(nc.vector.tensor_copy(hd[:, ACS, :], k.psum[0][:, 0:64]))
            s(nc.vector.tensor_tensor(w[:, BACK, :], k.psum[1][:, 0:64], hd[:, ACS, :], ALU.subtract))
            dve.wait_ge(done, 4)
            s(nc.vector.tensor_tensor(hd[:, DT_END, :], hd[:, DT, :], w[:, EXPD, :], ALU.mult))



def stage_ssd(nc, k, y, hd):
    with ExitStack() as ctx:
        def sb(name, shape):
            return ctx.enter_context(nc.sbuf_tensor("ssd_" + name, shape, F32))

        def sem(name):
            return ctx.enter_context(nc.semaphore("ssd_" + name))
        bt, ct, xs = sb("b", [P, T]), sb("c", [P, T]), sb("x", [P, 4, T])
        hv = sb("hv", [P, 5, 2, 8])
        bt_tok = sb("b_tok", [P, P])
        xdt = sb("xdt", [P, 2, 8, 64])
        xend = sb("xend", [P, 8, 64])
        cb = sb("cb", [P, 2, P])
        seg = sb("seg", [P, 4, 4, P])
        cdec = sb("cdec", [P, 2, 4, P])
        state = sb("state", [P, 512])
        staged, turned, rows_up = sem("staged"), sem("turned"), sem("rows_up")
        evac, masked, decayed, weighted = sem("evac"), sem("masked"), sem("decayed"), sem("weighted")
        cdone, states_up, state_down, y_up, y_down = sem("cdone"), sem("states_up"), sem("state_down"), sem("y_up"), \
            sem("y_down")
        rowed = sem("rowed")
        ident = const(k, "ident")
        block = ctx.enter_context(nc.Block())

        @block.gpsimd
        def _(pool):
            with pool.Fori(0, 4) as g:
                pool.wait_ge(y_down, g * 2)
                nc.gpsimd.tensor_copy(bt[:].unsqueeze(1), y[:, bass.ds(g + ST_B, 1), :]).then_inc(staged, 1)
                nc.gpsimd.tensor_copy(ct[:].unsqueeze(1), y[:, bass.ds(g + ST_C, 1), :]).then_inc(staged, 1)
                for r in (DT, DA, ACS, DT_END):
                    nc.gpsimd.tensor_copy(hv[:, r, :, :], hd[:, r, :].rearrange("p (c h) -> p c h", c=2)[
                        :, :, bass.ds(g * 8, 8)]).then_inc(staged, 1)
                nc.gpsimd.tensor_copy(xs[:], y[:, bass.ds(g * 4 + ST_XS, 4), :]).then_inc(staged, 1)

        @block.tensor
        def _(pe):
            with pe.Fori(0, 4) as g:
                pe.wait_ge(staged, g * 7 + 7)
                for c in range(2):
                    for i in range(4):
                        pe.transpose(k.psum[c][:, i * P:(i + 1) * P], xs[:, i, c * P:(c + 1) * P], ident)
                for c in range(2):
                    pe.matmul(k.psum[2][:, c * P:(c + 1) * P], bt[:, c * P:(c + 1) * P], ct[:, c * P:(c + 1) * P],
                              start=True, stop=True)
                pe.transpose(k.psum[2][:, 2 * P:3 * P], bt[:, 0:P], ident).then_inc(turned, 1)
                for b in range(4):
                    c, half = b // 2, b % 2
                    for i in range(4):
                        col = hv[:, DA, c, half * 4 + i:half * 4 + i + 1].to_broadcast([P, P])
                        mm = pe.matmul(k.psum[4 + b][:, i * P:(i + 1) * P], col, const(k, "tri"), start=True,
                                       stop=True)
                    mm.then_inc(rows_up, 1)
                pe.wait_ge(evac, g * 5 + 5)
                pe.matmul(k.psum[3][:], bt_tok[:], xend[:].rearrange("p h d -> p (h d)"), start=True,
                          stop=True).then_inc(states_up, 1)
                for c in range(2):
                    for i in range(4):
                        if i % 2 == 0:
                            pe.wait_ge(weighted, g * 4 + (2 * c + i // 2 + 1))
                        if c == 1 and i == 0:
                            pe.wait_ge(state_down, g + 1)
                            pe.wait_ge(cdone, g * 2 + 2)
                        for e in range(2):
                            hh = 2 * i + e
                            out = k.psum[c][e * 64:(e + 1) * 64, i * P:(i + 1) * P]
                            mm = pe.matmul(out, xdt[:, c, hh, :], seg[:, 2 * c + hh // 4, hh % 4, :], start=True,
                                           stop=(c == 0), skip_group_check=True)
                            if c == 1:
                                mm = pe.matmul(out, state[:, hh * 64:(hh + 1) * 64], cdec[:, hh // 4, hh % 4, :],
                                               start=False, stop=True, skip_group_check=True)
                    mm.then_inc(y_up, 1)

        @block.vector
        def _(dve):
            with dve.Fori(0, 4) as g:
                dve.wait_ge(turned, g + 1)
                for c in range(2):
                    xt = k.psum[c][:].rearrange("p (h d) -> p h d", h=8)
                    nc.vector.tensor_tensor(xdt[:, c, :, :], xt, hv[:, DT, c, :].unsqueeze(2).to_broadcast(
                        [P, 8, 64]), ALU.mult).then_inc(evac, 1)
                nc.vector.tensor_tensor(xend[:], k.psum[0][:].rearrange("p (h d) -> p h d", h=8),
                                        hv[:, DT_END, 0, :].unsqueeze(2).to_broadcast([P, 8, 64]),
                                        ALU.mult).then_inc(evac, 1)
                nc.vector.tensor_copy(cb[:].rearrange("p c l -> p (c l)"), k.psum[2][:, 0:2 * P]).then_inc(evac, 1)
                nc.vector.tensor_copy(bt_tok[:], k.psum[2][:, 2 * P:3 * P]).then_inc(evac, 1)
                for b in range(4):
                    c, half = b // 2, b % 2
                    dve.wait_ge(rows_up, g * 4 + (b + 1))
                    for i in range(4):
                        ins = nc.vector.scalar_tensor_tensor(
                            seg[:, b, i, :], k.psum[4 + b][:, i * P:(i + 1) * P],
                            hv[:, ACS, c, half * 4 + i:half * 4 + i + 1], const(k, "neg"), ALU.subtract, ALU.add)
                    ins.then_inc(masked, 1)
                for b in range(4):
                    dve.wait_ge(decayed, g * 4 + (b + 1))
                    if b == 0:
                        dve.wait_ge(evac, g * 5 + 5)
                    nc.vector.tensor_tensor(seg[:, b, :, :], seg[:, b, :, :], cb[:, b // 2, :].unsqueeze(
                        1).to_broadcast([P, 4, P]), ALU.mult).then_inc(weighted, 1)
                for half in range(2):
                    dve.wait_ge(rowed, g * 2 + (half + 1))
                    nc.vector.tensor_tensor(cdec[:, half, :, :], cdec[:, half, :, :], ct[:, P:2 * P].unsqueeze(
                        1).to_broadcast([P, 4, P]), ALU.mult).then_inc(cdone, 1)
                for c in range(2):
                    dve.wait_ge(y_up, g * 2 + (c + 1))
                    for i in range(4):
                        ins = nc.vector.scalar_tensor_tensor(
                            y[:, bass.ds(g * 4 + (ST_XS + i), 1), c * P:(c + 1) * P],
                            xs[:, i:i + 1, c * P:(c + 1) * P],
                            k.par[:, bass.ds(g * 4 + (PAR["dskip"] + i), 1)],
                            k.psum[c][:, i * P:(i + 1) * P].unsqueeze(1), ALU.mult, ALU.add)
                    ins.then_inc(y_down, 1)

        @block.scalar
        def _(act):
            with act.Fori(0, 4) as g:
                for b in range(4):
                    act.wait_ge(masked, g * 4 + (b + 1))
                    nc.scalar.activation(seg[:, b, :, :], seg[:, b, :, :], ACT.Exp).then_inc(decayed, 1)
                    if b >= 2:
                        nc.scalar.activation(cdec[:, b - 2, :, :].rearrange("p h l -> p (h l)"),
                                             k.psum[4 + b][:], ACT.Exp).then_inc(rowed, 1)
                act.wait_ge(states_up, g + 1)
                nc.scalar.copy(state[:], k.psum[3][:]).then_inc(state_down, 1)


def stage_ssm_gate(nc, k, y):
    with ExitStack() as ctx:
        half_done = ctx.enter_context(nc.semaphore("gate_done"))
        block = ctx.enter_context(nc.Block())

        @block.vector
        def _(dve):
            for lo, hi in ((0, 4), (4, 8), (8, 12), (12, 16)):
                nc.vector.tensor_tensor(y[:, ST_XS + lo:ST_XS + hi, :], y[:, ST_XS + lo:ST_XS + hi, :],
                                        y[:, lo:hi, :], ALU.mult)
    stage_norm(nc, k, y[:, ST_XS:ST_XS + 16, :], 16, T, row(k, "ssmg", 0, 16), None,
               y[:, ST_XS:ST_XS + 16, :], None, "ssm")


def stage_bias_table(nc, k, a, table):
    with ExitStack() as ctx:
        rel = ctx.enter_context(nc.sbuf_tensor("bias_rel", [32, 48], F32))
        onehot = ctx.enter_context(nc.sbuf_tensor("bias_onehot", [32, 384], F32))
        neg = ctx.enter_context(nc.sbuf_tensor("bias_neg", [48, 384], F32))
        flat = ctx.enter_context(nc.sbuf_tensor("bias_flat", [48, 384], F32))
        landed = ctx.enter_context(nc.semaphore("bias_landed"))
        looked_up = ctx.enter_context(nc.semaphore("bias_looked_up"))
        masked = ctx.enter_context(nc.semaphore("bias_masked"))
        kept = ctx.enter_context(nc.semaphore("bias_kept"))
        block = ctx.enter_context(nc.Block())

        @block.sync
        def _(sp):
            sp.dma_start(rel[:], a["rel_table"]).then_inc(landed, 16)
            sp.dma_start(onehot[:], a["bias_onehot"]).then_inc(landed, 16)
            sp.dma_start(neg[:], a["bias_neg"]).then_inc(landed, 16)
            sp.wait_ge(masked, 1)
            sp.dma_start(table, flat[:]).then_inc(kept, 16)
            sp.wait_ge(kept, 16)

        @block.tensor
        def _(pe):
            pe.wait_ge(landed, 48)
            pe.matmul(k.psum[0][0:48, 0:384], rel[:], onehot[:], start=True, stop=True).then_inc(looked_up, 1)

        @block.vector
        def _(dve):
            dve.wait_ge(looked_up, 1)
            nc.vector.tensor_tensor(flat[:], k.psum[0][0:48, 0:384], neg[:], ALU.add).then_inc(masked, 1)


def stage_attention(nc, k, a, y):
    table = nc.dram_tensor("bias_table", (48, 384), F32)
    stage_bias_table(nc, k, a, table.ap())
    NQ = 3 * T + 3 * P
    with ExitStack() as ctx:
        def sb(name, shape):
            return ctx.enter_context(nc.sbuf_tensor("att_" + name, shape, F32))

        def sem(name):
            return ctx.enter_context(nc.semaphore("att_" + name))
        half = sb("half", [P, 6])
        q2 = sb("q", [P, 2, 3, T])
        kst, vst = sb("k", [P, T]), sb("v", [P, T])
        vtok = sb("vtok", [P, 2, P])
        bias = y[:, 0:12, :].rearrange("p (u e g) v -> p u e g v", u=2, e=2)
        prob = sb("prob", [P, 2, NQ])
        stat = sb("stat", [P, 2, 6])
        diag = sb("diag", [P, 2, 2, P])
        ptok = sb("ptok", [P, 2, 3 * P])
        landed0, landed1 = sem("bias_even"), sem("bias_odd")
        half_landed = sem("half_landed")
        staged, q_up, scored, added = sem("staged"), sem("q_up"), sem("scored"), sem("added")
        maxed, exped, normed = sem("maxed"), sem("exped"), sem("normed")
        v_up, v_down, turned, p_down, o_up, o_down = sem("v_up"), sem("v_down"), sem("turned"), sem("p_down"), \
            sem("o_up"), sem("o_down")
        step = sem("step")
        ident = const(k, "ident")
        TURNS = 4

        with nc.Block() as block:
            @block.sync
            def _(sp):
                sp.dma_start(half[:], a["half_masks"]).then_inc(half_landed, 16)
                sp.wait_ge(half_landed, 16)
        block = ctx.enter_context(nc.Block())

        @block.sync
        def _(sp):
            with sp.Fori(0, TURNS) as t:
                for u in range(2):
                    sp.wait_ge(added, t * 4 + 0)
                    for e in range(2):
                        for g in range(3):
                            src = bass.AP(table, (t * 2 + u) * 768 + (g * 16 * 384 + e * 384),
                                          [[1, P], [1, T]])
                            sp.dma_start(bias[:, u, e, g, :], src).then_inc(landed0 if u == 0 else landed1, 16)

        @block.scalar
        def _(act):
            with act.Fori(0, TURNS) as t:
                for u in range(2):
                    i = t * 2 + u
                    act.wait_ge(o_up, i * 2)
                    act.wait_ge(v_up, i)
                    for e in range(2):
                        nc.scalar.activation(
                            q2[:, e, :, ::-1], y[:, ST_Q:ST_Q + 24, :].rearrange("p (g h) t -> p g h t", g=3)[
                                :, :, bass.ds(i, 1), :].rearrange("p g o t -> p g (o t)"),
                            ACT.Copy, scale=half[:, e:e + 1]).then_inc(q_up, 1)
                    for e in range(2):
                        n = i * 2 + e
                        act.wait_ge(maxed, n + 1)
                        p0 = prob[:, e, 3 * T:]
                        nc.scalar.activation(prob[:, e, 0:3 * T], prob[:, e, 0:3 * T], ACT.Exp,
                                             bias=stat[:, e, 1:2], accum_out=stat[:, e, 3:4])
                        nc.scalar.activation(p0, p0, ACT.Exp, bias=stat[:, e, 0:1],
                                             accum_out=stat[:, e, 2:3]).then_inc(exped, 1)
                    for e in range(2):
                        n = i * 2 + e
                        act.wait_ge(turned, n + 1)
                        nc.scalar.copy(ptok[:, e, :], k.psum[6][:, 0:3 * P]).then_inc(p_down, 1)

        @block.gpsimd
        def _(pool):
            with pool.Fori(0, TURNS) as t:
                for u in range(2):
                    i = t * 2 + u
                    pool.wait_ge(o_up, i * 2)
                    pool.wait_ge(v_up, i)
                    nc.gpsimd.tensor_copy(kst[:].unsqueeze(1), y[:, bass.ds(i + ST_K, 1), :]).then_inc(staged, 1)
                    nc.gpsimd.tensor_copy(vst[:].unsqueeze(1), y[:, bass.ds(i + ST_V, 1), :]).then_inc(staged, 1)

        @block.tensor
        def _(pe):
            with pe.Fori(0, TURNS) as t:
                for u in range(2):
                    i = t * 2 + u
                    pe.wait_ge(staged, i * 2 + 2)
                    for e in range(2):
                        pe.wait_ge(q_up, i * 2 + (e + 1))
                        pe.wait_ge(added, i * 2)
                        for g in range(3):
                            pe.matmul(k.psum[3 * e + g // 2][:, (g % 2) * T:(g % 2 + 1) * T], q2[:, e, g, 0:P],
                                      kst[:], start=True, stop=True)
                        for g in range(3):
                            mm = pe.matmul(k.psum[3 * e + 2][:, g * P:(g + 1) * P], q2[:, e, g, P:2 * P], kst[:, 0:P],
                                           start=True, stop=True)
                        mm.then_inc(scored, 1)
                    pe.wait_ge(o_down, i)
                    for c in range(2):
                        mm = pe.transpose(k.psum[7][:, c * P:(c + 1) * P], vst[:, c * P:(c + 1) * P], ident)
                    mm.then_inc(v_up, 1)
                    for e in range(2):
                        n = i * 2 + e
                        pe.wait_ge(normed, n + 1)
                        if e == 1:
                            pe.wait_ge(p_down, i * 2 + 1)
                        for blk, keys in ((0, 1), (1, 2)):
                            for kb in range(keys):
                                at = (blk + kb) * P
                                for g in range(3):
                                    lo = (3 * T + g * P) if blk == 0 else (g * T + kb * P)
                                    mm = pe.matmul(k.psum[6][:, at:at + P], prob[:, e, lo:lo + P],
                                                   diag[:, e, blk, :], start=(g == 0), stop=(g == 2))
                        mm.then_inc(turned, 1)
                    for e in range(2):
                        n = i * 2 + e
                        pe.wait_ge(p_down, n + 1)
                        pe.wait_ge(v_down, i + 1)
                        out = k.psum[7][e * 64:(e + 1) * 64, :]
                        pe.matmul(out[:, 0:P], vtok[:, 0, e * 64:(e + 1) * 64], ptok[:, e, 0:P], start=True,
                                  stop=True)
                        for kb in range(2):
                            mm = pe.matmul(out[:, P:2 * P], vtok[:, kb, e * 64:(e + 1) * 64],
                                           ptok[:, e, (1 + kb) * P:(2 + kb) * P], start=(kb == 0), stop=(kb == 1))
                        mm.then_inc(o_up, 1)

        @block.vector
        def _(dve):
            with dve.Fori(0, TURNS) as t:
                s = Steps(dve, step, t * 8)
                for u in range(2):
                    i = t * 2 + u
                    dve.wait_ge(landed0 if u == 0 else landed1, t * 96 + 96)
                    for e in range(2):
                        dve.wait_ge(scored, i * 2 + (e + 1))
                        dve.wait_ge(turned, i * 2)
                        pe1 = prob[:, e, 0:3 * T].rearrange("p (g v) -> p g v", g=3)
                        pe0 = prob[:, e, 3 * T:].rearrange("p (g v) -> p g v", g=3)
                        nc.vector.scalar_tensor_tensor(pe1[:, 0:2, :], k.psum[3 * e][:].rearrange(
                            "p (g v) -> p g v", g=2), 0.125, bias[:, u, e, 0:2, :], ALU.mult, ALU.add)
                        nc.vector.scalar_tensor_tensor(pe1[:, 2:3, :], k.psum[3 * e + 1][:, 0:T].unsqueeze(1),
                                                       0.125, bias[:, u, e, 2:3, :], ALU.mult, ALU.add)
                        nc.vector.scalar_tensor_tensor(pe0, k.psum[3 * e + 2][:, 0:3 * P].rearrange(
                            "p (g v) -> p g v", g=3), 0.125, bias[:, u, e, :, P:2 * P], ALU.mult,
                            ALU.add).then_inc(added, 1)
                        dve.wait_ge(added, i * 2 + (e + 1))
                        nc.vector.tensor_reduce(stat[:, e, 4:5], prob[:, e, 3 * T:], AX, ALU.max)
                        s(nc.vector.tensor_reduce(stat[:, e, 5:6], prob[:, e, 0:3 * T], AX, ALU.max))
                        nc.vector.tensor_scalar(stat[:, e, 0:2], stat[:, e, 4:6], -1.0, None,
                                                ALU.mult).then_inc(maxed, 1)
                    dve.wait_ge(v_up, i + 1)
                    nc.vector.tensor_copy(vtok[:].rearrange("p c v -> p (c v)"), k.psum[7][:, 0:T]).then_inc(
                        v_down, 1)
                    for e in range(2):
                        dve.wait_ge(exped, i * 2 + (e + 1))
                        s(nc.vector.reciprocal(stat[:, e, 4:6], stat[:, e, 2:4]))
                        nc.vector.tensor_scalar(diag[:, e, 0, :], const(k, "flip"), stat[:, e, 4:5], None, ALU.mult)
                        nc.vector.tensor_scalar(diag[:, e, 1, :], const(k, "flip"), stat[:, e, 5:6], None,
                                                ALU.mult).then_inc(normed, 1)
                    dve.wait_ge(o_up, i * 2 + 2)
                    nc.vector.tensor_copy(y[:, bass.ds(i + ST_Q, 1), :], k.psum[7][:, 0:T].unsqueeze(
                        1)).then_inc(o_down, 1)
                assert s.n == 8


def stage_out(nc, k, first, rhs, gain):
    groups = 2
    per = -(-len(rhs) // KT)
    with ExitStack() as ctx:
        done = ctx.enter_context(nc.semaphore("out_done"))
        block = ctx.enter_context(nc.Block())

        @block.sync
        def _(sp):
            load_ahead(k, sp, first, groups * per)

        @block.tensor
        def _(pe):
            n = first
            for grp in range(groups):
                for part in range(per):
                    kts = range(min(KT, len(rhs) - part * KT))
                    wait_slot(k, pe, n)
                    for i in range(4):
                        for kt in kts:
                            mm = pe.matmul(k.psum[grp * 4 + i][:, 0:T], ring_tile(k, n, kt, i * P),
                                           rhs[part * KT + kt], start=(part == 0 and kt == 0),
                                           stop=(part == per - 1 and kt == kts[-1]))
                    mm.then_inc(k.slot_used, 1)
                    n += 1

        @block.vector
        def _(dve):
            for grp in range(groups):
                dve.wait_ge(k.slot_used, first + (grp + 1) * per)
                for i in range(4):
                    m = grp * 4 + i
                    nc.vector.scalar_tensor_tensor(k.x[:, m, :], k.psum[m][:, 0:T], gain[:, m:m + 1], k.x[:, m, :],
                                                   ALU.mult, ALU.add)


def stage_ffn(nc, k, h, up, down, gain, which):
    count = FT // 2
    turns = count // RING
    with ExitStack() as lay:
        hid = lay.enter_context(nc.sbuf_tensor(f"ffn_hidden{which}", [P, FT, T], F32))
        with ExitStack() as ctx:
            gate = ctx.enter_context(nc.sbuf_tensor(f"ffn_gate{which}", [P, 2, 512], F32))
            gated = ctx.enter_context(nc.semaphore("ffn_gated"))
            stored = ctx.enter_context(nc.semaphore("ffn_stored"))
            block = ctx.enter_context(nc.Block())

            def over_slots(eng, one):
                with eng.Fori(0, turns) as t:
                    for j in range(RING):
                        one(j, t)
                for j in range(turns * RING, count):
                    one(j, 0)

            @block.sync
            def _(sp):
                load_ahead(k, sp, up, count)

            @block.tensor
            def _(pe):
                rhs = [h[:, kt, :] for kt in range(KT)]

                def one(j, t):
                    pe.wait_ge(stored, t * RING + (j + 1))
                    b = 2 * (j % 2)
                    outs = [k.psum[b + i // 2][:, (i % 2) * T:(i % 2 + 1) * T] for i in range(4)]
                    slot_products(k, pe, up + j, t, rhs, outs).then_inc(k.slot_used, 1)
                over_slots(pe, one)

            @block.scalar
            def _(act):
                def one(j, t):
                    act.wait_ge(k.slot_used, t * RING + (up + j + 1))
                    act.wait_ge(stored, t * RING + (j + 1))
                    nc.scalar.activation(gate[:, j % 2, :], k.psum[2 * (j % 2)][:], ACT.Silu).then_inc(gated, 1)
                over_slots(act, one)

            @block.vector
            def _(dve):
                dve.sem_inc(stored, 2)

                def one(j, t):
                    dve.wait_ge(gated, t * RING + (j + 1))
                    nc.vector.tensor_tensor(hid[:, bass.ds(t * 8 + 2 * j, 2), :].rearrange("p a t -> p (a t)"),
                                            gate[:, j % 2, :], k.psum[2 * (j % 2) + 1][:], ALU.mult).then_inc(
                                                stored, 1)
                over_slots(dve, one)
        stage_out(nc, k, down, [hid[:, i, :] for i in range(FT)], gain)


def stage_conformer(nc, k, h):
    NS = 4
    with ExitStack() as lay:
        u = lay.enter_context(nc.sbuf_tensor("cv_u", [P, KT, T], F32))
        v = lay.enter_context(nc.sbuf_tensor("cv_v", [P, KT, T], F32))
        sq = lay.enter_context(nc.sbuf_tensor("cv_sq", [P, KT, T], F32))
        first = FIRST["pw1"]
        with ExitStack() as ctx:
            sig = ctx.enter_context(nc.sbuf_tensor("cv_sig", [P, KT, T], F32))
            gated = ctx.enter_context(nc.semaphore("cv_gated"))
            block = ctx.enter_context(nc.Block())

            @block.sync
            def _(sp):
                load_ahead(k, sp, first, NS)

            @block.tensor
            def _(pe):
                rhs = [h[:, kt, :] for kt in range(KT)]
                for j in range(NS):
                    outs = [k.psum[2 * j + i // 2][:, (i % 2) * T:(i % 2 + 1) * T] for i in range(4)]
                    slot_products(k, pe, first + j, 0, rhs, outs).then_inc(k.slot_used, 1)

            @block.scalar
            def _(act):
                for j in range(NS):
                    act.wait_ge(k.slot_used, first + j + 1)
                    for i in range(2):
                        m = 2 * j + i
                        nc.scalar.activation(sig[:, m, :], k.psum[2 * j + 1][:, i * T:(i + 1) * T], ACT.Sigmoid,
                                             bias=row(k, "pw1b", 8 + m)).then_inc(gated, 1)

            @block.vector
            def _(dve):
                for m in range(KT):
                    dve.wait_ge(gated, m + 1)
                    nc.vector.scalar_tensor_tensor(u[:, m, :], k.psum[2 * (m // 2)][:, (m % 2) * T:(m % 2 + 1) * T],
                                                   row(k, "pw1b", m), sig[:, m, :], ALU.add, ALU.mult)
        with ExitStack() as ctx:
            step = ctx.enter_context(nc.semaphore("cv_step"))
            block = ctx.enter_context(nc.Block())

            @block.vector
            def _(dve):
                G = 2
                with dve.Fori(0, KT // G) as t:
                    s = Steps(dve, step, t * (TAPS * G))
                    for tap in range(TAPS):
                        for j in range(G):
                            i = t * G + j
                            src, acc = u[:, bass.ds(i, 1), :], v[:, bass.ds(i, 1), :]

                            def w(c):
                                return k.par[:, bass.ds(i * (TAPS + 1) + (PAR["dw"] + c), 1)]
                            if tap == 0:
                                ins = nc.vector.tensor_scalar(acc, src, w(TAPS - 1), w(TAPS), ALU.mult, ALU.add)
                            else:
                                ins = nc.vector.scalar_tensor_tensor(
                                    v[:, bass.ds(i, 1), tap:], u[:, bass.ds(i, 1), :T - tap], w(TAPS - 1 - tap),
                                    v[:, bass.ds(i, 1), tap:], ALU.mult, ALU.add)
                            ins.then_inc(step, 1)
                            s.n += 1
                        dve.wait_ge(step, s.done + s.n)
        with ExitStack() as ctx:
            mean = ctx.enter_context(nc.sbuf_tensor("cv_mean", [P, 2, T], F32))
            meant = ctx.enter_context(nc.semaphore("cv_meant"))
            centred = ctx.enter_context(nc.semaphore("cv_centred"))
            squared = ctx.enter_context(nc.semaphore("cv_squared"))
            summed = ctx.enter_context(nc.semaphore("cv_summed"))
            step = ctx.enter_context(nc.semaphore("cv_lnstep"))
            rooted = ctx.enter_context(nc.semaphore("cv_rooted"))
            scaled = ctx.enter_context(nc.semaphore("cv_scaled"))
            block = ctx.enter_context(nc.Block())

            @block.tensor
            def _(pe):
                for i in range(KT):
                    mm = pe.matmul(k.psum[0][:, 0:T], const(k, "ones"), v[:, i, :], start=(i == 0), stop=(i == 7))
                mm.then_inc(meant, 1)
                pe.wait_ge(squared, 1)
                for i in range(KT):
                    mm = pe.matmul(k.psum[1][:, 0:T], const(k, "ones"), sq[:, i, :], start=(i == 0), stop=(i == 7))
                mm.then_inc(summed, 1)

            @block.vector
            def _(dve):
                s = Steps(dve, step)
                dve.wait_ge(meant, 1)
                s(nc.vector.tensor_scalar(mean[:, 0, :], k.psum[0][:, 0:T], 1.0 / D, None, ALU.mult))
                nc.vector.tensor_tensor(v[:], v[:], mean[:, 0:1, :].to_broadcast([P, KT, T]),
                                        ALU.subtract).then_inc(centred, 1)
                dve.wait_ge(summed, 1)
                s(nc.vector.tensor_scalar(mean[:, 1, :], k.psum[1][:, 0:T], 1.0 / D, EPS, ALU.mult, ALU.add))
                dve.wait_ge(rooted, 1)
                s(nc.vector.reciprocal(mean[:, 1, :], mean[:, 1, :]))
                nc.vector.tensor_tensor(v[:], v[:], mean[:, 1:2, :].to_broadcast([P, KT, T]),
                                        ALU.mult).then_inc(scaled, 1)

            @block.scalar
            def _(act):
                act.wait_ge(centred, 1)
                nc.scalar.activation(sq[:], v[:], ACT.Square).then_inc(squared, 1)
                act.wait_ge(step, 2)
                nc.scalar.activation(mean[:, 1, :], mean[:, 1, :], ACT.Sqrt).then_inc(rooted, 1)
                act.wait_ge(scaled, 1)
                for i in range(KT):
                    nc.scalar.activation(u[:, i, :], v[:, i, :], ACT.Silu, bias=row(k, "lnb", i),
                                         scale=row(k, "lng", i))
        first = FIRST["pw2"]
        with ExitStack() as ctx:
            biased = ctx.enter_context(nc.semaphore("cv_biased"))
            block = ctx.enter_context(nc.Block())

            @block.sync
            def _(sp):
                load_ahead(k, sp, first, 2)

            @block.tensor
            def _(pe):
                rhs = [u[:, kt, :] for kt in range(KT)]
                for j in range(2):
                    outs = [k.psum[4 * j + i][:, 0:T] for i in range(4)]
                    slot_products(k, pe, first + j, 0, rhs, outs).then_inc(k.slot_used, 1)

            @block.scalar
            def _(act):
                for m in range(KT):
                    act.wait_ge(k.slot_used, first + m // 4 + 1)
                    nc.scalar.activation(v[:, m, :], k.psum[m][:, 0:T], ACT.Identity,
                                         bias=row(k, "pw2b", m)).then_inc(biased, 1)

            @block.vector
            def _(dve):
                for m in range(KT):
                    dve.wait_ge(biased, m + 1)
                    nc.vector.scalar_tensor_tensor(k.x[:, m, :], v[:, m, :], k.mod[:, 64 + m:65 + m], k.x[:, m, :],
                                                   ALU.mult, ALU.add)


GN_EPS = 64e-5
CH = 128
NCH = 2 * T // CH
SH, SC, GT = 0, 8, 16


def mod2(k, layer, part, ctx=False):
    c = 48 * ctx + 24 * layer + part
    return k.mod[:, c:c + 8]


def stage_shift(nc, k, h, xx):
    hs, xs = (b[:].rearrange("p k (s t) -> p (k s) t", s=2) for b in (h, xx))
    with ExitStack() as ctx:
        step = ctx.enter_context(nc.semaphore("shift_step"))
        block = ctx.enter_context(nc.Block())

        @block.vector
        def _(dve):
            s = Steps(dve, step)
            s(nc.vector.tensor_scalar(xs, hs, -1.0, None, ALU.mult))
            s(nc.vector.scalar_tensor_tensor(xs[:, :, 1:], hs[:, :, :T - 1], 0.5, xs[:, :, 1:], ALU.mult, ALU.add))
            s(nc.vector.scalar_tensor_tensor(xs[:, :, :T - 1], hs[:, :, 1:], 0.5, xs[:, :, :T - 1], ALU.mult,
                                             ALU.add))


def stage_rwkv_in(nc, k, a, h, xx, lora, kept):
    R, K, V, G, W, A = range(6)
    first = FIRST["rkvg"]
    with ExitStack() as ctx:
        l0 = ctx.enter_context(nc.sbuf_tensor("mixed0", [P, KT, 512], F32))
        l1 = ctx.enter_context(nc.sbuf_tensor("mixed1", [P, KT, 512], F32))
        w1 = ctx.enter_context(nc.sbuf_tensor("lora_in_sb", [P, KT, 256], F32))
        outb = ctx.enter_context(nc.sbuf_tensor("proj_out", [P, 2, 4, 512], F32))
        w1_landed = ctx.enter_context(nc.semaphore("lora_in_landed"))
        mixed = ctx.enter_context(nc.semaphore("mixed"))
        lora_up = ctx.enter_context(nc.semaphore("lora_up"))
        evac = ctx.enter_context(nc.semaphore("proj_evac"))
        kept0 = ctx.enter_context(nc.semaphore("proj_kept_even"))
        kept1 = ctx.enter_context(nc.semaphore("proj_kept_odd"))
        spare_kept = ctx.enter_context(nc.semaphore("proj_kept_spare"))
        block = ctx.enter_context(nc.Block())
        order = [(W, l0), (A, l1), (R, l0), (K, l1), (V, l0), (G, xx)]

        @block.sync
        def _(sp):
            sp.dma_start(w1[:], a["lora_in"]).then_inc(w1_landed, 16)
            load_ahead(k, sp, first, 4)

        @block.vector
        def _(dve):
            for n, (j, buf) in enumerate(order):
                if n in (2, 3):
                    dve.wait_ge(lora_up, n - 1)
                if n == 4:
                    dve.wait_ge(k.slot_used, first + 2)
                if n == 5:
                    dve.wait_ge(mixed, KT * n)
                for i in range(KT):
                    nc.vector.scalar_tensor_tensor(buf[:, i, :], xx[:, i, :], row(k, "mu", 8 * j + i), h[:, i, :],
                                                   ALU.mult, ALU.add).then_inc(mixed, 1)

        @block.tensor
        def _(pe):
            pe.wait_ge(w1_landed, 16)
            for n in range(2):
                pe.wait_ge(mixed, KT * (n + 1))
                for kt in range(KT):
                    mm = pe.matmul(k.psum[n][:], w1[:, kt, n * P:(n + 1) * P], order[n][1][:, kt, :],
                                   start=(kt == 0), stop=(kt == KT - 1))
                mm.then_inc(lora_up, 1)
            for j in range(8):
                n = 2 + j // 2
                pe.wait_ge(mixed, KT * (n + 1))
                if j >= 2:
                    pe.wait_ge(evac, 2 + 4 * (j - 1))
                elif j == 0:
                    pe.wait_ge(evac, 2)
                outs = [k.psum[4 * (j % 2) + i][:] for i in range(4)]
                rhs = [order[n][1][:, kt, :] for kt in range(KT)]
                slot_products(k, pe, first + j, 0, rhs, outs).then_inc(k.slot_used, 1)

        @block.scalar
        def _(act):
            act.wait_ge(lora_up, 1)
            for d in range(2):
                rows = slice(64 * d, 64 * d + 64)
                ins = nc.scalar.activation(lora[rows, d, 0, :], k.psum[0][rows, :], ACT.Tanh)
            ins.then_inc(evac, 1)
            act.wait_ge(lora_up, 2)
            for d in range(2):
                rows = slice(64 * d, 64 * d + 64)
                ins = nc.scalar.copy(lora[rows, d, 1, :], k.psum[1][rows, :])
            ins.then_inc(evac, 1)
            for j in range(8):
                act.wait_ge(k.slot_used, first + j + 1)
                if j >= 2:
                    act.wait_ge((kept0, kept1)[j % 2], 16 * (j // 2))
                for i in range(4):
                    nc.scalar.copy(outb[:, j % 2, i, :], k.psum[4 * (j % 2) + i][:]).then_inc(evac, 1)

        @block.gpsimd
        def _(pool):
            nc.gpsimd.memset(lora[64:P, 0, :, :], 0.0)
            nc.gpsimd.memset(lora[0:64, 1, :, :], 0.0)
            pool.dma_start(kept[KT], h[:, 0:4, :]).then_inc(spare_kept, 16)
            for j in range(8):
                pool.wait_ge(evac, 2 + 4 * (j + 1))
                pool.dma_start(kept[4 * (j % 2):4 * (j % 2) + 4, :, j // 2, :].rearrange("t p n -> p t n"),
                               outb[:, j % 2, :, :]).then_inc((kept0, kept1)[j % 2], 16)
            pool.wait_ge(kept0, 64)
            pool.wait_ge(kept1, 64)
            pool.wait_ge(spare_kept, 16)


class Track:

    def __init__(self, sem, items, marks):
        self.sem, self.n, self.seen = sem, 0, {}
        self.names, self.item_of = [], {}
        for i, item in enumerate(items):
            for name in marks(item):
                assert name not in self.item_of, name
                self.names.append(name)
                self.item_of[name] = i
        self.at = {name: i + 1 for i, name in enumerate(self.names)}

    def start(self, eng):
        if self.names:
            eng.sem_inc(self.sem, len(self.names))

    def mark(self, ins, name):
        assert self.names[self.n] == name, (self.names[self.n], name)
        self.n += 1
        ins.then_inc(self.sem, 1)

    def wait(self, eng, turn, here, *names, apart=False):
        counts = [self.at[n] + (len(self.names) if self.item_of[n] <= here else 0) for n in names if n in self.at]
        count = max(counts, default=0)
        if count > self.seen.get(id(eng), 0):
            self.seen[id(eng)] = count
            eng.wait_ge(self.sem, turn * len(self.names) + count)
        if apart:
            eng.nop(nofuse=True)


LEVELS = range(1, 7)
ORDER = [[0, 1, 2, 3], [1, 0, 3, 2]]
PREP = ["lw", "cum", "half", "mid", "dif", "blend", "kd", "b", "ksum"]


def prep_items(p):
    return [("lora", p)] + [("el", p, n) for n in PREP[:3]] + [("eh", p)] + [("el", p, n) for n in PREP[3:5]] + \
        [("exps", p)] + [("el", p, n) for n in PREP[5:]] + [("fin", p)]


def serial_items(s):
    return [(kind, s, q) for q in range(NCH) for kind in ("X", "SA", "U", "Y")]


def merge(*lists):
    total = max(len(x) for x in lists)
    keyed = [((i + 0.5) / len(x), n, item) for n, x in enumerate(lists) for i, item in enumerate(x)]
    return [item for _, _, item in sorted(keyed, key=lambda z: (z[0], z[1]))]


def section(d):
    s = p = 1 - d
    head = [("g", d, e, m) for e in range(2) for m in range(4)]
    head = merge(head, [("bup", d), ("keep", d)])
    body = []
    for e in range(2):
        body += [("T", d, e)]
    for lv in LEVELS:
        body += [(kind, d, lv, e) for kind in (("W", "Pt", "Tr") if lv < 6 else ("W", "Pt")) for e in range(2)]
    if d == 0:
        side = serial_items(s) + [("read0",), ("read1",), ("read2",), ("vtok",)]
        prep = prep_items(p)
    else:
        side = serial_items(s)
        prep = [("bonus",), ("stage",), ("kk",)] + prep_items(p)
    return head + merge(body, side, prep)


def marks(item):
    k, rest = item[0], item[1:]
    n = "".join(str(x) for x in rest)
    none = []
    return {
        "g": lambda: ([f"m{n}"] + ([f"i{rest[0]}0{rest[1]}"] if rest[-1:] == (0,) else []), none, [f"g{n}"], none),
        "bup": lambda: (none, [f"btok{n}", f"ktok{n}"], [f"bup{n}", f"kup{n}"], none),
        "keep": lambda: (none, none, none, [f"keep{n}"]),
        "T": lambda: ([f"t{rest[0]}0{rest[-1]}"], none, [f"T{n}"], none),
        "W": lambda: (none, [f"Wc{n}"], [f"W{n}"], none),
        "Pt": lambda: ([f"t{n}"], none, [f"Pt{n}"], [f"eyeM{rest[0]}"] if rest[1:] == (6, 1) else none),
        "Tr": lambda: (none, [f"Mc{n}"], [f"Tr{n}"], none),
        "X": lambda: ([f"ze{n}", f"x{n}"], none, [f"X{n}"], none),
        "SA": lambda: ([f"sa{n}", f"sb{n}"], none, [f"SA{n}"], [f"eyeT{rest[0]}"] if rest[1:] == (3,) else none),
        "U": lambda: ([f"z{n}"], none, [f"U{n}"], none),
        "Y": lambda: ([f"y{n}"], none, [f"Y{n}"], none),
        "lora": lambda: (none, [f"sigw{n}", f"siga{n}"], [f"lora{n}"], none),
        "el": lambda: ([rest[1] + str(rest[0])] if len(rest) > 1 else none, none, none, none),
        "eh": lambda: (none, [f"eh{n}"], none, none),
        "exps": lambda: (none, [f"ee{n}", f"ei{n}", f"en{n}"], none, none),
        "fin": lambda: ([f"at{n}", f"rt{n}", f"bt{n}", f"kt{n}", f"E{n}"], [f"am{n}", f"rm{n}"], none, none),
        "bonus": lambda: (["rk", "bon"], ["silu"], ["bonus"], none),
        "stage": lambda: (none, none, none, ["staged"]),
        "kk": lambda: (["omka", "kkraw", "kksq", "kkmax", "kkrec", "kk"], ["norm"], ["squp"], none),
        "read0": lambda: (["mean", "xc"], ["ysq"], ["mean"], none),
        "read1": lambda: (["var", "yrec"], ["yroot"], ["var"], none),
        "read2": lambda: (["yn", "ynl", "ysum", "o"], none, none, none),
        "vtok": lambda: (["vm"], ["vtok"], ["vup"], none),
    }[k]()


def stage_rwkv_scan(nc, k, a, lora, kept, o):
    HALF_E = -math.exp(-0.5)
    with ExitStack() as ctx:
        flat = k.ring[:].rearrange("p r s -> p (r s)")
        used = [0]

        def in_ring(*shape):
            n = int(np.prod(shape))
            ap = flat[:, used[0]:used[0] + n]
            used[0] += n
            assert used[0] <= RING * SLOT
            if len(shape) == 1:
                return ap
            names = "abcd"[:len(shape)]
            return ap.rearrange(f"p ({' '.join(names)}) -> p {' '.join(names)}", **dict(zip(names, shape)))

        def sb(name, *shape, dt=F32):
            return ctx.enter_context(nc.sbuf_tensor("rw_" + name, [P, *shape], dt))

        def sem(name):
            return ctx.enter_context(nc.semaphore("rw_" + name))
        MT, AKT, RBT, RKT = (in_ring(2, 2, NCH, P) for _ in range(4))
        AB, M, Wb = (in_ring(2, NCH, P) for _ in range(3))
        at2, rt2 = in_ring(2, 512), in_ring(2, 512)
        vtok2 = in_ring(2, NCH, P)
        tin = in_ring(4, 512)
        lora_out, tri, lvl, starts = sb("lora_out", 2, 9 * P), sb("tri", 4, P), sb("lvl", 2, 7, P, dt=U8), \
            sb("starts", 512)
        half2 = sb("half2", 6)
        pre, w2, rp, omka = sb("pre", 4, 512), sb("w2", 2, P), sb("rp", 9), sb("omka", 1)
        kk, sq, lw, av, mid, dif, kd, bb, ksum, ee, ei, en, at, rt, bt, kt_, yf, bonv, sg, tmp = (
            sb(n, 512) for n in ("kk", "sq", "lw", "av", "mid", "dif", "kd", "bb", "ksum", "ee", "ei", "en", "at",
                                 "rt", "bt", "kt", "yf", "bonv", "sg", "tmp"))
        hs_, eh, dec = sb("half", NCH), sb("eh", NCH), sb("dec", 4)
        atS, rtS, decS = sb("atS", 2, 512), sb("rtS", 2, 512), sb("decS", 2, 4)
        btok, ktok, vtok = sb("btok", 2, NCH, P), sb("ktok", 2, NCH, P), sb("vtok", NCH, P)
        xs2, sas2, sas = sb("xs2", 2, P), sb("sas2", 2, P), sb("sas", P)
        z, ze = sb("z", P), sb("ze", P)
        consts = sem("consts")
        ident, headones = const(k, "ident"), const(k, "headones")
        W0, A0, KK_, KA, RK_, LG, LB = 0, 2, 4, 5, 6, 7, 8
        rr, kx, vv, gg = (tin[:, i, :] for i in range(4))
        b = k.psum
        HALVES = [slice(0, 64), slice(64, 128)]

        def chunks(ap):
            return ap.rearrange("p (c t) -> p c t", c=NCH)

        def diagonal(buf):
            f = buf[:].rearrange("p e v -> p (e v)")
            return bass.AP(f.tensor, f.offset, [list(f.ap[0]), [192, 2], [1, 64]])

        wide = pre[:].rearrange("p j n -> p (j n)")[:, 0:14 * P].bitcast(I32)
        with nc.Block() as block:
            @block.sync
            def _(sp):
                sp.dma_start(lora_out[:], a["lora_out"]).then_inc(consts, 16)
                sp.dma_start(tri[:].rearrange("p m f -> p (m f)"), a["tri_masks"]).then_inc(consts, 16)
                sp.dma_start(wide, a["level_masks"]).then_inc(consts, 16)
                sp.dma_start(starts[:], a["chunk_starts"]).then_inc(consts, 16)
                sp.dma_start(half2[:], a["half_masks"]).then_inc(consts, 16)
                sp.wait_ge(consts, 80)

            @block.vector
            def _(dve):
                for buf in (MT, AKT, RBT, RKT):
                    nc.vector.memset(buf[:, 1, :, :, :], 0.0)
                for buf in (vtok2, vtok[:], xs2[:], sas2[:], z[:], yf[:], decS[:], bonv[:], sg[:]):
                    nc.vector.memset(buf, 0.0)
                dve.wait_ge(consts, 80)
                nc.vector.tensor_copy(lvl[:].rearrange("p u l f -> p (u l f)"), wide)

            @block.gpsimd
            def _(pool):
                for buf in (atS, rtS):
                    nc.gpsimd.memset(buf[:, 1, :], 0.0)
                for buf in (btok, ktok):
                    nc.gpsimd.memset(buf[:, 1, :, :], 0.0)
                src = ident.unsqueeze(1).to_broadcast([P, 2 * NCH, P])
                nc.gpsimd.tensor_copy(M.rearrange("p e c f -> p (e c) f"), src)
                nc.gpsimd.tensor_copy(MT[:, 0, :, :, :].rearrange("p e c f -> p (e c) f"), src)

        def run(items, turns, part):
            with ExitStack() as inner:
                dv, ac, pt, pl = (Track(inner.enter_context(nc.semaphore(f"rw_{n}_{part}")), items,
                                        lambda item, i=i: marks(item)[i]) for i, n in enumerate(
                                            ("dve", "act", "pe", "pool")))
                pre_landed = inner.enter_context(nc.semaphore(f"rw_pre_{part}"))
                block = inner.enter_context(nc.Block())

                def loop(eng, body):
                    if turns:
                        with eng.Fori(0, turns) as t:
                            body(t)
                    else:
                        body(0)
                next_tile = 1 if turns else 0

                @block.sync
                def _(sp):
                    def body(t):
                        if ("stage",) in items:
                            pl.wait(sp, t, items.index(("stage",)) - 1, "staged")
                            sp.dma_start(pre[:].unsqueeze(1), kept[bass.ds(t + next_tile, 1), :, :, :].rearrange(
                                "o p j n -> p o j n")).then_inc(pre_landed, 16)
                    loop(sp, body)

                @block.gpsimd
                def _(pool):
                    pl.start(pool)
                    eye = ident.unsqueeze(1).to_broadcast([P, 2 * NCH, P])

                    def body(t):
                        for i, item in enumerate(items):
                            kind, d = item[0], item[1] if len(item) > 1 else None
                            if kind == "keep":
                                dv.wait(pool, t, i, f"E{d}")
                                pt.wait(pool, t, i, f"Y{d}3", apart=True)
                                nc.gpsimd.tensor_copy(atS[:, d, :], at[:])
                                nc.gpsimd.tensor_copy(decS[:, d, 0:3], dec[:, 0:3])
                                pl.mark(nc.gpsimd.tensor_copy(rtS[:, d, :], rt[:]), f"keep{d}")
                            elif kind == "Pt" and item[2:] == (6, 1) and part == "loop":
                                pt.wait(pool, t, i, f"Pt{d}61", apart=True)
                                pl.mark(nc.gpsimd.tensor_copy(M.rearrange("p e c f -> p (e c) f"), eye), f"eyeM{d}")
                            elif kind == "SA" and item[2] == 3 and part == "loop":
                                pt.wait(pool, t, i, f"SA{d}3", apart=True)
                                pl.mark(nc.gpsimd.tensor_copy(MT[:, d, :, :, :].rearrange(
                                    "p e c f -> p (e c) f"), eye), f"eyeT{d}")
                            elif kind == "stage":
                                pool.wait_ge(pre_landed, t * 16 + 16)
                                pt.wait(pool, t, i, "vup")
                                ac.wait(pool, t, i, "silu")
                                dv.wait(pool, t, i, "bon", apart=True)
                                nc.gpsimd.tensor_copy(tin, pre[:])
                                nc.gpsimd.tensor_copy(w2[:], lora_out[:, :, bass.ds((t + next_tile) * P, P)])
                                pl.mark(nc.gpsimd.tensor_copy(
                                    rp[:], k.par[:, bass.ds((t + next_tile) * 9 + PAR["rw"], 9)]), "staged")
                    loop(pool, body)

                @block.scalar
                def _(act):
                    ac.start(act)

                    def body(t):
                        for i, item in enumerate(items):
                            kind, d = item[0], item[1] if len(item) > 1 else None
                            n = "".join(str(x) for x in item[1:])
                            if kind == "bup":
                                for dst, bk, up, name in ((btok, 4, "bup", "btok"), (ktok, 5, "kup", "ktok")):
                                    pt.wait(act, t, i, f"{up}{d}", f"Y{d}3")
                                    ac.mark(nc.scalar.copy(dst[:, d, :, :].rearrange("p c t -> p (c t)"),
                                                           b[bk][:]), f"{name}{d}")
                            elif kind in ("W", "Tr"):
                                lv, e = item[2:]
                                pt.wait(act, t, i, f"{kind}{n}")
                                bk = (2 * (lv % 2) + e) if kind == "W" else (2 * (lv % 2) + e)
                                dst = Wb if kind == "W" else M
                                ac.mark(nc.scalar.copy(dst[:, e, :, :].rearrange("p c t -> p (c t)"), b[bk][:]),
                                        f"{kind[0].replace('T', 'M')}c{n}")
                            elif kind == "lora":
                                pt.wait(act, t, i, f"lora{d}")
                                dv.wait(act, t, i, f"b{1 - d}")
                                ac.mark(nc.scalar.activation(lw[:], b[4][:], ACT.Sigmoid,
                                                             bias=rp[:, W0 + d:W0 + d + 1]), f"sigw{d}")
                                ac.mark(nc.scalar.activation(av[:], b[5][:], ACT.Sigmoid,
                                                             bias=rp[:, A0 + d:A0 + d + 1]), f"siga{d}")
                            elif kind == "eh":
                                dv.wait(act, t, i, f"half{d}", f"E{1 - d}")
                                ac.mark(nc.scalar.activation(eh[:], hs_[:], ACT.Exp), f"eh{d}")
                            elif kind == "exps":
                                dv.wait(act, t, i, f"dif{d}", f"kt{1 - d}")
                                before, upto, sign = (dif, mid, 1.0) if d == 0 else (mid, dif, -1.0)
                                ac.mark(nc.scalar.activation(ee[:], before[:], ACT.Exp, scale=sign), f"ee{d}")
                                ac.mark(nc.scalar.activation(ei[:], upto[:], ACT.Exp, scale=sign), f"ei{d}")
                                ac.mark(nc.scalar.activation(en[:], upto[:], ACT.Exp, scale=-sign), f"en{d}")
                            elif kind == "fin":
                                for src, dst, dn, name in ((at, at2, "at", "am"), (rt, rt2, "rt", "rm")):
                                    dv.wait(act, t, i, f"{dn}{d}")
                                    nc.scalar.activation(dst[:, 0, :], src[:], ACT.Copy, scale=half2[:, 0:1])
                                    ac.mark(nc.scalar.activation(dst[:, 1, :], src[:], ACT.Copy,
                                                                 scale=half2[:, 1:2]), f"{name}{d}")
                            elif kind == "bonus":
                                dv.wait(act, t, i, "o")
                                ac.mark(nc.scalar.activation(sg[:], gg, ACT.Silu), "silu")
                            elif kind == "kk":
                                pt.wait(act, t, i, "squp")
                                ac.mark(nc.scalar.activation(sq[:], b[4][:], ACT.Sqrt), "norm")
                            elif kind == "read0":
                                dv.wait(act, t, i, "xc")
                                ac.mark(nc.scalar.activation(tmp[:], yf[:], ACT.Square), "ysq")
                            elif kind == "read1":
                                dv.wait(act, t, i, "var")
                                ac.mark(nc.scalar.activation(tmp[:], tmp[:], ACT.Sqrt), "yroot")
                            elif kind == "vtok":
                                pt.wait(act, t, i, "vup")
                                ac.mark(nc.scalar.copy(vtok[:].rearrange("p c t -> p (c t)"), b[7][:]), "vtok")
                    loop(act, body)

                @block.tensor
                def _(pe):
                    pt.start(pe)

                    def each(out, lhs, rhs):
                        for c in range(NCH):
                            mm = pe.matmul(out[:, c * CH:(c + 1) * CH], lhs(c), rhs(c), start=True, stop=True)
                        return mm

                    def turned(out, src):
                        for c in range(NCH):
                            mm = pe.transpose(out[:, c * CH:(c + 1) * CH], src(c), ident)
                        return mm

                    def cols(buf):
                        return lambda c: buf[:, c * CH:(c + 1) * CH]

                    def body(t):
                        for i, item in enumerate(items):
                            kind, d = item[0], item[1] if len(item) > 1 else None
                            n = "".join(str(x) for x in item[1:])
                            if kind == "g":
                                e, m = item[2:]
                                if (e, m) == (0, 0):
                                    ac.wait(pe, t, i, f"rm{d}")
                                dv.wait(pe, t, i, f"kt{d}", f"m{d}0{m}" if e else f"t{1 - d}6{m % 2}")
                                lhs, rhs = ((at2[:, e, :], bt[:]), (kt_[:], at2[:, e, :]), (bt[:], rt2[:, e, :]),
                                            (kt_[:], rt2[:, e, :]))[m]
                                pt.mark(each(b[m], cols(lhs), cols(rhs)), f"g{n}")
                            elif kind == "bup":
                                ac.wait(pe, t, i, f"siga{d}")
                                dv.wait(pe, t, i, "bon", f"kt{d}")
                                pt.mark(turned(b[4], cols(bt)), f"bup{d}")
                                pt.mark(turned(b[5], cols(kt_)), f"kup{d}")
                            elif kind == "T":
                                e = item[2]
                                dv.wait(pe, t, i, f"m{d}{e}0", f"m{d}1{e}")
                                pt.mark(turned(b[e], lambda c: AB[:, e, c, :]), f"T{n}")
                            elif kind == "W":
                                lv, e = item[2:]
                                dv.wait(pe, t, i, f"t{d}{lv - 1}{e}", f"m{d}1{2 + e}")
                                pt.mark(each(b[2 * (lv % 2) + e], lambda c: AB[:, e, c, :],
                                             lambda c: MT[:, d, e, c, :]), f"W{n}")
                            elif kind == "Pt":
                                lv, e = item[2:]
                                if lv == 1:
                                    dv.wait(pe, t, i, f"i{d}0{e}")
                                    ac.wait(pe, t, i, f"Wc{n}")
                                else:
                                    ac.wait(pe, t, i, f"Wc{n}", f"Mc{d}{lv - 1}{e}")
                                pt.mark(each(b[2 - 2 * (lv % 2) + e], lambda c: M[:, e, c, :],
                                             lambda c: Wb[:, e, c, :]), f"Pt{n}")
                            elif kind == "Tr":
                                lv, e = item[2:]
                                dv.wait(pe, t, i, f"t{n}")
                                pt.mark(turned(b[2 * (lv % 2) + e], lambda c: MT[:, d, e, c, :]), f"Tr{n}")
                            elif kind == "X":
                                q = item[2]
                                c = ORDER[d][q]
                                if q == 0:
                                    pl.wait(pe, t, i, f"keep{d}")
                                    ac.wait(pe, t, i, f"ktok{d}")
                                dv.wait(pe, t, i, f"t{d}61", "vm", f"ze{n}")
                                pe.matmul(b[6][:, 0:P], atS[:, d, c * CH:(c + 1) * CH], z[:], start=True, stop=False)
                                for e in range(2):
                                    mm = pe.matmul(b[6][:, 0:P], AKT[:, d, e, c, :], vtok2[:, e, c, :], start=False,
                                                   stop=(e == 1))
                                pt.mark(mm, f"X{n}")
                            elif kind == "SA":
                                q = item[2]
                                c = ORDER[d][q]
                                dv.wait(pe, t, i, f"x{n}")
                                for e in range(2):
                                    mm = pe.matmul(b[6][:, P:2 * P], MT[:, d, e, c, :], xs2[:, e, :],
                                                   start=(e == 0), stop=(e == 1))
                                pt.mark(mm, f"SA{n}")
                                dv.wait(pe, t, i, f"y{d}{q - 1}" if q else ("y03" if d else "y13"), "yrec")
                                ac.wait(pe, t, i, "vtok")
                                pe.matmul(b[7][:, 0:P], z[:], rtS[:, d, c * CH:(c + 1) * CH], start=True, stop=False)
                                for e in range(2):
                                    pe.matmul(b[7][:, 0:P], vtok2[:, e, c, :], RKT[:, d, e, c, :], start=False,
                                              stop=False)
                            elif kind == "U":
                                c = ORDER[d][item[2]]
                                dv.wait(pe, t, i, f"sa{n}")
                                pe.matmul(b[6][:, 2 * P:3 * P], ktok[:, d, c, :], vtok[:, c, :], start=True, stop=False)
                                pt.mark(pe.matmul(b[6][:, 2 * P:3 * P], btok[:, d, c, :], sas[:], start=False,
                                                  stop=True), f"U{n}")
                            elif kind == "Y":
                                c = ORDER[d][item[2]]
                                dv.wait(pe, t, i, f"sb{n}")
                                for e in range(2):
                                    mm = pe.matmul(b[7][:, 0:P], sas2[:, e, :], RBT[:, d, e, c, :], start=False,
                                                   stop=(e == 1))
                                pt.mark(mm, f"Y{n}")
                            elif kind == "lora":
                                pl.wait(pe, t, i, "staged")
                                ac.wait(pe, t, i, f"ktok{1 - d}", *(["norm"] if d == 0 else []))
                                pe.matmul(b[4][:], w2[:, 0, :], lora[:, d, 0, :], start=True, stop=True)
                                pt.mark(pe.matmul(b[5][:], w2[:, 1, :], lora[:, d, 1, :], start=True, stop=True),
                                        f"lora{d}")
                            elif kind == "bonus":
                                dv.wait(pe, t, i, "rk")
                                ac.wait(pe, t, i, "ktok1")
                                pt.mark(pe.matmul(b[5][:], headones, ksum[:], start=True, stop=True), "bonus")
                            elif kind == "kk":
                                dv.wait(pe, t, i, "kksq")
                                ac.wait(pe, t, i, "btok1")
                                pt.mark(pe.matmul(b[4][:], headones, sq[:], start=True, stop=True), "squp")
                            elif kind == "read0":
                                dv.wait(pe, t, i, "y13", "z13")
                                pt.mark(pe.matmul(b[6][:], headones, yf[:], start=True, stop=True), "mean")
                            elif kind == "read1":
                                ac.wait(pe, t, i, "ysq")
                                pt.mark(pe.matmul(b[7][:], headones, tmp[:], start=True, stop=True), "var")
                            elif kind == "vtok":
                                dv.wait(pe, t, i, "var")
                                pt.mark(turned(b[7], cols(vv)), "vup")
                    loop(pe, body)

                @block.vector
                def _(dve):
                    v = nc.vector
                    dv.start(dve)
                    strict, incl, ab = (0, 2), (1, 3), (2, 0)

                    def mask(j):
                        return tri[:, j:j + 1, :].to_broadcast([P, NCH, P])

                    def level(d, mt_side, lv):
                        u = d if mt_side else 1 - d
                        return lvl[:, u, lv:lv + 1, :].to_broadcast([P, NCH, P])

                    def body(t):
                        def do(i, ins, name, wait=True):
                            dv.mark(ins, name)
                            if wait:
                                dv.wait(dve, t, i, name)
                        for i, item in enumerate(items):
                            kind, d = item[0], item[1] if len(item) > 1 else None
                            n = "".join(str(x) for x in item[1:])
                            if kind == "g":
                                e, m = item[2:]
                                pt.wait(dve, t, i, f"g{n}")
                                dst = (AB[:, e, :, :], AKT[:, d, e, :, :], RBT[:, d, e, :, :], RKT[:, d, e, :, :])[m]
                                mj = (ab, strict, incl, incl)[m][d]
                                if m == 0:
                                    pl.wait(dve, t, i, f"eyeM{1 - d}")
                                do(i, v.tensor_tensor(dst, chunks(b[m][:]), mask(mj), ALU.mult), f"m{n}", False)
                                if m == 0:
                                    dv.wait(dve, t, i, f"m{n}", apart=True)
                                    do(i, v.copy_predicated(M[:, e, :, :], level(d, False, 0), AB[:, e, :, :]),
                                       f"i{d}0{e}", False)
                            elif kind == "T":
                                e = item[2]
                                pl.wait(dve, t, i, f"eyeT{d}")
                                pt.wait(dve, t, i, f"T{n}", apart=True)
                                do(i, v.copy_predicated(MT[:, d, e, :, :], level(d, True, 0), chunks(b[e][:])),
                                   f"t{d}0{e}", False)
                            elif kind == "Pt":
                                lv, e = item[2:]
                                pt.wait(dve, t, i, f"Pt{n}", apart=True)
                                do(i, v.copy_predicated(MT[:, d, e, :, :], level(d, True, lv),
                                                        chunks(b[2 - 2 * (lv % 2) + e][:])), f"t{n}", False)
                            elif kind == "X":
                                q = item[2]
                                if q == 0:
                                    pl.wait(dve, t, i, f"keep{d}")
                                    pt.wait(dve, t, i, f"Y{1 - d}3")
                                    do(i, v.memset(z[:], 0.0), f"ze{n}", False)
                                else:
                                    dv.wait(dve, t, i, f"z{d}{q - 1}")
                                    do(i, v.tensor_scalar(ze[:], z[:], decS[:, d, min(q, 2):min(q, 2) + 1], None,
                                                          ALU.mult), f"ze{n}", False)
                                pt.wait(dve, t, i, f"X{n}")
                                do(i, v.tensor_copy(diagonal(xs2), b[6][:, 0:P].rearrange("p (e v) -> p e v", e=2)),
                                   f"x{n}", False)
                            elif kind == "SA":
                                pt.wait(dve, t, i, f"SA{n}")
                                do(i, v.tensor_copy(sas[:], b[6][:, P:2 * P]), f"sa{n}")
                                do(i, v.tensor_copy(diagonal(sas2), sas[:].rearrange("p (e v) -> p e v", e=2)),
                                   f"sb{n}", False)
                            elif kind == "U":
                                q = item[2]
                                pt.wait(dve, t, i, f"U{n}")
                                if q == 0:
                                    v.tensor_scalar(z[HALVES[0], HALVES[0]], b[6][HALVES[0], 2 * P:2 * P + 64],
                                                    decS[HALVES[0], d, 0:1], None, ALU.mult)
                                    ins = v.tensor_scalar(z[HALVES[1], HALVES[1]], b[6][HALVES[1], 2 * P + 64:3 * P],
                                                          decS[HALVES[1], d, 0:1], None, ALU.mult)
                                else:
                                    qq = min(q, 2)
                                    dv.wait(dve, t, i, f"ze{n}")
                                    v.scalar_tensor_tensor(
                                        z[HALVES[0], HALVES[0]], b[6][HALVES[0], 2 * P:2 * P + 64],
                                        decS[HALVES[0], d, qq:qq + 1], ze[HALVES[0], HALVES[0]], ALU.mult, ALU.add)
                                    ins = v.scalar_tensor_tensor(
                                        z[HALVES[1], HALVES[1]], b[6][HALVES[1], 2 * P + 64:3 * P],
                                        decS[HALVES[1], d, qq:qq + 1], ze[HALVES[1], HALVES[1]], ALU.mult, ALU.add)
                                do(i, ins, f"z{n}", False)
                            elif kind == "Y":
                                c = ORDER[d][item[2]]
                                dst = yf[:, c * CH:(c + 1) * CH]
                                pt.wait(dve, t, i, f"Y{n}")
                                if d == 0:
                                    do(i, v.tensor_copy(dst, b[7][:, 0:P]), f"y{n}", False)
                                else:
                                    do(i, v.tensor_tensor(dst, b[7][:, 0:P], dst, ALU.add), f"y{n}", False)
                            elif kind == "el":
                                name = item[2]
                                key = name + str(d)
                                if name == "lw":
                                    ac.wait(dve, t, i, f"sigw{d}")
                                    do(i, v.tensor_scalar(lw[:], lw[:], HALF_E, None, ALU.mult), key)
                                elif name == "cum":
                                    ac.wait(dve, t, i, f"en{1 - d}")
                                    do(i, v.tensor_tensor_scan(mid[:], starts[:], lw[:], 0.0, ALU.mult, ALU.add), key)
                                elif name == "half":
                                    do(i, v.tensor_scalar(hs_[:], chunks(mid[:])[:, :, CH - 1], 0.5, None, ALU.mult),
                                       key)
                                elif name == "mid":
                                    do(i, v.tensor_tensor(chunks(mid[:]), chunks(mid[:]), hs_[:].unsqueeze(
                                        2).to_broadcast([P, NCH, CH]), ALU.subtract), key)
                                elif name == "dif":
                                    do(i, v.tensor_tensor(dif[:], mid[:], lw[:], ALU.subtract), key, False)
                                elif name == "blend":
                                    ac.wait(dve, t, i, f"siga{d}")
                                    do(i, v.tensor_scalar(kd[:], av[:], rp[:, KA:KA + 1], omka[:, 0:1], ALU.mult,
                                                          ALU.add), key)
                                elif name == "kd":
                                    do(i, v.tensor_tensor(kd[:], kx, kd[:], ALU.mult), key)
                                elif name == "b":
                                    do(i, v.tensor_tensor(bb[:], kk[:], av[:], ALU.mult), key, False)
                                elif d == 0:
                                    do(i, v.tensor_copy(ksum[:], kd[:]), key, False)
                                else:
                                    do(i, v.tensor_tensor(ksum[:], ksum[:], kd[:], ALU.add), key, False)
                            elif kind == "fin":
                                pt.wait(dve, t, i, f"g{1 - d}03", f"g{1 - d}13", f"kup{1 - d}")
                                pl.wait(dve, t, i, f"keep{1 - d}")
                                ac.wait(dve, t, i, f"en{d}")
                                dv.wait(dve, t, i, f"b{d}")
                                do(i, v.scalar_tensor_tensor(at[:], kk[:], -1.0, ee[:], ALU.mult, ALU.mult), f"at{d}",
                                   False)
                                do(i, v.tensor_tensor(rt[:], rr, ei[:], ALU.mult), f"rt{d}", False)
                                do(i, v.tensor_tensor(bt[:], bb[:], en[:], ALU.mult), f"bt{d}", False)
                                do(i, v.tensor_tensor(kt_[:], kd[:], en[:], ALU.mult), f"kt{d}", False)
                                for q in range(3):
                                    c0, c1 = ORDER[d][q:q + 2]
                                    ins = v.tensor_tensor(dec[:, q:q + 1], eh[:, c0:c0 + 1], eh[:, c1:c1 + 1],
                                                          ALU.mult)
                                do(i, ins, f"E{d}", False)
                            elif kind == "bonus":
                                dv.wait(dve, t, i, "ksum1")
                                do(i, v.scalar_tensor_tensor(ksum[:], rr, rp[:, RK_:RK_ + 1], ksum[:], ALU.mult,
                                                             ALU.mult), "rk", False)
                                pt.wait(dve, t, i, "bonus")
                                do(i, v.tensor_tensor(bonv[:], b[5][:], vv, ALU.mult), "bon", False)
                            elif kind == "kk":
                                pl.wait(dve, t, i, "staged")
                                do(i, v.tensor_scalar(omka[:], rp[:, KA:KA + 1], -1.0, 1.0, ALU.mult, ALU.add),
                                   "omka", False)
                                do(i, v.tensor_scalar(kk[:], kx, rp[:, KK_:KK_ + 1], None, ALU.mult), "kkraw")
                                do(i, v.tensor_tensor(sq[:], kk[:], kk[:], ALU.mult), "kksq", False)
                                ac.wait(dve, t, i, "norm")
                                do(i, v.tensor_scalar(sq[:], sq[:], 1e-12, None, ALU.max), "kkmax")
                                do(i, v.reciprocal(sq[:], sq[:]), "kkrec")
                                do(i, v.tensor_tensor(kk[:], kk[:], sq[:], ALU.mult), "kk")
                            elif kind == "read0":
                                pt.wait(dve, t, i, "mean")
                                do(i, v.tensor_scalar(tmp[:], b[6][:], 1.0 / 64, None, ALU.mult), "mean")
                                do(i, v.tensor_tensor(yf[:], yf[:], tmp[:], ALU.subtract), "xc")
                            elif kind == "read1":
                                pt.wait(dve, t, i, "var")
                                do(i, v.tensor_scalar(tmp[:], b[7][:], 1.0 / 64, GN_EPS, ALU.mult, ALU.add), "var",
                                   False)
                                ac.wait(dve, t, i, "yroot")
                                do(i, v.reciprocal(tmp[:], tmp[:]), "yrec")
                            elif kind == "read2":
                                do(i, v.tensor_tensor(yf[:], yf[:], tmp[:], ALU.mult), "yn")
                                g, bi = ((k.par[:, bass.ds(t * 9 + (PAR["rw"] + j - 9), 1)] for j in (LG, LB))
                                         if turns else (row(k, "rw", 9 * (KT - 1) + j) for j in (LG, LB)))
                                do(i, v.tensor_scalar(yf[:], yf[:], g, bi, ALU.mult, ALU.add), "ynl")
                                do(i, v.tensor_tensor(yf[:], yf[:], bonv[:], ALU.add), "ysum")
                                dst = o[:, bass.ds(t, 1), :] if turns else o[:, KT:KT + 1, :]
                                do(i, v.tensor_tensor(dst, yf[:].unsqueeze(1), sg[:].unsqueeze(1), ALU.mult), "o",
                                   False)
                            elif kind == "vtok":
                                ac.wait(dve, t, i, "vtok")
                                f = vtok2.rearrange("p e c f -> p e c f")
                                v.tensor_copy(f[:, 0, :, 0:64], vtok[:, :, 0:64])
                                do(i, v.tensor_copy(f[:, 1, :, 64:P], vtok[:, :, 64:P]), "vm", False)
                    loop(dve, body)

        run([("stage",), ("kk",)] + prep_items(0), 0, "first")
        run(section(0) + section(1), KT, "loop")
        run(serial_items(1) + [("read0",), ("read1",), ("read2",)], 0, "last")


def stage_rwkv_out(nc, k, o):
    first = FIRST["rwout"]
    with ExitStack() as ctx:
        block = ctx.enter_context(nc.Block())

        @block.sync
        def _(sp):
            for n in range(first, first + RING):
                sp.dma_start(k.ring[:, n % RING, :], k.stream[n]).then_inc(k.slot_landed[n % RING], 16)
            load_ahead(k, sp, first, 2)

        @block.tensor
        def _(pe):
            rhs = [o[:, 1 + kt, :] for kt in range(KT)]
            for j in range(2):
                slot_products(k, pe, first + j, 0, rhs, [k.psum[4 * j + i][:] for i in range(4)]).then_inc(
                    k.slot_used, 1)

        @block.vector
        def _(dve):
            for m in range(KT):
                dve.wait_ge(k.slot_used, first + m // 4 + 1)
                for dst, cols, c in ((k.ctx, slice(0, T), True), (k.x, slice(T, 2 * T), False)):
                    nc.vector.scalar_tensor_tensor(dst[:, m, :], k.psum[m][:, cols],
                                                   mod2(k, 0, GT, c)[:, m:m + 1], dst[:, m, :], ALU.mult, ALU.add)


def second_block(nc, k, a):
    stage_mod(nc, k, (FIRST["mod2"], 12), [k.cs[:, 8:16], k.cs[:, 16:24]], [k.mod[:, 0:48], k.mod[:, 48:96]],
              row(k, "modb0", 0, 48))
    stage_scales(nc, k, [(k.gain[:, 8 * i:8 * i + 8], mod2(k, i // 2, SC, i % 2 == 1),
                          row(k, f"norm2_{i // 2}", 0, 8)) for i in range(4)])
    kept = nc.dram_tensor("rwkv_projections", (KT + 1, P, 4, 512), F32).ap()
    with ExitStack() as lay:
        lora = lay.enter_context(nc.sbuf_tensor("lora", [P, 2, 2, 512], F32))
        with ExitStack() as inner:
            h = inner.enter_context(nc.sbuf_tensor("h_both", [P, KT, 512], F32))
            stage_norm(nc, k, k.ctx[:], KT, T, k.gain[:, 8:16], mod2(k, 0, SH, True), h[:, :, 0:T], None, "rwc")
            stage_norm(nc, k, k.x[:], KT, T, k.gain[:, 0:8], mod2(k, 0, SH), h[:, :, T:2 * T], None, "rwx")
            xx = inner.enter_context(nc.sbuf_tensor("shifted", [P, KT, 512], F32))
            stage_shift(nc, k, h, xx)
            stage_rwkv_in(nc, k, a, h, xx, lora, kept)
        o = lay.enter_context(nc.sbuf_tensor("rwkv_o", [P, KT + 1, 512], F32))
        stage_rwkv_scan(nc, k, a, lora, kept, o)
        stage_rwkv_out(nc, k, o)
    stage_mla(nc, k, a)
    stage_norm(nc, k, k.x[:], KT, T, row(k, "final2", 0, 8), None, k.x, None, "final2")


def stage_mla_in(nc, k, a, h, rope, qc, kvc, kpe, gate):
    first = FIRST["mlain"]
    X = slice(T, 2 * T)
    with ExitStack() as ctx:
        turned = ctx.enter_context(nc.sbuf_tensor("kpe_turned", [P, T], F32))
        act_evac = ctx.enter_context(nc.semaphore("mlain_act_evac"))
        step = ctx.enter_context(nc.semaphore("mlain_step"))
        b = k.psum
        block = ctx.enter_context(nc.Block())

        @block.sync
        def _(sp):
            load_ahead(k, sp, first, 4)

        @block.tensor
        def _(pe):
            both, x_only = [h[:, kt, :] for kt in range(KT)], [h[:, kt, X] for kt in range(KT)]

            def tile(n, i, out, rhs):
                for kt in range(KT):
                    mm = pe.matmul(out, ring_tile(k, n, kt, i * P), rhs[kt], start=(kt == 0), stop=(kt == KT - 1))
                return mm
            wait_slot(k, pe, first)
            for i in range(3):
                tile(first, i, b[i // 2][:, (i % 2) * T:(i % 2 + 1) * T], x_only)
            tile(first, 3, b[2][:], both).then_inc(k.slot_used, 1)
            wait_slot(k, pe, first + 1)
            for i in range(3):
                mm = tile(first + 1, i, b[3 + i][:], both)
            mm.then_inc(k.slot_used, 1)
            for j in range(2):
                wait_slot(k, pe, first + 2 + j)
                if j == 1:
                    pe.wait_ge(act_evac, 2)
                for i in range(4):
                    mm = tile(first + 2 + j, i, b[(6, 0)[j] + i // 2][:, (i % 2) * T:(i % 2 + 1) * T], x_only)
                mm.then_inc(k.slot_used, 1)

        @block.scalar
        def _(act):
            act.wait_ge(k.slot_used, first + 1)
            nc.scalar.copy(qc[:, 0:2, :].rearrange("p i t -> p (i t)"), b[0][:]).then_inc(act_evac, 1)
            nc.scalar.copy(qc[:, 2, :], b[1][:, 0:T]).then_inc(act_evac, 1)
            act.wait_ge(k.slot_used, first + 2)
            for i in range(2):
                nc.scalar.copy(kvc[:, i, :], b[3 + i][:])
            for j in range(2):
                act.wait_ge(k.slot_used, first + 3 + j)
                for i in range(2):
                    nc.scalar.activation(gate[:, 4 * j + 2 * i:4 * j + 2 * i + 2, :].rearrange("p i t -> p (i t)"),
                                         b[(6, 0)[j] + i][:], ACT.Silu)

        @block.vector
        def _(dve):
            s = Steps(dve, step)
            dve.wait_ge(k.slot_used, first + 2)
            nc.vector.tensor_copy(kpe[:, 0:T], b[2][:, 0:T])
            nc.vector.tensor_tensor(kpe[:, X], b[2][:, X], rope[:, 0, :], ALU.mult)
            s(nc.vector.tensor_tensor(turned[:], b[5][:, X], rope[:, 1, :], ALU.mult))
            nc.vector.tensor_tensor(kpe[:, X], kpe[:, X], turned[:], ALU.add)


def stage_mla_up(nc, k, rope, qc, kvc, kn, v, qn, qp):
    first = FIRST["mlab"]
    with ExitStack() as ctx:
        turned = ctx.enter_context(nc.sbuf_tensor("qp_turned", [P, 4, T], F32))
        act_evac = ctx.enter_context(nc.semaphore("mlaup_act"))
        dve_evac = ctx.enter_context(nc.semaphore("mlaup_dve"))
        done = ctx.enter_context(nc.semaphore("mlaup_pe"))
        b = k.psum
        block = ctx.enter_context(nc.Block())

        @block.sync
        def _(sp):
            load_ahead(k, sp, first, 3)

        @block.tensor
        def _(pe):
            w = k.ring[:, first % RING, :]
            wait_slot(k, pe, first)
            for m in range(8):
                for kt in range(2):
                    mm = pe.matmul(b[m][:], w[:, kt * D + m * P:kt * D + (m + 1) * P], kvc[:, kt, :],
                                   start=(kt == 0), stop=(kt == 1))
                mm.then_inc(done, 1)
            for c in range(4):
                for n in range(2):
                    pe.wait_ge(act_evac, 2 * c + n + 1)
                    for kt in range(2):
                        mm = pe.matmul(b[2 * c + n][:], kvc[:, kt, c * P:(c + 1) * P],
                                       w[:, 2 * D + kt * D + n * 512:2 * D + kt * D + (n + 1) * 512],
                                       start=(kt == 0), stop=(kt == 1))
                    mm.then_inc(done, 1)
            for sl, (lo, tiles, banks) in enumerate((((0, D), 8, range(0, 4)), ((0, 512), 8, range(4, 8)))):
                wait_slot(k, pe, first + 1 + sl)
                w = k.ring[:, (first + 1 + sl) % RING, :]
                for m in range(tiles):
                    bk = banks[m // 2]
                    if m % 2 == 0:
                        pe.wait_ge(dve_evac, bk + 1)
                    for kt in range(3):
                        if sl == 0:
                            at = kt * D + m * P
                        else:
                            at = (m // 4) * 1536 + kt * 512 + (m % 4) * P
                        mm = pe.matmul(b[bk][:, (m % 2) * T:(m % 2 + 1) * T], w[:, at:at + P], qc[:, kt, :],
                                       start=(kt == 0), stop=(kt == 2))
                if sl == 0:
                    mm.then_inc(k.slot_used, 2)
                else:
                    mm.then_inc(k.slot_used, 1)

        @block.scalar
        def _(act):
            for m in range(8):
                act.wait_ge(done, m + 1)
                nc.scalar.copy(kn[:, m, :], b[m][:]).then_inc(act_evac, 1)
            act.wait_ge(k.slot_used, first + 2)
            for i in range(4):
                nc.scalar.copy(qn[:, 2 * i:2 * i + 2, :].rearrange("p i t -> p (i t)"), b[i][:])

        @block.vector
        def _(dve):
            for c in range(4):
                for n in range(2):
                    dve.wait_ge(done, 8 + 2 * c + n + 1)
                    nc.vector.tensor_copy(v[:, c, n * 512:(n + 1) * 512], b[2 * c + n][:]).then_inc(dve_evac, 1)
            dve.wait_ge(k.slot_used, first + 3)
            cos, sin = (rope[:, i:i + 1, :].to_broadcast([P, 2, T]) for i in range(2))
            for i in range(2):
                nc.vector.tensor_tensor(qp[:, 2 * i:2 * i + 2, :], b[4 + i][:].rearrange("p (i t) -> p i t", i=2),
                                        cos, ALU.mult)
                nc.vector.tensor_tensor(turned[:, 2 * i:2 * i + 2, :], b[6 + i][:].rearrange(
                    "p (i t) -> p i t", i=2), sin, ALU.mult).then_inc(dve_evac, 1)
            dve.wait_ge(dve_evac, 10)
            nc.vector.tensor_tensor(qp[:], qp[:], turned[:], ALU.add)


def stage_mla_attention(nc, k, half, kn, v, qn, qp, kpe, gate):
    SCALE = 1.0 / math.sqrt(96.0)
    NK = 2 * T
    with ExitStack() as ctx:
        def sb(name, shape):
            return ctx.enter_context(nc.sbuf_tensor("mla_" + name, shape, F32))

        def sem(name):
            return ctx.enter_context(nc.semaphore("mla_" + name))
        qm = sb("q", [P, 4, 2, T])
        kst, vst = sb("k", [P, 2, NK]), sb("v", [P, 4, 2 * P])
        prob = sb("prob", [P, 2, NK])
        stat = sb("stat", [P, 8, 3])
        diag = sb("diag", [P, 2, P])
        ptok = sb("ptok", [P, 2, NK])
        staged, q_up, scored, maxed, exped, normed = (sem(n) for n in ("staged", "q_up", "scored", "maxed", "exped",
                                                                        "normed"))
        turned, p_down, o_up, o_down, step = (sem(n) for n in ("turned", "p_down", "o_up", "o_down", "step"))
        ident = const(k, "ident")
        U = 8
        block = ctx.enter_context(nc.Block())

        @block.gpsimd
        def _(pool):
            with pool.Fori(0, 4) as t:
                pool.wait_ge(o_up, t * U)
                pool.nop(nofuse=True)
                nc.gpsimd.tensor_copy(kst[:], kn[:, bass.ds(t * 2, 2), :]).then_inc(staged, 1)
                nc.gpsimd.tensor_copy(vst[:], v[:, :, bass.ds(t * 2 * P, 2 * P)]).then_inc(staged, 1)

        @block.scalar
        def _(act):
            with act.Fori(0, 4) as t:
                act.wait_ge(o_up, t * U)
                for hh in range(4):
                    nc.scalar.activation(qm[:, hh, 0:1, :], qn[:, bass.ds(t * 2 + hh // 2, 1), :], ACT.Copy,
                                         scale=half[:, hh % 2:hh % 2 + 1])
                    nc.scalar.activation(qm[:, hh, 1:2, :], qp[:, bass.ds(t, 1), :], ACT.Copy,
                                         scale=half[:, 2 + hh:3 + hh]).then_inc(q_up, 1)
                for u in range(U + 1):
                    if u < U:
                        act.wait_ge(maxed, t * U + (u + 1))
                        act.wait_ge(turned, t * U + max(u - 1, 0))
                        nc.scalar.activation(prob[:, u % 2, :], k.psum[u % 4][:], ACT.Exp, scale=SCALE,
                                             bias=stat[:, u, 0:1], accum_out=stat[:, u, 1:2]).then_inc(exped, 1)
                    if u >= 1:
                        act.wait_ge(turned, t * U + u)
                        nc.scalar.copy(ptok[:, (u - 1) % 2, :], k.psum[4 + (u - 1) % 2][:]).then_inc(p_down, 1)

        @block.tensor
        def _(pe):
            with pe.Fori(0, 4) as t:
                pe.wait_ge(staged, t * 2 + 2)

                def turn(u):
                    pe.wait_ge(normed, t * U + (u + 1))
                    pe.wait_ge(p_down, t * U + max(u - 1, 0))
                    for c in range(4):
                        mm = pe.matmul(k.psum[4 + u % 2][:, c * P:(c + 1) * P], prob[:, u % 2, c * P:(c + 1) * P],
                                       diag[:, u % 2, :], start=True, stop=True)
                    mm.then_inc(turned, 1)

                def values(u):
                    hh, e, qb = u // 2, (u // 2) % 2, u % 2
                    pe.wait_ge(p_down, t * U + (u + 1))
                    if u % 4 == 0:
                        pe.wait_ge(o_down, t * 2 + 0)
                    for c in range(4):
                        mm = pe.matmul(k.psum[6 + hh // 2][e * 64:(e + 1) * 64, qb * P:(qb + 1) * P],
                                       vst[:, c, hh * 64:(hh + 1) * 64], ptok[:, u % 2, c * P:(c + 1) * P],
                                       start=(c == 0), stop=(c == 3))
                    mm.then_inc(o_up, 1)
                for u in range(U + 2):
                    if u < U:
                        hh, qb = u // 2, u % 2
                        pe.wait_ge(q_up, t * 4 + (hh + 1))
                        pe.wait_ge(exped, t * U + max(u - 3, 0))
                        pe.matmul(k.psum[u % 4][:], qm[:, hh, 0, qb * P:(qb + 1) * P], kst[:, hh // 2, :],
                                  start=True, stop=False)
                        pe.matmul(k.psum[u % 4][:], qm[:, hh, 1, qb * P:(qb + 1) * P], kpe[:], start=False,
                                  stop=True).then_inc(scored, 1)
                    if u >= 1 and u - 1 < U:
                        turn(u - 1)
                    if u >= 2:
                        values(u - 2)

        @block.vector
        def _(dve):
            with dve.Fori(0, 4) as t:
                s = Steps(dve, step, t * 16)

                def output(i):
                    dve.wait_ge(o_up, t * U + 4 * (i + 1))
                    g = gate[:, bass.ds(t * 2 + i, 1), :]
                    nc.vector.tensor_tensor(g, k.psum[6 + i][:, 0:T].unsqueeze(1), g, ALU.mult).then_inc(o_down, 1)

                def norm(u):
                    dve.wait_ge(exped, t * U + (u + 1))
                    s(nc.vector.reciprocal(stat[:, u, 2:3], stat[:, u, 1:2]))
                    dve.wait_ge(turned, t * U + max(u - 1, 0))
                    nc.vector.tensor_scalar(diag[:, u % 2, :], ident, stat[:, u, 2:3], None,
                                            ALU.mult).then_inc(normed, 1)
                for u in range(U + 1):
                    if u < U:
                        dve.wait_ge(scored, t * U + (u + 1))
                        s(nc.vector.tensor_reduce(stat[:, u, 2:3], k.psum[u % 4][:], AX, ALU.max))
                        nc.vector.tensor_scalar(stat[:, u, 0:1], stat[:, u, 2:3], -SCALE, None,
                                                ALU.mult).then_inc(maxed, 1)
                    if u >= 1:
                        norm(u - 1)
                for i in range(2):
                    output(i)


def stage_mla(nc, k, a):
    with ExitStack() as lay:
        def sb(name, shape):
            return lay.enter_context(nc.sbuf_tensor("mla_" + name, shape, F32))
        rope, half = sb("rope", [P, 2, T]), sb("half", [P, 6])
        qc, kvc, kpe, gate = sb("qc", [P, 3, T]), sb("kvc", [P, 2, 512]), sb("kpe", [P, 512]), sb("gate", [P, KT, T])
        with nc.semaphore("mla_consts") as landed, nc.Block() as block:
            @block.sync
            def _(sp):
                sp.dma_start(rope[:], a["rope"].rearrange("p (i t) -> p i t", i=2)).then_inc(landed, 16)
                sp.dma_start(half[:], a["half_masks"]).then_inc(landed, 16)
                sp.wait_ge(landed, 32)
        with ExitStack() as inner:
            h = inner.enter_context(nc.sbuf_tensor("mla_h", [P, KT, 512], F32))
            stage_norm(nc, k, k.ctx[:], KT, T, k.gain[:, 24:32], mod2(k, 1, SH, True), h[:, :, 0:T], None, "mlac")
            stage_norm(nc, k, k.x[:], KT, T, k.gain[:, 16:24], mod2(k, 1, SH), h[:, :, T:2 * T], None, "mlax")
            stage_mla_in(nc, k, a, h, rope, qc, kvc, kpe, gate)
        stage_norm(nc, k, qc[:], 3, T, row(k, "qg", 0, 3), None, qc, None, "mlaq")
        stage_norm(nc, k, kvc[:], 2, 512, row(k, "kvg", 0, 2), None, kvc, None, "mlakv")
        kn, v, qn, qp = sb("kn", [P, KT, 512]), sb("vt", [P, 4, D]), sb("qn", [P, KT, T]), sb("qp", [P, 4, T])
        stage_mla_up(nc, k, rope, qc, kvc, kn, v, qn, qp)
        stage_mla_attention(nc, k, half, kn, v, qn, qp, kpe, gate)
        stage_out(nc, k, FIRST["mlaout"], [gate[:, i, :] for i in range(KT)], mod2(k, 1, GT))


def build(nc, a, out):
    with ExitStack() as top:
        k = Core()
        k.stream = a["stream"]
        k.ring = top.enter_context(nc.sbuf_tensor("ring", [P, RING, SLOT], F32))
        k.par = top.enter_context(nc.sbuf_tensor("par", [P, NPAR], F32))
        k.con = top.enter_context(nc.sbuf_tensor("con", [P, NCON], F32))
        k.cs = top.enter_context(nc.sbuf_tensor("cs", [P, 24], F32))
        k.x = top.enter_context(nc.sbuf_tensor("x", [P, KT, T], F32))
        k.ctx = top.enter_context(nc.sbuf_tensor("ctx", [P, KT, T], F32))
        k.mod = top.enter_context(nc.sbuf_tensor("mod", [P, 96], F32))
        k.gain = top.enter_context(nc.sbuf_tensor("gain", [P, 32], F32))
        k.psum = [top.enter_context(nc.psum_tensor(f"bank{b}", [P, 512], F32)) for b in range(8)]
        k.slot_landed = [top.enter_context(nc.semaphore(f"slot_landed{s}")) for s in range(RING)]
        k.slot_used = top.enter_context(nc.semaphore("slot_used"))
        k.first_stage_sem = k.slot_used.num + 1

        stage_setup(nc, k, a)
        first_block(nc, k, a)
        stage_clear(nc, k)
        second_block(nc, k, a)
        stage_store(nc, k, out)


def stage_clear(nc, k):
    with nc.Block() as block:
        @block.sync
        def _(sp):
            sp.sem_clear(range(k.first_stage_sem, 256))


def stage_store(nc, k, out):
    with nc.semaphore("out_stored") as stored, nc.Block() as block:
        @block.sync
        def _(sp):
            sp.dma_start(out, k.x[:]).then_inc(stored, 16)
            sp.wait_ge(stored, 16)


def first_block(nc, k, a):
    with ExitStack() as lay:
        h = lay.enter_context(nc.sbuf_tensor("h", [P, KT, T], F32))
        stage_mod(nc, k, (FIRST["mod0"], 12), [k.cs[:, 0:8]], [k.mod[:, 0:48]], row(k, "adab0", 0, 48))
        stage_scales(nc, k, [(k.gain[:, 0:8], k.mod[:, 8:16], row(k, "nmix0", 0, 8)),
                             (k.gain[:, 8:16], k.mod[:, 32:40], row(k, "nffn0", 0, 8))])
        stage_norm(nc, k, k.x[:], KT, T, k.gain[:, 0:8], k.mod[:, 0:8], h, None, "mix0")
        stage_hybrid(nc, k, a, h)
        stage_norm(nc, k, k.x[:], KT, T, k.gain[:, 8:16], k.mod[:, 24:32], h, None, "ffn0")
        stage_ffn(nc, k, h, FIRST["up0"], FIRST["down0"], k.mod[:, 40:48], 0)
        stage_mod(nc, k, (FIRST["mod1"], 12), [k.cs[:, 0:8]], [k.mod[:, 48:96]], row(k, "adab1", 0, 48))
        stage_scales(nc, k, [(k.gain[:, 0:8], k.mod[:, 56:64], row(k, "nmix1", 0, 8)),
                             (k.gain[:, 8:16], k.mod[:, 80:88], row(k, "nffn1", 0, 8))])
        stage_norm(nc, k, k.x[:], KT, T, k.gain[:, 0:8], k.mod[:, 48:56], h, None, "mix1")
        stage_conformer(nc, k, h)
        stage_norm(nc, k, k.x[:], KT, T, k.gain[:, 8:16], k.mod[:, 72:80], h, None, "ffn1")
        stage_ffn(nc, k, h, FIRST["up1"], FIRST["down1"], k.mod[:, 88:96], 1)
        stage_norm(nc, k, k.x[:], KT, T, row(k, "final1", 0, 8), None, k.x, None, "final1")


def stage_hybrid(nc, k, a, h):
    with ExitStack() as lay:
        y = lay.enter_context(nc.sbuf_tensor("y", [P, NY, T], F32))
        dtok = lay.enter_context(nc.sbuf_tensor("dtok", [P, 2 * HEADS], F32))
        stage_hyin(nc, k, h, y, a, dtok)
        stage_conv4(nc, k, y)
        with ExitStack() as inner:
            hd = inner.enter_context(nc.sbuf_tensor("headvals", [P, 8, 2 * HEADS], F32))
            stage_dt(nc, k, a, dtok, hd)
            stage_ssd(nc, k, y, hd)
        stage_ssm_gate(nc, k, y)
        stage_attention(nc, k, a, y)
        rhs = [y[:, ST_XS + i, :] for i in range(16)] + [y[:, ST_Q + i, :] for i in range(8)]
        stage_out(nc, k, FIRST["hyout"], rhs, k.mod[:, 16:24])


def _cols(w):
    return w.reshape(w.shape[0] // P, P, w.shape[1]).transpose(1, 0, 2)


def _slots(w, groups=None):
    kk, n = w.shape
    kslots, nslots = -(-kk // D), -(-n // 512)
    full = np.zeros((kslots * D, nslots * 512), w.dtype)
    full[:kk, :n] = w
    return full.reshape(kslots, KT, P, nslots, 512).transpose(3, 0, 2, 1, 4).reshape(-1, P, SLOT)


def _pairs(a, b, width=256):
    n = a.shape[1] // width
    both = np.stack([a.reshape(D, n, width), b.reshape(D, n, width)], 2)
    return both.reshape(D, 2 * a.shape[1])


def _one_slot(parts):
    flat = np.concatenate([p.reshape(P, -1) for p in parts], 1)
    out = np.zeros((1, P, SLOT), flat.dtype)
    out[0, :, :flat.shape[1]] = flat
    return out


def lay_stream(i):
    s = [_slots(i["ada_w"][0]), None, _slots(i["hy_w_out"][0]),
         _slots(_pairs(i["ffn_w_gate"][0], i["ffn_w_up"][0])), _slots(i["ffn_w_down"][0]),
         _slots(i["ada_w"][1]), _slots(_pairs(*np.split(i["cv_w_pw1"][0], 2, 1))), _slots(i["cv_w_pw2"][0]),
         _slots(_pairs(i["ffn_w_gate"][1], i["ffn_w_up"][1])), _slots(i["ffn_w_down"][1]),
         _slots(i["mod_w_2"][0]), _slots(i["mod_w_2"][1])]
    w = i["hy_w_in"][0]
    s[1] = _slots(np.concatenate([w[:, :DI + CONV_DIM], w[:, DI + CONV_DIM + HEADS:]], 1))
    s += [_slots(i["rwkv_w_in_2"][0][j]) for j in range(4)] + [_slots(i["rwkv_w_out_2"][0])]
    w = i["mla_w_in_2"][0]
    qc, kvc, kpe, gate = w[:, :384], w[:, 384:640], w[:, 640:672], w[:, 672:]
    swapped = np.concatenate([kpe[:, 16:], kpe[:, :16]], 1)
    s += [_slots(np.concatenate([qc] + [kpe] * 4, 1)), _slots(np.concatenate([kvc] + [swapped] * 4, 1)),
          _slots(gate)]
    kvb = i["mla_w_kvb_2"][0].reshape(256, 16, 2, 64)
    qb = i["mla_w_qb_2"][0].reshape(384, 16, 96)
    s += [_one_slot([_cols(kvb[:, :, 0].reshape(256, 1024)), _cols(kvb[:, :, 1].reshape(256, 1024))]),
          _one_slot([_cols(qb[:, :, :64].reshape(384, 1024))]),
          _one_slot([_cols(qb[:, :, 64:].reshape(384, 512)),
                     _cols(np.concatenate([qb[:, :, 80:], qb[:, :, 64:80]], 2).reshape(384, 512))]),
          _slots(i["mla_w_out_2"][0])]
    stream = np.concatenate(s, 0)
    assert stream.shape == (NSLOTS, P, SLOT), (stream.shape, NSLOTS)
    return stream


def _rows(*vectors):
    return np.concatenate([v.reshape(-1, P).T for v in vectors], 1)


def lay_par(i):
    conv = np.stack([*i["hy_conv_w"][0], i["hy_conv_b"][0]], 0)
    dw = np.stack([*i["cv_w_dw"][0], i["cv_b_dw"][0]], 0)
    rw = np.stack([i["rwkv_w0_2"][0, 0], i["rwkv_w0_2"][0, 1], i["rwkv_a0_2"][0, 0], i["rwkv_a0_2"][0, 1],
                   i["rwkv_k_k_2"][0], i["rwkv_k_a_2"][0], i["rwkv_r_k_2"][0].reshape(-1),
                   i["rwkv_lnx_g_2"][0], i["rwkv_lnx_b_2"][0]], 0)

    def tilewise(m):
        return m.reshape(m.shape[0], -1, P).transpose(1, 0, 2)
    par = _rows(i["c"], i["c_2"], i["c_ctx_2"], i["ada_b"][0], i["ada_b"][1], i["mod_b_2"][0], i["mod_b_2"][1],
                i["norm_mix_g"][0], i["norm_mix_g"][1], i["norm_ffn_g"][0], i["norm_ffn_g"][1],
                i["final_norm_g"], tilewise(conv), np.repeat(i["hy_d_skip"][0], 64), i["hy_ssm_norm_g"][0],
                i["cv_b_pw1"][0], tilewise(dw), i["cv_ln_g"][0], i["cv_ln_b"][0], i["cv_b_pw2"][0],
                i["norm_g_2"][0], i["norm_g_2"][1], i["rwkv_mu_2"][0], i["final_g_2"], i["mla_q_norm_g_2"][0],
                i["mla_kv_norm_g_2"][0], tilewise(rw), np.zeros((9 * P,), rw.dtype))
    assert par.shape == (P, NPAR), (par.shape, NPAR)
    return par


def t5_bucket(dist):
    n = np.maximum(dist, 1).astype(np.float32)
    large = np.float32(16) + np.log(n / np.float32(16)) / np.float32(math.log(2048 / 16)) * np.float32(16)
    return np.where(dist < 16, dist, np.minimum(large.astype(np.int32), 31))


def constants():
    p, f = np.arange(P)[:, None], np.arange(P)[None, :]
    f32 = np.float32
    out = {}
    out["con"] = np.concatenate([(p == f), np.ones((P, P)), (p // 64 == f // 64), (p <= f),
                                 np.where(f >= p, 0.0, NEG), (p + f == P - 1)], 1).astype(f32)
    dist = 255 - np.arange(384)
    bucket = t5_bucket(np.maximum(dist, 0))
    onehot = ((np.arange(32)[:, None] == bucket[None]) & (dist >= 0)[None]).astype(f32)
    allowed = [(dist >= 0) & (dist <= 128), (dist >= 0) & (dist % 4 == 0), (dist >= 0) & (dist % 16 == 0)]
    negs = np.concatenate([np.where(np.tile(a, (16, 1)), 0.0, NEG) for a in allowed], 0).astype(f32)
    out["bias_onehot"], out["bias_neg"] = onehot, negs
    out["tri_masks"] = np.concatenate([p < f, p <= f, p > f, p >= f], 1).astype(f32)
    levels = []
    for upper in (True, False):
        for lv in range(7):
            i, j = p >> lv, f >> lv
            levels.append((i % 2 == 0) & (j == i + 1) if upper else (j % 2 == 0) & (i == j + 1))
    out["level_masks"] = np.concatenate(levels, 1).astype(np.int32)
    out["chunk_starts"] = np.broadcast_to((np.arange(512) % P != 0), (P, 512)).astype(f32).copy()
    out["half_masks"] = np.concatenate([p < 64, p >= 64] + [p // 32 == q for q in range(4)], 1).astype(f32)
    tok = np.arange(T)
    inv = (1.0 / (f32(10000.0) ** (np.arange(0, 16, 2, dtype=f32) / f32(16)))).astype(f32)
    ang = np.concatenate([(tok // 64).astype(f32)[:, None] * inv, (tok % 64).astype(f32)[:, None] * inv], 1)
    cos, sin = np.cos(ang).T.astype(f32), np.sin(ang).T.astype(f32)
    out["rope"] = np.tile(np.concatenate([np.concatenate([cos, cos]), np.concatenate([-sin, sin])], 1), (4, 1))
    return out


def lay_inputs(i):
    def tokens(x):
        return _cols(np.ascontiguousarray(x.reshape(T, D).T))
    w = i["hy_w_in"][0]
    out = constants()
    out["stream"] = lay_stream(i)
    out["par"] = lay_par(i)
    out["xt"], out["ctxt"] = tokens(i["x"]), tokens(i["ctx_2"])
    out["wdt"] = _cols(w[:, DI + CONV_DIM:DI + CONV_DIM + HEADS])
    out["headrow"] = np.concatenate([np.broadcast_to(i["hy_dt_bias"][0], (P, HEADS)),
                                     np.broadcast_to(i["hy_a_log"][0], (P, HEADS))], 1)
    out["rel_table"] = i["rel_table"]
    w1 = np.concatenate([*i["rwkv_w1_2"][0], *i["rwkv_a1_2"][0]], 1)
    out["lora_in"] = _cols(w1)
    out["lora_out"] = np.zeros((P, 2, D + P), w.dtype)
    out["lora_out"][:, :, :D] = np.stack([i["rwkv_w2_2"][0].reshape(P, D), i["rwkv_a2_2"][0].reshape(P, D)], 1)
    return {n: np.ascontiguousarray(v) for n, v in out.items()}


def kernel(**inputs):
    import concourse.bacc as bacc
    from concourse.bass_utils import run_bass_kernel_spmd

    nc = bacc.Bacc("TRN2", target_bir_lowering=False, num_devices=1)
    arrays = lay_inputs({n: np.asarray(v) for n, v in inputs.items()})
    aps = {n: nc.dram_tensor("in_" + n, v.shape, mybir.dt.from_np(v.dtype), kind="ExternalInput").ap()
           for n, v in arrays.items()}
    out = nc.dram_tensor("out_0_dram", (P, KT, T), F32, kind="ExternalOutput").ap()
    build(nc, aps, out)
    r = run_bass_kernel_spmd(nc, [{"in_" + n: v for n, v in arrays.items()}], core_ids=[0])
    got = r.results[0]["out_0_dram"]
    return got.transpose(2, 1, 0).reshape(1, T, D)
```

```python
import math
from contextlib import ExitStack

import numpy as np

import concourse.bass as bass
from concourse import mybir

F32 = mybir.dt.float32
U8 = mybir.dt.uint8
I32 = mybir.dt.int32
ACT = mybir.ActivationFunctionType
ALU = mybir.AluOpType
AX = mybir.AxisListType.X

P = 128
D = 1024
T = 256
KT = D // P
RING = 4
SLOT = KT * 512
EPS = 1e-6
NEG = -1e30

DI = 2048
CONV_DIM = 3072
HEADS = 32
ST_Z, ST_XS, ST_B, ST_C, ST_Q, ST_K, ST_V = 0, 16, 32, 36, 40, 64, 72
NY = 80
FFN = 2816
FT = FFN // P
TAPS = 31

_PAR_SIZES = [("c", 8), ("c2", 8), ("cctx", 8), ("adab0", 48), ("adab1", 48), ("modb0", 24), ("modb1", 24),
              ("nmix0", 8), ("nmix1", 8), ("nffn0", 8), ("nffn1", 8), ("final1", 8),
              ("conv", 24 * 5), ("dskip", 16), ("ssmg", 16), ("pw1b", 16), ("dw", 8 * 32), ("lng", 8),
              ("lnb", 8), ("pw2b", 8), ("norm2_0", 8), ("norm2_1", 8), ("mu", 48), ("final2", 8), ("qg", 3),
              ("kvg", 2), ("rw", 9 * 9)]
PAR = {}
NPAR = 0
for _name, _n in _PAR_SIZES:
    PAR[_name] = NPAR
    NPAR += _n

_SLOTS = [("mod0", 4), ("hyin", 20), ("hyout", 6), ("up0", 11), ("down0", 6), ("pw1", 4), ("pw2", 2),
          ("up1", 11), ("down1", 6), ("rkvg", 8), ("rwout", 2), ("mlain", 4), ("mlab", 3),
          ("mlaout", 2)]
FIRST = {}
NSLOTS = 0
for _name, _n in _SLOTS:
    FIRST[_name] = NSLOTS
    NSLOTS += _n

_CONST_SIZES = [("ident", 128), ("ones", 128), ("headones", 128), ("tri", 128), ("neg", 128), ("flip", 128)]
CON = {}
NCON = 0
for _name, _n in _CONST_SIZES:
    CON[_name] = NCON
    NCON += _n


class Steps:

    def __init__(self, eng, sem, done=0):
        self.eng, self.sem, self.done, self.n = eng, sem, done, 0

    def __call__(self, ins):
        self.n += 1
        ins.then_inc(self.sem, 1)
        self.eng.wait_ge(self.sem, self.done + self.n)


class Core:
    pass


def psum_tiles(k):
    return [k.psum[b] for b in range(8)]


def wait_slot(k, eng, n, turn=0):
    eng.wait_ge(k.slot_landed[n % RING], turn * 16 + 16 * (n // RING + 1))


def load_ahead(k, sp, first, count):
    def one(n, turn):
        sp.wait_ge(k.slot_used, turn * RING + (n + 1))
        sp.dma_start(k.ring[:, n % RING, :], k.stream[turn * RING + (n + RING)]).then_inc(
            k.slot_landed[n % RING], 16)

    count = min(count, NSLOTS - RING - first)
    turns = count // RING
    if turns > 1:
        with sp.Fori(0, turns) as t:
            for j in range(RING):
                one(first + j, t)
        for j in range(turns * RING, count):
            one(first + j, 0)
    else:
        for j in range(count):
            one(first + j, 0)


def ring_tile(k, n, kt, col, width=P):
    return k.ring[:, n % RING, kt * 512 + col:kt * 512 + col + width]


def row(k, name, i=0, n=1):
    c = PAR[name] + i
    return k.par[:, c:c + n]


def const(k, name):
    return k.con[:, CON[name]:CON[name] + P]


def stage_setup(nc, k, a):
    with ExitStack() as ctx:
        landed = ctx.enter_context(nc.semaphore("setup_landed"))
        silu_done = ctx.enter_context(nc.semaphore("setup_silu"))
        block = ctx.enter_context(nc.Block())

        @block.sync
        def _(sp):
            sp.dma_start(k.par[:], a["par"]).then_inc(landed, 16)
            sp.dma_start(k.con[:], a["con"]).then_inc(landed, 16)
            for n in range(RING):
                sp.dma_start(k.ring[:, n, :], k.stream[n]).then_inc(k.slot_landed[n], 16)
            sp.dma_start(k.x[:], a["xt"]).then_inc(k.x_landed, 16)
            sp.wait_ge(landed, 32)

        @block.scalar
        def _(act):
            act.wait_ge(landed, 32)
            nc.scalar.activation(k.cs[:], row(k, "c", 0, 24), ACT.Silu).then_inc(silu_done, 1)


def stage_mod(nc, k, first, vec, out, bias):
    with ExitStack() as ctx:
        part = ctx.enter_context(nc.sbuf_tensor(f"mod_part{first}", [P, RING, 512], F32))
        summed = ctx.enter_context(nc.semaphore("mod_summed"))
        step = ctx.enter_context(nc.semaphore("mod_step"))
        block = ctx.enter_context(nc.Block())

        @block.sync
        def _(sp):
            load_ahead(k, sp, first, RING)
            sp.wait_ge(k.x_landed, 16)

        @block.vector
        def _(dve):
            s = Steps(dve, step)
            for j in range(RING):
                wait_slot(k, dve, first + j)
                w = k.ring[:, (first + j) % RING, :]
                for kt in range(KT):
                    acc = part[:, j, :]
                    if kt == 0:
                        s(nc.vector.tensor_scalar(acc, w[:, 0:512], vec[:, 0:1], None, ALU.mult))
                    else:
                        ins = nc.vector.scalar_tensor_tensor(
                            acc, w[:, kt * 512:kt * 512 + 512], vec[:, kt:kt + 1], acc, ALU.mult, ALU.add)
                        if kt < KT - 1:
                            s(ins)
                        else:
                            ins.then_inc(summed, 1)
            dve.wait_ge(k.slot_used, first + RING)
            nc.vector.tensor_tensor(out, k.psum[0][:, 0:4 * RING], bias, ALU.add)

        @block.tensor
        def _(pe):
            for j in range(RING):
                pe.wait_ge(summed, j + 1)
                for q in range(4):
                    mm = pe.matmul(k.psum[0][:, j * 4 + q:j * 4 + q + 1], part[:, j, q * P:(q + 1) * P],
                                   const(k, "ones")[:, 0:1], start=True, stop=True)
                mm.then_inc(k.slot_used, 1)


def stage_mod_bias(nc, k, out, bias):
    with nc.Block() as block:
        @block.vector
        def _(dve):
            for v, dst in enumerate(out):
                nc.vector.tensor_tensor(dst, k.next_mod[:, v, :], bias, ALU.add)


def stage_mod_rest(nc, k):
    with nc.Block() as block:
        @block.vector
        def _(dve):
            nc.vector.tensor_tensor(k.mod[:, 16:48], k.mod[:, 16:48], row(k, "adab0", 16, 32), ALU.add)


def stage_norm(nc, k, src, nt, width, scale, bias, dst, name):
    stage_norms(nc, k, [(src, scale, bias, dst)], nt, width, name)


def stage_norms(nc, k, jobs, nt, width, name):
    count = len(jobs)
    with ExitStack() as ctx:
        sq = ctx.enter_context(nc.sbuf_tensor(f"norm_sq_{name}", [P, count, nt, width], F32))
        rstd = ctx.enter_context(nc.sbuf_tensor(f"norm_rstd_{name}", [P, count, width], F32))
        squared = ctx.enter_context(nc.semaphore("norm_squared"))
        summed = ctx.enter_context(nc.semaphore("norm_summed"))
        step = ctx.enter_context(nc.semaphore("norm_step"))
        rooted = ctx.enter_context(nc.semaphore("norm_rooted"))
        block = ctx.enter_context(nc.Block())
        half = nt // 2

        @block.scalar
        def _(act):
            for n, (src, *_) in enumerate(jobs):
                for lo, hi in ((0, half), (half, nt)):
                    nc.scalar.activation(sq[:, n, lo:hi, :], src[:, lo:hi, :], ACT.Square).then_inc(squared, 1)
            for n in range(count):
                act.wait_ge(step, n + 1)
                nc.scalar.activation(rstd[:, n, :], rstd[:, n, :], ACT.Sqrt).then_inc(rooted, 1)
            for n, (src, scale, bias, dst) in enumerate(jobs):
                if bias is not None:
                    act.wait_ge(step, count + 2 * n + 2)
                    for i in range(1, nt, 2):
                        nc.scalar.activation(dst[:, i, :], sq[:, n, i, :], ACT.Identity, bias=bias[:, i:i + 1],
                                             scale=scale[:, i:i + 1])

        @block.tensor
        def _(pe):
            for n in range(count):
                for i in range(nt):
                    if i == 0:
                        pe.wait_ge(squared, 2 * n + 1)
                    if i == half:
                        pe.wait_ge(squared, 2 * n + 2)
                    mm = pe.matmul(k.psum[n][:, 0:width], const(k, "ones"), sq[:, n, i, :], start=(i == 0),
                                   stop=(i == nt - 1))
                mm.then_inc(summed, 1)

        @block.vector
        def _(dve):
            s = Steps(dve, step)
            for n in range(count):
                dve.wait_ge(summed, n + 1)
                s(nc.vector.tensor_scalar(rstd[:, n, :], k.psum[n][:, 0:width], 1.0 / (nt * P), EPS, ALU.mult,
                                          ALU.add))
            for n, (src, scale, bias, dst) in enumerate(jobs):
                dve.wait_ge(rooted, n + 1)
                s(nc.vector.reciprocal(rstd[:, n, :], rstd[:, n, :]))
                s(nc.vector.tensor_tensor(sq[:, n, :, :], src, rstd[:, n:n + 1, :].to_broadcast([P, nt, width]),
                                          ALU.mult))
                for i in range(0, nt, 2 if bias is not None else 1):
                    if bias is not None:
                        nc.vector.tensor_scalar(dst[:, i, :], sq[:, n, i, :], scale[:, i:i + 1], bias[:, i:i + 1],
                                                ALU.mult, ALU.add)
                    else:
                        nc.vector.tensor_scalar(dst[:, i, :], sq[:, n, i, :], scale[:, i:i + 1], None, ALU.mult)


def stage_scales(nc, k, pairs):
    with ExitStack() as ctx:
        block = ctx.enter_context(nc.Block())

        @block.vector
        def _(dve):
            for out, sc, g in pairs:
                nc.vector.scalar_tensor_tensor(out, sc, 1.0, g, ALU.add, ALU.mult)


def slot_products(k, pe, n, turn, rhs, outs, kts=range(KT), start=True, stop=True, width=P):
    wait_slot(k, pe, n, turn)
    for i, out in enumerate(outs):
        for kt in kts:
            mm = pe.matmul(out, ring_tile(k, n, kt, i * P), rhs[kt], start=start and kt == kts[0],
                           stop=stop and kt == kts[-1])
    return mm


def stage_hyin(nc, k, h, y, a, dtok):
    first = FIRST["hyin"]
    mod_w = k.ctx[:].rearrange("p i t -> p (i t)")
    vec = k.cs[:, 0:8]
    PHASES = ((0, 2, True, False), (2, 2, True, True), (4, 1, False, True))
    with ExitStack() as ctx:
        wdt = ctx.enter_context(nc.sbuf_tensor("hyin_wdt", [P, KT, HEADS], F32))
        part = ctx.enter_context(nc.sbuf_tensor("hyin_mod_part", [P, 2, 512], F32))
        acc = ctx.enter_context(nc.sbuf_tensor("conv_acc", [P, 2, T], F32))

        def sem(name):
            return ctx.enter_context(nc.semaphore(name))
        wdt_landed, stored_dve, stored_act, dt_done = (sem(n) for n in ("wdt_landed", "hyin_stored_dve",
                                                                        "hyin_stored_act", "hyin_dt"))
        mod_landed = k.by_pool["hyin_mod_landed"]
        mod_half, mod_step, mod_up, mod_stored = (sem("hmod_" + n) for n in ("half", "step", "up", "stored"))
        conv_step, conv_summed, conv_stored = (sem(n) for n in ("conv_step", "conv_summed", "conv_stored"))
        block = ctx.enter_context(nc.Block())

        def over_phases(eng, one, between=None):
            for t0, turns, mod, conv in PHASES:
                if turns > 1:
                    with eng.Fori(0, turns) as t:
                        for j in range(RING):
                            one(t, j, t0, mod, conv)
                else:
                    for j in range(RING):
                        one(0, j, t0, mod, conv)
                if between is not None and t0 == 0:
                    between()

        @block.sync
        def _(sp):
            sp.dma_start(wdt[:], a["wdt"]).then_inc(wdt_landed, 16)
            load_ahead(k, sp, first, 20)

        @block.gpsimd
        def _(pool):
            pool.dma_start(mod_w, a["mod_rest"][0]).then_inc(mod_landed, 16)

            def load(t, j):
                pool.wait_ge(mod_half, t * RING + (j + 1))
                pool.dma_start(mod_w, a["mod_rest"][t * RING + (j + 1)]).then_inc(mod_landed, 16)
            with pool.Fori(0, 3) as t:
                for j in range(RING):
                    load(t, j)
            for j in range(3 * RING, 4 * RING - 1):
                load(0, j)

        @block.tensor
        def _(pe):
            rhs = [h[:, kt, :] for kt in range(KT)]
            pe.sem_inc(mod_up, 2)
            pe.wait_ge(wdt_landed, 16)
            for c in range(2):
                for kt in range(KT):
                    mm = pe.matmul(k.psum[7][:, c * HEADS:(c + 1) * HEADS], h[:, kt, c * P:(c + 1) * P],
                                   wdt[:, kt, :], start=(kt == 0), stop=(kt == KT - 1))
            mm.then_inc(dt_done, 1)

            def one(t, j, t0, mod, conv):
                pe.wait_ge(stored_dve, t * RING + (RING * t0 + j + 1))
                pe.wait_ge(stored_act, t * RING + (RING * t0 + j + 1))
                b = 2 * (j % 2)
                outs = [k.psum[b + i // 2][:, (i % 2) * T:(i % 2 + 1) * T] for i in range(4)]
                slot_products(k, pe, first + RING * t0 + j, t, rhs, outs).then_inc(k.slot_used, 1)
                if mod and j % 2 == 1:
                    pe.wait_ge(mod_half, t * RING + (RING * t0 + j + 1))
                    if j == 1:
                        pe.wait_ge(mod_stored, t + (t0 + 1))
                    for q in range(4):
                        mm = pe.matmul(k.psum[4][:, (j // 2) * 4 + q:(j // 2) * 4 + q + 1],
                                       part[:, j // 2, q * P:(q + 1) * P], const(k, "ones")[:, 0:1],
                                       start=True, stop=True)
                    mm.then_inc(mod_up, 1)
            over_phases(pe, one)

        @block.vector
        def _(dve):
            dve.wait_ge(dt_done, 1)
            nc.vector.tensor_copy(dtok[:], k.psum[7][:, 0:2 * HEADS])
            dve.sem_inc(stored_dve, 2)

            def half_slot(t, j, t0):
                n = RING * t0 + j
                dve.wait_ge(mod_landed, t * (16 * RING) + 16 * (n + 1))
                acc_m = part[:, j // 2, :]
                if j % 2 == 0:
                    dve.wait_ge(mod_up, t * 2 + (n // 2 + 1))
                else:
                    dve.wait_ge(mod_half, t * RING + n)
                s = Steps(dve, mod_step, t * (3 * RING) + 3 * n)
                for q in range(4):
                    kt = 4 * (j % 2) + q
                    w = mod_w[:, q * 512:(q + 1) * 512]
                    if kt == 0:
                        ins = nc.vector.tensor_scalar(acc_m, w, vec[:, 0:1], None, ALU.mult)
                    else:
                        ins = nc.vector.scalar_tensor_tensor(acc_m, w, vec[:, kt:kt + 1], acc_m, ALU.mult, ALU.add)
                    if q < 3:
                        s(ins)
                    else:
                        ins.then_inc(mod_half, 1)

            def convolve(t, j, t0):
                p = RING * (t0 - 2) + j
                dve.wait_ge(stored_act, t * 2 + (2 + 4 + p // 2 + 1))
                dve.wait_ge(stored_dve, t * 2 + (2 + 4 + p // 2 + 1))
                done = 6 * p
                for tap in range(4):
                    for e in range(2):
                        i = t * (2 * RING) + (2 * p + e)
                        src = y[:, bass.ds(i + ST_XS, 1), :]
                        dst = acc[:, e:e + 1, :]

                        def w(c):
                            return k.par[:, bass.ds(i * 5 + (PAR["conv"] + c), 1)]
                        if tap == 0:
                            dve.wait_ge(conv_stored, t * (2 * RING) + (2 * p + e + 1))
                            ins = nc.vector.tensor_scalar(dst, src, w(3), w(4), ALU.mult, ALU.add)
                        else:
                            ins = nc.vector.scalar_tensor_tensor(
                                dst[:, :, tap:], src[:, :, :T - tap], w(3 - tap), dst[:, :, tap:], ALU.mult, ALU.add)
                        ins.then_inc(conv_summed if tap == 3 else conv_step, 1)
                    if tap < 3:
                        done += 2
                        dve.wait_ge(conv_step, t * (6 * RING) + done)

            def one(t, j, t0, mod, conv):
                if mod:
                    half_slot(t, j, t0)
                if conv:
                    convolve(t, j, t0)
                n = RING * t0 + j
                dve.wait_ge(k.slot_used, t * RING + (first + n + 1))
                nc.vector.tensor_copy(y[:, bass.ds(t * 16 + 4 * n, 2), :],
                                      k.psum[2 * (j % 2)][:]).then_inc(stored_dve, 1)
            over_phases(dve, one)

        @block.scalar
        def _(act):
            act.sem_inc(stored_act, 2)
            act.sem_inc(mod_stored, 1)
            act.sem_inc(conv_stored, 2)

            def one(t, j, t0, mod, conv):
                n = RING * t0 + j
                if conv:
                    p = RING * (t0 - 2) + j
                    for e in range(2):
                        act.wait_ge(conv_summed, t * (2 * RING) + (2 * p + e + 1))
                        nc.scalar.activation(y[:, bass.ds(t * (2 * RING) + (2 * p + e + ST_XS), 1), :],
                                             acc[:, e:e + 1, :], ACT.Silu).then_inc(conv_stored, 1)
                act.wait_ge(k.slot_used, t * RING + (first + n + 1))
                nc.scalar.copy(y[:, bass.ds(t * 16 + 4 * n + 2, 2), :],
                               k.psum[2 * (j % 2) + 1][:]).then_inc(stored_act, 1)
                if mod and j == RING - 1:
                    act.wait_ge(mod_up, t * 2 + (2 * t0 + 4))
                    nc.scalar.copy(k.mod[:, bass.ds(t * 8 + (16 + 8 * t0), 8)],
                                   k.psum[4][:, 0:8]).then_inc(mod_stored, 1)

            def gates():
                act.wait_ge(stored_dve, 2 + 8)
                act.wait_ge(stored_act, 2 + 8)
                for q in range(4):
                    nc.scalar.activation(y[:, 4 * q:4 * q + 4, :], y[:, 4 * q:4 * q + 4, :], ACT.Silu)
            over_phases(act, one, gates)


DT, DA, ACS, TOTAL, DT_END = range(5)


def stage_dt(nc, k, a, dtok, hd):
    with ExitStack() as ctx:
        hrow = ctx.enter_context(nc.sbuf_tensor("headrow", [P, 2, HEADS], F32))
        w = ctx.enter_context(nc.sbuf_tensor("dt_work", [P, 8, 2 * HEADS], F32))
        landed = ctx.enter_context(nc.semaphore("headrow_landed"))
        step = ctx.enter_context(nc.semaphore("dt_step"))
        done = ctx.enter_context(nc.semaphore("dt_act"))
        summed = ctx.enter_context(nc.semaphore("dt_summed"))
        dt_ready = ctx.enter_context(nc.semaphore("dt_ready"))
        block = ctx.enter_context(nc.Block())
        RAW, ABS, EXPD, ONEP, LOG1, BACK, ZERO, AROW = range(8)

        def both(ap):
            return ap.unsqueeze(1).to_broadcast([P, 2, HEADS])

        def v(i):
            return w[:, i, :].rearrange("p (c h) -> p c h", c=2)

        @block.sync
        def _(sp):
            sp.dma_start(hrow[:], a["headrow"].rearrange("p (r h) -> p r h", r=2)).then_inc(landed, 16)

        @block.scalar
        def _(act):
            act.wait_ge(landed, 16)
            nc.scalar.activation(w[:, AROW, 0:HEADS], hrow[:, 1, :], ACT.Exp).then_inc(done, 1)
            act.wait_ge(step, 2)
            nc.scalar.activation(w[:, EXPD, :], w[:, ABS, :], ACT.Exp, scale=-1.0).then_inc(done, 1)
            act.wait_ge(step, 3)
            nc.scalar.activation(w[:, LOG1, :], w[:, ONEP, :], ACT.Ln).then_inc(done, 1)
            act.wait_ge(step, 13)
            nc.scalar.activation(w[:, EXPD, :], w[:, BACK, :], ACT.Exp).then_inc(done, 1)

        @block.tensor
        def _(pe):
            pe.wait_ge(step, 11)
            pe.matmul(k.psum[0][:, 0:64], const(k, "tri"), hd[:, DA, :], start=True, stop=True)
            pe.matmul(k.psum[1][:, 0:64], const(k, "ones"), hd[:, DA, :], start=True, stop=True).then_inc(summed, 1)

        @block.vector
        def _(dve):
            s = Steps(dve, step)
            dve.wait_ge(landed, 16)
            s(nc.vector.tensor_tensor(v(RAW), dtok[:].rearrange("p (c h) -> p c h", c=2), both(hrow[:, 0, :]), ALU.add))
            s(nc.vector.scalar_tensor_tensor(w[:, ABS, :], w[:, RAW, :], -1.0, w[:, RAW, :], ALU.mult, ALU.max))
            dve.wait_ge(done, 2)
            s(nc.vector.tensor_scalar(w[:, ONEP, :], w[:, EXPD, :], 1.0, None, ALU.add))
            s(nc.vector.tensor_scalar(w[:, BACK, :], w[:, ONEP, :], -1.0, None, ALU.add))
            s(nc.vector.tensor_scalar(w[:, ZERO, :], w[:, BACK, :], 0.0, None, ALU.is_equal))
            s(nc.vector.tensor_tensor(w[:, BACK, :], w[:, BACK, :], w[:, ZERO, :], ALU.add))
            dve.wait_ge(done, 3)
            s(nc.vector.tensor_tensor(w[:, LOG1, :], w[:, LOG1, :], w[:, ZERO, :], ALU.add))
            s(nc.vector.reciprocal(w[:, BACK, :], w[:, BACK, :]))
            s(nc.vector.tensor_tensor(w[:, LOG1, :], w[:, LOG1, :], w[:, BACK, :], ALU.mult))
            s(nc.vector.tensor_tensor(w[:, LOG1, :], w[:, LOG1, :], w[:, EXPD, :], ALU.mult))
            nc.vector.scalar_tensor_tensor(hd[:, DT, :], w[:, RAW, :], 0.0, w[:, LOG1, :], ALU.max,
                                           ALU.add).then_inc(dt_ready, 1)
            dve.wait_ge(dt_ready, 1)
            dve.wait_ge(done, 1)
            s(nc.vector.scalar_tensor_tensor(hd[:, DA, :].rearrange("p (c h) -> p c h", c=2),
                                             hd[:, DT, :].rearrange("p (c h) -> p c h", c=2), -1.0,
                                             both(w[:, AROW, 0:HEADS]), ALU.mult, ALU.mult))
            dve.wait_ge(summed, 1)
            s(nc.vector.tensor_copy(hd[:, ACS, :], k.psum[0][:, 0:64]))
            s(nc.vector.tensor_tensor(w[:, BACK, :], k.psum[1][:, 0:64], hd[:, ACS, :], ALU.subtract))
            dve.wait_ge(done, 4)
            s(nc.vector.tensor_tensor(hd[:, DT_END, :], hd[:, DT, :], w[:, EXPD, :], ALU.mult))



def stage_ssd(nc, k, y, hd):
    with ExitStack() as ctx:
        def sb(name, shape):
            return ctx.enter_context(nc.sbuf_tensor("ssd_" + name, shape, F32))

        def sem(name):
            return ctx.enter_context(nc.semaphore("ssd_" + name))
        bt_, ct_ = sb("b", [P, 2, T]), sb("c", [P, 2, T])
        xs_ = k.ctx[:].rearrange("p (u i) t -> p u i t", u=2)
        hv_ = sb("hv", [P, 2, 5, 2, 8])
        bt_tok = sb("b_tok", [P, P])
        xdt = sb("xdt", [P, 2, 8, 64])
        xend = sb("xend", [P, 8, 64])
        cb = sb("cb", [P, 2, P])
        seg = sb("seg", [P, 4, 4, P])
        cdec = sb("cdec", [P, 2, 4, P])
        state = sb("state", [P, 512])
        staged, turned, rows_up = sem("staged"), sem("turned"), sem("rows_up")
        evac, masked, decayed, weighted = sem("evac"), sem("masked"), sem("decayed"), sem("weighted")
        cdone, states_up, state_down, y_up, y_down = sem("cdone"), sem("states_up"), sem("state_down"), sem("y_up"), \
            sem("y_down")
        rowed = sem("rowed")
        ident = const(k, "ident")
        block = ctx.enter_context(nc.Block())

        @block.gpsimd
        def _(pool):
            with pool.Fori(0, 2) as gg:
                for u in range(2):
                    g = gg * 2 + u
                    bt, ct, xs, hv = bt_[:, u, :], ct_[:, u, :], xs_[:, u, :, :], hv_[:, u, :, :, :]
                    pool.wait_ge(y_down, g * 2 + 2)
                    nc.gpsimd.tensor_copy(bt.unsqueeze(1), y[:, bass.ds(g + ST_B, 1), :]).then_inc(staged, 1)
                    nc.gpsimd.tensor_copy(ct.unsqueeze(1), y[:, bass.ds(g + ST_C, 1), :]).then_inc(staged, 1)
                    for r in (DT, DA, ACS, DT_END):
                        nc.gpsimd.tensor_copy(hv[:, r, :, :], hd[:, r, :].rearrange("p (c h) -> p c h", c=2)[
                            :, :, bass.ds(g * 8, 8)]).then_inc(staged, 1)
                    nc.gpsimd.tensor_copy(xs, y[:, bass.ds(g * 4 + ST_XS, 4), :]).then_inc(staged, 1)

        @block.tensor
        def _(pe):
            with pe.Fori(0, 2) as gg:
                for u in range(2):
                    g = gg * 2 + u
                    bt, ct, xs, hv = bt_[:, u, :], ct_[:, u, :], xs_[:, u, :, :], hv_[:, u, :, :, :]
                    pe.wait_ge(staged, g * 7 + 7)
                    for c in range(2):
                        pe.wait_ge(y_down, g * 2 + (c + 3))
                        for i in range(4):
                            pe.transpose(k.psum[c][:, i * P:(i + 1) * P], xs[:, i, c * P:(c + 1) * P], ident)
                    for c in range(2):
                        pe.matmul(k.psum[2][:, c * P:(c + 1) * P], bt[:, c * P:(c + 1) * P], ct[:, c * P:(c + 1) * P],
                                  start=True, stop=True)
                    pe.transpose(k.psum[2][:, 2 * P:3 * P], bt[:, 0:P], ident).then_inc(turned, 1)
                    for b in range(4):
                        c, half = b // 2, b % 2
                        for i in range(4):
                            col = hv[:, DA, c, half * 4 + i:half * 4 + i + 1].to_broadcast([P, P])
                            mm = pe.matmul(k.psum[4 + b][:, i * P:(i + 1) * P], col, const(k, "tri"), start=True,
                                           stop=True)
                        mm.then_inc(rows_up, 1)
                    pe.wait_ge(evac, g * 5 + 5)
                    pe.matmul(k.psum[3][:], bt_tok[:], xend[:].rearrange("p h d -> p (h d)"), start=True,
                              stop=True).then_inc(states_up, 1)
                    for c in range(2):
                        for i in range(4):
                            if i % 2 == 0:
                                pe.wait_ge(weighted, g * 4 + (2 * c + i // 2 + 1))
                            if c == 1 and i == 0:
                                pe.wait_ge(state_down, g + 1)
                                pe.wait_ge(cdone, g * 2 + 2)
                            for e in range(2):
                                hh = 2 * i + e
                                out = k.psum[c][e * 64:(e + 1) * 64, i * P:(i + 1) * P]
                                mm = pe.matmul(out, xdt[:, c, hh, :], seg[:, 2 * c + hh // 4, hh % 4, :], start=True,
                                               stop=(c == 0), skip_group_check=True)
                                if c == 1:
                                    mm = pe.matmul(out, state[:, hh * 64:(hh + 1) * 64], cdec[:, hh // 4, hh % 4, :],
                                                   start=False, stop=True, skip_group_check=True)
                        mm.then_inc(y_up, 1)

        @block.vector
        def _(dve):
            dve.sem_inc(y_down, 4)
            with dve.Fori(0, 2) as gg:
                for u in range(2):
                    g = gg * 2 + u
                    bt, ct, xs, hv = bt_[:, u, :], ct_[:, u, :], xs_[:, u, :, :], hv_[:, u, :, :, :]
                    dve.wait_ge(turned, g + 1)
                    for c in range(2):
                        xt = k.psum[c][:].rearrange("p (h d) -> p h d", h=8)
                        nc.vector.tensor_tensor(xdt[:, c, :, :], xt, hv[:, DT, c, :].unsqueeze(2).to_broadcast(
                            [P, 8, 64]), ALU.mult).then_inc(evac, 1)
                    nc.vector.tensor_tensor(xend[:], k.psum[0][:].rearrange("p (h d) -> p h d", h=8),
                                            hv[:, DT_END, 0, :].unsqueeze(2).to_broadcast([P, 8, 64]),
                                            ALU.mult).then_inc(evac, 1)
                    nc.vector.tensor_copy(cb[:].rearrange("p c l -> p (c l)"), k.psum[2][:, 0:2 * P]).then_inc(evac, 1)
                    nc.vector.tensor_copy(bt_tok[:], k.psum[2][:, 2 * P:3 * P]).then_inc(evac, 1)
                    for b in range(4):
                        c, half = b // 2, b % 2
                        dve.wait_ge(rows_up, g * 4 + (b + 1))
                        for i in range(4):
                            ins = nc.vector.scalar_tensor_tensor(
                                seg[:, b, i, :], k.psum[4 + b][:, i * P:(i + 1) * P],
                                hv[:, ACS, c, half * 4 + i:half * 4 + i + 1], const(k, "neg"), ALU.subtract, ALU.add)
                        ins.then_inc(masked, 1)
                    for b in range(4):
                        dve.wait_ge(decayed, g * 4 + (b + 1))
                        if b == 0:
                            dve.wait_ge(evac, g * 5 + 5)
                        nc.vector.tensor_tensor(seg[:, b, :, :], seg[:, b, :, :], cb[:, b // 2, :].unsqueeze(
                            1).to_broadcast([P, 4, P]), ALU.mult).then_inc(weighted, 1)
                    for half in range(2):
                        dve.wait_ge(rowed, g * 2 + (half + 1))
                        nc.vector.tensor_tensor(cdec[:, half, :, :], cdec[:, half, :, :], ct[:, P:2 * P].unsqueeze(
                            1).to_broadcast([P, 4, P]), ALU.mult).then_inc(cdone, 1)
                    for c in range(2):
                        dve.wait_ge(y_up, g * 2 + (c + 1))
                        for i in range(4):
                            ins = nc.vector.scalar_tensor_tensor(
                                y[:, bass.ds(g * 4 + (ST_XS + i), 1), c * P:(c + 1) * P],
                                xs[:, i:i + 1, c * P:(c + 1) * P],
                                k.par[:, bass.ds(g * 4 + (PAR["dskip"] + i), 1)],
                                k.psum[c][:, i * P:(i + 1) * P].unsqueeze(1), ALU.mult, ALU.add)
                        ins.then_inc(y_down, 1)

        @block.scalar
        def _(act):
            with act.Fori(0, 2) as gg:
                for u in range(2):
                    g = gg * 2 + u
                    for b in range(4):
                        act.wait_ge(masked, g * 4 + (b + 1))
                        nc.scalar.activation(seg[:, b, :, :], seg[:, b, :, :], ACT.Exp).then_inc(decayed, 1)
                        if b >= 2:
                            nc.scalar.activation(cdec[:, b - 2, :, :].rearrange("p h l -> p (h l)"),
                                                 k.psum[4 + b][:], ACT.Exp).then_inc(rowed, 1)
                    act.wait_ge(states_up, g + 1)
                    nc.scalar.copy(state[:], k.psum[3][:]).then_inc(state_down, 1)


def stage_ssm_gate(nc, k, y):
    with ExitStack() as ctx:
        half_done = ctx.enter_context(nc.semaphore("gate_done"))
        block = ctx.enter_context(nc.Block())

        @block.vector
        def _(dve):
            for lo, hi in ((0, 4), (4, 8), (8, 12), (12, 16)):
                nc.vector.tensor_tensor(y[:, ST_XS + lo:ST_XS + hi, :], y[:, ST_XS + lo:ST_XS + hi, :],
                                        y[:, lo:hi, :], ALU.mult)
    stage_norm(nc, k, y[:, ST_XS:ST_XS + 16, :], 16, T, row(k, "ssmg", 0, 16), None,
               y[:, ST_XS:ST_XS + 16, :], "ssm")


def stage_bias_table(nc, k, a, table):
    with ExitStack() as ctx:
        rel = ctx.enter_context(nc.sbuf_tensor("bias_rel", [32, 48], F32))
        onehot = ctx.enter_context(nc.sbuf_tensor("bias_onehot", [32, 384], F32))
        neg = ctx.enter_context(nc.sbuf_tensor("bias_neg", [48, 384], F32))
        flat = ctx.enter_context(nc.sbuf_tensor("bias_flat", [48, 384], F32))
        landed = ctx.enter_context(nc.semaphore("bias_landed"))
        looked_up = ctx.enter_context(nc.semaphore("bias_looked_up"))
        masked = ctx.enter_context(nc.semaphore("bias_masked"))
        kept = ctx.enter_context(nc.semaphore("bias_kept"))
        block = ctx.enter_context(nc.Block())

        @block.sync
        def _(sp):
            sp.dma_start(rel[:], a["rel_table"]).then_inc(landed, 16)
            sp.dma_start(onehot[:], a["bias_onehot"]).then_inc(landed, 16)
            sp.dma_start(neg[:], a["bias_neg"]).then_inc(landed, 16)
            sp.wait_ge(masked, 1)
            sp.dma_start(table, flat[:]).then_inc(kept, 16)
            sp.wait_ge(kept, 16)

        @block.tensor
        def _(pe):
            pe.wait_ge(landed, 48)
            pe.matmul(k.psum[0][0:48, 0:384], rel[:], onehot[:], start=True, stop=True).then_inc(looked_up, 1)

        @block.vector
        def _(dve):
            dve.wait_ge(looked_up, 1)
            nc.vector.tensor_tensor(flat[:], k.psum[0][0:48, 0:384], neg[:], ALU.add).then_inc(masked, 1)


def stage_attention(nc, k, a, y):
    table = nc.dram_tensor("bias_table", (48, 384), F32)
    stage_bias_table(nc, k, a, table.ap())
    NQ = 3 * T + 3 * P
    with ExitStack() as ctx:
        def sb(name, shape):
            return ctx.enter_context(nc.sbuf_tensor("att_" + name, shape, F32))

        def sem(name):
            return ctx.enter_context(nc.semaphore("att_" + name))
        half = sb("half", [P, 6])
        q2 = sb("q", [P, 2, 3, T])
        kst, vst = sb("k", [P, T]), sb("v", [P, T])
        vtok = sb("vtok", [P, 2, P])
        bias = y[:, 0:12, :].rearrange("p (u e g) v -> p u e g v", u=2, e=2)
        prob = sb("prob", [P, 2, 2, NQ])
        stat = sb("stat", [P, 2, 2, 6])
        diag = sb("diag", [P, 2, 2, P])
        ptok = sb("ptok", [P, 2, 3 * P])
        landed0, landed1 = sem("bias_even"), sem("bias_odd")
        half_landed = sem("half_landed")
        staged, q_up, scored, added = sem("staged"), sem("q_up"), sem("scored"), sem("added")
        maxed, exped, normed = sem("maxed"), sem("exped"), sem("normed")
        v_up, v_down, turned, p_down, o_up, o_down = sem("v_up"), sem("v_down"), sem("turned"), sem("p_down"), \
            sem("o_up"), sem("o_down")
        step = sem("step")
        ident = const(k, "ident")
        ADDED0, O_DOWN0, TURNED0, NORMED0, SCORED0, V_UP0 = 4, 1, 4, 2, 2, 1
        TURNS = 4

        with nc.Block() as block:
            @block.sync
            def _(sp):
                sp.dma_start(half[:], a["half_masks"]).then_inc(half_landed, 16)
                sp.wait_ge(half_landed, 16)
        block = ctx.enter_context(nc.Block())

        @block.sync
        def _(sp):
            with sp.Fori(0, TURNS) as t:
                for u in range(2):
                    sp.wait_ge(added, t * 4 + (2 * u + 2))
                    for e in range(2):
                        for g in range(3):
                            src = bass.AP(table, (t * 2 + u) * 768 + (g * 16 * 384 + e * 384),
                                          [[1, P], [1, T]])
                            sp.dma_start(bias[:, u, e, g, :], src).then_inc(landed0 if u == 0 else landed1, 16)

        @block.scalar
        def _(act):
            def operands(i):
                act.wait_ge(scored, i * 2 + SCORED0)
                for e in range(2):
                    nc.scalar.activation(
                        q2[:, e, :, ::-1], y[:, ST_Q:ST_Q + 24, :].rearrange("p (g h) t -> p g h t", g=3)[
                            :, :, bass.ds(i, 1), :].rearrange("p g o t -> p g (o t)"),
                        ACT.Copy, scale=half[:, e:e + 1]).then_inc(q_up, 1)

            def exps(i, u):
                for e in range(2):
                    act.wait_ge(maxed, i * 2 + (e + 1))
                    p0 = prob[:, u, e, 3 * T:]
                    nc.scalar.activation(prob[:, u, e, 0:3 * T], prob[:, u, e, 0:3 * T], ACT.Exp,
                                         bias=stat[:, u, e, 1:2], accum_out=stat[:, u, e, 3:4])
                    nc.scalar.activation(p0, p0, ACT.Exp, bias=stat[:, u, e, 0:1],
                                         accum_out=stat[:, u, e, 2:3]).then_inc(exped, 1)

            def probs(i):
                for e in range(2):
                    act.wait_ge(turned, i * 2 + (e + 1 + TURNED0))
                    nc.scalar.copy(ptok[:, e, :], k.psum[6][:, 0:3 * P]).then_inc(p_down, 1)
            operands(0)
            exps(0, 0)
            with act.Fori(0, TURNS - 1) as t:
                for u in range(2):
                    operands(t * 2 + (u + 1))
                    probs(t * 2 + u)
                    exps(t * 2 + (u + 1), 1 - u)
            i = 2 * TURNS - 1
            operands(i)
            probs(i - 1)
            exps(i, 1)
            probs(i)

        @block.gpsimd
        def _(pool):
            with pool.Fori(0, TURNS) as t:
                for u in range(2):
                    i = t * 2 + u
                    pool.wait_ge(scored, i * 2 + SCORED0)
                    pool.nop(nofuse=True)
                    nc.gpsimd.tensor_copy(kst[:].unsqueeze(1), y[:, bass.ds(i + ST_K, 1), :]).then_inc(staged, 1)
                    pool.wait_ge(v_up, i + V_UP0)
                    pool.nop(nofuse=True)
                    nc.gpsimd.tensor_copy(vst[:].unsqueeze(1), y[:, bass.ds(i + ST_V, 1), :]).then_inc(staged, 1)

        @block.tensor
        def _(pe):
            pe.sem_inc(scored, SCORED0)
            pe.sem_inc(v_up, V_UP0)
            pe.sem_inc(turned, TURNED0)

            def scores(i):
                pe.wait_ge(staged, i * 2 + 1)
                for e in range(2):
                    pe.wait_ge(q_up, i * 2 + (e + 1))
                    pe.wait_ge(added, i * 2 + (e - 1 + ADDED0))
                    for g in range(3):
                        pe.matmul(k.psum[3 * e + g // 2][:, (g % 2) * T:(g % 2 + 1) * T], q2[:, e, g, 0:P],
                                  kst[:], start=True, stop=True)
                    for g in range(3):
                        mm = pe.matmul(k.psum[3 * e + 2][:, g * P:(g + 1) * P], q2[:, e, g, P:2 * P], kst[:, 0:P],
                                       start=True, stop=True)
                    mm.then_inc(scored, 1)

            def values(i, u):
                pe.wait_ge(staged, i * 2 + 2)
                pe.wait_ge(o_down, i + O_DOWN0)
                for c in range(2):
                    mm = pe.transpose(k.psum[7][:, c * P:(c + 1) * P], vst[:, c * P:(c + 1) * P], ident)
                mm.then_inc(v_up, 1)
                for e in range(2):
                    pe.wait_ge(normed, i * 2 + (e + 1))
                    if e == 1:
                        pe.wait_ge(p_down, i * 2 + 1)
                    for blk, keys in ((0, 1), (1, 2)):
                        for kb in range(keys):
                            at = (blk + kb) * P
                            for g in range(3):
                                lo = (3 * T + g * P) if blk == 0 else (g * T + kb * P)
                                mm = pe.matmul(k.psum[6][:, at:at + P], prob[:, u, e, lo:lo + P],
                                               diag[:, e, blk, :], start=(g == 0), stop=(g == 2))
                    mm.then_inc(turned, 1)
                for e in range(2):
                    pe.wait_ge(p_down, i * 2 + (e + 1))
                    pe.wait_ge(v_down, i + 1)
                    out = k.psum[7][e * 64:(e + 1) * 64, :]
                    pe.matmul(out[:, 0:P], vtok[:, 0, e * 64:(e + 1) * 64], ptok[:, e, 0:P], start=True,
                              stop=True)
                    for kb in range(2):
                        mm = pe.matmul(out[:, P:2 * P], vtok[:, kb, e * 64:(e + 1) * 64],
                                       ptok[:, e, (1 + kb) * P:(2 + kb) * P], start=(kb == 0), stop=(kb == 1))
                    mm.then_inc(o_up, 1)
            scores(0)
            with pe.Fori(0, TURNS - 1) as t:
                for u in range(2):
                    scores(t * 2 + (u + 1))
                    values(t * 2 + u, u)
            scores(2 * TURNS - 1)
            values(2 * TURNS - 2, 0)
            values(2 * TURNS - 1, 1)

        @block.vector
        def _(dve):
            dve.sem_inc(added, ADDED0)
            dve.sem_inc(o_down, O_DOWN0)

            def scores(i, u, t16):
                dve.wait_ge(landed0 if u == 0 else landed1, t16 + 96)
                s = Steps(dve, step, i * 4)
                for e in range(2):
                    dve.wait_ge(scored, i * 2 + (e + 1 + SCORED0))
                    dve.wait_ge(turned, i * 2 + (e - 3 + TURNED0))
                    pe1 = prob[:, u, e, 0:3 * T].rearrange("p (g v) -> p g v", g=3)
                    pe0 = prob[:, u, e, 3 * T:].rearrange("p (g v) -> p g v", g=3)
                    nc.vector.scalar_tensor_tensor(pe1[:, 0:2, :], k.psum[3 * e][:].rearrange(
                        "p (g v) -> p g v", g=2), 0.125, bias[:, u, e, 0:2, :], ALU.mult, ALU.add)
                    nc.vector.scalar_tensor_tensor(pe1[:, 2:3, :], k.psum[3 * e + 1][:, 0:T].unsqueeze(1),
                                                   0.125, bias[:, u, e, 2:3, :], ALU.mult, ALU.add)
                    nc.vector.scalar_tensor_tensor(pe0, k.psum[3 * e + 2][:, 0:3 * P].rearrange(
                        "p (g v) -> p g v", g=3), 0.125, bias[:, u, e, :, P:2 * P], ALU.mult,
                        ALU.add).then_inc(added, 1)
                    dve.wait_ge(added, i * 2 + (e + 1 + ADDED0))
                    nc.vector.tensor_reduce(stat[:, u, e, 4:5], prob[:, u, e, 3 * T:], AX, ALU.max)
                    s(nc.vector.tensor_reduce(stat[:, u, e, 5:6], prob[:, u, e, 0:3 * T], AX, ALU.max))
                    nc.vector.tensor_scalar(stat[:, u, e, 0:2], stat[:, u, e, 4:6], -1.0, None,
                                            ALU.mult).then_inc(maxed, 1)

            def norms(i, u):
                s = Steps(dve, step, i * 4 + 2)
                for e in range(2):
                    dve.wait_ge(exped, i * 2 + (e + 1))
                    s(nc.vector.reciprocal(stat[:, u, e, 4:6], stat[:, u, e, 2:4]))
                    dve.wait_ge(turned, i * 2 + (e - 1 + TURNED0))
                    nc.vector.tensor_scalar(diag[:, e, 0, :], const(k, "flip"), stat[:, u, e, 4:5], None, ALU.mult)
                    nc.vector.tensor_scalar(diag[:, e, 1, :], const(k, "flip"), stat[:, u, e, 5:6], None,
                                            ALU.mult).then_inc(normed, 1)

            def output(i):
                dve.wait_ge(v_up, i + (1 + V_UP0))
                nc.vector.tensor_copy(vtok[:].rearrange("p c v -> p (c v)"), k.psum[7][:, 0:T]).then_inc(
                    v_down, 1)
                dve.wait_ge(o_up, i * 2 + 2)
                nc.vector.tensor_copy(y[:, bass.ds(i + ST_Q, 1), :], k.psum[7][:, 0:T].unsqueeze(
                    1)).then_inc(o_down, 1)
            scores(0, 0, 0)
            norms(0, 0)
            with dve.Fori(0, TURNS - 1) as t:
                for u in range(2):
                    scores(t * 2 + (u + 1), 1 - u, t * 96 + 96 * u)
                    output(t * 2 + u)
                    norms(t * 2 + (u + 1), 1 - u)
            i = 2 * TURNS - 1
            scores(i, 1, (TURNS - 1) * 96)
            output(i - 1)
            norms(i, 1)
            output(i)


def stage_out(nc, k, first, rhs, gain):
    groups = 2
    per = -(-len(rhs) // KT)
    with ExitStack() as ctx:
        done = ctx.enter_context(nc.semaphore("out_done"))
        block = ctx.enter_context(nc.Block())

        @block.sync
        def _(sp):
            load_ahead(k, sp, first, groups * per)

        @block.tensor
        def _(pe):
            n = first
            for grp in range(groups):
                for part in range(per):
                    kts = range(min(KT, len(rhs) - part * KT))
                    wait_slot(k, pe, n)
                    for i in range(4):
                        for kt in kts:
                            mm = pe.matmul(k.psum[grp * 4 + i][:, 0:T], ring_tile(k, n, kt, i * P),
                                           rhs[part * KT + kt], start=(part == 0 and kt == 0),
                                           stop=(part == per - 1 and kt == kts[-1]))
                    mm.then_inc(k.slot_used, 1)
                    n += 1

        @block.vector
        def _(dve):
            for grp in range(groups):
                dve.wait_ge(k.slot_used, first + (grp + 1) * per)
                for i in range(4):
                    m = grp * 4 + i
                    nc.vector.scalar_tensor_tensor(k.x[:, m, :], k.psum[m][:, 0:T], gain[:, m:m + 1], k.x[:, m, :],
                                                   ALU.mult, ALU.add)


def stage_ffn(nc, k, h, up, down, gain, which, mods, vectors):
    count = FT // 2
    turns = count // RING
    NM, nv = 12, len(vectors)
    with ExitStack() as lay:
        hid = lay.enter_context(nc.sbuf_tensor(f"ffn_hidden{which}", [P, FT, T], F32))
        with ExitStack() as ctx:
            gate = ctx.enter_context(nc.sbuf_tensor(f"ffn_gate{which}", [P, 2, 512], F32))
            gated = ctx.enter_context(nc.semaphore("ffn_gated"))
            stored = ctx.enter_context(nc.semaphore("ffn_stored"))
            mod_w = ctx.enter_context(nc.sbuf_tensor(f"next_w{which}", [P, 2, SLOT], F32))
            part = ctx.enter_context(nc.sbuf_tensor(f"next_part{which}", [P, 2, nv, 512], F32))
            mod_landed = [k.by_pool[f"ffn{which}_{i}_landed"] for i in ("even", "odd")]
            mod_summed = ctx.enter_context(nc.semaphore("mod_summed"))
            mod_step = ctx.enter_context(nc.semaphore("mod_step"))
            mod_up = ctx.enter_context(nc.semaphore("mod_up"))
            mod_stored = ctx.enter_context(nc.semaphore("mod_stored"))
            block = ctx.enter_context(nc.Block())

            def over_slots(eng, one):
                with eng.Fori(0, turns) as t:
                    for j in range(RING):
                        one(j, t)
                for j in range(turns * RING, count):
                    one(j, 0)

            @block.sync
            def _(sp):
                load_ahead(k, sp, up, count)

            @block.gpsimd
            def _(pool):
                for n in range(2):
                    pool.dma_start(mod_w[:, n, :], mods[n]).then_inc(mod_landed[n], 16)

                def load(j, t):
                    pool.wait_ge(mod_summed, t * RING + (j + 1))
                    pool.dma_start(mod_w[:, j % 2, :], mods[t * RING + (j + 2)]).then_inc(mod_landed[j % 2], 16)
                with pool.Fori(0, turns) as t:
                    for j in range(RING):
                        load(j, t)
                for j in range(turns * RING, NM - 2):
                    load(j, 0)

            @block.tensor
            def _(pe):
                rhs = [h[:, kt, :] for kt in range(KT)]
                pe.sem_inc(mod_up, 2)

                def mod(j, t):
                    pe.wait_ge(mod_summed, t * RING + (j + 1))
                    if j % RING == 0:
                        pe.wait_ge(mod_stored, t * nv + nv * (j // RING + 1))
                    for v in range(nv):
                        for q in range(4):
                            c = (j % RING) * 4 + q
                            mm = pe.matmul(k.psum[4 + v][:, c:c + 1], part[:, j % 2, v, q * P:(q + 1) * P],
                                           const(k, "ones")[:, 0:1], start=True, stop=True)
                    mm.then_inc(mod_up, 1)

                def one(j, t):
                    pe.wait_ge(stored, t * RING + (j + 1))
                    b = 2 * (j % 2)
                    outs = [k.psum[b + i // 2][:, (i % 2) * T:(i % 2 + 1) * T] for i in range(4)]
                    slot_products(k, pe, up + j, t, rhs, outs).then_inc(k.slot_used, 1)
                    mod(j, t)
                over_slots(pe, one)
                mod(NM - 1, 0)

            @block.scalar
            def _(act):
                act.sem_inc(mod_stored, nv)

                def one(j, t):
                    act.wait_ge(k.slot_used, t * RING + (up + j + 1))
                    act.wait_ge(stored, t * RING + (j + 1))
                    nc.scalar.activation(gate[:, j % 2, :], k.psum[2 * (j % 2)][:], ACT.Silu).then_inc(gated, 1)
                    if j == RING - 1:
                        store(j, t)

                def store(j, t):
                    act.wait_ge(mod_up, t * RING + (j + 3))
                    for v in range(nv):
                        nc.scalar.copy(k.next_mod[:, v, bass.ds(t * 16 + (j - 3) * 4, 16)],
                                       k.psum[4 + v][:, 0:16]).then_inc(mod_stored, 1)
                over_slots(act, one)
                store(NM - 1, 0)

            @block.vector
            def _(dve):
                dve.sem_inc(stored, 2)

                def mod(j, t):
                    dve.wait_ge(mod_landed[j % 2], t * 32 + 16 * (j // 2 + 1))
                    dve.wait_ge(mod_up, t * RING + (j + 1))
                    s = Steps(dve, mod_step, t * (RING * (KT - 1) * nv) + j * (KT - 1) * nv)
                    w = mod_w[:, j % 2, :]
                    for kt in range(KT):
                        for v, vec in enumerate(vectors):
                            acc = part[:, j % 2, v, :]
                            if kt == 0:
                                ins = nc.vector.tensor_scalar(acc, w[:, 0:512], vec[:, 0:1], None, ALU.mult)
                            else:
                                ins = nc.vector.scalar_tensor_tensor(
                                    acc, w[:, kt * 512:kt * 512 + 512], vec[:, kt:kt + 1], acc, ALU.mult, ALU.add)
                            if kt < KT - 1:
                                ins.then_inc(mod_step, 1)
                                s.n += 1
                            elif v == nv - 1:
                                ins.then_inc(mod_summed, 1)
                        if kt < KT - 1:
                            dve.wait_ge(mod_step, s.done + s.n)

                def one(j, t):
                    if j <= turns * RING:
                        mod(j, t)
                    if j >= turns * RING:
                        mod(j + 1, 0)
                    dve.wait_ge(gated, t * RING + (j + 1))
                    nc.vector.tensor_tensor(hid[:, bass.ds(t * 8 + 2 * j, 2), :].rearrange("p a t -> p (a t)"),
                                            gate[:, j % 2, :], k.psum[2 * (j % 2) + 1][:], ALU.mult).then_inc(
                                                stored, 1)
                over_slots(dve, one)
        stage_out(nc, k, down, [hid[:, i, :] for i in range(FT)], gain)


def stage_conformer(nc, k, a, h):
    NS = 4
    PAD = TAPS - 1
    ON_PE = (5, 6, 7)
    with ExitStack() as lay:
        u = lay.enter_context(nc.sbuf_tensor("cv_u", [P, KT, PAD + T], F32))
        v = lay.enter_context(nc.sbuf_tensor("cv_v", [P, KT, T], F32))
        sq = lay.enter_context(nc.sbuf_tensor("cv_sq", [P, KT, T], F32))
        first = FIRST["pw1"]
        with ExitStack() as ctx:
            sig = sq
            diag = ctx.enter_context(nc.sbuf_tensor("cv_diag", [P, len(ON_PE), TAPS, P], F32))
            sigmoid = ctx.enter_context(nc.semaphore("cv_sigmoid"))
            gated = ctx.enter_context(nc.semaphore("cv_gated"))
            diag_made = ctx.enter_context(nc.semaphore("cv_diag_made"))
            convolved = ctx.enter_context(nc.semaphore("cv_convolved"))
            padded = ctx.enter_context(nc.semaphore("cv_padded"))
            step = ctx.enter_context(nc.semaphore("cv_step"))
            ctx_landed = ctx.enter_context(nc.semaphore("ctx_landed"))
            block = ctx.enter_context(nc.Block())

            @block.sync
            def _(sp):
                load_ahead(k, sp, first, NS)
                sp.dma_start(k.ctx[:], a["ctxt"]).then_inc(ctx_landed, 16)
                sp.wait_ge(ctx_landed, 16)

            @block.gpsimd
            def _(pool):
                nc.gpsimd.memset(u[:, :, 0:PAD], 0.0).then_inc(padded, 1)
                for n, i in enumerate(ON_PE):
                    nc.gpsimd.tensor_tensor(
                        diag[:, n, :, :], const(k, "ident").unsqueeze(1).to_broadcast([P, TAPS, P]),
                        row(k, "dw", i * (TAPS + 1), TAPS).unsqueeze(2).to_broadcast([P, TAPS, P]),
                        ALU.mult).then_inc(diag_made, 1)

            @block.tensor
            def _(pe):
                rhs = [h[:, kt, :] for kt in range(KT)]
                for j in range(NS):
                    outs = [k.psum[2 * j + i // 2][:, (i % 2) * T:(i % 2 + 1) * T] for i in range(4)]
                    slot_products(k, pe, first + j, 0, rhs, outs).then_inc(k.slot_used, 1)
                pe.wait_ge(padded, 1)
                pe.wait_ge(gated, KT)
                for n, i in enumerate(ON_PE):
                    pe.wait_ge(diag_made, n + 1)
                    for c in range(TAPS):
                        mm = pe.matmul(k.psum[2 * n][:, 0:T], diag[:, n, c, :], u[:, i, c:c + T], start=(c == 0),
                                       stop=(c == TAPS - 1))
                    mm.then_inc(convolved, 1)

            @block.scalar
            def _(act):
                for j in range(NS):
                    act.wait_ge(k.slot_used, first + j + 1)
                    for i in range(2):
                        m = 2 * j + i
                        nc.scalar.activation(sig[:, m, :], k.psum[2 * j + 1][:, i * T:(i + 1) * T], ACT.Sigmoid,
                                             bias=row(k, "pw1b", 8 + m)).then_inc(sigmoid, 1)
                for n, i in enumerate(ON_PE):
                    act.wait_ge(convolved, n + 1)
                    nc.scalar.activation(v[:, i, :], k.psum[2 * n][:, 0:T], ACT.Identity,
                                         bias=row(k, "dw", i * (TAPS + 1) + TAPS))

            @block.vector
            def _(dve):
                done = 0
                U = 5

                def gate(tiles):
                    for m in tiles:
                        dve.wait_ge(sigmoid, m + 1)
                        nc.vector.scalar_tensor_tensor(
                            u[:, m, PAD:], k.psum[2 * (m // 2)][:, (m % 2) * T:(m % 2 + 1) * T], row(k, "pw1b", m),
                            sig[:, m, :], ALU.add, ALU.mult).then_inc(gated, 1)

                def convolve(tiles, done):
                    g = len(tiles)
                    for i in tiles:
                        nc.vector.tensor_scalar(v[:, i, :], u[:, i, PAD:], row(k, "dw", i * (TAPS + 1) + PAD),
                                                row(k, "dw", i * (TAPS + 1) + TAPS), ALU.mult, ALU.add).then_inc(
                                                    step, 1)
                    dve.wait_ge(step, done + g)
                    with dve.Fori(0, PAD // U) as t:
                        s = Steps(dve, step, t * (U * g) + (done + g))
                        for j in range(U):
                            for i in tiles:
                                nc.vector.scalar_tensor_tensor(
                                    v[:, i:i + 1, :], u[:, i:i + 1, bass.ds(t * U + j, T)],
                                    k.par[:, bass.ds(t * U + (PAR["dw"] + i * (TAPS + 1) + j), 1)], v[:, i:i + 1, :],
                                    ALU.mult, ALU.add).then_inc(step, 1)
                                s.n += 1
                            dve.wait_ge(step, s.done + s.n)
                    return done + g * TAPS
                gate([0, 1])
                dve.wait_ge(padded, 1)
                dve.wait_ge(gated, 2)
                done = convolve([0, 1], done)
                gate(range(2, KT))
                dve.wait_ge(gated, KT)
                done = convolve([2, 3], done)
                convolve([4], done)
        with ExitStack() as ctx:
            mean = ctx.enter_context(nc.sbuf_tensor("cv_mean", [P, 2, T], F32))
            meant = ctx.enter_context(nc.semaphore("cv_meant"))
            centred = ctx.enter_context(nc.semaphore("cv_centred"))
            squared = ctx.enter_context(nc.semaphore("cv_squared"))
            summed = ctx.enter_context(nc.semaphore("cv_summed"))
            step = ctx.enter_context(nc.semaphore("cv_lnstep"))
            rooted = ctx.enter_context(nc.semaphore("cv_rooted"))
            scaled = ctx.enter_context(nc.semaphore("cv_scaled"))
            block = ctx.enter_context(nc.Block())

            @block.tensor
            def _(pe):
                for i in range(KT):
                    mm = pe.matmul(k.psum[0][:, 0:T], const(k, "ones"), v[:, i, :], start=(i == 0), stop=(i == 7))
                mm.then_inc(meant, 1)
                pe.wait_ge(squared, 1)
                for i in range(KT):
                    mm = pe.matmul(k.psum[1][:, 0:T], const(k, "ones"), sq[:, i, :], start=(i == 0), stop=(i == 7))
                mm.then_inc(summed, 1)

            @block.vector
            def _(dve):
                s = Steps(dve, step)
                dve.wait_ge(meant, 1)
                s(nc.vector.tensor_scalar(mean[:, 0, :], k.psum[0][:, 0:T], 1.0 / D, None, ALU.mult))
                nc.vector.tensor_tensor(v[:], v[:], mean[:, 0:1, :].to_broadcast([P, KT, T]),
                                        ALU.subtract).then_inc(centred, 1)
                dve.wait_ge(summed, 1)
                s(nc.vector.tensor_scalar(mean[:, 1, :], k.psum[1][:, 0:T], 1.0 / D, EPS, ALU.mult, ALU.add))
                dve.wait_ge(rooted, 1)
                s(nc.vector.reciprocal(mean[:, 1, :], mean[:, 1, :]))
                nc.vector.tensor_tensor(v[:], v[:], mean[:, 1:2, :].to_broadcast([P, KT, T]),
                                        ALU.mult).then_inc(scaled, 1)

            @block.scalar
            def _(act):
                act.wait_ge(centred, 1)
                nc.scalar.activation(sq[:], v[:], ACT.Square).then_inc(squared, 1)
                act.wait_ge(step, 2)
                nc.scalar.activation(mean[:, 1, :], mean[:, 1, :], ACT.Sqrt).then_inc(rooted, 1)
                act.wait_ge(scaled, 1)
                for i in range(KT):
                    nc.scalar.activation(u[:, i, PAD:], v[:, i, :], ACT.Silu, bias=row(k, "lnb", i),
                                         scale=row(k, "lng", i))
        first = FIRST["pw2"]
        with ExitStack() as ctx:
            biased = ctx.enter_context(nc.semaphore("cv_biased"))
            block = ctx.enter_context(nc.Block())

            @block.sync
            def _(sp):
                load_ahead(k, sp, first, 2)

            @block.tensor
            def _(pe):
                rhs = [u[:, kt, PAD:] for kt in range(KT)]
                for j in range(2):
                    outs = [k.psum[4 * j + i][:, 0:T] for i in range(4)]
                    slot_products(k, pe, first + j, 0, rhs, outs).then_inc(k.slot_used, 1)

            @block.scalar
            def _(act):
                for m in range(KT):
                    act.wait_ge(k.slot_used, first + m // 4 + 1)
                    nc.scalar.activation(v[:, m, :], k.psum[m][:, 0:T], ACT.Identity,
                                         bias=row(k, "pw2b", m)).then_inc(biased, 1)

            @block.vector
            def _(dve):
                for m in range(KT):
                    dve.wait_ge(biased, m + 1)
                    nc.vector.scalar_tensor_tensor(k.x[:, m, :], v[:, m, :], k.mod[:, 64 + m:65 + m], k.x[:, m, :],
                                                   ALU.mult, ALU.add)


GN_EPS = 64e-5
CH = 128
NCH = 2 * T // CH
SH, SC, GT = 0, 8, 16


def mod2(k, layer, part, ctx=False):
    c = 48 * ctx + 24 * layer + part
    return k.mod[:, c:c + 8]


def stage_shift(nc, k, a, h, xx, w1):
    hs, xs = (b[:].rearrange("p k (s t) -> p (k s) t", s=2) for b in (h, xx))
    with ExitStack() as ctx:
        step = ctx.enter_context(nc.semaphore("shift_step"))
        block = ctx.enter_context(nc.Block())

        @block.sync
        def _(sp):
            sp.dma_start(w1[:], a["lora_in"]).then_inc(k.w1_landed, 16)

        @block.vector
        def _(dve):
            s = Steps(dve, step)
            s(nc.vector.tensor_scalar(xs, hs, -1.0, None, ALU.mult))
            s(nc.vector.scalar_tensor_tensor(xs[:, :, 1:], hs[:, :, :T - 1], 0.5, xs[:, :, 1:], ALU.mult, ALU.add))
            s(nc.vector.scalar_tensor_tensor(xs[:, :, :T - 1], hs[:, :, 1:], 0.5, xs[:, :, :T - 1], ALU.mult,
                                             ALU.add))


def stage_rwkv_in(nc, k, h, xx, w1, lora, kept):
    R, K, V, G, W, A = range(6)
    first = FIRST["rkvg"]
    with ExitStack() as ctx:
        l0 = ctx.enter_context(nc.sbuf_tensor("mixed0", [P, KT, 512], F32))
        l1 = ctx.enter_context(nc.sbuf_tensor("mixed1", [P, KT, 512], F32))
        outb = ctx.enter_context(nc.sbuf_tensor("proj_out", [P, 2, 4, 512], F32))
        mixed = ctx.enter_context(nc.semaphore("mixed"))
        lora_up = ctx.enter_context(nc.semaphore("lora_up"))
        evac = ctx.enter_context(nc.semaphore("proj_evac"))
        kept0 = k.by_pool["proj_even_kept"]
        kept1 = k.by_pool["proj_odd_kept"]
        spare_kept = k.by_pool["proj_spare_kept"]
        block = ctx.enter_context(nc.Block())
        order = [(W, l0), (A, l1), (R, l0), (K, l1), (V, l0), (G, xx)]

        @block.sync
        def _(sp):
            load_ahead(k, sp, first, 4)

        @block.vector
        def _(dve):
            for n, (j, buf) in enumerate(order):
                if n in (2, 3):
                    dve.wait_ge(lora_up, n - 1)
                if n == 4:
                    dve.wait_ge(k.slot_used, first + 2)
                if n == 5:
                    dve.wait_ge(mixed, KT * n)
                for i in range(KT):
                    nc.vector.scalar_tensor_tensor(buf[:, i, :], xx[:, i, :], row(k, "mu", 8 * j + i), h[:, i, :],
                                                   ALU.mult, ALU.add).then_inc(mixed, 1)

        @block.tensor
        def _(pe):
            pe.wait_ge(k.w1_landed, 16)
            for n in range(2):
                pe.wait_ge(mixed, KT * (n + 1))
                for kt in range(KT):
                    mm = pe.matmul(k.psum[n][:], w1[:, kt, n * P:(n + 1) * P], order[n][1][:, kt, :],
                                   start=(kt == 0), stop=(kt == KT - 1))
                mm.then_inc(lora_up, 1)
            for j in range(8):
                n = 2 + j // 2
                pe.wait_ge(mixed, KT * (n + 1))
                if j >= 2:
                    pe.wait_ge(evac, 2 + 4 * (j - 1))
                elif j == 0:
                    pe.wait_ge(evac, 2)
                outs = [k.psum[4 * (j % 2) + i][:] for i in range(4)]
                rhs = [order[n][1][:, kt, :] for kt in range(KT)]
                slot_products(k, pe, first + j, 0, rhs, outs).then_inc(k.slot_used, 1)

        @block.scalar
        def _(act):
            act.wait_ge(lora_up, 1)
            for d in range(2):
                rows = slice(64 * d, 64 * d + 64)
                ins = nc.scalar.activation(lora[rows, d, 0, :], k.psum[0][rows, :], ACT.Tanh)
            ins.then_inc(evac, 1)
            act.wait_ge(lora_up, 2)
            for d in range(2):
                rows = slice(64 * d, 64 * d + 64)
                ins = nc.scalar.copy(lora[rows, d, 1, :], k.psum[1][rows, :])
            ins.then_inc(evac, 1)
            for j in range(8):
                act.wait_ge(k.slot_used, first + j + 1)
                if j >= 2:
                    act.wait_ge((kept0, kept1)[j % 2], 16 * (j // 2))
                for i in range(4):
                    nc.scalar.copy(outb[:, j % 2, i, :], k.psum[4 * (j % 2) + i][:]).then_inc(evac, 1)

        @block.gpsimd
        def _(pool):
            nc.gpsimd.memset(lora[64:P, 0, :, :], 0.0)
            nc.gpsimd.memset(lora[0:64, 1, :, :], 0.0)
            pool.dma_start(kept[KT], h[:, 0:4, :]).then_inc(spare_kept, 16)
            for j in range(8):
                pool.wait_ge(evac, 2 + 4 * (j + 1))
                pool.dma_start(kept[4 * (j % 2):4 * (j % 2) + 4, :, j // 2, :].rearrange("t p n -> p t n"),
                               outb[:, j % 2, :, :]).then_inc((kept0, kept1)[j % 2], 16)
            pool.wait_ge(kept0, 64)
            pool.wait_ge(kept1, 64)
            pool.wait_ge(spare_kept, 16)


class Track:

    def __init__(self, sem, items, marks):
        self.sem, self.n, self.seen = sem, 0, {}
        self.names, self.item_of = [], {}
        for i, item in enumerate(items):
            for name in marks(item):
                assert name not in self.item_of, name
                self.names.append(name)
                self.item_of[name] = i
        self.at = {name: i + 1 for i, name in enumerate(self.names)}

    def start(self, eng):
        if self.names:
            eng.sem_inc(self.sem, len(self.names))

    def mark(self, ins, name):
        assert self.names[self.n] == name, (self.names[self.n], name)
        self.n += 1
        ins.then_inc(self.sem, 1)

    def wait(self, eng, turn, here, *names, apart=False):
        counts = [self.at[n] + (len(self.names) if self.item_of[n] <= here else 0) for n in names if n in self.at]
        count = max(counts, default=0)
        if count > self.seen.get(id(eng), 0):
            self.seen[id(eng)] = count
            eng.wait_ge(self.sem, turn * len(self.names) + count)
        if apart:
            eng.nop(nofuse=True)


LEVELS = range(1, 7)
ORDER = [[0, 1, 2, 3], [1, 0, 3, 2]]
READOUT = [(f"read{i}",) for i in range(4)] + [("yrec", q) for q in range(4)] + [("read4",), ("read5",)]
KKNORM = [("kk0",), ("kk1",)] + [("kkrec", q) for q in range(4)] + [("kk2",)]
BONUS = [("bonus0",), ("bonus1",), ("bonus2",), ("stage",)]
PREP = ["lw", "cum", "half", "mid", "dif", "blend", "kd", "b", "ksum"]


def prep_items(p):
    return [("lora", p)] + [("el", p, n) for n in PREP[:3]] + [("eh", p)] + [("el", p, n) for n in PREP[3:5]] + \
        [("exps", p)] + [("el", p, n) for n in PREP[5:]] + \
        [("fin", p, n) for n in ("at", "rt", "bt", "kt")]


def serial_items(s):
    return [(kind, s, q) for q in range(NCH) for kind in ("X", "SA", "U", "Y") if (kind, q) != ("U", NCH - 1)]


def merge(*lists):
    keyed = [(share * (i + 0.5) / len(x), n, item) for n, (share, x) in enumerate(lists) for i, item in enumerate(x)]
    return [item for _, _, item in sorted(keyed, key=lambda z: (z[0], z[1]))]


def section(d):
    s = p = 1 - d
    head = [("g", d, e, m) for e in range(2) for m in range(4)]
    head = merge((1, head), (1, [("keep", d), ("bup", d)] + (BONUS[1:] if d else [])))
    body = []
    for e in range(2):
        body += [("T", d, e)]
    for lv in LEVELS:
        body += [("W", d, lv, e) for e in range(2)] + [("Tr", d, lv - 1, e) for e in range(2) if lv > 1] + [
            ("Pt", d, lv, e) for e in range(2)]
    if d == 0:
        side = serial_items(s) + READOUT + [("vtok0",), ("vtok1",), BONUS[0]]
        prep = prep_items(p)
    else:
        side = serial_items(s)
        prep = [("stage2",)] + KKNORM + prep_items(p)
    return head + merge((1, body), (1.1, side), (0.75, prep))


def marks(item):
    k, rest = item[0], item[1:]
    n = "".join(str(x) for x in rest)
    none = []
    return {
        "g": lambda: ([f"m{n}"] + ([f"i{rest[0]}0{rest[1]}"] if rest[-1:] == (0,) else []), none, [f"g{n}"], none),
        "bup": lambda: (none, [f"btok{n}", f"ktok{n}"], [f"bup{n}", f"kup{n}"], none),
        "keep": lambda: (none, none, none, [f"keep{n}"]),
        "T": lambda: ([f"t{rest[0]}0{rest[-1]}"], none, [f"T{n}"], none),
        "W": lambda: (none, [f"Wc{n}"], [f"W{n}"], none),
        "Pt": lambda: ([f"t{n}"], none, [f"Pt{n}"], [f"eyeM{rest[0]}"] if rest[1:] == (6, 1) else none),
        "Tr": lambda: (none, [f"Mc{n}"], [f"Tr{n}"], none),
        "X": lambda: ([f"x{n}"] if rest[-1:] in ((0,), (3,)) else [f"ze{n}", f"x{n}"], none, [f"X{n}"], none),
        "SA": lambda: ([f"sa{n}", f"sb{n}"], none, [f"SA{n}"], [f"eyeT{rest[0]}"] if rest[1:] == (3,) else none),
        "U": lambda: ([f"z{n}"], none, [f"U{n}"], none),
        "Y": lambda: ([f"y{n}"], none, [f"Y{n}"], none),
        "lora": lambda: (none, [f"sigw{n}", f"siga{n}"], [f"lora{n}"], none),
        "el": lambda: ([rest[1] + str(rest[0])] if len(rest) > 1 else none, none, none, none),
        "eh": lambda: (none, [f"eh{n}"], none, none),
        "exps": lambda: (none, [f"ee{n}", f"ei{n}", f"en{n}"], none, none),
        "fin": lambda: ([rest[-1] + str(rest[0])] + ([f"E{rest[0]}"] if rest[-1:] == ("kt",) else []),
                [f"{rest[-1][0]}m{rest[0]}"] if rest[-1:] in (("at",), ("rt",)) else none, none, none),
        "bonus0": lambda: (["rk"], none, none, none),
        "bonus1": lambda: (none, ["silu"], ["bonus"], none),
        "bonus2": lambda: (["bon"], none, none, none),
        "stage": lambda: (none, ["kstaged"], none, ["staged"]),
        "stage2": lambda: (none, ["rstaged"], none, none),
        "kk0": lambda: (["omka", "kkraw", "kksq"], none, none, none),
        "kk1": lambda: (none, ["norm"], ["squp"], none),
        "kkrec": lambda: ((["kkmax"] if rest == (0,) else []) + [f"kkrec{n}"], none, none, none),
        "kk2": lambda: (["kk"], none, none, none),
        "read0": lambda: (none, none, ["mean"], none),
        "read1": lambda: (["mean", "xc"], none, none, none),
        "read2": lambda: (none, ["ysq"], ["var"], none),
        "read3": lambda: (["var"], ["yroot"], none, none),
        "yrec": lambda: ([f"yrec{n}"], none, none, none),
        "read4": lambda: (["yn", "ynl"], none, none, none),
        "read5": lambda: (["ysum", "o"], none, none, none),
        "vtok0": lambda: (none, ["vtok"], ["vup"], none),
        "vtok1": lambda: (["vm"], none, none, none),
    }[k]()


def stage_rwkv_scan(nc, k, a, lora, kept, o):
    HALF_E = -math.exp(-0.5)
    with ExitStack() as ctx:
        flat = k.ring[:].rearrange("p r s -> p (r s)")
        used = [0]

        def in_ring(*shape):
            n = int(np.prod(shape))
            ap = flat[:, used[0]:used[0] + n]
            used[0] += n
            assert used[0] <= RING * SLOT
            if len(shape) == 1:
                return ap
            names = "abcd"[:len(shape)]
            return ap.rearrange(f"p ({' '.join(names)}) -> p {' '.join(names)}", **dict(zip(names, shape)))

        def sb(name, *shape, dt=F32):
            return ctx.enter_context(nc.sbuf_tensor("rw_" + name, [P, *shape], dt))

        def sem(name):
            return ctx.enter_context(nc.semaphore("rw_" + name))
        MT, AKT, RBT, RKT = (in_ring(2, 2, NCH, P) for _ in range(4))
        AB, M, Wb = (in_ring(2, NCH, P) for _ in range(3))
        at2, rt2 = in_ring(2, 512), in_ring(2, 512)
        vtok2 = in_ring(2, NCH, P)
        tin = in_ring(4, 512)
        lora_out, tri, lvl, starts = sb("lora_out", 2, 9 * P), sb("tri", 4, P), sb("lvl", 2, 7, P, dt=U8), \
            sb("starts", 512)
        half2 = sb("half2", 6)
        pre, w2, rp, omka = sb("pre", 4, 512), sb("w2", 2, P), sb("rp", 9), sb("omka", 1)
        kk, sq, lw, av, mid, dif, kd, bb, ksum, ee, ei, en, at, rt, bt, kt_, yf, bonv, sg, tmp = (
            sb(n, 512) for n in ("kk", "sq", "lw", "av", "mid", "dif", "kd", "bb", "ksum", "ee", "ei", "en", "at",
                                 "rt", "bt", "kt", "yf", "bonv", "sg", "tmp"))
        hs_, eh, dec = sb("half", NCH), sb("eh", NCH), sb("dec", 4)
        atS, rtS, decS = sb("atS", 2, 512), sb("rtS", 2, 512), sb("decS", 2, 4)
        btok, ktok, vtok = sb("btok", 2, NCH, P), sb("ktok", 2, NCH, P), sb("vtok", NCH, P)
        xs2, sas2, sas = sb("xs2", 2, P), sb("sas2", 2, P), sb("sas", P)
        z, ze = sb("z", P), sb("ze", P)
        consts = sem("consts")
        ident, headones = const(k, "ident"), const(k, "headones")
        W0, A0, KK_, KA, RK_, LG, LB = 0, 2, 4, 5, 6, 7, 8
        rr, kx, vv, gg = (tin[:, i, :] for i in range(4))
        b = k.psum
        HALVES = [slice(0, 64), slice(64, 128)]

        def chunks(ap):
            return ap.rearrange("p (c t) -> p c t", c=NCH)

        def diagonal(buf):
            f = buf[:].rearrange("p e v -> p (e v)")
            return bass.AP(f.tensor, f.offset, [list(f.ap[0]), [192, 2], [1, 64]])

        wide = pre[:].rearrange("p j n -> p (j n)")[:, 0:14 * P].bitcast(I32)
        with nc.Block() as block:
            @block.sync
            def _(sp):
                sp.dma_start(lora_out[:], a["lora_out"]).then_inc(consts, 16)
                sp.dma_start(tri[:].rearrange("p m f -> p (m f)"), a["tri_masks"]).then_inc(consts, 16)
                sp.dma_start(wide, a["level_masks"]).then_inc(consts, 16)
                sp.dma_start(starts[:], a["chunk_starts"]).then_inc(consts, 16)
                sp.dma_start(half2[:], a["half_masks"]).then_inc(consts, 16)
                sp.wait_ge(consts, 80)

            @block.vector
            def _(dve):
                for buf in (MT, AKT, RBT, RKT):
                    nc.vector.memset(buf[:, 1, :, :, :], 0.0)
                for buf in (vtok2, vtok[:], xs2[:], sas2[:], z[:], yf[:], decS[:], bonv[:], sg[:]):
                    nc.vector.memset(buf, 0.0)
                dve.wait_ge(consts, 80)
                nc.vector.tensor_copy(lvl[:].rearrange("p u l f -> p (u l f)"), wide)

            @block.gpsimd
            def _(pool):
                for buf in (atS, rtS):
                    nc.gpsimd.memset(buf[:, 1, :], 0.0)
                for buf in (btok, ktok):
                    nc.gpsimd.memset(buf[:, 1, :, :], 0.0)
                src = ident.unsqueeze(1).to_broadcast([P, 2 * NCH, P])
                nc.gpsimd.tensor_copy(M.rearrange("p e c f -> p (e c) f"), src)
                nc.gpsimd.tensor_copy(MT[:, 0, :, :, :].rearrange("p e c f -> p (e c) f"), src)

        def run(items, turns, part):
            with ExitStack() as inner:
                dv, ac, pt, pl = (Track(inner.enter_context(nc.semaphore(f"rw_{n}_{part}")), items,
                                        lambda item, i=i: marks(item)[i]) for i, n in enumerate(
                                            ("dve", "act", "pe", "pool")))
                pre_landed = inner.enter_context(nc.semaphore(f"rw_pre_{part}"))
                block = inner.enter_context(nc.Block())

                def loop(eng, body):
                    if turns:
                        with eng.Fori(0, turns) as t:
                            body(t)
                    else:
                        body(0)
                next_tile = 1 if turns else 0

                @block.sync
                def _(sp):
                    def body(t):
                        if ("stage",) in items:
                            ac.wait(sp, t, -1, "rstaged")
                            sp.dma_start(pre[:].unsqueeze(1), kept[bass.ds(t + next_tile, 1), :, :, :].rearrange(
                                "o p j n -> p o j n")).then_inc(pre_landed, 16)
                    loop(sp, body)

                @block.gpsimd
                def _(pool):
                    pl.start(pool)
                    eye = ident.unsqueeze(1).to_broadcast([P, 2 * NCH, P])

                    def body(t):
                        for i, item in enumerate(items):
                            kind, d = item[0], item[1] if len(item) > 1 else None
                            if kind == "keep":
                                dv.wait(pool, t, i, f"E{d}", f"z{d}2")
                                pt.wait(pool, t, i, f"Y{d}3", apart=True)
                                nc.gpsimd.tensor_copy(atS[:, d, :], at[:])
                                nc.gpsimd.tensor_copy(decS[:, d, 0:3], dec[:, 0:3])
                                pl.mark(nc.gpsimd.tensor_copy(rtS[:, d, :], rt[:]), f"keep{d}")
                            elif kind == "Pt" and item[2:] == (6, 1) and part == "loop":
                                pt.wait(pool, t, i, f"Pt{d}61", apart=True)
                                pl.mark(nc.gpsimd.tensor_copy(M.rearrange("p e c f -> p (e c) f"), eye), f"eyeM{d}")
                            elif kind == "SA" and item[2] == 3 and part == "loop":
                                pt.wait(pool, t, i, f"SA{d}3", apart=True)
                                pl.mark(nc.gpsimd.tensor_copy(MT[:, d, :, :, :].rearrange(
                                    "p e c f -> p (e c) f"), eye), f"eyeT{d}")
                            elif kind == "stage":
                                pt.wait(pool, t, i, "lora1")
                                ac.wait(pool, t, i, "siga1")
                                dv.wait(pool, t, i, "rk", apart=True)
                                nc.gpsimd.tensor_copy(w2[:], lora_out[:, :, bass.ds((t + next_tile) * P, P)])
                                pl.mark(nc.gpsimd.tensor_copy(
                                    rp[:], k.par[:, bass.ds((t + next_tile) * 9 + PAR["rw"], 9)]), "staged")
                    loop(pool, body)

                @block.scalar
                def _(act):
                    ac.start(act)

                    def body(t):
                        for i, item in enumerate(items):
                            kind, d = item[0], item[1] if len(item) > 1 else None
                            n = "".join(str(x) for x in item[1:])
                            if kind == "bup":
                                for dst, bk, up, name in ((btok, 4, "bup", "btok"), (ktok, 5, "kup", "ktok")):
                                    pt.wait(act, t, i, f"{up}{d}", f"Y{d}3")
                                    ac.mark(nc.scalar.copy(dst[:, d, :, :].rearrange("p c t -> p (c t)"),
                                                           b[bk][:]), f"{name}{d}")
                            elif kind in ("W", "Tr"):
                                lv, e = item[2:]
                                pt.wait(act, t, i, f"{kind}{n}")
                                bk = (2 * (lv % 2) + e) if kind == "W" else (2 * (lv % 2) + e)
                                dst = Wb if kind == "W" else M
                                ac.mark(nc.scalar.copy(dst[:, e, :, :].rearrange("p c t -> p (c t)"), b[bk][:]),
                                        f"{kind[0].replace('T', 'M')}c{n}")
                            elif kind == "lora":
                                pt.wait(act, t, i, f"lora{d}")
                                dv.wait(act, t, i, f"b{1 - d}")
                                ac.mark(nc.scalar.activation(lw[:], b[4][:], ACT.Sigmoid,
                                                             bias=rp[:, W0 + d:W0 + d + 1]), f"sigw{d}")
                                ac.mark(nc.scalar.activation(av[:], b[5][:], ACT.Sigmoid,
                                                             bias=rp[:, A0 + d:A0 + d + 1]), f"siga{d}")
                            elif kind == "eh":
                                dv.wait(act, t, i, f"half{d}", f"E{1 - d}")
                                ac.mark(nc.scalar.activation(eh[:], hs_[:], ACT.Exp), f"eh{d}")
                            elif kind == "exps":
                                dv.wait(act, t, i, f"dif{d}", f"kt{1 - d}")
                                before, upto, sign = (dif, mid, 1.0) if d == 0 else (mid, dif, -1.0)
                                ac.mark(nc.scalar.activation(ee[:], before[:], ACT.Exp, scale=sign), f"ee{d}")
                                ac.mark(nc.scalar.activation(ei[:], upto[:], ACT.Exp, scale=sign), f"ei{d}")
                                ac.mark(nc.scalar.activation(en[:], upto[:], ACT.Exp, scale=-sign), f"en{d}")
                            elif kind == "fin":
                                if item[2] in ("at", "rt"):
                                    src, dst = {"at": (at, at2), "rt": (rt, rt2)}[item[2]]
                                    dv.wait(act, t, i, f"{item[2]}{d}")
                                    nc.scalar.activation(dst[:, 0, :], src[:], ACT.Copy, scale=half2[:, 0:1])
                                    ac.mark(nc.scalar.activation(dst[:, 1, :], src[:], ACT.Copy,
                                                                 scale=half2[:, 1:2]), f"{item[2][0]}m{d}")
                            elif kind == "stage":
                                act.wait_ge(pre_landed, t * 16 + 16)
                                dv.wait(act, t, i, "bon")
                                ac.mark(nc.scalar.copy(kx, pre[:, 1, :]), "kstaged")
                            elif kind == "stage2":
                                ac.wait(act, t, i, "silu")
                                pt.wait(act, t, i, "vup")
                                for j in (0, 2, 3):
                                    ins = nc.scalar.copy(tin[:, j, :], pre[:, j, :])
                                ac.mark(ins, "rstaged")
                            elif kind == "bonus1":
                                dv.wait(act, t, i, "o")
                                ac.mark(nc.scalar.activation(sg[:], gg, ACT.Silu), "silu")
                            elif kind == "kk1":
                                pt.wait(act, t, i, "squp")
                                ac.mark(nc.scalar.activation(sq[:], b[4][:], ACT.Sqrt), "norm")
                            elif kind == "read2":
                                dv.wait(act, t, i, "xc")
                                ac.mark(nc.scalar.activation(tmp[:], yf[:], ACT.Square), "ysq")
                            elif kind == "read3":
                                dv.wait(act, t, i, "var")
                                ac.mark(nc.scalar.activation(tmp[:], tmp[:], ACT.Sqrt), "yroot")
                            elif kind == "vtok0":
                                pt.wait(act, t, i, "vup")
                                ac.mark(nc.scalar.copy(vtok[:].rearrange("p c t -> p (c t)"), b[7][:]), "vtok")
                    loop(act, body)

                @block.tensor
                def _(pe):
                    pt.start(pe)

                    def each(out, lhs, rhs):
                        for c in range(NCH):
                            mm = pe.matmul(out[:, c * CH:(c + 1) * CH], lhs(c), rhs(c), start=True, stop=True)
                        return mm

                    def turned(out, src):
                        for c in range(NCH):
                            mm = pe.transpose(out[:, c * CH:(c + 1) * CH], src(c), ident)
                        return mm

                    def cols(buf):
                        return lambda c: buf[:, c * CH:(c + 1) * CH]

                    def body(t):
                        for i, item in enumerate(items):
                            kind, d = item[0], item[1] if len(item) > 1 else None
                            n = "".join(str(x) for x in item[1:])
                            if kind == "g":
                                e, m = item[2:]
                                if e == 0 and m < 2:
                                    ac.wait(pe, t, i, f"rm{d}", f"Wc{1 - d}6{m}")
                                    dv.wait(pe, t, i, f"kt{d}")
                                else:
                                    dv.wait(pe, t, i, f"m{d}0{m}" if e else f"t{1 - d}6{m - 2}")
                                lhs, rhs = ((at2[:, e, :], bt[:]), (kt_[:], at2[:, e, :]), (bt[:], rt2[:, e, :]),
                                            (kt_[:], rt2[:, e, :]))[m]
                                pt.mark(each(b[m], cols(lhs), cols(rhs)), f"g{n}")
                            elif kind == "bup":
                                ac.wait(pe, t, i, f"siga{d}")
                                dv.wait(pe, t, i, f"kt{d}")
                                pt.mark(turned(b[4], cols(bt)), f"bup{d}")
                                pt.mark(turned(b[5], cols(kt_)), f"kup{d}")
                            elif kind == "T":
                                e = item[2]
                                dv.wait(pe, t, i, f"m{d}{e}0", f"m{d}1{e}")
                                pt.mark(turned(b[e], lambda c: AB[:, e, c, :]), f"T{n}")
                            elif kind == "W":
                                lv, e = item[2:]
                                dv.wait(pe, t, i, f"t{d}{lv - 1}{e}", f"m{d}1{2 + e}")
                                pt.mark(each(b[2 * (lv % 2) + e], lambda c: AB[:, e, c, :],
                                             lambda c: MT[:, d, e, c, :]), f"W{n}")
                            elif kind == "Pt":
                                lv, e = item[2:]
                                if lv == 1:
                                    dv.wait(pe, t, i, f"i{d}0{e}")
                                    ac.wait(pe, t, i, f"Wc{n}")
                                else:
                                    ac.wait(pe, t, i, f"Wc{n}", f"Mc{d}{lv - 1}{e}")
                                pt.mark(each(b[2 - 2 * (lv % 2) + e], lambda c: M[:, e, c, :],
                                             lambda c: Wb[:, e, c, :]), f"Pt{n}")
                            elif kind == "Tr":
                                lv, e = item[2:]
                                dv.wait(pe, t, i, f"t{n}")
                                pt.mark(turned(b[2 * (lv % 2) + e], lambda c: MT[:, d, e, c, :]), f"Tr{n}")
                            elif kind == "X":
                                q = item[2]
                                c = ORDER[d][q]
                                if q == 0:
                                    ac.wait(pe, t, i, f"ktok{d}")
                                    pl.wait(pe, t, i, f"keep{d}")
                                dv.wait(pe, t, i, f"t{d}61", "vm", *([f"z{d}{q - 1}"] if q else [f"sa{1 - d}3", "mean"]))
                                if q:
                                    pe.matmul(b[6][:, 0:P], atS[:, d, c * CH:(c + 1) * CH], z[:], start=True,
                                              stop=False)
                                for e in range(2):
                                    mm = pe.matmul(b[6][:, 0:P], AKT[:, d, e, c, :], vtok2[:, e, c, :],
                                                   start=(q == 0 and e == 0), stop=(e == 1))
                                pt.mark(mm, f"X{n}")
                            elif kind == "SA":
                                q = item[2]
                                c = ORDER[d][q]
                                dv.wait(pe, t, i, f"x{n}")
                                for e in range(2):
                                    mm = pe.matmul(b[6][:, P:2 * P], MT[:, d, e, c, :], xs2[:, e, :],
                                                   start=(e == 0), stop=(e == 1))
                                pt.mark(mm, f"SA{n}")
                                dv.wait(pe, t, i, f"y{d}{q - 1}" if q else ("y03" if d else "y13"), "var", "bon")
                                ac.wait(pe, t, i, "vtok")
                                if q:
                                    pe.matmul(b[7][:, 0:P], z[:], rtS[:, d, c * CH:(c + 1) * CH], start=True,
                                              stop=False)
                                for e in range(2):
                                    pe.matmul(b[7][:, 0:P], vtok2[:, e, c, :], RKT[:, d, e, c, :],
                                              start=(q == 0 and e == 0), stop=False)
                            elif kind == "U":
                                c = ORDER[d][item[2]]
                                dv.wait(pe, t, i, f"sa{n}")
                                pe.matmul(b[6][:, 2 * P:3 * P], ktok[:, d, c, :], vtok[:, c, :], start=True, stop=False)
                                pt.mark(pe.matmul(b[6][:, 2 * P:3 * P], btok[:, d, c, :], sas[:], start=False,
                                                  stop=True), f"U{n}")
                            elif kind == "Y":
                                c = ORDER[d][item[2]]
                                dv.wait(pe, t, i, f"sb{n}")
                                for e in range(2):
                                    mm = pe.matmul(b[7][:, 0:P], sas2[:, e, :], RBT[:, d, e, c, :], start=False,
                                                   stop=(e == 1))
                                pt.mark(mm, f"Y{n}")
                            elif kind == "lora":
                                pl.wait(pe, t, i, "staged")
                                ac.wait(pe, t, i, f"ktok{1 - d}", *(["norm"] if d == 0 else []))
                                pe.matmul(b[4][:], w2[:, 0, :], lora[:, d, 0, :], start=True, stop=True)
                                pt.mark(pe.matmul(b[5][:], w2[:, 1, :], lora[:, d, 1, :], start=True, stop=True),
                                        f"lora{d}")
                            elif kind == "bonus1":
                                dv.wait(pe, t, i, "rk")
                                ac.wait(pe, t, i, "vtok")
                                pt.mark(pe.matmul(b[7][:], headones, ksum[:], start=True, stop=True), "bonus")
                            elif kind == "kk1":
                                dv.wait(pe, t, i, "kksq")
                                ac.wait(pe, t, i, "btok1")
                                pt.mark(pe.matmul(b[4][:], headones, sq[:], start=True, stop=True), "squp")
                            elif kind == "read0":
                                dv.wait(pe, t, i, "y13")
                                pt.mark(pe.matmul(b[6][:], headones, yf[:], start=True, stop=True), "mean")
                            elif kind == "read2":
                                ac.wait(pe, t, i, "ysq")
                                pt.mark(pe.matmul(b[7][:], headones, tmp[:], start=True, stop=True), "var")
                            elif kind == "vtok0":
                                dv.wait(pe, t, i, "var")
                                pt.mark(turned(b[7], cols(vv)), "vup")
                    loop(pe, body)

                @block.vector
                def _(dve):
                    v = nc.vector
                    dv.start(dve)
                    strict, incl, ab = (0, 2), (1, 3), (2, 0)

                    def mask(j):
                        return tri[:, j:j + 1, :].to_broadcast([P, NCH, P])

                    def level(d, mt_side, lv):
                        u = d if mt_side else 1 - d
                        return lvl[:, u, lv:lv + 1, :].to_broadcast([P, NCH, P])

                    def body(t):
                        def do(i, ins, name, wait=True):
                            dv.mark(ins, name)
                            if wait:
                                dv.wait(dve, t, i, name)
                        for i, item in enumerate(items):
                            kind, d = item[0], item[1] if len(item) > 1 else None
                            n = "".join(str(x) for x in item[1:])
                            if kind == "g":
                                e, m = item[2:]
                                pt.wait(dve, t, i, f"g{n}")
                                dst = (AB[:, e, :, :], AKT[:, d, e, :, :], RBT[:, d, e, :, :], RKT[:, d, e, :, :])[m]
                                mj = (ab, strict, incl, incl)[m][d]
                                if m == 0:
                                    pl.wait(dve, t, i, f"eyeM{1 - d}")
                                do(i, v.tensor_tensor(dst, chunks(b[m][:]), mask(mj), ALU.mult), f"m{n}", False)
                                if m == 0:
                                    dv.wait(dve, t, i, f"m{n}", apart=True)
                                    do(i, v.copy_predicated(M[:, e, :, :], level(d, False, 0), AB[:, e, :, :]),
                                       f"i{d}0{e}", False)
                            elif kind == "T":
                                e = item[2]
                                pl.wait(dve, t, i, f"eyeT{d}")
                                pt.wait(dve, t, i, f"T{n}", apart=True)
                                do(i, v.copy_predicated(MT[:, d, e, :, :], level(d, True, 0), chunks(b[e][:])),
                                   f"t{d}0{e}", False)
                            elif kind == "Pt":
                                lv, e = item[2:]
                                pt.wait(dve, t, i, f"Pt{n}", apart=True)
                                do(i, v.copy_predicated(MT[:, d, e, :, :], level(d, True, lv),
                                                        chunks(b[2 - 2 * (lv % 2) + e][:])), f"t{n}", False)
                            elif kind == "X":
                                q = item[2]
                                if q in (1, 2):
                                    dv.wait(dve, t, i, f"z{d}{q - 1}")
                                    do(i, v.tensor_scalar(ze[:], z[:], decS[:, d, q:q + 1], None, ALU.mult),
                                       f"ze{n}", False)
                                pt.wait(dve, t, i, f"X{n}")
                                do(i, v.tensor_copy(diagonal(xs2), b[6][:, 0:P].rearrange("p (e v) -> p e v", e=2)),
                                   f"x{n}", False)
                            elif kind == "SA":
                                pt.wait(dve, t, i, f"SA{n}")
                                do(i, v.tensor_copy(sas[:], b[6][:, P:2 * P]), f"sa{n}")
                                do(i, v.tensor_copy(diagonal(sas2), sas[:].rearrange("p (e v) -> p e v", e=2)),
                                   f"sb{n}", False)
                            elif kind == "U":
                                q = item[2]
                                pt.wait(dve, t, i, f"U{n}")
                                pl.wait(dve, t, i, f"keep{d}")
                                if q == 0:
                                    v.tensor_scalar(z[HALVES[0], HALVES[0]], b[6][HALVES[0], 2 * P:2 * P + 64],
                                                    decS[HALVES[0], d, 0:1], None, ALU.mult)
                                    ins = v.tensor_scalar(z[HALVES[1], HALVES[1]], b[6][HALVES[1], 2 * P + 64:3 * P],
                                                          decS[HALVES[1], d, 0:1], None, ALU.mult)
                                else:
                                    dv.wait(dve, t, i, f"ze{n}")
                                    v.scalar_tensor_tensor(
                                        z[HALVES[0], HALVES[0]], b[6][HALVES[0], 2 * P:2 * P + 64],
                                        decS[HALVES[0], d, q:q + 1], ze[HALVES[0], HALVES[0]], ALU.mult, ALU.add)
                                    ins = v.scalar_tensor_tensor(
                                        z[HALVES[1], HALVES[1]], b[6][HALVES[1], 2 * P + 64:3 * P],
                                        decS[HALVES[1], d, q:q + 1], ze[HALVES[1], HALVES[1]], ALU.mult, ALU.add)
                                do(i, ins, f"z{n}", False)
                            elif kind == "Y":
                                c = ORDER[d][item[2]]
                                dst = yf[:, c * CH:(c + 1) * CH]
                                pt.wait(dve, t, i, f"Y{n}")
                                if d == 0:
                                    do(i, v.tensor_copy(dst, b[7][:, 0:P]), f"y{n}", False)
                                else:
                                    do(i, v.tensor_tensor(dst, b[7][:, 0:P], dst, ALU.add), f"y{n}", False)
                            elif kind == "el":
                                name = item[2]
                                key = name + str(d)
                                if name == "lw":
                                    ac.wait(dve, t, i, f"sigw{d}")
                                    do(i, v.tensor_scalar(lw[:], lw[:], HALF_E, None, ALU.mult), key)
                                elif name == "cum":
                                    ac.wait(dve, t, i, f"en{1 - d}")
                                    do(i, v.tensor_tensor_scan(mid[:], starts[:], lw[:], 0.0, ALU.mult, ALU.add), key)
                                elif name == "half":
                                    do(i, v.tensor_scalar(hs_[:], chunks(mid[:])[:, :, CH - 1], 0.5, None, ALU.mult),
                                       key)
                                elif name == "mid":
                                    do(i, v.tensor_tensor(chunks(mid[:]), chunks(mid[:]), hs_[:].unsqueeze(
                                        2).to_broadcast([P, NCH, CH]), ALU.subtract), key)
                                elif name == "dif":
                                    do(i, v.tensor_tensor(dif[:], mid[:], lw[:], ALU.subtract), key, False)
                                elif name == "blend":
                                    ac.wait(dve, t, i, f"siga{d}")
                                    do(i, v.tensor_scalar(kd[:], av[:], rp[:, KA:KA + 1], omka[:, 0:1], ALU.mult,
                                                          ALU.add), key)
                                elif name == "kd":
                                    do(i, v.tensor_tensor(kd[:], kx, kd[:], ALU.mult), key)
                                elif name == "b":
                                    do(i, v.tensor_tensor(bb[:], kk[:], av[:], ALU.mult), key, False)
                                elif d == 0:
                                    do(i, v.tensor_copy(ksum[:], kd[:]), key, False)
                                else:
                                    do(i, v.tensor_tensor(ksum[:], ksum[:], kd[:], ALU.add), key, False)
                            elif kind == "fin":
                                name = item[2]
                                pt.wait(dve, t, i, f"g{1 - d}03", f"g{1 - d}13", f"kup{1 - d}")
                                pl.wait(dve, t, i, f"keep{1 - d}")
                                if name == "at":
                                    ac.wait(dve, t, i, f"en{d}")
                                    dv.wait(dve, t, i, f"b{d}")
                                    do(i, v.scalar_tensor_tensor(at[:], kk[:], -1.0, ee[:], ALU.mult, ALU.mult),
                                       f"at{d}", False)
                                    continue
                                if name == "rt":
                                    ac.wait(dve, t, i, "rstaged")
                                dst, x, y = {"rt": (rt[:], rr, ei[:]), "bt": (bt[:], bb[:], en[:]),
                                             "kt": (kt_[:], kd[:], en[:])}[name]
                                do(i, v.tensor_tensor(dst, x, y, ALU.mult), f"{name}{d}", False)
                                if name != "kt":
                                    continue
                                for q in range(3):
                                    c0, c1 = ORDER[d][q:q + 2]
                                    ins = v.tensor_tensor(dec[:, q:q + 1], eh[:, c0:c0 + 1], eh[:, c1:c1 + 1],
                                                          ALU.mult)
                                do(i, ins, f"E{d}", False)
                            elif kind == "bonus0":
                                dv.wait(dve, t, i, "ksum1")
                                do(i, v.scalar_tensor_tensor(ksum[:], rr, rp[:, RK_:RK_ + 1], ksum[:], ALU.mult,
                                                             ALU.mult), "rk", False)
                            elif kind == "bonus2":
                                pt.wait(dve, t, i, "bonus")
                                do(i, v.tensor_tensor(bonv[:], b[7][:], vv, ALU.mult), "bon", False)
                            elif kind == "kk0":
                                pl.wait(dve, t, i, "staged")
                                ac.wait(dve, t, i, "kstaged")
                                do(i, v.tensor_scalar(omka[:], rp[:, KA:KA + 1], -1.0, 1.0, ALU.mult, ALU.add),
                                   "omka", False)
                                do(i, v.tensor_scalar(kk[:], kx, rp[:, KK_:KK_ + 1], None, ALU.mult), "kkraw")
                                do(i, v.tensor_tensor(sq[:], kk[:], kk[:], ALU.mult), "kksq", False)
                            elif kind == "kkrec":
                                piece = slice(item[1] * CH, (item[1] + 1) * CH)
                                if item[1] == 0:
                                    ac.wait(dve, t, i, "norm")
                                    do(i, v.tensor_scalar(sq[:], sq[:], 1e-12, None, ALU.max), "kkmax")
                                do(i, v.reciprocal(sq[:, piece], sq[:, piece]), f"kkrec{n}", False)
                            elif kind == "kk2":
                                dv.wait(dve, t, i, "kkrec3")
                                do(i, v.tensor_tensor(kk[:], kk[:], sq[:], ALU.mult), "kk")
                            elif kind == "read1":
                                pt.wait(dve, t, i, "mean")
                                do(i, v.tensor_scalar(tmp[:], b[6][:], 1.0 / 64, None, ALU.mult), "mean")
                                do(i, v.tensor_tensor(yf[:], yf[:], tmp[:], ALU.subtract), "xc")
                            elif kind == "read3":
                                pt.wait(dve, t, i, "var")
                                do(i, v.tensor_scalar(tmp[:], b[7][:], 1.0 / 64, GN_EPS, ALU.mult, ALU.add), "var",
                                   False)
                            elif kind == "yrec":
                                piece = slice(item[1] * CH, (item[1] + 1) * CH)
                                if item[1] == 0:
                                    ac.wait(dve, t, i, "yroot")
                                do(i, v.reciprocal(tmp[:, piece], tmp[:, piece]), f"yrec{n}", False)
                            elif kind == "read4":
                                dv.wait(dve, t, i, "yrec3")
                                do(i, v.tensor_tensor(yf[:], yf[:], tmp[:], ALU.mult), "yn")
                                g, bi = ((k.par[:, bass.ds(t * 9 + (PAR["rw"] + j - 9), 1)] for j in (LG, LB))
                                         if turns else (row(k, "rw", 9 * (KT - 1) + j) for j in (LG, LB)))
                                do(i, v.tensor_scalar(yf[:], yf[:], g, bi, ALU.mult, ALU.add), "ynl")
                            elif kind == "read5":
                                do(i, v.tensor_tensor(yf[:], yf[:], bonv[:], ALU.add), "ysum")
                                dst = o[:, bass.ds(t, 1), :] if turns else o[:, KT:KT + 1, :]
                                do(i, v.tensor_tensor(dst, yf[:].unsqueeze(1), sg[:].unsqueeze(1), ALU.mult), "o",
                                   False)
                            elif kind == "vtok1":
                                ac.wait(dve, t, i, "vtok")
                                f = vtok2.rearrange("p e c f -> p e c f")
                                v.tensor_copy(f[:, 0, :, 0:64], vtok[:, :, 0:64])
                                do(i, v.tensor_copy(f[:, 1, :, 64:P], vtok[:, :, 64:P]), "vm", False)
                    loop(dve, body)

        run([("stage",), ("stage2",)] + KKNORM + prep_items(0), 0, "first")
        run(section(0) + section(1), KT, "loop")
        run(serial_items(1) + READOUT, 0, "last")


def stage_rwkv_out(nc, k, o):
    first = FIRST["rwout"]
    with ExitStack() as ctx:
        block = ctx.enter_context(nc.Block())

        @block.sync
        def _(sp):
            for n in range(first, first + RING):
                sp.dma_start(k.ring[:, n % RING, :], k.stream[n]).then_inc(k.slot_landed[n % RING], 16)
            load_ahead(k, sp, first, 2)

        @block.tensor
        def _(pe):
            rhs = [o[:, 1 + kt, :] for kt in range(KT)]
            for j in range(2):
                slot_products(k, pe, first + j, 0, rhs, [k.psum[4 * j + i][:] for i in range(4)]).then_inc(
                    k.slot_used, 1)

        @block.vector
        def _(dve):
            for m in range(KT):
                dve.wait_ge(k.slot_used, first + m // 4 + 1)
                for dst, cols, c in ((k.ctx, slice(0, T), True), (k.x, slice(T, 2 * T), False)):
                    nc.vector.scalar_tensor_tensor(dst[:, m, :], k.psum[m][:, cols],
                                                   mod2(k, 0, GT, c)[:, m:m + 1], dst[:, m, :], ALU.mult, ALU.add)


def second_block(nc, k, a):
    stage_mod_bias(nc, k, [k.mod[:, 0:48], k.mod[:, 48:96]], row(k, "modb0", 0, 48))
    stage_scales(nc, k, [(k.gain[:, 8 * i:8 * i + 8], mod2(k, i // 2, SC, i % 2 == 1),
                          row(k, f"norm2_{i // 2}", 0, 8)) for i in range(4)])
    kept = nc.dram_tensor("rwkv_projections", (KT + 1, P, 4, 512), F32).ap()
    with ExitStack() as lay:
        lora = lay.enter_context(nc.sbuf_tensor("lora", [P, 2, 2, 512], F32))
        with ExitStack() as inner:
            h = inner.enter_context(nc.sbuf_tensor("h_both", [P, KT, 512], F32))
            stage_norms(nc, k, [(k.ctx[:], k.gain[:, 8:16], mod2(k, 0, SH, True), h[:, :, 0:T]),
                                (k.x[:], k.gain[:, 0:8], mod2(k, 0, SH), h[:, :, T:2 * T])], KT, T, "rwkv")
            xx = inner.enter_context(nc.sbuf_tensor("shifted", [P, KT, 512], F32))
            w1 = inner.enter_context(nc.sbuf_tensor("lora_in_sb", [P, KT, 256], F32))
            stage_shift(nc, k, a, h, xx, w1)
            stage_rwkv_in(nc, k, h, xx, w1, lora, kept)
        o = lay.enter_context(nc.sbuf_tensor("rwkv_o", [P, KT + 1, 512], F32))
        stage_rwkv_scan(nc, k, a, lora, kept, o)
        stage_rwkv_out(nc, k, o)
    stage_mla(nc, k, a)
    stage_norm(nc, k, k.x[:], KT, T, row(k, "final2", 0, 8), None, k.x, "final2")


def stage_mla_in(nc, k, a, h, rope, qc, kvc, kpe, gate):
    first = FIRST["mlain"]
    X = slice(T, 2 * T)
    with ExitStack() as ctx:
        turned = ctx.enter_context(nc.sbuf_tensor("kpe_turned", [P, T], F32))
        act_evac = ctx.enter_context(nc.semaphore("mlain_act_evac"))
        step = ctx.enter_context(nc.semaphore("mlain_step"))
        b = k.psum
        block = ctx.enter_context(nc.Block())

        @block.sync
        def _(sp):
            load_ahead(k, sp, first, 4)

        @block.tensor
        def _(pe):
            both, x_only = [h[:, kt, :] for kt in range(KT)], [h[:, kt, X] for kt in range(KT)]

            def tile(n, i, out, rhs):
                for kt in range(KT):
                    mm = pe.matmul(out, ring_tile(k, n, kt, i * P), rhs[kt], start=(kt == 0), stop=(kt == KT - 1))
                return mm
            wait_slot(k, pe, first)
            for i in range(3):
                tile(first, i, b[i // 2][:, (i % 2) * T:(i % 2 + 1) * T], x_only)
            tile(first, 3, b[2][:], both).then_inc(k.slot_used, 1)
            wait_slot(k, pe, first + 1)
            for i in range(3):
                mm = tile(first + 1, i, b[3 + i][:], both)
            mm.then_inc(k.slot_used, 1)
            for j in range(2):
                wait_slot(k, pe, first + 2 + j)
                if j == 1:
                    pe.wait_ge(act_evac, 2)
                for i in range(4):
                    mm = tile(first + 2 + j, i, b[(6, 0)[j] + i // 2][:, (i % 2) * T:(i % 2 + 1) * T], x_only)
                mm.then_inc(k.slot_used, 1)

        @block.scalar
        def _(act):
            act.wait_ge(k.slot_used, first + 1)
            nc.scalar.copy(qc[:, 0:2, :].rearrange("p i t -> p (i t)"), b[0][:]).then_inc(act_evac, 1)
            nc.scalar.copy(qc[:, 2, :], b[1][:, 0:T]).then_inc(act_evac, 1)
            act.wait_ge(k.slot_used, first + 2)
            for i in range(2):
                nc.scalar.copy(kvc[:, i, :], b[3 + i][:])
            for j in range(2):
                act.wait_ge(k.slot_used, first + 3 + j)
                for i in range(2):
                    nc.scalar.activation(gate[:, 4 * j + 2 * i:4 * j + 2 * i + 2, :].rearrange("p i t -> p (i t)"),
                                         b[(6, 0)[j] + i][:], ACT.Silu)

        @block.vector
        def _(dve):
            s = Steps(dve, step)
            dve.wait_ge(k.slot_used, first + 2)
            nc.vector.tensor_copy(kpe[:, 0:T], b[2][:, 0:T])
            nc.vector.tensor_tensor(kpe[:, X], b[2][:, X], rope[:, 0, :], ALU.mult)
            s(nc.vector.tensor_tensor(turned[:], b[5][:, X], rope[:, 1, :], ALU.mult))
            nc.vector.tensor_tensor(kpe[:, X], kpe[:, X], turned[:], ALU.add)


def stage_mla_up(nc, k, rope, qc, kvc, kn, v, qn, qp):
    first = FIRST["mlab"]
    with ExitStack() as ctx:
        turned = ctx.enter_context(nc.sbuf_tensor("qp_turned", [P, 4, T], F32))
        act_evac = ctx.enter_context(nc.semaphore("mlaup_act"))
        dve_evac = ctx.enter_context(nc.semaphore("mlaup_dve"))
        done = ctx.enter_context(nc.semaphore("mlaup_pe"))
        b = k.psum
        block = ctx.enter_context(nc.Block())

        @block.sync
        def _(sp):
            load_ahead(k, sp, first, 3)

        @block.tensor
        def _(pe):
            w = k.ring[:, first % RING, :]
            wait_slot(k, pe, first)
            for m in range(8):
                for kt in range(2):
                    mm = pe.matmul(b[m][:], w[:, kt * D + m * P:kt * D + (m + 1) * P], kvc[:, kt, :],
                                   start=(kt == 0), stop=(kt == 1))
                mm.then_inc(done, 1)
            for c in range(4):
                for n in range(2):
                    pe.wait_ge(act_evac, 2 * c + n + 1)
                    for kt in range(2):
                        mm = pe.matmul(b[2 * c + n][:], kvc[:, kt, c * P:(c + 1) * P],
                                       w[:, 2 * D + kt * D + n * 512:2 * D + kt * D + (n + 1) * 512],
                                       start=(kt == 0), stop=(kt == 1))
                    mm.then_inc(done, 1)
            for sl, (lo, tiles, banks) in enumerate((((0, D), 8, range(0, 4)), ((0, 512), 8, range(4, 8)))):
                wait_slot(k, pe, first + 1 + sl)
                w = k.ring[:, (first + 1 + sl) % RING, :]
                for m in range(tiles):
                    bk = banks[m // 2]
                    if m % 2 == 0:
                        pe.wait_ge(dve_evac, bk + 1)
                    for kt in range(3):
                        if sl == 0:
                            at = kt * D + m * P
                        else:
                            at = (m // 4) * 1536 + kt * 512 + (m % 4) * P
                        mm = pe.matmul(b[bk][:, (m % 2) * T:(m % 2 + 1) * T], w[:, at:at + P], qc[:, kt, :],
                                       start=(kt == 0), stop=(kt == 2))
                if sl == 0:
                    mm.then_inc(k.slot_used, 2)
                else:
                    mm.then_inc(k.slot_used, 1)

        @block.scalar
        def _(act):
            for m in range(8):
                act.wait_ge(done, m + 1)
                nc.scalar.copy(kn[:, m, :], b[m][:]).then_inc(act_evac, 1)
            act.wait_ge(k.slot_used, first + 2)
            for i in range(4):
                nc.scalar.copy(qn[:, 2 * i:2 * i + 2, :].rearrange("p i t -> p (i t)"), b[i][:])

        @block.vector
        def _(dve):
            for c in range(4):
                for n in range(2):
                    dve.wait_ge(done, 8 + 2 * c + n + 1)
                    nc.vector.tensor_copy(v[:, c, n * 512:(n + 1) * 512], b[2 * c + n][:]).then_inc(dve_evac, 1)
            dve.wait_ge(k.slot_used, first + 3)
            cos, sin = (rope[:, i:i + 1, :].to_broadcast([P, 2, T]) for i in range(2))
            for i in range(2):
                nc.vector.tensor_tensor(qp[:, 2 * i:2 * i + 2, :], b[4 + i][:].rearrange("p (i t) -> p i t", i=2),
                                        cos, ALU.mult)
                nc.vector.tensor_tensor(turned[:, 2 * i:2 * i + 2, :], b[6 + i][:].rearrange(
                    "p (i t) -> p i t", i=2), sin, ALU.mult).then_inc(dve_evac, 1)
            dve.wait_ge(dve_evac, 10)
            nc.vector.tensor_tensor(qp[:], qp[:], turned[:], ALU.add)


def stage_mla_attention(nc, k, half, kn, v, qn, qp, kpe, gate):
    SCALE = 1.0 / math.sqrt(96.0)
    NK = 2 * T
    with ExitStack() as ctx:
        def sb(name, shape):
            return ctx.enter_context(nc.sbuf_tensor("mla_" + name, shape, F32))

        def sem(name):
            return ctx.enter_context(nc.semaphore("mla_" + name))
        U = 16
        TURNS = 2
        qm = sb("q", [P, 8, 2, T])
        kst, vst = sb("k", [P, 2, 2, NK]), sb("v", [P, 2, 4, 2 * P])
        prob = sb("prob", [P, 4, NK])
        stat = sb("stat", [P, U, 3])
        diag = sb("diag", [P, 4, P])
        ptok = sb("ptok", [P, 2, NK])
        staged, q_up, scored, maxed, exped, normed = (sem(n) for n in ("staged", "q_up", "scored", "maxed", "exped",
                                                                        "normed"))
        turned, p_down, o_up, o_down, step = (sem(n) for n in ("turned", "p_down", "o_up", "o_down", "step"))
        TURNED0, P_DOWN0, EXPED0, O_UP0, O_DOWN0 = 4, 2, 4, U, 2
        ident = const(k, "ident")
        block = ctx.enter_context(nc.Block())

        @block.gpsimd
        def _(pool):
            with pool.Fori(0, TURNS) as t:
                for f in range(2):
                    pool.wait_ge(o_up, t * U + (8 * f + 8))
                    pool.nop(nofuse=True)
                    nc.gpsimd.tensor_copy(kst[:, f, :, :], kn[:, bass.ds(t * 4 + 2 * f, 2), :]).then_inc(staged, 1)
                    nc.gpsimd.tensor_copy(vst[:, f, :, :], v[:, :, bass.ds(t * (4 * P) + 2 * f * P, 2 * P)]).then_inc(
                        staged, 1)

        @block.scalar
        def _(act):
            act.sem_inc(p_down, P_DOWN0)
            act.sem_inc(exped, EXPED0)
            with act.Fori(0, TURNS) as t:
                def queries(heads):
                    for hh in heads:
                        nc.scalar.activation(qm[:, hh, 0:1, :], qn[:, bass.ds(t * 4 + hh // 2, 1), :], ACT.Copy,
                                             scale=half[:, hh % 2:hh % 2 + 1])
                        nc.scalar.activation(qm[:, hh, 1:2, :], qp[:, bass.ds(t * 2 + hh // 4, 1), :], ACT.Copy,
                                             scale=half[:, 2 + hh % 4:3 + hh % 4]).then_inc(q_up, 1)
                queries(range(2))
                for u in range(U + 2):
                    if u < U:
                        act.wait_ge(maxed, t * U + (u + 1))
                        act.wait_ge(turned, t * U + (u - 3 + TURNED0))
                        nc.scalar.activation(prob[:, u % 4, :], k.psum[u % 4][:], ACT.Exp, scale=SCALE,
                                             bias=stat[:, u, 0:1], accum_out=stat[:, u, 1:2]).then_inc(exped, 1)
                    if u % 2 == 0 and u // 2 + 2 < 8:
                        queries([u // 2 + 2])
                    if u >= 2:
                        act.wait_ge(turned, t * U + (u - 1 + TURNED0))
                        nc.scalar.copy(ptok[:, u % 2, :], k.psum[4 + u % 2][:]).then_inc(p_down, 1)

        @block.tensor
        def _(pe):
            pe.sem_inc(turned, TURNED0)
            pe.sem_inc(o_up, O_UP0)
            with pe.Fori(0, TURNS) as t:
                def turn(u):
                    pe.wait_ge(normed, t * U + (u + 1))
                    pe.wait_ge(p_down, t * U + (u - 1 + P_DOWN0))
                    for c in range(4):
                        mm = pe.matmul(k.psum[4 + u % 2][:, c * P:(c + 1) * P], prob[:, u % 4, c * P:(c + 1) * P],
                                       diag[:, u % 4, :], start=True, stop=True)
                    mm.then_inc(turned, 1)

                def values(u):
                    hh, e, qb = u // 2, (u // 2) % 2, u % 2
                    pe.wait_ge(p_down, t * U + (u + 1 + P_DOWN0))
                    if u % 4 == 0:
                        pe.wait_ge(o_down, t * 4 + (u // 4 - 1 + O_DOWN0))
                    for c in range(4):
                        mm = pe.matmul(k.psum[6 + hh // 2 % 2][e * 64:(e + 1) * 64, qb * P:(qb + 1) * P],
                                       vst[:, hh // 4, c, (hh % 4) * 64:(hh % 4 + 1) * 64],
                                       ptok[:, u % 2, c * P:(c + 1) * P], start=(c == 0), stop=(c == 3))
                    mm.then_inc(o_up, 1)
                for u in range(U + 3):
                    if u < U:
                        hh, qb = u // 2, u % 2
                        if u % 8 == 0:
                            pe.wait_ge(staged, t * 4 + (u // 4 + 2))
                        pe.wait_ge(q_up, t * 8 + (hh + 1))
                        pe.wait_ge(exped, t * U + (u - 3 + EXPED0))
                        pe.matmul(k.psum[u % 4][:], qm[:, hh, 0, qb * P:(qb + 1) * P], kst[:, hh // 4, hh // 2 % 2, :],
                                  start=True, stop=False)
                        pe.matmul(k.psum[u % 4][:], qm[:, hh, 1, qb * P:(qb + 1) * P], kpe[:], start=False,
                                  stop=True).then_inc(scored, 1)
                    if u >= 2 and u - 2 < U:
                        turn(u - 2)
                    if u >= 3:
                        values(u - 3)

        @block.vector
        def _(dve):
            dve.sem_inc(o_down, O_DOWN0)
            with dve.Fori(0, TURNS) as t:
                s = Steps(dve, step, t * (2 * U))

                def output(i):
                    dve.wait_ge(o_up, t * U + (4 * (i + 1) + O_UP0))
                    g = gate[:, bass.ds(t * 4 + i, 1), :]
                    nc.vector.tensor_tensor(g, k.psum[6 + i % 2][:, 0:T].unsqueeze(1), g, ALU.mult).then_inc(
                        o_down, 1)

                def norm(u):
                    dve.wait_ge(exped, t * U + (u + 1 + EXPED0))
                    s(nc.vector.reciprocal(stat[:, u, 2:3], stat[:, u, 1:2]))
                    dve.wait_ge(turned, t * U + (u - 3 + TURNED0))
                    nc.vector.tensor_scalar(diag[:, u % 4, :], ident, stat[:, u, 2:3], None,
                                            ALU.mult).then_inc(normed, 1)
                for u in range(U + 1):
                    if u < U:
                        dve.wait_ge(scored, t * U + (u + 1))
                        s(nc.vector.tensor_reduce(stat[:, u, 2:3], k.psum[u % 4][:], AX, ALU.max))
                        nc.vector.tensor_scalar(stat[:, u, 0:1], stat[:, u, 2:3], -SCALE, None,
                                                ALU.mult).then_inc(maxed, 1)
                    if u >= 1:
                        norm(u - 1)
                    if u >= 7 and u % 4 == 3:
                        output(u // 4 - 1)
                output(3)


def stage_mla(nc, k, a):
    with ExitStack() as lay:
        def sb(name, shape):
            return lay.enter_context(nc.sbuf_tensor("mla_" + name, shape, F32))
        rope, half = sb("rope", [P, 2, T]), sb("half", [P, 6])
        qc, kvc, kpe, gate = sb("qc", [P, 3, T]), sb("kvc", [P, 2, 512]), sb("kpe", [P, 512]), sb("gate", [P, KT, T])
        with nc.semaphore("mla_consts") as landed, nc.Block() as block:
            @block.sync
            def _(sp):
                sp.dma_start(rope[:], a["rope"].rearrange("p (i t) -> p i t", i=2)).then_inc(landed, 16)
                sp.dma_start(half[:], a["half_masks"]).then_inc(landed, 16)
                sp.wait_ge(landed, 32)
        with ExitStack() as inner:
            h = inner.enter_context(nc.sbuf_tensor("mla_h", [P, KT, 512], F32))
            stage_norms(nc, k, [(k.ctx[:], k.gain[:, 24:32], mod2(k, 1, SH, True), h[:, :, 0:T]),
                                (k.x[:], k.gain[:, 16:24], mod2(k, 1, SH), h[:, :, T:2 * T])], KT, T, "mla")
            stage_mla_in(nc, k, a, h, rope, qc, kvc, kpe, gate)
        stage_norm(nc, k, qc[:], 3, T, row(k, "qg", 0, 3), None, qc, "mlaq")
        stage_norm(nc, k, kvc[:], 2, 512, row(k, "kvg", 0, 2), None, kvc, "mlakv")
        kn, v, qn, qp = sb("kn", [P, KT, 512]), sb("vt", [P, 4, D]), sb("qn", [P, KT, T]), sb("qp", [P, 4, T])
        stage_mla_up(nc, k, rope, qc, kvc, kn, v, qn, qp)
        stage_mla_attention(nc, k, half, kn, v, qn, qp, kpe, gate)
        stage_out(nc, k, FIRST["mlaout"], [gate[:, i, :] for i in range(KT)], mod2(k, 1, GT))


def build(nc, a, out):
    with ExitStack() as top:
        k = Core()
        k.stream = a["stream"]
        k.ring = top.enter_context(nc.sbuf_tensor("ring", [P, RING, SLOT], F32))
        k.par = top.enter_context(nc.sbuf_tensor("par", [P, NPAR], F32))
        k.con = top.enter_context(nc.sbuf_tensor("con", [P, NCON], F32))
        k.cs = top.enter_context(nc.sbuf_tensor("cs", [P, 24], F32))
        k.x = top.enter_context(nc.sbuf_tensor("x", [P, KT, T], F32))
        k.ctx = top.enter_context(nc.sbuf_tensor("ctx", [P, KT, T], F32))
        k.mod = top.enter_context(nc.sbuf_tensor("mod", [P, 96], F32))
        k.next_mod = top.enter_context(nc.sbuf_tensor("next_mod", [P, 2, 48], F32))
        k.gain = top.enter_context(nc.sbuf_tensor("gain", [P, 32], F32))
        k.psum = [top.enter_context(nc.psum_tensor(f"bank{b}", [P, 512], F32)) for b in range(8)]
        k.slot_landed = [top.enter_context(nc.semaphore(f"slot_landed{s}")) for s in range(RING)]
        k.slot_used = top.enter_context(nc.semaphore("slot_used"))
        k.x_landed = top.enter_context(nc.semaphore("x_landed"))
        k.w1_landed = top.enter_context(nc.semaphore("lora_in_landed"))
        k.by_pool = {n: top.enter_context(nc.semaphore(n)) for n in (
            "hyin_mod_landed", "ffn0_even_landed", "ffn0_odd_landed", "ffn1_even_landed", "ffn1_odd_landed",
            "proj_even_kept", "proj_odd_kept", "proj_spare_kept")}
        k.first_stage_sem = max(m.num for m in k.by_pool.values()) + 1

        stage_setup(nc, k, a)
        first_block(nc, k, a)
        stage_clear(nc, k)
        second_block(nc, k, a)
        stage_store(nc, k, out)


def stage_clear(nc, k):
    with nc.Block() as block:
        @block.sync
        def _(sp):
            sp.sem_clear(range(k.first_stage_sem, 256))


def stage_store(nc, k, out):
    with nc.semaphore("out_stored") as stored, nc.Block() as block:
        @block.sync
        def _(sp):
            sp.dma_start(out, k.x[:]).then_inc(stored, 16)
            sp.wait_ge(stored, 16)


def first_block(nc, k, a):
    with ExitStack() as lay:
        h = lay.enter_context(nc.sbuf_tensor("h", [P, KT, T], F32))
        stage_mod(nc, k, FIRST["mod0"], k.cs[:, 0:8], k.mod[:, 0:16], row(k, "adab0", 0, 16))
        stage_scales(nc, k, [(k.gain[:, 0:8], k.mod[:, 8:16], row(k, "nmix0", 0, 8))])
        stage_norm(nc, k, k.x[:], KT, T, k.gain[:, 0:8], k.mod[:, 0:8], h, "mix0")
        stage_hybrid(nc, k, a, h)
        stage_scales(nc, k, [(k.gain[:, 8:16], k.mod[:, 32:40], row(k, "nffn0", 0, 8))])
        stage_norm(nc, k, k.x[:], KT, T, k.gain[:, 8:16], k.mod[:, 24:32], h, "ffn0")
        stage_ffn(nc, k, h, FIRST["up0"], FIRST["down0"], k.mod[:, 40:48], 0, a["mod_stream"][0], [k.cs[:, 0:8]])
        stage_mod_bias(nc, k, [k.mod[:, 48:96]], row(k, "adab1", 0, 48))
        stage_scales(nc, k, [(k.gain[:, 0:8], k.mod[:, 56:64], row(k, "nmix1", 0, 8)),
                             (k.gain[:, 8:16], k.mod[:, 80:88], row(k, "nffn1", 0, 8))])
        stage_norm(nc, k, k.x[:], KT, T, k.gain[:, 0:8], k.mod[:, 48:56], h, "mix1")
        stage_conformer(nc, k, a, h)
        stage_norm(nc, k, k.x[:], KT, T, k.gain[:, 8:16], k.mod[:, 72:80], h, "ffn1")
        stage_ffn(nc, k, h, FIRST["up1"], FIRST["down1"], k.mod[:, 88:96], 1, a["mod_stream"][1],
                  [k.cs[:, 8:16], k.cs[:, 16:24]])
        stage_norm(nc, k, k.x[:], KT, T, row(k, "final1", 0, 8), None, k.x, "final1")


def stage_hybrid(nc, k, a, h):
    with ExitStack() as lay:
        y = lay.enter_context(nc.sbuf_tensor("y", [P, NY, T], F32))
        dtok = lay.enter_context(nc.sbuf_tensor("dtok", [P, 2 * HEADS], F32))
        stage_hyin(nc, k, h, y, a, dtok)
        stage_mod_rest(nc, k)
        with ExitStack() as inner:
            hd = inner.enter_context(nc.sbuf_tensor("headvals", [P, 8, 2 * HEADS], F32))
            stage_dt(nc, k, a, dtok, hd)
            stage_ssd(nc, k, y, hd)
        stage_ssm_gate(nc, k, y)
        stage_attention(nc, k, a, y)
        rhs = [y[:, ST_XS + i, :] for i in range(16)] + [y[:, ST_Q + i, :] for i in range(8)]
        stage_out(nc, k, FIRST["hyout"], rhs, k.mod[:, 16:24])


def _cols(w):
    return w.reshape(w.shape[0] // P, P, w.shape[1]).transpose(1, 0, 2)


def _slots(w, groups=None):
    kk, n = w.shape
    kslots, nslots = -(-kk // D), -(-n // 512)
    full = np.zeros((kslots * D, nslots * 512), w.dtype)
    full[:kk, :n] = w
    return full.reshape(kslots, KT, P, nslots, 512).transpose(3, 0, 2, 1, 4).reshape(-1, P, SLOT)


def _pairs(a, b, width=256):
    n = a.shape[1] // width
    both = np.stack([a.reshape(D, n, width), b.reshape(D, n, width)], 2)
    return both.reshape(D, 2 * a.shape[1])


def _one_slot(parts):
    flat = np.concatenate([p.reshape(P, -1) for p in parts], 1)
    out = np.zeros((1, P, SLOT), flat.dtype)
    out[0, :, :flat.shape[1]] = flat
    return out


def lay_stream(i):
    s = [_slots(i["ada_w"][0][:, :2 * D]), None, _slots(i["hy_w_out"][0]),
         _slots(_pairs(i["ffn_w_gate"][0], i["ffn_w_up"][0])), _slots(i["ffn_w_down"][0]),
         _slots(_pairs(*np.split(i["cv_w_pw1"][0], 2, 1))), _slots(i["cv_w_pw2"][0]),
         _slots(_pairs(i["ffn_w_gate"][1], i["ffn_w_up"][1])), _slots(i["ffn_w_down"][1])]
    w = i["hy_w_in"][0]
    s[1] = _slots(np.concatenate([w[:, :DI + CONV_DIM], w[:, DI + CONV_DIM + HEADS:]], 1))
    s += [_slots(i["rwkv_w_in_2"][0][j]) for j in range(4)] + [_slots(i["rwkv_w_out_2"][0])]
    w = i["mla_w_in_2"][0]
    qc, kvc, kpe, gate = w[:, :384], w[:, 384:640], w[:, 640:672], w[:, 672:]
    swapped = np.concatenate([kpe[:, 16:], kpe[:, :16]], 1)
    s += [_slots(np.concatenate([qc] + [kpe] * 4, 1)), _slots(np.concatenate([kvc] + [swapped] * 4, 1)),
          _slots(gate)]
    kvb = i["mla_w_kvb_2"][0].reshape(256, 16, 2, 64)
    qb = i["mla_w_qb_2"][0].reshape(384, 16, 96)
    s += [_one_slot([_cols(kvb[:, :, 0].reshape(256, 1024)), _cols(kvb[:, :, 1].reshape(256, 1024))]),
          _one_slot([_cols(qb[:, :, :64].reshape(384, 1024))]),
          _one_slot([_cols(qb[:, :, 64:].reshape(384, 512)),
                     _cols(np.concatenate([qb[:, :, 80:], qb[:, :, 64:80]], 2).reshape(384, 512))]),
          _slots(i["mla_w_out_2"][0])]
    stream = np.concatenate(s, 0)
    assert stream.shape == (NSLOTS, P, SLOT), (stream.shape, NSLOTS)
    return stream


def _rows(*vectors):
    return np.concatenate([v.reshape(-1, P).T for v in vectors], 1)


def lay_par(i):
    conv = np.stack([*i["hy_conv_w"][0], i["hy_conv_b"][0]], 0)
    dw = np.stack([*i["cv_w_dw"][0], i["cv_b_dw"][0]], 0)
    rw = np.stack([i["rwkv_w0_2"][0, 0], i["rwkv_w0_2"][0, 1], i["rwkv_a0_2"][0, 0], i["rwkv_a0_2"][0, 1],
                   i["rwkv_k_k_2"][0], i["rwkv_k_a_2"][0], i["rwkv_r_k_2"][0].reshape(-1),
                   i["rwkv_lnx_g_2"][0], i["rwkv_lnx_b_2"][0]], 0)

    def tilewise(m):
        return m.reshape(m.shape[0], -1, P).transpose(1, 0, 2)
    par = _rows(i["c"], i["c_2"], i["c_ctx_2"], i["ada_b"][0], i["ada_b"][1], i["mod_b_2"][0], i["mod_b_2"][1],
                i["norm_mix_g"][0], i["norm_mix_g"][1], i["norm_ffn_g"][0], i["norm_ffn_g"][1],
                i["final_norm_g"], tilewise(conv), np.repeat(i["hy_d_skip"][0], 64), i["hy_ssm_norm_g"][0],
                i["cv_b_pw1"][0], tilewise(dw), i["cv_ln_g"][0], i["cv_ln_b"][0], i["cv_b_pw2"][0],
                i["norm_g_2"][0], i["norm_g_2"][1], i["rwkv_mu_2"][0], i["final_g_2"], i["mla_q_norm_g_2"][0],
                i["mla_kv_norm_g_2"][0], tilewise(rw), np.zeros((9 * P,), rw.dtype))
    assert par.shape == (P, NPAR), (par.shape, NPAR)
    return par


def t5_bucket(dist):
    n = np.maximum(dist, 1).astype(np.float32)
    large = np.float32(16) + np.log(n / np.float32(16)) / np.float32(math.log(2048 / 16)) * np.float32(16)
    return np.where(dist < 16, dist, np.minimum(large.astype(np.int32), 31))


def constants():
    p, f = np.arange(P)[:, None], np.arange(P)[None, :]
    f32 = np.float32
    out = {}
    out["con"] = np.concatenate([(p == f), np.ones((P, P)), (p // 64 == f // 64), (p <= f),
                                 np.where(f >= p, 0.0, NEG), (p + f == P - 1)], 1).astype(f32)
    dist = 255 - np.arange(384)
    bucket = t5_bucket(np.maximum(dist, 0))
    onehot = ((np.arange(32)[:, None] == bucket[None]) & (dist >= 0)[None]).astype(f32)
    allowed = [(dist >= 0) & (dist <= 128), (dist >= 0) & (dist % 4 == 0), (dist >= 0) & (dist % 16 == 0)]
    negs = np.concatenate([np.where(np.tile(a, (16, 1)), 0.0, NEG) for a in allowed], 0).astype(f32)
    out["bias_onehot"], out["bias_neg"] = onehot, negs
    out["tri_masks"] = np.concatenate([p < f, p <= f, p > f, p >= f], 1).astype(f32)
    levels = []
    for upper in (True, False):
        for lv in range(7):
            i, j = p >> lv, f >> lv
            levels.append((i % 2 == 0) & (j == i + 1) if upper else (j % 2 == 0) & (i == j + 1))
    out["level_masks"] = np.concatenate(levels, 1).astype(np.int32)
    out["chunk_starts"] = np.broadcast_to((np.arange(512) % P != 0), (P, 512)).astype(f32).copy()
    out["half_masks"] = np.concatenate([p < 64, p >= 64] + [p // 32 == q for q in range(4)], 1).astype(f32)
    tok = np.arange(T)
    inv = (1.0 / (f32(10000.0) ** (np.arange(0, 16, 2, dtype=f32) / f32(16)))).astype(f32)
    ang = np.concatenate([(tok // 64).astype(f32)[:, None] * inv, (tok % 64).astype(f32)[:, None] * inv], 1)
    cos, sin = np.cos(ang).T.astype(f32), np.sin(ang).T.astype(f32)
    out["rope"] = np.tile(np.concatenate([np.concatenate([cos, cos]), np.concatenate([-sin, sin])], 1), (4, 1))
    return out


def lay_inputs(i):
    def tokens(x):
        return _cols(np.ascontiguousarray(x.reshape(T, D).T))
    w = i["hy_w_in"][0]
    out = constants()
    out["stream"] = lay_stream(i)
    rest = _slots(i["ada_w"][0][:, 2 * D:])
    out["mod_rest"] = rest.reshape(-1, P, 2, SLOT // 2).transpose(0, 2, 1, 3).reshape(-1, P, SLOT // 2)
    out["mod_stream"] = np.stack([_slots(i["ada_w"][1]), np.concatenate([_slots(m) for m in i["mod_w_2"]], 0)], 0)
    out["par"] = lay_par(i)
    out["xt"], out["ctxt"] = tokens(i["x"]), tokens(i["ctx_2"])
    out["wdt"] = _cols(w[:, DI + CONV_DIM:DI + CONV_DIM + HEADS])
    out["headrow"] = np.concatenate([np.broadcast_to(i["hy_dt_bias"][0], (P, HEADS)),
                                     np.broadcast_to(i["hy_a_log"][0], (P, HEADS))], 1)
    out["rel_table"] = i["rel_table"]
    w1 = np.concatenate([*i["rwkv_w1_2"][0], *i["rwkv_a1_2"][0]], 1)
    out["lora_in"] = _cols(w1)
    out["lora_out"] = np.zeros((P, 2, D + P), w.dtype)
    out["lora_out"][:, :, :D] = np.stack([i["rwkv_w2_2"][0].reshape(P, D), i["rwkv_a2_2"][0].reshape(P, D)], 1)
    return {n: np.ascontiguousarray(v) for n, v in out.items()}


def kernel(**inputs):
    import concourse.bacc as bacc
    from concourse.bass_utils import run_bass_kernel_spmd

    nc = bacc.Bacc("TRN2", target_bir_lowering=False, num_devices=1)
    arrays = lay_inputs({n: np.asarray(v) for n, v in inputs.items()})
    aps = {n: nc.dram_tensor("in_" + n, v.shape, mybir.dt.from_np(v.dtype), kind="ExternalInput").ap()
           for n, v in arrays.items()}
    out = nc.dram_tensor("out_0_dram", (P, KT, T), F32, kind="ExternalOutput").ap()
    build(nc, aps, out)
    r = run_bass_kernel_spmd(nc, [{"in_" + n: v for n, v in arrays.items()}], core_ids=[0])
    got = r.results[0]["out_0_dram"]
    return got.transpose(2, 1, 0).reshape(1, T, D)
```
